# Optimizing a Trainium2 kernel written in Bass

```python
import math
import jax, jax.numpy as jnp
from jax import lax
import numpy as np

D_MODEL = 1024
BATCH = 1
SEQ = 512
DEPTH = 1
DEC_BATCH = 8
DEC_SEQ = 16
PAST_LEN = 512

CHUNK = 64
QBLOCK = 128
DA_HEADS = 4
DA_DV = D_MODEL // 2 // DA_HEADS
DA_DH = DA_DV // 2
DA_QK = DA_HEADS * 2 * DA_DH
DA_WIDTH = DA_HEADS * DA_DV
GDN_HEADS = 4
GDN_DV = D_MODEL // 2 // GDN_HEADS
GDN_DK = GDN_DV
GDN_WIDTH = GDN_HEADS * GDN_DV
GDN_QKV = GDN_HEADS * (2 * GDN_DK + GDN_DV)
CONV_W = 4
IN_COLS = 2 * DA_QK + DA_WIDTH + GDN_QKV + 2 * GDN_HEADS + GDN_WIDTH
MIX_WIDTH = DA_WIDTH + GDN_WIDTH
X_HEADS = 4
X_DH = D_MODEL // X_HEADS
N_MEM = 256
N_GROUPS = 4
E_PER_GROUP = 8
N_EXPERTS = N_GROUPS * E_PER_GROUP
TOP_K = 2
D_EXPERT = 256
NORM_EPS = 1e-6
NEG_INF = -1e30

kernel_name = 'hybrid_diffattn_gdn_hmoe_stream_step'

def rmsnorm(x, g):
    xf = x.astype(jnp.float32)
    y = xf * lax.rsqrt(jnp.mean(xf * xf, axis=-1, keepdims=True) + NORM_EPS)
    return (y * g.astype(jnp.float32)).astype(x.dtype)

def l2norm(x):
    xf = x.astype(jnp.float32)
    return xf * lax.rsqrt(jnp.sum(xf * xf, axis=-1, keepdims=True) + NORM_EPS)

def diff_attn_core(q, k, v, q_pos, k_pos, lam):
    s = jnp.einsum('bqhmd,bkhmd->bhmqk', q, k).astype(jnp.float32) * (DA_DH ** -0.5)
    visible = (q_pos[:, None] // CHUNK) >= (k_pos[None, :] // CHUNK)
    p = jax.nn.softmax(jnp.where(visible, s, NEG_INF), axis=-1)
    a = p[:, :, 0] - lam * p[:, :, 1]
    return jnp.einsum('bhqk,bkhe->bqhe', a.astype(v.dtype), v)

def diff_attn_prompt(q, k, v, lam):
    B, T = q.shape[0], q.shape[1]
    nb = T // QBLOCK
    qb = jnp.moveaxis(q.reshape((B, nb, QBLOCK) + q.shape[2:]), 1, 0)
    k_pos = jnp.arange(T)

    def one_block(args):
        q_blk, start = args
        return diff_attn_core(q_blk, k, v, start + jnp.arange(QBLOCK), k_pos, lam)

    o = lax.map(one_block, (qb, jnp.arange(nb) * QBLOCK))
    return jnp.moveaxis(o, 0, 1).reshape((B, T) + o.shape[3:])

def causal_short_conv(x, prev, conv_w):
    T = x.shape[1]
    xp = jnp.concatenate([prev.astype(x.dtype), x], axis=1)
    y = sum(xp[:, j:j + T] * conv_w[j] for j in range(CONV_W))
    return jax.nn.silu(y), xp[:, xp.shape[1] - (CONV_W - 1):]

def gated_delta_rule(q, k, v, g, beta, s0):
    f32 = jnp.float32
    B, T, H, DK = k.shape
    DV = v.shape[-1]
    n = -(-T // CHUNK)
    pad = n * CHUNK - T

    def to_blocks(a):
        a = a.astype(f32)
        a = jnp.pad(a, [(0, 0), (0, pad)] + [(0, 0)] * (a.ndim - 2))
        a = a.reshape((B, n, CHUNK) + a.shape[2:])
        return jnp.moveaxis(a, (1, 2), (0, 3))

    qc = to_blocks(q) * (DK ** -0.5)
    kc, vc, bc = to_blocks(k), to_blocks(v), to_blocks(beta)
    gc = jnp.cumsum(to_blocks(g), axis=-1)
    idx = jnp.arange(CHUNK)
    causal = idx[:, None] >= idx[None, :]
    strict = idx[:, None] > idx[None, :]
    decay = jnp.exp(jnp.where(causal, gc[..., :, None] - gc[..., None, :], NEG_INF))
    kb = kc * bc[..., None]
    lower = jnp.where(strict, jnp.einsum('nbhid,nbhjd->nbhij', kb, kc) * decay, 0.0)
    eye = jnp.eye(CHUNK, dtype=f32)
    t_inv = lax.linalg.triangular_solve(eye + lower, jnp.broadcast_to(eye, lower.shape),
                                        left_side=True, lower=True, unit_diagonal=True)
    u = jnp.einsum('nbhij,nbhjd->nbhid', t_inv, vc * bc[..., None])
    w = jnp.einsum('nbhij,nbhjd->nbhid', t_inv, kb * jnp.exp(gc)[..., None])
    a_intra = jnp.einsum('nbhid,nbhjd->nbhij', qc, kc) * decay
    q_dec = qc * jnp.exp(gc)[..., None]
    k_tail = kc * jnp.exp(gc[..., -1:] - gc)[..., None]
    g_last = jnp.exp(gc[..., -1])

    def block_step(s, xs):
        u_i, w_i, a_i, q_i, kt_i, gl_i = xs
        v_new = u_i - jnp.einsum('bhck,bhkv->bhcv', w_i, s)
        o_i = jnp.einsum('bhck,bhkv->bhcv', q_i, s) + jnp.einsum('bhij,bhjv->bhiv', a_i, v_new)
        s = s * gl_i[..., None, None] + jnp.einsum('bhck,bhcv->bhkv', kt_i, v_new)
        return s, o_i

    s_fin, o = lax.scan(block_step, s0.astype(f32), (u, w, a_intra, q_dec, k_tail, g_last))
    o = jnp.moveaxis(o, (0, 3), (1, 2)).reshape(B, n * CHUNK, H, DV)[:, :T]
    return o, s_fin

def memory_kv(mem, g_mem, w_ck, w_cv):
    B, M = mem.shape[0], mem.shape[1]
    m = rmsnorm(mem, g_mem)
    return ((m @ w_ck).reshape(B, M, X_HEADS, X_DH), (m @ w_cv).reshape(B, M, X_HEADS, X_DH))

def cross_attn(h, mem_k, mem_v, w_cq, w_co):
    B, T, _ = h.shape
    q = (h @ w_cq).reshape(B, T, X_HEADS, X_DH)
    s = jnp.einsum('bqhd,bmhd->bhqm', q, mem_k).astype(jnp.float32) * (X_DH ** -0.5)
    p = jax.nn.softmax(s, axis=-1).astype(h.dtype)
    o = jnp.einsum('bhqm,bmhd->bqhd', p, mem_v)
    return o.reshape(B, T, X_HEADS * X_DH) @ w_co

def hier_moe(x, w_grp, b_grp, w_rt, b_rt, w_gate, w_up, w_down):
    N = x.shape[0]
    grp_prob = jax.nn.softmax((x @ w_grp).astype(jnp.float32) + b_grp.astype(jnp.float32), axis=-1)
    g_top, g_idx = lax.top_k(grp_prob, 1)
    e_logits = ((x @ w_rt).astype(jnp.float32) + b_rt.astype(jnp.float32)).reshape(N, N_GROUPS, E_PER_GROUP)
    in_grp = jnp.take_along_axis(e_logits, g_idx[:, :, None], axis=1)[:, 0]
    e_top, e_idx = lax.top_k(in_grp, TOP_K)
    e_w = jax.nn.softmax(e_top, axis=-1) * g_top
    flat = g_idx * E_PER_GROUP + e_idx
    comb = jnp.sum(jax.nn.one_hot(flat, N_EXPERTS, dtype=jnp.float32) * e_w[..., None], axis=1).astype(x.dtype)
    out = jnp.zeros_like(x)
    for gi in range(N_GROUPS):
        sl = slice(gi * E_PER_GROUP, (gi + 1) * E_PER_GROUP)
        hg = jax.nn.silu(jnp.einsum('nd,edf->nef', x, w_gate[sl])) * jnp.einsum('nd,edf->nef', x, w_up[sl])
        out = out + jnp.einsum('nef,efd->nd', hg * comb[:, sl, None], w_down[sl])
    return out

def trunk_layer(x, mem_k, mem_v, past_k, past_v, conv_prev, s_prev, lam_init,
                g_mix, w_in, lam_q1, lam_k1, lam_q2, lam_k2, g_subln, conv_w, a_log, dt_bias,
                g_gdn_out, w_out, g_cross, w_cq, w_co, g_ffn, w_grp, b_grp, w_rt, b_rt,
                w_gate, w_up, w_down):
    f32 = jnp.float32
    B, T, _ = x.shape
    h = rmsnorm(x, g_mix)
    sizes = (DA_QK, DA_QK, DA_WIDTH, GDN_QKV, GDN_HEADS, GDN_HEADS, GDN_WIDTH)
    cuts = [int(c) for c in np.cumsum(sizes)[:-1]]
    dq, dk, dv, gqkv, ga, gb, gz = jnp.split(h @ w_in, cuts, axis=-1)

    dq = dq.reshape(B, T, DA_HEADS, 2, DA_DH)
    dk = dk.reshape(B, T, DA_HEADS, 2 * DA_DH)
    dv = dv.reshape(B, T, DA_HEADS, DA_DV)
    lam = (jnp.exp(jnp.sum(lam_q1.astype(f32) * lam_k1.astype(f32)))
           - jnp.exp(jnp.sum(lam_q2.astype(f32) * lam_k2.astype(f32))) + lam_init)
    if past_k is None:
        o_da = diff_attn_prompt(dq, dk.reshape(B, T, DA_HEADS, 2, DA_DH), dv, lam)
    else:
        P = past_k.shape[1]
        k_all = jnp.concatenate([past_k.astype(dk.dtype), dk], axis=1).reshape(B, P + T, DA_HEADS, 2, DA_DH)
        v_all = jnp.concatenate([past_v.astype(dv.dtype), dv], axis=1)
        o_da = diff_attn_core(dq, k_all, v_all, P + jnp.arange(T), jnp.arange(P + T), lam)
    o_da = rmsnorm(o_da, g_subln) * (1.0 - lam_init)

    if conv_prev is None:
        conv_prev = jnp.zeros((B, CONV_W - 1, GDN_QKV), x.dtype)
    if s_prev is None:
        s_prev = jnp.zeros((B, GDN_HEADS, GDN_DK, GDN_DV), f32)
    c, conv_new = causal_short_conv(gqkv, conv_prev, conv_w)
    cq, ck, cv = jnp.split(c, [GDN_HEADS * GDN_DK, 2 * GDN_HEADS * GDN_DK], axis=-1)
    cq = l2norm(cq.reshape(B, T, GDN_HEADS, GDN_DK))
    ck = l2norm(ck.reshape(B, T, GDN_HEADS, GDN_DK))
    cv = cv.reshape(B, T, GDN_HEADS, GDN_DV)
    g = -jnp.exp(a_log.astype(f32)) * jax.nn.softplus(ga.astype(f32) + dt_bias.astype(f32))
    beta = jax.nn.sigmoid(gb.astype(f32))
    o_g, s_new = gated_delta_rule(cq, ck, cv, g, beta, s_prev)
    o_g = rmsnorm(o_g.astype(x.dtype), g_gdn_out) * jax.nn.silu(gz.reshape(B, T, GDN_HEADS, GDN_DV))

    mix = jnp.concatenate([o_da.reshape(B, T, DA_WIDTH), o_g.reshape(B, T, GDN_WIDTH)], axis=-1)
    x = x + mix @ w_out
    x = x + cross_attn(rmsnorm(x, g_cross), mem_k, mem_v, w_cq, w_co)
    x = x + hier_moe(rmsnorm(x, g_ffn).reshape(B * T, D_MODEL), w_grp, b_grp, w_rt, b_rt,
                     w_gate, w_up, w_down).reshape(B, T, D_MODEL)
    return x, (dk, dv, conv_new, s_new.astype(x.dtype))

def setup_inputs(seed: int = 0) -> dict:
    key = jax.random.key(seed)
    ks = iter(jax.random.split(key, 48))
    f32 = jnp.float32
    L = DEPTH

    def nrm(shape, scale=1.0):
        return jax.random.normal(next(ks), shape, f32) * scale

    def gain(shape):
        return 1.0 + 0.01 * jax.random.normal(next(ks), shape, f32)

    dt = jnp.exp(jax.random.uniform(next(ks), (L, GDN_HEADS), f32, math.log(1e-3), math.log(1e-1)))
    a_log = jnp.log(jax.random.uniform(next(ks), (L, GDN_HEADS), f32, 1.0, 16.0))
    return {
        'x_prompt': nrm((BATCH, SEQ, D_MODEL)),
        'x_sample': nrm((DEC_BATCH, DEC_SEQ, D_MODEL)),
        'cache_diff_k': nrm((L, DEC_BATCH, PAST_LEN, DA_HEADS, 2 * DA_DH)),
        'cache_diff_v': nrm((L, DEC_BATCH, PAST_LEN, DA_HEADS, DA_DV)),
        'state_gdn_conv': nrm((L, DEC_BATCH, CONV_W - 1, GDN_QKV)),
        'state_gdn': nrm((L, DEC_BATCH, GDN_HEADS, GDN_DK, GDN_DV), 0.1),
        'cache_mem_k': nrm((L, DEC_BATCH, N_MEM, X_HEADS, X_DH)),
        'cache_mem_v': nrm((L, DEC_BATCH, N_MEM, X_HEADS, X_DH)),
        'mem_prompt': nrm((BATCH, N_MEM, D_MODEL)),
        'g_mix': gain((L, D_MODEL)),
        'w_in': nrm((L, D_MODEL, IN_COLS), D_MODEL ** -0.5),
        'lam_q1': nrm((L, DA_DH), 0.1),
        'lam_k1': nrm((L, DA_DH), 0.1),
        'lam_q2': nrm((L, DA_DH), 0.1),
        'lam_k2': nrm((L, DA_DH), 0.1),
        'g_subln': gain((L, DA_DV)),
        'conv_w': nrm((L, CONV_W, GDN_QKV), CONV_W ** -0.5),
        'a_log': a_log,
        'dt_bias': dt + jnp.log(-jnp.expm1(-dt)),
        'g_gdn_out': gain((L, GDN_DV)),
        'w_out': nrm((L, MIX_WIDTH, D_MODEL), MIX_WIDTH ** -0.5),
        'g_cross': gain((L, D_MODEL)),
        'g_mem': gain((L, D_MODEL)),
        'w_ck': nrm((L, D_MODEL, X_HEADS * X_DH), D_MODEL ** -0.5),
        'w_cv': nrm((L, D_MODEL, X_HEADS * X_DH), D_MODEL ** -0.5),
        'w_cq': nrm((L, D_MODEL, X_HEADS * X_DH), D_MODEL ** -0.5),
        'w_co': nrm((L, X_HEADS * X_DH, D_MODEL), (X_HEADS * X_DH) ** -0.5),
        'g_ffn': gain((L, D_MODEL)),
        'w_grp': nrm((L, D_MODEL, N_GROUPS), D_MODEL ** -0.5),
        'b_grp': nrm((L, N_GROUPS), 0.01),
        'w_rt': nrm((L, D_MODEL, N_EXPERTS), D_MODEL ** -0.5),
        'b_rt': nrm((L, N_EXPERTS), 0.01),
        'w_gate': nrm((L, N_EXPERTS, D_MODEL, D_EXPERT), D_MODEL ** -0.5),
        'w_up': nrm((L, N_EXPERTS, D_MODEL, D_EXPERT), D_MODEL ** -0.5),
        'w_down': nrm((L, N_EXPERTS, D_EXPERT, D_MODEL), D_EXPERT ** -0.5),
        'g_final': gain((D_MODEL,)),
    }

def reference(x_prompt, x_sample, cache_diff_k, cache_diff_v, state_gdn_conv, state_gdn,
              cache_mem_k, cache_mem_v, mem_prompt,
              g_mix, w_in, lam_q1, lam_k1, lam_q2, lam_k2, g_subln, conv_w, a_log, dt_bias,
              g_gdn_out, w_out, g_cross, g_mem, w_ck, w_cv, w_cq, w_co, g_ffn,
              w_grp, b_grp, w_rt, b_rt, w_gate, w_up, w_down, g_final):
    xp, xs = x_prompt, x_sample
    pk, pv, pc, ps, pmk, pmv, sk, sv, sc, ss = ([] for _ in range(10))
    for l in range(DEPTH):
        lam_init = 0.8 - 0.6 * math.exp(-0.3 * l)
        lw = (g_mix[l], w_in[l], lam_q1[l], lam_k1[l], lam_q2[l], lam_k2[l], g_subln[l], conv_w[l],
              a_log[l], dt_bias[l], g_gdn_out[l], w_out[l], g_cross[l], w_cq[l], w_co[l], g_ffn[l],
              w_grp[l], b_grp[l], w_rt[l], b_rt[l], w_gate[l], w_up[l], w_down[l])
        mk, mv = memory_kv(mem_prompt, g_mem[l], w_ck[l], w_cv[l])
        xp, (k_p, v_p, c_p, s_p) = trunk_layer(xp, mk, mv, None, None, None, None, lam_init, *lw)
        pk.append(k_p); pv.append(v_p); pc.append(c_p); ps.append(s_p); pmk.append(mk); pmv.append(mv)
        xs, (k_s, v_s, c_s, s_s) = trunk_layer(xs, cache_mem_k[l], cache_mem_v[l], cache_diff_k[l],
                                               cache_diff_v[l], state_gdn_conv[l], state_gdn[l],
                                               lam_init, *lw)
        sk.append(k_s); sv.append(v_s); sc.append(c_s); ss.append(s_s)
    y_prompt = rmsnorm(xp, g_final)
    y_sample = rmsnorm(xs, g_final)
    return (y_prompt, y_sample,
            jnp.stack(pk), jnp.stack(pv), jnp.stack(pc), jnp.stack(ps), jnp.stack(pmk), jnp.stack(pmv),
            jnp.stack(sk), jnp.stack(sv), jnp.stack(sc), jnp.stack(ss))


_drawn_inputs = setup_inputs


def setup_inputs(seed=0):
    import zlib

    import numpy as np

    out = dict(_drawn_inputs(seed))
    spreads = {}
    factors = {'g_subln': 4.47,
     'g_gdn_out': 3.097,
     'g_cross': 6.621,
     'g_mem': 4.96,
     'g_ffn': 2.834,
     'b_grp': 3.818,
     'b_rt': 3.171,
     'g_final': 5.895}
    for name, (base, spread) in spreads.items():
        noise = np.random.default_rng([zlib.crc32(name.encode()), seed]).standard_normal(out[name].shape)
        drawn = base * np.exp(spread * noise) if base else spread * noise
        out[name] = __import__('jax').numpy.asarray(drawn.astype(out[name].dtype))
    for name, factor in factors.items():
        out[name] = (out[name] * factor).astype(out[name].dtype)
    return out
```

```python
from contextlib import ExitStack

import numpy as np

import concourse.bass as bass
from concourse import mybir

F32 = mybir.dt.float32
U32 = mybir.dt.uint32
ALU = mybir.AluOpType
ACT = mybir.ActivationFunctionType
AX = mybir.AxisListType

P = 128
D = 1024
KC = D // P
NT = 5
NTP = 4
SEQ = 512
NB = 8
TB = 16
PAST = 512
H = 4
MEM = 256
CONV = 4
NG, NE, TOPK = 4, 32, 2
EPG = NE // NG
FE = 256
CAP = 80
MAXBLK = (NT * P * TOPK) // CAP + NE
BLKPAD = MAXBLK + 1
NBLK = BLKPAD + 3
NSLOT = NBLK * CAP
NPAIR = TOPK * NT * P
EPS = 1e-6
BIG = 1.0e30
LAM_INIT = 0.8 - 0.6
GW = 3 + SEQ + NB * (TB + 3)
GS = 3 + SEQ



def constant_columns():
    p = np.arange(P)[:, None]
    f = np.arange(P)[None, :]
    same = p // TB == f // TB
    cols = {}
    cols["ident"] = (p == f) * 1.0
    cols["ones"] = np.ones((P, P))
    cols["cum_p"] = (p <= f) * 1.0
    cols["cum_s"] = ((p <= f) & same) * 1.0
    cols["low_p"] = np.where(f < p, 0.0, -BIG)
    cols["low_s"] = np.where((f < p) & same, 0.0, -BIG)
    cols["up_p"] = np.where(f >= p, 0.0, -BIG)
    cols["up_s"] = np.where((f >= p) & same, 0.0, -BIG)
    cols["blk16"] = same * 1.0
    for s in (32, 64, 128):
        cols[f"lev{s}"] = ((p // s == f // s) & (p // (s // 2) > f // (s // 2))) * 1.0
    cols["stream_off"] = np.repeat(np.where(np.arange(NB)[:, None] == f // TB, 0.0, -BIG).reshape(1, -1), P, 0)
    cols["stream_row"] = (p // TB == np.arange(NB)[None, :]) * 1.0
    row = np.arange(P)
    h, m, q = row // 32, (row // 16) % 2, row % 16
    cols["pick"] = (h * 16 + q)[:, None] == np.arange(64)[None, :]
    cols["map0"] = (m == 0)[:, None]
    cols["map1"] = (m == 1)[:, None]
    cols["capacities"] = np.repeat(CAP * np.arange(NT * P // CAP)[None] * 1.0, P, 0)
    cols["minus_one"] = np.full((P, 1), -1.0)
    cols["eps"] = np.full((P, 1), EPS)
    cols["minus_half"] = np.full((P, 8), -0.5)
    cols["qk_scale"] = np.repeat(np.array([[P] * 4 + [1.0] * 4]), P, 0)
    cols["iota8"] = np.repeat(np.arange(8.0)[None], P, 0)
    cols["group"] = np.repeat((np.arange(NE) // EPG)[None] * 1.0, P, 0)
    cols["iota32"] = np.repeat(np.arange(NE)[None] * 1.0, P, 0)
    cols["block"] = np.repeat(np.arange(BLKPAD + 1)[None] * 1.0, P, 0)
    cols["pair"] = p + P * np.arange(TOPK * NT)[None, :]
    slot = np.arange(NSLOT)
    cols["empty"] = np.zeros((P, NBLK))
    cols["empty"][:CAP] = (NPAIR + slot % (2 * CAP)).reshape(CAP, NBLK)
    return {k: np.asarray(v, np.float32) for k, v in cols.items()}


CONST = constant_columns()
CONST_AT, _at = {}, 0
for _k, _v in CONST.items():
    CONST_AT[_k] = (_at, _v.shape[1])
    _at += _v.shape[1]
NCONST = _at


class Steps:

    def __init__(self, sem, name, names):
        self.groups = []
        self.of = {}
        for i, group in enumerate(names.split("|")):
            group = group.split()
            self.groups.append([sem(f"{name}{i or ''}"), len(group), 0])
            for k, step in enumerate(group):
                assert step not in self.of
                self.of[step] = (i, k)

    def arm(self, eng):
        for sem, n, _ in self.groups:
            eng.sem_inc(sem, 2 * n)

    def __getitem__(self, name):
        return self.groups[self.of[name][0]][0]

    def after(self, it, name):
        i, k = self.of[name]
        n = self.groups[i][1]
        return it * n + (k + 1 + 2 * n)

    def step(self, name):
        i, k = self.of[name]
        group = self.groups[i]
        assert group[2] % group[1] == k, (name, k, group)
        group[2] += 1
        return group[0]




def weight_jobs():
    own = lambda what: [(what, t, 0) for t in range(NT)]
    wide = lambda what, n: [(what, m, c) for m in range(n) for c in range(2)]
    project = (
        [("dq", m, c) for m in range(4) for c in range(2)] + own("dk") + own("dv")
        + [("conv", m, c) for m in range(12) for c in range(2)] + own("gz") + [("gab", 0, 0)]
    )
    mix = [("mix", t, n) for n in range(2) for t in range(NT)]
    memory = [("mk", t, n) for n in range(2) for t in range(2)] + [("mv", t, n) for n in range(2) for t in range(2)]
    return {"project": project, "mix": mix, "memory": memory, "cq": wide("cq", KC),
            "co": [("co", t, n) for n in range(2) for t in range(NT)]}


JOBS = weight_jobs()
ORDER = [job for group in ("project", "mix", "memory", "cq", "co") for job in JOBS[group]]
NJBANK = 4


def evacuator(n):
    return "dve" if ORDER[n][0] in ("mix", "co") or n % 2 else "act"


TAKEN = {e: np.cumsum([evacuator(n) == e for n in range(len(ORDER))]).tolist() for e in ("act", "dve")}
FIRST_OF = {}
for _n, _job in enumerate(ORDER):
    FIRST_OF.setdefault(_job[0], _n)
LAST_OF = {job[0]: n for n, job in enumerate(ORDER)}

UNIT = {}
for _n, _u in enumerate(
    ["dq", "dk", "dv", "conv0", "conv1", "conv2", "gz"] + [f"da{b}" for b in range(NB)]
    + ["mix0", "mix1", "mk0", "mk1", "mv0", "mv1", "cq0", "cq1"] + [f"x{b}" for b in range(NB)]
    + ["co0", "co1"]
):
    UNIT[_u] = _n
WSLOT = 6 * D


def unit_of(job):
    what, a, b = job
    if what == "conv":
        return UNIT[f"conv{a // 4}"]
    if what in ("mix", "mk", "mv", "co"):
        return UNIT[f"{what}{b}"]
    if what == "cq":
        return UNIT[f"cq{a // 4}"]
    return None if what == "gab" else UNIT[what]


GDN_ACT = "stage sq0 sq1 EG eg D DT qT Mt M2 M2t M4 M4t M8 T0 T1 T2 w osq mix"
GDN_PE = ("tokqk tokv cum gcum chq chk kk kq Mt sq2 sq2t x1 sq4 sq4t x2 sq8 x3 "
          "T0 BX0 Y0 T1 BX1 Y1 T2 BX2 Y2 w vn o s oT")
GDN_DVE = ("gb gB gc S SD SU ss ssq qk0 qk1 kT vb be kbg kl ktail L0 L AT M B0 X0 X1 X2 X3 "
           "W0 Y0 B1 W1 Y1 B2 W2 Y2 qd vn sg s oss oms on og oz")
GDN_POOL = "rn orn"


def build_encoder_step(nc, a):
    ctx = ExitStack()
    with ctx:
        def sb(name, shape, dt=F32):
            return ctx.enter_context(nc.sbuf_tensor("sb_" + name, shape, dt))

        def sem(name):
            return ctx.enter_context(nc.semaphore(name))

        def steps(name, names):
            return Steps(sem, name, names)

        const = sb("const", [P, NCONST])
        x_buf = sb("x", [P, NT * D])
        x = x_buf[:, :].rearrange("p (t d) -> p t d", t=NT)
        act_a = sb("act_a", [P, KC, NT * P])
        act_b = sb("act_b", [P, KC * NT * P])
        attn = sb("attn", [P, 3 * NT * 512])
        conv = sb("conv", [P, 12 * GW])
        gz = sb("gz", [P, NT, 512])
        W = sb("W", [P, 2, WSLOT])
        scr = sb("scr", [P, 3, D])
        small = sb("small", [P, 768])
        gains = sb("gains", [P, 4, KC])
        gdn_g = sb("gdn_g", [P, 2 * 128])
        convw = sb("convw", [P, 12, CONV])
        w_gab = sb("w_gab", [P, KC, 8])

        def C(name, h=None):
            at, n = CONST_AT[name]
            v = const[:, at:at + n]
            return v if h is None else v.unsqueeze(1).to_broadcast([P, h, n])

        free = [0]

        def little(n):
            free[0] += n
            assert free[0] <= 768
            return small[:, free[0] - n:free[0]]

        ident = C("ident")
        dq = attn[:, 0:2560].rearrange("p (h t) -> p h t", h=H)
        dk = attn[:, 2560:5120].rearrange("p (h t) -> p h t", h=H)
        dv = attn[:, 5120:7680].rearrange("p (t c) -> p t c", t=NT)
        dk_tok = act_b[:, 0:2560].rearrange("p (t c) -> p t c", t=NT)
        cv = conv[:, :].rearrange("p (m c) -> p m c", m=12)
        bank = [ctx.enter_context(nc.psum_tensor(f"bank{i}", [P, 512], F32)) for i in range(8)]

        def quarters(b):
            return b[:, :].rearrange("p (h c) -> p h c", h=4)

        s_const = sem("const_loaded")
        s_gain = sem("gains_loaded")
        s_x = [sem(f"x_loaded{t}") for t in range(NT)]
        s_w = [sem(f"w_loaded{k}") for k in range(2)]
        s_kv = [sem(f"kv_loaded{k}") for k in range(2)]
        s_hist = sem("conv_history_loaded")
        s_job = sem("jobs_computed")
        s_taken = {"act": sem("jobs_taken_by_act"), "dve": sem("jobs_taken_by_dve")}
        s_out = sem("outputs_stored")
        n_out = [0]

        def taken(n):
            return s_taken[evacuator(n)]

        def taken_count(n):
            return TAKEN[evacuator(n)][n]

        def all_taken(eng, last):
            for e in ("act", "dve"):
                if TAKEN[e][last]:
                    eng.wait_ge(s_taken[e], TAKEN[e][last])

        NORMS = {"mix": NT, "mem": 2, "cross": NT, "ffn": NT}
        n_act = {k: steps(f"norm_{k}_act", " ".join(f"sq{t}" for t in range(n))) for k, n in NORMS.items()}
        n_pool = {k: steps(f"norm_{k}_pool", "ms rstd " + " ".join(f"g{t}" for t in range(n) if k == "ffn"))
                  for k, n in NORMS.items()}
        n_dve = {k: steps(f"norm_{k}_dve", " ".join(
            f"xn{t}" + ("" if t == 0 else f" ev{t - 1}a ev{t - 1}b") for t in range(n)) + f" ev{n - 1}a ev{n - 1}b")
            for k, n in NORMS.items()}
        n_pe = {k: steps(f"norm_{k}_pe", " ".join(f"tr{t}a tr{t}b" for t in range(n))) for k, n in NORMS.items()}
        ss = little(8)
        rstd = little(8)

        def norm_act(act, k, src, ready):
            s = n_act[k]
            s.arm(act)
            for t in range(NORMS[k]):
                act.wait_ge(*ready(t))
                nc.scalar.activation(scr[:, 2, :], src(t), ACT.Square, accum_out=ss[:, t:t + 1]).then_inc(s.step(f"sq{t}"), 1)
                act.wait_ge(s[f"sq{t}"], s.after(0, f"sq{t}"))

        def norm_pool(pool, k):
            s, n = n_pool[k], NORMS[k]
            s.arm(pool)
            pool.wait_ge(n_act[k][f"sq{n - 1}"], n_act[k].after(0, f"sq{n - 1}"))
            nc.gpsimd.tensor_scalar(rstd[:, 0:n], ss[:, 0:n], 1.0 / D, EPS, ALU.mult, ALU.add).then_inc(s.step("ms"), 1)
            pool.wait_ge(s["ms"], s.after(0, "ms"))
            nc.gpsimd.tensor_tensor(rstd[:, 0:n], rstd[:, 0:n], C("minus_half")[:, 0:n], ALU.pow).then_inc(s.step("rstd"), 1)

        def norm_dve(dve, k, src, gain, dst):
            s, n = n_dve[k], NORMS[k]
            s.arm(dve)
            dve.wait_ge(n_pool[k]["rstd"], n_pool[k].after(0, "rstd"))
            for t in range(n + 1):
                if t < n:
                    if t >= 2:
                        dve.wait_ge(n_pe[k][f"tr{t - 2}b"], n_pe[k].after(0, f"tr{t - 2}b"))
                        if k == "ffn":
                            dve.wait_ge(n_pool[k][f"g{t - 2}"], n_pool[k].after(0, f"g{t - 2}"))
                    nc.vector.tensor_scalar(scr[:, t % 2, :], src(t), rstd[:, t:t + 1], None, ALU.mult).then_inc(s.step(f"xn{t}"), 1)
                if t >= 1:
                    for i, ab in enumerate("ab"):
                        dve.wait_ge(n_pe[k][f"tr{t - 1}{ab}"], n_pe[k].after(0, f"tr{t - 1}{ab}"))
                        o = dst[:, 4 * i:4 * i + 4, (t - 1) * P:t * P]
                        g = gain[:, 4 * i:4 * i + 4].unsqueeze(2).to_broadcast([P, 4, P])
                        nc.vector.tensor_tensor(o, quarters(bank[4 + 2 * ((t - 1) % 2) + i]), g, ALU.mult).then_inc(s.step(f"ev{t - 1}{ab}"), 1)

        def norm_pe(pe, k):
            s = n_pe[k]
            s.arm(pe)
            for t in range(NORMS[k]):
                pe.wait_ge(n_dve[k][f"xn{t}"], n_dve[k].after(0, f"xn{t}"))
                for i, ab in enumerate("ab"):
                    if t >= 2:
                        pe.wait_ge(n_dve[k][f"ev{t - 2}{ab}"], n_dve[k].after(0, f"ev{t - 2}{ab}"))
                    for c in range(4):
                        q = 4 * i + c
                        mm = nc.tensor.transpose(quarters(bank[4 + 2 * (t % 2) + i])[:, c, :], scr[:, t % 2, q * P:(q + 1) * P], ident)
                    mm.then_inc(s.step(f"tr{t}{ab}"), 1)

        def x_tile(t):
            return x[:, t, :]

        def slot(n):
            return W[:, n % 2, 0:4096].rearrange("p (c n) -> p c n", c=KC)

        def run_jobs(pe, names, src):
            for n, job in enumerate(ORDER):
                what, ja, jb = job
                if what not in names:
                    continue
                unit = unit_of(job)
                first = n == 0 or unit_of(ORDER[n - 1]) != unit
                if unit is not None and first:
                    pe.wait_ge(s_w[unit % 2], 16 * W_COUNT[unit])
                if n >= NJBANK:
                    pe.wait_ge(taken(n - NJBANK), taken_count(n - NJBANK))
                out = bank[n % NJBANK]
                for c in range(KC):
                    if what in ("dq", "conv", "cq"):
                        cols = slice(0, 512) if jb == 0 else slice(512, 640)
                        m = ja % 4
                        mm = nc.tensor.matmul(out[:, 0:cols.stop - cols.start], slot(unit)[:, c, m * P:(m + 1) * P],
                                              src[:, c, cols], start=c == 0, stop=c == KC - 1)
                    elif what == "gab":
                        continue
                    else:
                        mm = nc.tensor.matmul(out[:, :], src[:, c, ja * P:(ja + 1) * P], slot(unit)[:, c, :],
                                              start=c == 0, stop=c == KC - 1)
                if what == "gab":
                    for t in range(NT):
                        for c in range(KC):
                            mm = nc.tensor.matmul(out[:, 8 * t:8 * t + 8], src[:, c, t * P:(t + 1) * P], w_gab[:, c, :],
                                                  start=c == 0, stop=c == KC - 1)
                mm.then_inc(s_job, 1)

        gab = little(8 * NT)

        def take_jobs(me, eng, names, dst):
            for n, job in enumerate(ORDER):
                if job[0] not in names or evacuator(n) != me:
                    continue
                eng.wait_ge(s_job, n + 1)
                for i, (o, b, scale) in enumerate(dst(job, bank[n % NJBANK])):
                    if job[0] in ("mix", "co"):
                        ins = nc.vector.tensor_tensor(o, b, o, ALU.add)
                    elif me == "act":
                        ins = nc.scalar.mul(o, b, scale) if scale != 1.0 else nc.scalar.copy(o, b)
                    elif scale != 1.0:
                        ins = nc.vector.tensor_scalar(o, b, scale, None, ALU.mult)
                    else:
                        ins = nc.vector.tensor_copy(o, b)
                ins.then_inc(s_taken[me], 1)

        def project_dst(job, b):
            what, ja, jb = job
            n = 512 if jb == 0 else P
            at = 512 * jb
            if what == "dq":
                return [(dq[:, ja, at:at + n], b[:, 0:n], 0.125)]
            if what == "conv":
                if jb == 0:
                    return [(cv[:, ja, 3:GS], b[:, :], 1.0)]
                return [(cv[:, ja, GS:GW].rearrange("p (b c) -> p b c", b=NB)[:, :, 3:],
                         b[:, 0:P].rearrange("p (b c) -> p b c", b=NB), 1.0)]
            if what == "gab":
                return [(gab, b[:, 0:8 * NT], 1.0)]
            return [({"dk": dk_tok, "dv": dv, "gz": gz}[what][:, ja, :], b[:, :], 1.0)]

        W_COUNT, _count = {}, [0, 0]
        for name, n in UNIT.items():
            if not (name[0:2] == "da" or name[0] == "x"):
                _count[n % 2] += 1
                W_COUNT[n] = _count[n % 2]

        LAST_JOB = {unit_of(job): n for n, job in enumerate(ORDER)}

        def load_weight(eng, name, src, cols):
            n = UNIT[name]
            for s in (das, xs):
                b = n - 2 - s.first_unit
                if 0 <= b < NB:
                    eng.wait_ge(s.pe["pv"], s.pe.after(b, "pv"))
            if n - 2 in LAST_JOB:
                eng.wait_ge(s_job, LAST_JOB[n - 2] + 1)
            eng.dma_start(slot(n), src.rearrange("(c p) n -> p c n", p=P)[:, :, cols]).then_inc(s_w[n % 2], 16)

        lam4 = little(4 * 64)
        lamp = little(2)
        lame = little(2)
        nlam = little(1)
        row_sign = little(1)
        alog = little(4)
        dtb = little(4)
        nexp_a = little(4)
        glog = little(4 * NT)
        beta = little(4 * NT)
        tz, te = little(4 * NT), little(4 * NT)
        eps = C("eps")

        hist = act_b[0:NB * 3, 2560:4096]
        tails = act_b[:, 4096:4096 + 12 * 27].rearrange("p (m c) -> p m c", m=12)
        tails_tok = act_b[0:27, 2560:4096]

        p_dve = steps("prep_dve", "lam0 lam1 nlam sign sign2 hist tail0 tail1 kT0 kT1 kT2 kT3 kT4 tt0 tt1 tt2 "
                                  "na z az sp0 sp1 g b1 b2 gsub")
        p_act = steps("prep_act", "lam ea e l eb")
        p_pe = steps("prep_pe", "hist kT0 kT1 kT2 kT3 kT4 tt0 tt1 tt2")
        p_pool = steps("prep_pool", "zero")
        s_small = sem("small_loaded")

        def prep_sync_load(sp):
            for i, n in enumerate(("lam_q1", "lam_k1", "lam_q2", "lam_k2")):
                sp.dma_start(lam4[:, 64 * i:64 * i + 64], a[n][0].partition_broadcast(P)).then_inc(s_small, 16)
            sp.dma_start(alog, a["a_log"][0].partition_broadcast(P)).then_inc(s_small, 16)
            sp.dma_start(dtb, a["dt_bias"][0].partition_broadcast(P)).then_inc(s_small, 16)
            sp.dma_start(gdn_g[:, 0:128], a["g_subln"][0].partition_broadcast(P)).then_inc(s_small, 16)
            sp.dma_start(gdn_g[:, 128:256], a["g_gdn_out"][0].partition_broadcast(P)).then_inc(s_small, 16)
            for m in range(CONV):
                sp.dma_start(convw[:, :, m], a["conv_w"][0][m].rearrange("(m p) -> p m", p=P),
                             allow_slow_non_contiguous=True).then_inc(s_small, 16)
            sp.dma_start(w_gab[:, :, :], a["w_in"][0].rearrange("(c p) n -> p c n", p=P)[:, :, 3072:3080]).then_inc(s_small, 16)

        N_SMALL = 16 * (4 + 2 + 2 + CONV + 1)

        def prep_pool_a(pool):
            p_pool.arm(pool)
            nc.gpsimd.memset(cv[:, :, 0:3], 0.0).then_inc(p_pool.step("zero"), 1)

        def prep_dve_a(dve):
            p_dve.arm(dve)
            dve.wait_ge(s_small, N_SMALL)
            dve.wait_ge(s_const, 16)
            l4 = lam4.rearrange("p (a b c) -> p a b c", a=2, b=2)
            nc.vector.tensor_tensor(l4[:, :, 0, :], l4[:, :, 0, :], l4[:, :, 1, :], ALU.mult).then_inc(p_dve.step("lam0"), 1)
            dve.wait_ge(p_dve["lam0"], p_dve.after(0, "lam0"))
            nc.vector.tensor_reduce(lamp, l4[:, :, 0, :], AX.X, ALU.add).then_inc(p_dve.step("lam1"), 1)
            dve.wait_ge(p_act["lam"], p_act.after(0, "lam"))
            nc.vector.scalar_tensor_tensor(nlam, lame[:, 1:2], -LAM_INIT, lame[:, 0:1], ALU.add, ALU.subtract).then_inc(p_dve.step("nlam"), 1)
            dve.wait_ge(p_dve["nlam"], p_dve.after(0, "nlam"))
            nc.vector.tensor_tensor(row_sign, C("map1"), nlam, ALU.mult).then_inc(p_dve.step("sign"), 1)
            dve.wait_ge(p_dve["sign"], p_dve.after(0, "sign"))
            nc.vector.tensor_tensor(row_sign, row_sign, C("map0"), ALU.add).then_inc(p_dve.step("sign2"), 1)
            dve.wait_ge(p_pe["hist"], p_pe.after(0, "hist"))
            for b in range(NB):
                ins = nc.vector.tensor_copy(cv[:, :, GS + 19 * b:GS + 19 * b + 3],
                                            bank[7][:, 0:288].rearrange("p (m r) -> p m r", m=12)[:, :, 3 * b:3 * b + 3])
            ins.then_inc(p_dve.step("hist"), 1)

        def prep_act_a(act):
            p_act.arm(act)
            act.wait_ge(p_dve["lam1"], p_dve.after(0, "lam1"))
            nc.scalar.activation(lame, lamp, ACT.Exp).then_inc(p_act.step("lam"), 1)
            nc.scalar.activation(nexp_a, alog, ACT.Exp).then_inc(p_act.step("ea"), 1)

        def prep_pe_a(pe):
            p_pe.arm(pe)
            pe.wait_ge(s_const, 16)
            pe.wait_ge(s_hist, 16)
            for m in range(12):
                mm = nc.tensor.transpose(bank[7][:, 24 * m:24 * m + 24], hist[:, m * P:(m + 1) * P], ident[0:24, 0:24])
            mm.then_inc(p_pe.step("hist"), 1)

        def prep_pe_b(pe):
            for t in range(NT):
                pe.wait_ge(taken(ORDER.index(("dk", t, 0))), taken_count(ORDER.index(("dk", t, 0))))
                if t >= 2:
                    pe.wait_ge(p_dve[f"kT{t - 2}"], p_dve.after(0, f"kT{t - 2}"))
                else:
                    pe.wait_ge(n_dve["mix"][f"ev{NT - 1}b"], n_dve["mix"].after(0, f"ev{NT - 1}b"))
                for h in range(H):
                    mm = nc.tensor.transpose(quarters(bank[4 + t % 2])[:, h, :], dk_tok[:, t, h * P:(h + 1) * P], ident)
                mm.then_inc(p_pe.step(f"kT{t}"), 1)
            pe.wait_ge(p_dve["tail1"], p_dve.after(0, "tail1"))
            for g in range(3):
                if g == 2:
                    pe.wait_ge(p_dve["tt0"], p_dve.after(0, "tt0"))
                for i in range(4):
                    mm = nc.tensor.transpose(bank[6 + g % 2][0:27, i * P:(i + 1) * P], tails[:, 4 * g + i, :], ident)
                mm.then_inc(p_pe.step(f"tt{g}"), 1)

        def prep_dve_b(dve):
            all_taken(dve, ORDER.index(("conv", 11, 1)))
            nc.vector.tensor_copy(tails[:, :, 0:3], cv[:, :, GS - 3:GS]).then_inc(p_dve.step("tail0"), 1)
            for b in range(NB):
                at = GS + 19 * b + 16
                ins = nc.vector.tensor_copy(tails[:, :, 3 + 3 * b:6 + 3 * b], cv[:, :, at:at + 3])
            ins.then_inc(p_dve.step("tail1"), 1)
            for t in range(NT):
                dve.wait_ge(p_pe[f"kT{t}"], p_pe.after(0, f"kT{t}"))
                nc.vector.tensor_copy(dk[:, :, t * P:(t + 1) * P], quarters(bank[4 + t % 2])).then_inc(p_dve.step(f"kT{t}"), 1)
            for g in range(3):
                dve.wait_ge(p_pe[f"tt{g}"], p_pe.after(0, f"tt{g}"))
                nc.vector.tensor_copy(tails_tok[:, g * 512:(g + 1) * 512], bank[6 + g % 2][0:27, :]).then_inc(p_dve.step(f"tt{g}"), 1)
            dve.wait_ge(p_act["ea"], p_act.after(0, "ea"))
            nc.vector.tensor_scalar(nexp_a, nexp_a, -1.0, None, ALU.mult).then_inc(p_dve.step("na"), 1)
            dve.wait_ge(p_dve["na"], p_dve.after(0, "na"))
            dve.wait_ge(taken(LAST_OF["gab"]), taken_count(LAST_OF["gab"]))
            g3 = gab.rearrange("p (t c) -> p t c", t=NT)

            def wide(v):
                return v.unsqueeze(1).to_broadcast([P, NT, 4])

            v3 = lambda v: v.rearrange("p (t c) -> p t c", t=NT)
            nc.vector.tensor_tensor(v3(tz), g3[:, :, 0:4], wide(dtb), ALU.add).then_inc(p_dve.step("z"), 1)
            dve.wait_ge(p_dve["z"], p_dve.after(0, "z"))
            nc.vector.scalar_tensor_tensor(te, tz, -1.0, tz, ALU.mult, ALU.max).then_inc(p_dve.step("az"), 1)
            dve.wait_ge(p_act["l"], p_act.after(0, "l"))
            nc.vector.tensor_scalar(tz, tz, 0.0, None, ALU.max).then_inc(p_dve.step("sp0"), 1)
            dve.wait_ge(p_dve["sp0"], p_dve.after(0, "sp0"))
            nc.vector.tensor_tensor(tz, tz, te, ALU.add).then_inc(p_dve.step("sp1"), 1)
            dve.wait_ge(p_dve["sp1"], p_dve.after(0, "sp1"))
            nc.vector.tensor_tensor(v3(glog), v3(tz), wide(nexp_a), ALU.mult).then_inc(p_dve.step("g"), 1)
            dve.wait_ge(p_act["eb"], p_act.after(0, "eb"))
            nc.vector.tensor_scalar(beta, beta, 1.0, None, ALU.add).then_inc(p_dve.step("b1"), 1)
            dve.wait_ge(p_dve["b1"], p_dve.after(0, "b1"))
            nc.vector.reciprocal(beta, beta).then_inc(p_dve.step("b2"), 1)
            nc.vector.tensor_scalar(gdn_g[:, 0:128], gdn_g[:, 0:128], 1.0 - LAM_INIT, None, ALU.mult).then_inc(p_dve.step("gsub"), 1)

        def prep_act_b(act):
            act.wait_ge(taken(LAST_OF["gab"]), taken_count(LAST_OF["gab"]))
            act.wait_ge(p_dve["az"], p_dve.after(0, "az"))
            nc.scalar.activation(te, te, ACT.Exp, scale=-1.0).then_inc(p_act.step("e"), 1)
            act.wait_ge(p_act["e"], p_act.after(0, "e"))
            nc.scalar.activation(te, te, ACT.Ln, bias=C("ones")[:, 0:1]).then_inc(p_act.step("l"), 1)
            nc.scalar.activation(beta.rearrange("p (t c) -> p t c", t=NT),
                                            gab.rearrange("p (t c) -> p t c", t=NT)[:, :, 4:8], ACT.Exp, scale=-1.0).then_inc(p_act.step("eb"), 1)

        NY = GW - 3
        c_pool = steps("conv_pool", "y0 u1 y1 u2 y2 u3 y3")
        c_act = steps("conv_act", "silu")

        def conv_pool_one(pool, m):
            y, u = scr[:, 0, 0:NY], scr[:, 1, 0:NY]
            nc.gpsimd.tensor_scalar(y, cv[:, m, 0:NY], convw[:, m, 0:1], None, ALU.mult).then_inc(c_pool.step("y0"), 1)
            pool.wait_ge(c_pool["y0"], c_pool.after(m, "y0"))
            for j in range(1, CONV):
                nc.gpsimd.tensor_scalar(u, cv[:, m, j:j + NY], convw[:, m, j:j + 1], None, ALU.mult).then_inc(c_pool.step(f"u{j}"), 1)
                pool.wait_ge(c_pool[f"u{j}"], c_pool.after(m, f"u{j}"))
                o = cv[:, m, 0:NY] if j == CONV - 1 else y
                nc.gpsimd.tensor_tensor(o, y, u, ALU.add).then_inc(c_pool.step(f"y{j}"), 1)
                pool.wait_ge(c_pool[f"y{j}"], c_pool.after(m, f"y{j}"))

        def conv_act(act):
            c_act.arm(act)
            act.wait_ge(c_pool["y3"], c_pool.after(11, "y3"))
            for m in range(0, 12, 3):
                nc.scalar.activation(cv[:, m:m + 3, 0:NY], cv[:, m:m + 3, 0:NY], ACT.Silu)
            nc.scalar.activation(gz[:, :, :], gz[:, :, :], ACT.Silu).then_inc(c_act.step("silu"), 1)

        UN = NTP * H
        d_pe = steps("da_pe", "sc | tr | pv")
        d_dve = steps("da_dve", "cut mx | r c2 a0 a")
        d_act = steps("da_act", "p0 p1 | aT")
        prob = [x_buf[:, 1024 * i:1024 * (i + 1)].rearrange("p (m k) -> p m k", m=2) for i in range(2)]
        aT = [x_buf[:, 2048 + 512 * i:2560 + 512 * i] for i in range(2)]
        osq, on = x_buf[:, 3072:3584], x_buf[:, 3584:4096]
        nmax = [little(2) for _ in range(2)]
        psum_p = [little(2) for _ in range(2)]
        pr = [little(2) for _ in range(2)]
        o_pe = steps("da_out_pe", "oT")
        o_act = steps("da_out_act", "sq mix")
        o_dve = steps("da_out_dve", "ss on og")
        o_pool = steps("da_out_pool", "ms rn")
        oss = little(4)

        def b4(v):
            return v.unsqueeze(2).to_broadcast([P, 4, P])

        def h4(v):
            return v.rearrange("p (h c) -> p h c", h=4)

        def da_pe(pe):
            d_pe.arm(pe)
            o_pe.arm(pe)
            for u in range(UN + 3):
                if u < UN:
                    t, h = divmod(u, H)
                    if u == 0:
                        all_taken(pe, len(JOBS["project"]) - 1)
                        pe.wait_ge(p_dve["kT4"], p_dve.after(0, "kT4"))
                    if u >= 2:
                        pe.wait_ge(d_act["p1"], d_act.after(u - 2, "p1"))
                    for m in range(2):
                        s = slice(64 * m, 64 * m + 64)
                        mm = nc.tensor.matmul(bank[2 * (u % 2) + m][:, 0:P * (t + 1)], dq[s, h, t * P:(t + 1) * P],
                                              dk[s, h, 0:P * (t + 1)], start=True, stop=True)
                    mm.then_inc(d_pe.step("sc"), 1)
                if 1 <= u <= UN:
                    v = u - 1
                    t = v // H
                    pe.wait_ge(d_dve["a"], d_dve.after(v, "a"))
                    if v >= 2:
                        pe.wait_ge(d_act["aT"], d_act.after(v - 2, "aT"))
                    else:
                        pe.wait_ge(p_dve["kT4"], p_dve.after(0, "kT4"))
                    for k in range(t + 1):
                        mm = nc.tensor.transpose(bank[4 + v % 2][:, k * P:(k + 1) * P], prob[v % 2][:, 0, k * P:(k + 1) * P], ident)
                    mm.then_inc(d_pe.step("tr"), 1)
                if 2 <= u < UN + 2:
                    v = u - 2
                    t, h = divmod(v, H)
                    pe.wait_ge(d_act["aT"], d_act.after(v, "aT"))
                    if h == 0 and t >= 2:
                        pe.wait_ge(o_act["mix"], o_act.after(t - 2, "mix"))
                    if v == 0:
                        pe.wait_ge(p_dve["tt2"], p_dve.after(0, "tt2"))
                    for k in range(t + 1):
                        mm = nc.tensor.matmul(bank[6 + t % 2][:, h * P:(h + 1) * P], aT[v % 2][:, k * P:(k + 1) * P],
                                              dv[:, k, h * P:(h + 1) * P], start=k == 0, stop=k == t)
                    mm.then_inc(d_pe.step("pv"), 1)
                if u >= 3 and (u - 3) % H == H - 1:
                    t = (u - 3) // H
                    pe.wait_ge(o_dve["og"], o_dve.after(t, "og"))
                    for h in range(H):
                        mm = nc.tensor.transpose(quarters(bank[6 + t % 2])[:, h, :], on[:, h * P:(h + 1) * P], ident)
                    mm.then_inc(o_pe.step("oT"), 1)

        def da_dve(dve):
            d_dve.arm(dve)
            o_dve.arm(dve)
            for u in range(UN + 3):
                if u < UN:
                    t = u // H
                    dve.wait_ge(d_pe["sc"], d_pe.after(u, "sc"))
                    for m in range(2):
                        ins = nc.vector.memset(bank[2 * (u % 2) + m][0:64, P * t + 64:P * t + 128], -BIG)
                    ins.then_inc(d_dve.step("cut"), 1)
                    dve.wait_ge(d_dve["cut"], d_dve.after(u, "cut"))
                    for m in range(2):
                        ins = nc.vector.tensor_reduce(nmax[u % 2][:, m:m + 1], bank[2 * (u % 2) + m][:, 0:P * (t + 1)],
                                                      AX.X, ALU.max, negate=True)
                    ins.then_inc(d_dve.step("mx"), 1)
                if 1 <= u <= UN:
                    v = u - 1
                    n = P * (v // H + 1)
                    q = v % 2
                    dve.wait_ge(d_act["p1"], d_act.after(v, "p1"))
                    nc.vector.reciprocal(pr[q], psum_p[q]).then_inc(d_dve.step("r"), 1)
                    dve.wait_ge(d_dve["r"], d_dve.after(v, "r"))
                    nc.vector.tensor_tensor(pr[q][:, 1:2], pr[q][:, 1:2], nlam, ALU.mult).then_inc(d_dve.step("c2"), 1)
                    dve.wait_ge(d_dve["c2"], d_dve.after(v, "c2"))
                    nc.vector.tensor_scalar(prob[q][:, 0, 0:n], prob[q][:, 0, 0:n], pr[q][:, 0:1], None, ALU.mult).then_inc(d_dve.step("a0"), 1)
                    dve.wait_ge(d_dve["a0"], d_dve.after(v, "a0"))
                    nc.vector.scalar_tensor_tensor(prob[q][:, 0, 0:n], prob[q][:, 1, 0:n], pr[q][:, 1:2],
                                                              prob[q][:, 0, 0:n], ALU.mult, ALU.add).then_inc(d_dve.step("a"), 1)
                if u >= 3 and (u - 3) % H == H - 1:
                    t = (u - 3) // H
                    head_norm_dve(dve, o_dve, o_act, o_pool, t, bank[6 + t % 2], gdn_g[:, 0:128])

        def head_norm_dve(dve, s, s_act, s_pool, t, b, gain):
            dve.wait_ge(s_act["sq"], s_act.after(t, "sq"))
            nc.vector.tensor_reduce(oss, h4(osq), AX.X, ALU.add).then_inc(s.step("ss"), 1)
            dve.wait_ge(s_pool["rn"], s_pool.after(t, "rn"))
            nc.vector.tensor_tensor(h4(on), h4(b[:, :]), b4(oss), ALU.mult).then_inc(s.step("on"), 1)
            dve.wait_ge(s["on"], s.after(t, "on"))
            nc.vector.tensor_tensor(h4(on), h4(on), gain.unsqueeze(1).to_broadcast([P, 4, P]), ALU.mult).then_inc(s.step("og"), 1)

        def head_norm_pool(pool, s, s_dve, t):
            pool.wait_ge(s_dve["ss"], s_dve.after(t, "ss"))
            nc.gpsimd.tensor_scalar(oss, oss, 1.0 / P, EPS, ALU.mult, ALU.add).then_inc(s.step("ms"), 1)
            pool.wait_ge(s["ms"], s.after(t, "ms"))
            nc.gpsimd.tensor_tensor(oss, oss, C("minus_half")[:, 0:4], ALU.pow).then_inc(s.step("rn"), 1)

        def da_act(act):
            d_act.arm(act)
            o_act.arm(act)
            for u in range(UN + 3):
                if u < UN:
                    n = P * (u // H + 1)
                    q = u % 2
                    act.wait_ge(d_dve["mx"], d_dve.after(u, "mx"))
                    if u >= 2:
                        act.wait_ge(d_pe["tr"], d_pe.after(u - 2, "tr"))
                    for m in range(2):
                        nc.scalar.activation(prob[q][:, m, 0:n], bank[2 * q + m][:, 0:n], ACT.Exp,
                                                        bias=nmax[q][:, m:m + 1], accum_out=psum_p[q][:, m:m + 1]).then_inc(d_act.step(f"p{m}"), 1)
                if 1 <= u <= UN:
                    v = u - 1
                    n = P * (v // H + 1)
                    act.wait_ge(d_pe["tr"], d_pe.after(v, "tr"))
                    if v >= 2:
                        act.wait_ge(d_pe["pv"], d_pe.after(v - 2, "pv"))
                    nc.scalar.copy(aT[v % 2][:, 0:n], bank[4 + v % 2][:, 0:n]).then_inc(d_act.step("aT"), 1)
                if u >= 2 and (u - 2) % H == H - 1:
                    t = (u - 2) // H
                    act.wait_ge(d_pe["pv"], d_pe.after(u - 2, "pv"))
                    nc.scalar.activation(osq, bank[6 + t % 2][:, :], ACT.Square).then_inc(o_act.step("sq"), 1)
                if u >= 3 and (u - 3) % H == H - 1:
                    t = (u - 3) // H
                    act.wait_ge(o_pe["oT"], o_pe.after(t, "oT"))
                    nc.scalar.copy(act_a[:, 0:4, t * P:(t + 1) * P], quarters(bank[6 + t % 2])).then_inc(o_act.step("mix"), 1)

        def da_pool(pool):
            o_pool.arm(pool)
            c_pool.arm(pool)
            all_taken(pool, ORDER.index(("conv", 11, 1)))
            pool.wait_ge(p_dve["tail1"], p_dve.after(0, "tail1"))
            for m in range(12):
                conv_pool_one(pool, m)
                if m % 3 == 2:
                    head_norm_pool(pool, o_pool, o_dve, m // 3)

        KT = [act_b[:, 0:2048], act_b[:, 2048:4096]]

        class Streams:
            def __init__(self, tag, KT, buf, first_unit):
                self.tag, self.first_unit = tag, first_unit
                self.cross = tag == "x"
                self.pe = steps(tag + "s_pe", "f0 f1 f2 f3 sc | pT pv")
                self.dve = steps(tag + "s_dve", "q f1 f3 " + ("mx | r pn pT" if self.cross else "sn mx mx2 mxm | sum r c cm pT"))
                self.act = steps(tag + "s_act", "f0 f2 " + ("p | o" if self.cross else "p pn | o"))
                self.zero = steps(tag + "s_zero", "z0 z1")
                self.KT = KT
                at = [buf]

                def take(n):
                    at[0] += n
                    return scratch_of(self)[:, at[0] - n:at[0]]

                self.q = [take(256).rearrange("p (c r) -> p c r", r=32) for _ in range(2)]
                self.P = [take(640) for _ in range(2)]
                self.sn = take(128)
                self.aT = take(320)
                self.cm = [take(64) for _ in range(2)]
                self.o = take(512)
                assert at[0] <= 3072
                self.mx = [little(4) for _ in range(2)]
                self.sum = [little(4) for _ in range(2)]

        def scratch_of(s):
            return x_buf if s.tag == "da" else attn

        das = Streams("da", KT, 0, UNIT["da0"])
        xs = Streams("x", [attn[:, 3584:5632], attn[:, 5632:7680]], 0, UNIT["x0"])
        da_oT = das.o.rearrange("p (h t) -> p h t", h=H)

        def loop(eng, body):
            body((0, 0), None)
            with eng.Fori(0, NB // 2 - 1) as i:
                body((2 * i + 1, 1), (2 * i, 0))
                body((2 * i + 2, 0), (2 * i + 1, 1))
            body((NB - 1, 1), (NB - 2, 0))
            body(None, (NB - 1, 1))

        def kv_slot(s, k):
            w = W[:, (s.first_unit + k) % 2, 0:4096]
            if s.cross:
                return (w[:, 0:2048].rearrange("p (m c) -> p m c", m=2), w[:, 2048:4096].rearrange("p (m c) -> p m c", m=2))
            return (w[:, 0:2048].rearrange("p (t c) -> p t c", t=4), w[:, 2048:4096].rearrange("p (t c) -> p t c", t=4))

        def kv_base(s):
            return 0 if s.tag == "da" else 32 * (NB // 2)

        def streams_sync(sp, s, ck, cvv):

            def one(b, k):
                if isinstance(b, int) and b < 2:
                    n = s.first_unit + b - 2
                    sp.wait_ge(s_job, LAST_JOB[n] + 1)
                else:
                    sp.wait_ge(s.pe["pv"], s.pe.after(b - 2, "pv"))
                kk, vv = kv_slot(s, k)
                at = (b if isinstance(b, int) else bass.ds(b, 1))

                def src(c):
                    v = c[0][b] if isinstance(b, int) else c[0][bass.ds(b, 1)].rearrange("o t h c -> (o t) h c")
                    return v.rearrange("(t p) h c -> p t (h c)", p=P)

                q = s_kv[k]
                sp.dma_start(kk, src(ck)).then_inc(q, 16)
                sp.dma_start(vv, src(cvv)).then_inc(q, 16)

            one(0, 0)
            one(1, 1)
            with sp.Fori(1, NB // 2) as i:
                one(sp.snap(2 * i), 0)
                one(sp.snap(2 * i + 1), 1)

        def kv_wait(eng, s, b, k):
            eng.wait_ge(s_kv[k], (b - k) * 16 + 32 + kv_base(s))

        def streams_pe(pe, s, ready):
            s.pe.arm(pe)
            ready(pe)
            x_ = s.cross

            def first(b, k):
                kk, _ = kv_slot(s, k)
                kv_wait(pe, s, b, k)
                for f in range(4):
                    if f == 0:
                        pe.wait_ge(s.act["f2"], s.act.after(b - 1, "f2"))
                    elif f == 1:
                        pe.wait_ge(s.dve["f3"], s.dve.after(b - 1, "f3"))
                    elif f == 2:
                        pe.wait_ge(s.act["f0"], s.act.after(b, "f0"))
                    else:
                        pe.wait_ge(s.dve["f1"], s.dve.after(b, "f1"))
                    for i in range(4):
                        src = kk[:, i % 2, (2 * f + i // 2) * P:(2 * f + i // 2 + 1) * P] if x_ else kk[:, i, f * P:(f + 1) * P]
                        mm = nc.tensor.transpose(quarters(bank[f % 2])[:, i, :], src, ident)
                    mm.then_inc(s.pe.step(f"f{f}"), 1)
                pe.wait_ge(s.act["f2"], s.act.after(b, "f2"))
                pe.wait_ge(s.dve["f3"], s.dve.after(b, "f3"))
                pe.wait_ge(s.act["p" if x_ else "pn"], s.act.after(b - 1, "p" if x_ else "pn"))
                if x_:
                    kt = s.KT[k].rearrange("p (c m) -> p c m", c=8)
                    for h in range(H):
                        for c in range(2):
                            mm = nc.tensor.matmul(bank[2][32 * h:32 * h + 32, 0:MEM], s.q[k][:, 2 * h + c, :], kt[:, 2 * h + c, :],
                                                  start=c == 0, stop=c == 1, skip_group_check=True)
                else:
                    kt = s.KT[k].rearrange("p (h m) -> p h m", h=H)
                    for h in range(H):
                        nc.tensor.matmul(bank[2][32 * h:32 * h + 32, :], s.q[k][:, h, :], kt[:, h, :], start=True, stop=True)
                        mm = nc.tensor.matmul(bank[3][32 * h:32 * h + 32, 0:P], s.q[k][:, h, :], dk[:, h, SEQ:], start=True, stop=True)
                mm.then_inc(s.pe.step("sc"), 1)

            def last(b, k):
                _, vv = kv_slot(s, k)
                pe.wait_ge(s.dve["pT"], s.dve.after(b - 1, "pT"))
                if x_:
                    pe.wait_ge(s.dve["pn"], s.dve.after(b, "pn"))
                    for m in range(2):
                        mm = nc.tensor.transpose(bank[4][:, m * P:(m + 1) * P], s.P[k][:, m * P:(m + 1) * P], ident)
                else:
                    pe.wait_ge(s.dve["cm"], s.dve.after(b, "cm"))
                    for c in range(5):
                        mm = nc.tensor.matmul(bank[4][:, 64 * c:64 * c + 64], s.P[k][:, c * P:(c + 1) * P], s.cm[k], start=True, stop=True)
                mm.then_inc(s.pe.step("pT"), 1)
                pe.wait_ge(s.dve["pT"], s.dve.after(b, "pT"))
                pe.wait_ge(s.act["o"], s.act.after(b - 1, "o"))
                if x_:
                    for c in range(8):
                        for m in range(2):
                            mm = nc.tensor.matmul(bank[5][:, 16 * c:16 * c + 16], vv[:, m, c * P:(c + 1) * P],
                                                  s.aT[:, m * P + 32 * (c // 2):m * P + 32 * (c // 2) + 16], start=m == 0, stop=m == 1)
                else:
                    for h in range(H):
                        for c in range(5):
                            v = vv[:, c, h * P:(h + 1) * P] if c < 4 else dv[:, 4, h * P:(h + 1) * P]
                            mm = nc.tensor.matmul(bank[5][:, 16 * h:16 * h + 16], v, s.aT[:, 64 * c + 16 * h:64 * c + 16 * h + 16],
                                                  start=c == 0, stop=c == 4)
                mm.then_inc(s.pe.step("pv"), 1)

            def body(f, l):
                if f:
                    first(*f)
                if l:
                    last(*l)

            loop(pe, body)

        def streams_dve(dve, s, ready):
            x_ = s.cross
            s.dve.arm(dve)
            ready(dve)
            s.zero.arm(dve)
            for k in range(2):
                nc.vector.memset(s.q[k], 0.0).then_inc(s.zero.step(f"z{k}"), 1)
                dve.wait_ge(s.zero[f"z{k}"], s.zero.after(0, f"z{k}"))

            def first(b, k):
                at = b * TB
                dve.wait_ge(s.pe["sc"], s.pe.after(b - 2, "sc"))
                if x_:
                    src = act_b[:, :].rearrange("p (c t) -> p c t", c=8)[:, :, bass.ds(at + SEQ, TB)]
                    nc.vector.tensor_copy(s.q[k][:, :, 0:16], src).then_inc(s.dve.step("q"), 1)
                else:
                    nc.vector.tensor_copy(s.q[k][0:64, 0:4, 0:16], dq[0:64, :, bass.ds(at + SEQ, TB)])
                    nc.vector.tensor_copy(s.q[k][64:128, 0:4, 16:32], dq[64:128, :, bass.ds(at + SEQ, TB)]).then_inc(s.dve.step("q"), 1)
                for f in (1, 3):
                    dve.wait_ge(s.pe[f"f{f}"], s.pe.after(b, f"f{f}"))
                    nc.vector.tensor_copy(s.KT[k][:, 512 * f:512 * f + 512], bank[f % 2][:, :]).then_inc(s.dve.step(f"f{f}"), 1)
                dve.wait_ge(s.pe["sc"], s.pe.after(b, "sc"))
                if x_:
                    nc.vector.tensor_reduce(s.mx[k][:, 0:1], bank[2][:, 0:MEM], AX.X, ALU.max, negate=True).then_inc(s.dve.step("mx"), 1)
                else:
                    w = C("stream_off")[:, bass.ds(b * P, P)]
                    dve.wait_ge(s.act["pn"], s.act.after(b - 1, "pn"))
                    nc.vector.tensor_tensor(s.sn, bank[3][:, 0:P], w, ALU.add).then_inc(s.dve.step("sn"), 1)
                    dve.wait_ge(s.dve["sn"], s.dve.after(b, "sn"))
                    nc.vector.tensor_reduce(s.mx[k][:, 1:2], bank[2][:, :], AX.X, ALU.max).then_inc(s.dve.step("mx"), 1)
                    nc.vector.tensor_reduce(s.mx[k][:, 2:3], s.sn, AX.X, ALU.max).then_inc(s.dve.step("mx2"), 1)
                    dve.wait_ge(s.dve["mx2"], s.dve.after(b, "mx2"))
                    nc.vector.scalar_tensor_tensor(s.mx[k][:, 0:1], s.mx[k][:, 1:2], s.mx[k][:, 2:3], C("minus_one"),
                                                              ALU.max, ALU.mult).then_inc(s.dve.step("mxm"), 1)

            def last(b, k):
                if x_:
                    dve.wait_ge(s.act["p"], s.act.after(b, "p"))
                    nc.vector.reciprocal(s.sum[k][:, 0:1], s.sum[k][:, 0:1]).then_inc(s.dve.step("r"), 1)
                    dve.wait_ge(s.dve["r"], s.dve.after(b, "r"))
                    nc.vector.tensor_scalar(s.P[k][:, 0:MEM], s.P[k][:, 0:MEM], s.sum[k][:, 0:1], None, ALU.mult).then_inc(s.dve.step("pn"), 1)
                else:
                    dve.wait_ge(s.act["pn"], s.act.after(b, "pn"))
                    nc.vector.tensor_tensor(s.sum[k][:, 2:3], s.sum[k][:, 0:1], s.sum[k][:, 1:2], ALU.add).then_inc(s.dve.step("sum"), 1)
                    dve.wait_ge(s.dve["sum"], s.dve.after(b, "sum"))
                    nc.vector.reciprocal(s.sum[k][:, 3:4], s.sum[k][:, 2:3]).then_inc(s.dve.step("r"), 1)
                    dve.wait_ge(s.dve["r"], s.dve.after(b, "r"))
                    nc.vector.tensor_tensor(s.sum[k][:, 2:3], s.sum[k][:, 3:4], row_sign, ALU.mult).then_inc(s.dve.step("c"), 1)
                    dve.wait_ge(s.dve["c"], s.dve.after(b, "c"))
                    nc.vector.tensor_scalar(s.cm[k], C("pick"), s.sum[k][:, 2:3], None, ALU.mult).then_inc(s.dve.step("cm"), 1)
                dve.wait_ge(s.pe["pT"], s.pe.after(b, "pT"))
                n = MEM if x_ else 320
                nc.vector.tensor_copy(s.aT[:, 0:n], bank[4][:, 0:n]).then_inc(s.dve.step("pT"), 1)

            def body(f, l):
                if f:
                    first(*f)
                if l:
                    last(*l)

            loop(dve, body)

        def streams_act(act, s, ready):
            x_ = s.cross
            s.act.arm(act)
            ready(act)

            def first(b, k):
                for f in (0, 2):
                    act.wait_ge(s.pe[f"f{f}"], s.pe.after(b, f"f{f}"))
                    if f == 0:
                        act.wait_ge(s.pe["sc"], s.pe.after(b - 2, "sc"))
                    nc.scalar.copy(s.KT[k][:, 512 * f:512 * f + 512], bank[f % 2][:, :]).then_inc(s.act.step(f"f{f}"), 1)
                act.wait_ge(s.pe["pT"], s.pe.after(b - 2, "pT"))
                if x_:
                    act.wait_ge(s.dve["mx"], s.dve.after(b, "mx"))
                    nc.scalar.activation(s.P[k][:, 0:MEM], bank[2][:, 0:MEM], ACT.Exp, bias=s.mx[k][:, 0:1], scale=1.0,
                                                    accum_out=s.sum[k][:, 0:1]).then_inc(s.act.step("p"), 1)
                else:
                    act.wait_ge(s.dve["mxm"], s.dve.after(b, "mxm"))
                    nc.scalar.activation(s.P[k][:, 0:512], bank[2][:, :], ACT.Exp, bias=s.mx[k][:, 0:1],
                                                    accum_out=s.sum[k][:, 0:1]).then_inc(s.act.step("p"), 1)
                    nc.scalar.activation(s.P[k][:, 512:640], s.sn, ACT.Exp, bias=s.mx[k][:, 0:1],
                                                    accum_out=s.sum[k][:, 1:2]).then_inc(s.act.step("pn"), 1)

            def last(b, k):
                act.wait_ge(s.pe["pv"], s.pe.after(b, "pv"))
                dst = act_a if x_ else da_oT
                n = 8 if x_ else 4
                cols = bass.ds(b * TB + (SEQ if x_ else 0), TB)
                nc.scalar.copy(dst[:, 0:n, cols], bank[5][:, 0:16 * n].rearrange("p (c t) -> p c t", c=n)).then_inc(s.act.step("o"), 1)

            def body(f, l):
                if f:
                    first(*f)
                if l:
                    last(*l)

            loop(act, body)

        t_pe = steps("da_s_pe", "turn oT")
        t_act = steps("da_s_act", "sq mix")
        t_dve = steps("da_s_dve", "ss on og")
        t_pool = steps("da_s_pool", "ms rn")

        def das_out_pe(pe):
            t_pe.arm(pe)
            pe.wait_ge(das.act["o"], das.act.after(NB - 1, "o"))
            for h in range(H):
                mm = nc.tensor.transpose(quarters(bank[6])[:, h, :], da_oT[:, h, :], ident)
            mm.then_inc(t_pe.step("turn"), 1)
            pe.wait_ge(t_dve["og"], t_dve.after(0, "og"))
            for h in range(H):
                mm = nc.tensor.transpose(quarters(bank[7])[:, h, :], on[:, h * P:(h + 1) * P], ident)
            mm.then_inc(t_pe.step("oT"), 1)

        def das_out_act(act):
            t_act.arm(act)
            act.wait_ge(t_pe["turn"], t_pe.after(0, "turn"))
            nc.scalar.activation(osq, bank[6][:, :], ACT.Square).then_inc(t_act.step("sq"), 1)
            act.wait_ge(t_pe["oT"], t_pe.after(0, "oT"))
            nc.scalar.copy(act_a[:, 0:4, SEQ:], quarters(bank[7])).then_inc(t_act.step("mix"), 1)

        g_act, g_pe, g_dve, g_pool = (steps("gdn_" + e, n) for e, n in
                                      (("act", GDN_ACT), ("pe", GDN_PE), ("dve", GDN_DVE), ("pool", GDN_POOL)))
        gs_act, gs_pe, gs_dve, gs_pool = (steps("gdn_s_" + e, n) for e, n in (
            ("act", "stage0 stage1 stage2 sq0 sq1 EG eg D DT qT Mt M2 M2t M4 M4t M8 w osq mix"),
            ("pe", "tokqk tokv cum gcum chq chk kk kq Mt sq2 sq2t x1 sq4 sq4t x2 sq8 x3 w oT"),
            ("dve", "gb gB gc S SD SU ss ssq qk0 qk1 kT vb be kbg kl ktail L0 L AT M X0 X1 X2 X3 qd oss oms on og oz"),
            ("pool", GDN_POOL)))
        gh_pe = steps("gdn_state_pe", "vn o s")
        gh_dve = steps("gdn_state_dve", "wM qM vn vM sg s0 s1")
        s_state = sem("states_loaded")

        stage = attn[:, 0:1536].rearrange("p (m t) -> p m t", m=12)
        qk_tok = attn[:, 1536:2560]
        qT, kT, vb, kbg, ktail, EG, SD, DT, S_, AT = (attn[:, 2560 + 512 * i:3072 + 512 * i] for i in range(10))
        gB, L, M, Mt, M2, M2t, X, Bm, T_, Wb = (x_buf[:, 512 * i:512 * i + 512] for i in range(10))
        scr_ = scr[:, :, :].rearrange("p a b -> p (a b)")
        wTn, qdT, vnew, gon, gsq = (scr_[:, 512 * i:512 * i + 512] for i in range(5))
        gsq2 = scr_[:, 2048:3072]
        state = act_b[:, 4096:4608]
        states = act_b[:, 0:4096].rearrange("p (h b v) -> p h b v", h=H, b=NB)
        wM = attn[:, 0:1024].rearrange("p (b t) -> p b t", b=NB)
        qM = qk_tok.rearrange("p (b t) -> p b t", b=NB)
        vM = x_buf[:, 1024:2048].rearrange("p (b t) -> p b t", b=NB)
        g_t, b_t, gc, eg, be, kl, goss = (little(4) for _ in range(7))
        rqk = little(8)

        def m4(name):
            return C(name, 4)

        def mul4(pe, out, lhs, rhs, start=True, stop=True):
            for h in range(H):
                mm = nc.tensor.matmul(quarters(out)[:, h, :], h4(lhs)[:, h, :], h4(rhs)[:, h, :], start=start, stop=stop)
            return mm

        def turn4(pe, out, src):
            for h in range(H):
                mm = nc.tensor.transpose(quarters(out)[:, h, :], h4(src)[:, h, :], ident)
            return mm

        def gdn_pe_tile(pe, t, sample):
            s, sa, sd = (gs_pe, gs_act, gs_dve) if sample else (g_pe, g_act, g_dve)
            cum = C("cum_s" if sample else "cum_p")
            pe.wait_ge(sa["stage2" if sample else "stage"], sa.after(t, "stage2" if sample else "stage"))
            pe.wait_ge(sd["s" if not sample else "oz"], sd.after(t - 1, "s" if not sample else "oz"))
            pe.wait_ge(sa["mix"], sa.after(t - 1, "mix"))
            for i in range(8):
                mm = nc.tensor.transpose(quarters(bank[i // 4])[:, i % 4, :], stage[:, i, :], ident)
            mm.then_inc(s.step("tokqk"), 1)
            for i in range(4):
                mm = nc.tensor.transpose(quarters(bank[2])[:, i, :], stage[:, 8 + i, :], ident)
            mm.then_inc(s.step("tokv"), 1)
            pe.wait_ge(sd["gB"], sd.after(t, "gB"))
            nc.tensor.matmul(bank[3][:, 0:4], cum, g_t, start=True, stop=True).then_inc(s.step("cum"), 1)
            for h in range(H):
                mm = nc.tensor.matmul(quarters(bank[4])[:, h, :], h4(gB)[:, h, :], cum, start=True, stop=True)
            mm.then_inc(s.step("gcum"), 1)
            pe.wait_ge(sd["qk1"], sd.after(t, "qk1"))
            turn4(pe, bank[0], qk_tok[:, 0:512]).then_inc(s.step("chq"), 1)
            turn4(pe, bank[1], qk_tok[:, 512:1024]).then_inc(s.step("chk"), 1)
            pe.wait_ge(sd["kT"], sd.after(t, "kT"))
            pe.wait_ge(sd["S"], sd.after(t, "S"))
            pe.wait_ge(sa["qT"], sa.after(t, "qT"))
            mul4(pe, bank[3], kT, kT).then_inc(s.step("kk"), 1)
            mul4(pe, bank[4], kT, qT).then_inc(s.step("kq"), 1)
            pe.wait_ge(sd["M"], sd.after(t, "M"))
            turn4(pe, bank[5], M).then_inc(s.step("Mt"), 1)
            pe.wait_ge(sa["Mt"], sa.after(t, "Mt"))
            mul4(pe, bank[6], Mt, M).then_inc(s.step("sq2"), 1)
            mul4(pe, bank[7], M, Mt).then_inc(s.step("sq2t"), 1)
            pe.wait_ge(sd["X0"], sd.after(t, "X0"))
            pe.wait_ge(sa["M2t"], sa.after(t, "M2t"))
            mul4(pe, bank[5], M2, X).then_inc(s.step("x1"), 1)
            mul4(pe, bank[6], M2t, M2).then_inc(s.step("sq4"), 1)
            mul4(pe, bank[7], M2, M2t).then_inc(s.step("sq4t"), 1)
            pe.wait_ge(sd["X1"], sd.after(t, "X1"))
            pe.wait_ge(sa["M4t"], sa.after(t, "M4t"))
            mul4(pe, bank[5], M, X).then_inc(s.step("x2"), 1)
            mul4(pe, bank[6], Mt, M).then_inc(s.step("sq8"), 1)
            pe.wait_ge(sd["X2"], sd.after(t, "X2"))
            pe.wait_ge(sa["M8"], sa.after(t, "M8"))
            mul4(pe, bank[5], M2, X).then_inc(s.step("x3"), 1)
            if not sample:
                for l in range(3):
                    pe.wait_ge(sd[f"B{l}"], sd.after(t, f"B{l}"))
                    if l == 0:
                        pe.wait_ge(sd["X3"], sd.after(t, "X3"))
                    turn4(pe, bank[6], X).then_inc(s.step(f"T{l}"), 1)
                    mul4(pe, bank[7], Bm, X).then_inc(s.step(f"BX{l}"), 1)
                    pe.wait_ge(sa[f"T{l}"], sa.after(t, f"T{l}"))
                    pe.wait_ge(sd[f"W{l}"], sd.after(t, f"W{l}"))
                    mul4(pe, bank[5], T_, Wb).then_inc(s.step(f"Y{l}"), 1)
            pe.wait_ge(sd["X3" if sample else "Y2"], sd.after(t, "X3" if sample else "Y2"))
            pe.wait_ge(sa["M8"], sa.after(t, "M8"))
            mul4(pe, bank[6], kbg, X).then_inc(s.step("w"), 1)

        def gdn_pe_prompt(pe):
            g_pe.arm(pe)

            def tile(t):
                gdn_pe_tile(pe, t, False)
                pe.wait_ge(g_act["w"], g_act.after(t, "w"))
                mm = None
                for h in range(H):
                    nc.tensor.matmul(quarters(bank[7])[:, h, :], h4(X)[:, h, :], h4(vb)[:, h, :], start=True, stop=False)
                    mm = nc.tensor.matmul(quarters(bank[7])[:, h, :], h4(wTn)[:, h, :], h4(state)[:, h, :], start=False, stop=True)
                mm.then_inc(g_pe.step("vn"), 1)
                pe.wait_ge(g_dve["vn"], g_dve.after(t, "vn"))
                for h in range(H):
                    nc.tensor.matmul(quarters(bank[0])[:, h, :], h4(qdT)[:, h, :], h4(state)[:, h, :], start=True, stop=False)
                    mm = nc.tensor.matmul(quarters(bank[0])[:, h, :], h4(AT)[:, h, :], h4(vnew)[:, h, :], start=False, stop=True)
                mm.then_inc(g_pe.step("o"), 1)
                mul4(pe, bank[1], ktail, vnew).then_inc(g_pe.step("s"), 1)
                pe.wait_ge(g_dve["oz"], g_dve.after(t, "oz"))
                turn4(pe, bank[2], gon).then_inc(g_pe.step("oT"), 1)

            with pe.Fori(0, NTP) as t:
                tile(t)

        def gdn_pe_sample(pe):
            gs_pe.arm(pe)
            gh_pe.arm(pe)
            pe.wait_ge(g_act["mix"], g_act.after(NTP - 1, "mix"))
            gdn_pe_tile(pe, 0, True)
            pe.wait_ge(s_state, 16 * H)
            for h in range(H):
                pe.wait_ge(gh_dve["qM"], gh_dve.after(h, "qM"))
                nc.tensor.matmul(quarters(bank[7])[:, h, :], h4(X)[:, h, :], h4(vb)[:, h, :], start=True, stop=False)
                for b in range(NB):
                    mm = nc.tensor.matmul(quarters(bank[7])[:, h, :], wM[:, b, :], states[:, h, b, :], start=False, stop=b == NB - 1)
                mm.then_inc(gh_pe.step("vn"), 1)
                pe.wait_ge(gh_dve["vM"], gh_dve.after(h, "vM"))
                for b in range(NB):
                    nc.tensor.matmul(quarters(bank[0])[:, h, :], qM[:, b, :], states[:, h, b, :], start=b == 0, stop=False)
                mm = nc.tensor.matmul(quarters(bank[0])[:, h, :], h4(AT)[:, h, :], h4(vnew)[:, h, :], start=False, stop=True)
                mm.then_inc(gh_pe.step("o"), 1)
                pe.wait_ge(gh_dve["s1"], gh_dve.after(h - 1, "s1"))
                for i in range(2):
                    mm = nc.tensor.matmul(bank[3 + i][:, :], h4(ktail)[:, h, :], vM[:, 4 * i:4 * i + 4, :], start=True, stop=True)
                mm.then_inc(gh_pe.step("s"), 1)
            pe.wait_ge(gs_dve["oz"], gs_dve.after(0, "oz"))
            turn4(pe, bank[2], gon).then_inc(gs_pe.step("oT"), 1)

        def tile_cols(t):
            return bass.ds(t * P, P) if not isinstance(t, int) else slice(t * P, t * P + P)

        def gdn_act_tile(act, t, sample):
            s, sp_, sd, spo = (gs_act, gs_pe, gs_dve, gs_pool) if sample else (g_act, g_pe, g_dve, g_pool)
            if sample:
                for i in range(3):
                    src = cv[:, 4 * i:4 * i + 4, GS:GW].rearrange("p m (b c) -> p m b c", b=NB)[:, :, :, 0:TB]
                    nc.scalar.copy(stage[:, 4 * i:4 * i + 4, :].rearrange("p m (b c) -> p m b c", b=NB), src).then_inc(s.step(f"stage{i}"), 1)
            else:
                act.wait_ge(sp_["tokv"], sp_.after(t - 1, "tokv"))
                nc.scalar.copy(stage[:, :, :], cv[:, :, tile_cols(t)]).then_inc(s.step("stage"), 1)
            act.wait_ge(sp_["tokqk"], sp_.after(t, "tokqk"))
            nc.scalar.activation(gsq2[:, 0:512], bank[0][:, :], ACT.Square).then_inc(s.step("sq0"), 1)
            nc.scalar.activation(gsq2[:, 512:1024], bank[1][:, :], ACT.Square).then_inc(s.step("sq1"), 1)
            act.wait_ge(sp_["gcum"], sp_.after(t, "gcum"))
            nc.scalar.activation(EG, bank[4][:, :], ACT.Exp).then_inc(s.step("EG"), 1)
            act.wait_ge(sd["gc"], sd.after(t, "gc"))
            nc.scalar.activation(eg, gc, ACT.Exp).then_inc(s.step("eg"), 1)
            act.wait_ge(sd["SU"], sd.after(t, "SU"))
            nc.scalar.activation(SD, SD, ACT.Exp).then_inc(s.step("D"), 1)
            nc.scalar.activation(DT, DT, ACT.Exp).then_inc(s.step("DT"), 1)
            act.wait_ge(sp_["chq"], sp_.after(t, "chq"))
            nc.scalar.copy(qT, bank[0][:, :]).then_inc(s.step("qT"), 1)
            act.wait_ge(sp_["Mt"], sp_.after(t, "Mt"))
            nc.scalar.copy(Mt, bank[5][:, :]).then_inc(s.step("Mt"), 1)
            for n in ("sq2", "sq4"):
                act.wait_ge(sp_[n], sp_.after(t, n))
                nc.scalar.copy(M2 if n == "sq2" else M, bank[6][:, :]).then_inc(s.step("M2" if n == "sq2" else "M4"), 1)
                act.wait_ge(sp_[n + "t"], sp_.after(t, n + "t"))
                nc.scalar.copy(M2t if n == "sq2" else Mt, bank[7][:, :]).then_inc(s.step("M2t" if n == "sq2" else "M4t"), 1)
            act.wait_ge(sp_["sq8"], sp_.after(t, "sq8"))
            nc.scalar.copy(M2, bank[6][:, :]).then_inc(s.step("M8"), 1)
            if not sample:
                for l in range(3):
                    act.wait_ge(sp_[f"T{l}"], sp_.after(t, f"T{l}"))
                    nc.scalar.copy(T_, bank[6][:, :]).then_inc(s.step(f"T{l}"), 1)
            act.wait_ge(sp_["w"], sp_.after(t, "w"))
            nc.scalar.copy(wTn, bank[6][:, :]).then_inc(s.step("w"), 1)
            if sample:
                act.wait_ge(gh_pe["o"], gh_pe.after(H - 1, "o"))
            else:
                act.wait_ge(sp_["o"], sp_.after(t, "o"))
            nc.scalar.activation(gsq, bank[0][:, :], ACT.Square).then_inc(s.step("osq"), 1)
            act.wait_ge(sp_["oT"], sp_.after(t, "oT"))
            dst = act_a[:, 4:8, SEQ:] if sample else act_a[:, 4:8, tile_cols(t)]
            nc.scalar.copy(dst, quarters(bank[2])).then_inc(s.step("mix"), 1)

        def gdn_act(act):
            g_act.arm(act)
            gs_act.arm(act)
            with act.Fori(0, NTP) as t:
                gdn_act_tile(act, t, False)
            gdn_act_tile(act, 0, True)

        def gdn_pool(pool):
            for s, sd, n in ((g_pool, g_dve, NTP), (gs_pool, gs_dve, 1)):
                s.arm(pool)

                def tile(t):
                    pool.wait_ge(sd["ssq"], sd.after(t, "ssq"))
                    nc.gpsimd.tensor_tensor(rqk, rqk, C("minus_half"), ALU.pow).then_inc(s.step("rn"), 1)
                    pool.wait_ge(sd["oms"], sd.after(t, "oms"))
                    nc.gpsimd.tensor_tensor(goss, goss, C("minus_half")[:, 0:4], ALU.pow).then_inc(s.step("orn"), 1)

                if n == 1:
                    tile(0)
                else:
                    with pool.Fori(0, n) as t:
                        tile(t)

        def gdn_dve_tile(dve, t, sample):
            s, sp_, sa, spo = (gs_dve, gs_pe, gs_act, gs_pool) if sample else (g_dve, g_pe, g_act, g_pool)
            sfx = "_s" if sample else "_p"
            tt = nc.vector.tensor_tensor
            gcols = slice(4 * (NT - 1), 4 * NT) if sample else bass.ds(t * 4, 4)
            nc.vector.tensor_copy(b_t, beta[:, gcols])
            nc.vector.tensor_copy(g_t, glog[:, gcols]).then_inc(s.step("gb"), 1)
            dve.wait_ge(s["gb"], s.after(t, "gb"))
            dve.wait_ge(sp_["gcum"], sp_.after(t - 1, "gcum"))
            nc.vector.tensor_copy(h4(gB), b4(g_t)).then_inc(s.step("gB"), 1)
            dve.wait_ge(sp_["gcum"], sp_.after(t, "gcum"))
            nc.vector.tensor_copy(gc, bank[3][:, 0:4]).then_inc(s.step("gc"), 1)
            dve.wait_ge(s["gc"], s.after(t, "gc"))
            dve.wait_ge(sa["eg"], sa.after(t, "eg"))
            tt(h4(S_), quarters(bank[4]), b4(gc), ALU.subtract).then_inc(s.step("S"), 1)
            dve.wait_ge(s["S"], s.after(t, "S"))
            tt(h4(SD), m4("low" + sfx), h4(S_), ALU.subtract).then_inc(s.step("SD"), 1)
            tt(h4(DT), m4("up" + sfx), h4(S_), ALU.add).then_inc(s.step("SU"), 1)
            dve.wait_ge(sa["sq1"], sa.after(t, "sq1"))
            nc.vector.tensor_reduce(rqk, gsq2.rearrange("p (h c) -> p h c", h=8), AX.X, ALU.add).then_inc(s.step("ss"), 1)
            dve.wait_ge(s["ss"], s.after(t, "ss"))
            nc.vector.scalar_tensor_tensor(rqk, rqk, EPS, C("qk_scale"), ALU.add, ALU.mult).then_inc(s.step("ssq"), 1)
            dve.wait_ge(spo["rn"], spo.after(t, "rn"))
            tt(h4(qk_tok[:, 0:512]), quarters(bank[0]), b4(rqk[:, 0:4]), ALU.mult).then_inc(s.step("qk0"), 1)
            tt(h4(qk_tok[:, 512:1024]), quarters(bank[1]), b4(rqk[:, 4:8]), ALU.mult).then_inc(s.step("qk1"), 1)
            dve.wait_ge(sp_["chk"], sp_.after(t, "chk"))
            nc.vector.tensor_copy(kT, bank[1][:, :]).then_inc(s.step("kT"), 1)
            tt(h4(vb), quarters(bank[2]), b4(b_t), ALU.mult).then_inc(s.step("vb"), 1)
            nc.vector.scalar_tensor_tensor(be, b_t, -1.0, eg, ALU.mult, ALU.mult).then_inc(s.step("be"), 1)
            dve.wait_ge(s["be"], s.after(t, "be"))
            tt(h4(kbg), h4(qk_tok[:, 512:1024]), b4(be), ALU.mult).then_inc(s.step("kbg"), 1)
            dve.wait_ge(sa["DT"], sa.after(t, "DT"))
            if sample:
                last = h4(DT)[:, :, TB - 1:P:TB]
                nc.vector.tensor_reduce(kl, last, AX.X, ALU.add).then_inc(s.step("kl"), 1)
                dve.wait_ge(s["kl"], s.after(t, "kl"))
            else:
                nc.vector.tensor_copy(kl, h4(DT)[:, :, P - 1]).then_inc(s.step("kl"), 1)
                dve.wait_ge(s["kl"], s.after(t, "kl"))
            tt(h4(ktail), h4(qk_tok[:, 512:1024]), b4(kl), ALU.mult).then_inc(s.step("ktail"), 1)
            dve.wait_ge(sp_["kk"], sp_.after(t, "kk"))
            tt(h4(L), quarters(bank[3]), h4(SD), ALU.mult).then_inc(s.step("L0"), 1)
            dve.wait_ge(s["L0"], s.after(t, "L0"))
            tt(h4(L), h4(L), b4(b_t), ALU.mult).then_inc(s.step("L"), 1)
            dve.wait_ge(s["L"], s.after(t, "L"))
            dve.wait_ge(sp_["kq"], sp_.after(t, "kq"))
            tt(h4(AT), quarters(bank[4]), h4(DT), ALU.mult).then_inc(s.step("AT"), 1)
            tt(h4(M), h4(L), m4("blk16"), ALU.mult).then_inc(s.step("M"), 1)
            if not sample:
                tt(h4(Bm), h4(L), m4("lev32"), ALU.mult).then_inc(s.step("B0"), 1)
            dve.wait_ge(sp_["Mt"], sp_.after(t, "Mt"))
            dve.wait_ge(sa["Mt"], sa.after(t, "Mt"))
            tt(h4(X), m4("ident"), quarters(bank[5]), ALU.subtract).then_inc(s.step("X0"), 1)
            for i in (1, 2, 3):
                dve.wait_ge(sp_[f"x{i}"], sp_.after(t, f"x{i}"))
                tt(h4(X), h4(X), quarters(bank[5]), ALU.add).then_inc(s.step(f"X{i}"), 1)
            if not sample:
                for l in range(3):
                    if l:
                        dve.wait_ge(sp_[f"BX{l - 1}"], sp_.after(t, f"BX{l - 1}"))
                        tt(h4(Bm), h4(L), m4(f"lev{32 << l}"), ALU.mult).then_inc(s.step(f"B{l}"), 1)
                    dve.wait_ge(sp_[f"BX{l}"], sp_.after(t, f"BX{l}"))
                    nc.vector.tensor_copy(Wb, bank[7][:, :]).then_inc(s.step(f"W{l}"), 1)
                    dve.wait_ge(sp_[f"Y{l}"], sp_.after(t, f"Y{l}"))
                    tt(h4(X), h4(X), quarters(bank[5]), ALU.subtract).then_inc(s.step(f"Y{l}"), 1)
            dve.wait_ge(sa["qT"], sa.after(t, "qT"))
            tt(qdT, qT, EG, ALU.mult).then_inc(s.step("qd"), 1)
            if not sample:
                dve.wait_ge(sp_["vn"], sp_.after(t, "vn"))
                nc.vector.tensor_copy(vnew, bank[7][:, :]).then_inc(s.step("vn"), 1)
                dve.wait_ge(sp_["o"], sp_.after(t, "o"))
                tt(h4(state), h4(state), b4(h4(EG)[:, :, P - 1]), ALU.mult).then_inc(s.step("sg"), 1)
                dve.wait_ge(s["sg"], s.after(t, "sg"))
                dve.wait_ge(sp_["s"], sp_.after(t, "s"))
                tt(state, state, bank[1][:, :], ALU.add).then_inc(s.step("s"), 1)
            else:
                gdn_dve_states(dve)
            dve.wait_ge(sa["osq"], sa.after(t, "osq"))
            nc.vector.tensor_reduce(goss, h4(gsq), AX.X, ALU.add).then_inc(s.step("oss"), 1)
            dve.wait_ge(s["oss"], s.after(t, "oss"))
            nc.vector.tensor_scalar(goss, goss, 1.0 / P, EPS, ALU.mult, ALU.add).then_inc(s.step("oms"), 1)
            dve.wait_ge(spo["orn"], spo.after(t, "orn"))
            tt(h4(gon), quarters(bank[0]), b4(goss), ALU.mult).then_inc(s.step("on"), 1)
            dve.wait_ge(s["on"], s.after(t, "on"))
            tt(h4(gon), h4(gon), gdn_g[:, 128:256].unsqueeze(1).to_broadcast([P, 4, P]), ALU.mult).then_inc(s.step("og"), 1)
            dve.wait_ge(s["og"], s.after(t, "og"))
            gate = gz[:, NT - 1, :] if sample else gz[:, bass.ds(t, 1), :].rearrange("p o c -> p (o c)")
            tt(gon, gon, gate, ALU.mult).then_inc(s.step("oz"), 1)

        def gdn_dve_states(dve):
            gh_dve.arm(dve)
            tt = nc.vector.tensor_tensor
            dve.wait_ge(gs_dve["qd"], gs_dve.after(0, "qd"))
            dve.wait_ge(gs_act["w"], gs_act.after(0, "w"))
            dve.wait_ge(s_state, 16 * H)
            off = C("stream_off").rearrange("p (b t) -> p b t", b=NB)
            for h in range(H):
                def over(v):
                    return h4(v)[:, h, :].unsqueeze(1).to_broadcast([P, NB, P])

                dve.wait_ge(gh_pe["vn"], gh_pe.after(h - 1, "vn"))
                nc.vector.scalar_tensor_tensor(wM, off, 0.0, over(wTn), ALU.is_equal, ALU.mult).then_inc(gh_dve.step("wM"), 1)
                dve.wait_ge(gh_pe["o"], gh_pe.after(h - 1, "o"))
                nc.vector.scalar_tensor_tensor(qM, off, 0.0, over(qdT), ALU.is_equal, ALU.mult).then_inc(gh_dve.step("qM"), 1)
                dve.wait_ge(gh_pe["vn"], gh_pe.after(h, "vn"))
                nc.vector.tensor_copy(h4(vnew)[:, h, :], quarters(bank[7])[:, h, :]).then_inc(gh_dve.step("vn"), 1)
                dve.wait_ge(gh_dve["vn"], gh_dve.after(h, "vn"))
                dve.wait_ge(gh_pe["s"], gh_pe.after(h - 1, "s"))
                tt(vM, over(vnew), C("stream_row").unsqueeze(2).to_broadcast([P, NB, P]), ALU.mult).then_inc(gh_dve.step("vM"), 1)
                dve.wait_ge(gh_pe["o"], gh_pe.after(h, "o"))
                last = h4(EG)[:, h, TB - 1:P:TB].unsqueeze(2).to_broadcast([P, NB, P])
                tt(states[:, h, :, :], states[:, h, :, :], last, ALU.mult).then_inc(gh_dve.step("sg"), 1)
                dve.wait_ge(gh_dve["sg"], gh_dve.after(h, "sg"))
                dve.wait_ge(gh_pe["s"], gh_pe.after(h, "s"))
                for i in range(2):
                    o = states[:, h, 4 * i:4 * i + 4, :]
                    tt(o, o, quarters(bank[3 + i]), ALU.add).then_inc(gh_dve.step(f"s{i}"), 1)

        def gdn_dve(dve):
            g_dve.arm(dve)
            gs_dve.arm(dve)
            g0.arm(dve)
            nc.vector.memset(state, 0.0).then_inc(g0.step("state"), 1)
            dve.wait_ge(g0["state"], g0.after(0, "state"))
            with dve.Fori(0, NTP) as t:
                gdn_dve_tile(dve, t, False)
            gdn_dve_tile(dve, 0, True)

        g0 = steps("gdn_state_zero", "state")

        mem_rows = act_b[:, 2048:4096].rearrange("p (t d) -> p t d", t=2)
        mem_act = act_b[:, 0:2048].rearrange("p (c t) -> p c t", c=KC)
        mk_tok = conv[:, 0:2048].rearrange("p (t d) -> p t d", t=2)
        mkT = conv[:, 2048:4096].rearrange("p (c m) -> p c m", c=KC)
        mv = conv[:, 4096:6144].rearrange("p (t d) -> p t d", t=2)
        m_pe = steps("mem_pe", "t0 t1 t2 t3")
        m_dve = steps("mem_dve", "t0 t1 t2 t3")
        s_mem = sem("memory_rows_loaded")
        s_xback = sem("x_reloaded")

        def mem_turn_pe(pe):
            m_pe.arm(pe)
            all_taken(pe, LAST_OF["mk"])
            for g in range(4):
                pe.wait_ge(n_dve["mem"]["ev1b"], n_dve["mem"].after(0, "ev1b"))
                if g >= 2:
                    pe.wait_ge(m_dve[f"t{g - 2}"], m_dve.after(0, f"t{g - 2}"))
                for i in range(4):
                    c, m = 2 * g + i // 2, i % 2
                    mm = nc.tensor.transpose(quarters(bank[4 + g % 2])[:, i, :], mk_tok[:, m, c * P:(c + 1) * P], ident)
                mm.then_inc(m_pe.step(f"t{g}"), 1)

        def mem_turn_dve(dve):
            m_dve.arm(dve)
            for g in range(4):
                dve.wait_ge(m_pe[f"t{g}"], m_pe.after(0, f"t{g}"))
                nc.vector.tensor_copy(mkT[:, 2 * g:2 * g + 2, :].rearrange("p a b -> p (a b)"), bank[4 + g % 2][:, :]).then_inc(m_dve.step(f"t{g}"), 1)

        xq = act_b[:, :].rearrange("p (c t) -> p c t", c=KC)
        x_pe = steps("xp_pe", "sc | tr0 tr1 pv0 pv1")
        x_dve = steps("xp_dve", "m0 m1 | r pn T1 o1")
        x_act = steps("xp_act", "p0 p1 p2 p3 | T0 o0")
        xP = [gz[:, 2 * i:2 * i + 2, :].rearrange("p a b -> p (a b)") for i in range(2)]
        xPT = [scr[:, i, :] for i in range(2)]
        xmx = [little(4) for _ in range(2)]
        xsum = [little(4) for _ in range(2)]

        def xp_pe(pe):
            x_pe.arm(pe)
            all_taken(pe, LAST_OF["cq"])
            pe.wait_ge(m_dve["t3"], m_dve.after(0, "t3"))
            pe.wait_ge(n_dve["cross"][f"ev{NT - 1}b"], n_dve["cross"].after(0, f"ev{NT - 1}b"))
            for u in range(NTP + 1):
                if u < NTP:
                    pe.wait_ge(x_act["p3"], x_act.after(u - 2, "p3"))
                    for h in range(H):
                        for c in range(2):
                            mm = nc.tensor.matmul(bank[2 * (u % 2) + h // 2][:, MEM * (h % 2):MEM * (h % 2) + MEM],
                                                  xq[:, 2 * h + c, u * P:(u + 1) * P], mkT[:, 2 * h + c, :], start=c == 0, stop=c == 1)
                    mm.then_inc(x_pe.step("sc"), 1)
                if u >= 1:
                    v = u - 1
                    pe.wait_ge(x_dve["pn"], x_dve.after(v, "pn"))
                    for g, s in ((0, x_act), (1, x_dve)):
                        pe.wait_ge(s[f"T{g}"], s.after(v - 1, f"T{g}"))
                        for i in range(4):
                            q = 4 * g + i
                            mm = nc.tensor.transpose(quarters(bank[4 + g])[:, i, :], xP[v % 2][:, q * P:(q + 1) * P], ident)
                        mm.then_inc(x_pe.step(f"tr{g}"), 1)
                    pe.wait_ge(x_act["T0"], x_act.after(v, "T0"))
                    pe.wait_ge(x_dve["T1"], x_dve.after(v, "T1"))
                    for g, s in ((0, x_act), (1, x_dve)):
                        pe.wait_ge(s[f"o{g}"], s.after(v - 1, f"o{g}"))
                        for i in range(4):
                            q = 4 * g + i
                            for m in range(2):
                                mm = nc.tensor.matmul(quarters(bank[6 + g])[:, i, :], mv[:, m, q * P:(q + 1) * P],
                                                      xPT[v % 2][:, (2 * (q // 2) + m) * P:(2 * (q // 2) + m + 1) * P], start=m == 0, stop=m == 1)
                        mm.then_inc(x_pe.step(f"pv{g}"), 1)

        def xp_dve(dve):
            x_dve.arm(dve)
            for u in range(NTP + 1):
                if u < NTP:
                    dve.wait_ge(x_pe["sc"], x_pe.after(u, "sc"))
                    for g in range(2):
                        ins = nc.vector.tensor_reduce(xmx[u % 2][:, 2 * g:2 * g + 2],
                                                      bank[2 * (u % 2) + g][:, :].rearrange("p (h m) -> p h m", h=2), AX.X, ALU.max, negate=True)
                        ins.then_inc(x_dve.step(f"m{g}"), 1)
                if u >= 1:
                    v = u - 1
                    dve.wait_ge(x_act["p3"], x_act.after(v, "p3"))
                    nc.vector.reciprocal(xsum[v % 2], xsum[v % 2]).then_inc(x_dve.step("r"), 1)
                    dve.wait_ge(x_dve["r"], x_dve.after(v, "r"))
                    pp = xP[v % 2].rearrange("p (h m) -> p h m", h=H)
                    nc.vector.tensor_tensor(pp, pp, xsum[v % 2].unsqueeze(2).to_broadcast([P, H, MEM]), ALU.mult).then_inc(x_dve.step("pn"), 1)
                    dve.wait_ge(x_pe["tr1"], x_pe.after(v, "tr1"))
                    nc.vector.tensor_copy(xPT[v % 2][:, 512:1024], bank[5][:, :]).then_inc(x_dve.step("T1"), 1)
                    dve.wait_ge(x_pe["pv1"], x_pe.after(v, "pv1"))
                    nc.vector.tensor_copy(act_a[:, 4:8, v * P:(v + 1) * P], quarters(bank[7])).then_inc(x_dve.step("o1"), 1)

        def xp_act(act):
            x_act.arm(act)
            for u in range(NTP + 1):
                if u < NTP:
                    q = u % 2
                    act.wait_ge(x_dve["m1"], x_dve.after(u, "m1"))
                    act.wait_ge(x_pe["tr1"], x_pe.after(u - 2, "tr1"))
                    for h in range(H):
                        c = slice(MEM * (h % 2), MEM * (h % 2) + MEM)
                        nc.scalar.activation(xP[q][:, MEM * h:MEM * h + MEM], bank[2 * q + h // 2][:, c], ACT.Exp,
                                                        bias=xmx[q][:, h:h + 1], accum_out=xsum[q][:, h:h + 1]).then_inc(x_act.step(f"p{h}"), 1)
                if u >= 1:
                    v = u - 1
                    act.wait_ge(x_pe["tr0"], x_pe.after(v, "tr0"))
                    nc.scalar.copy(xPT[v % 2][:, 0:512], bank[4][:, :]).then_inc(x_act.step("T0"), 1)
                    act.wait_ge(x_pe["pv0"], x_pe.after(v, "pv0"))
                    nc.scalar.copy(act_a[:, 0:4, v * P:(v + 1) * P], quarters(bank[6])).then_inc(x_act.step("o0"), 1)

        h_row = conv[:, 0:5 * D].rearrange("p (t d) -> p t d", t=NT)
        gffn_row = conv[:, 6144:7168]
        w_route = conv[:, 7168:7168 + 36 * KC].rearrange("p (c n) -> p c n", c=KC)
        b_route = conv[:, 7456:7492]
        at_r = [0]

        def rs(*shape):
            n = int(np.prod(shape))
            at_r[0] += n
            v = attn[:, at_r[0] - n:at_r[0]]
            if len(shape) == 2:
                v = v.rearrange("p (a b) -> p a b", a=shape[0])
            return v

        lg = rs(NT, 36)
        g_s, g_e, g_q = rs(NT, 4), rs(NT, 4), rs(NT, 4)
        gmax, gsum, gidx, m1, m2, i1, i2, ee, w1, w2, sl1, sl2 = (rs(NT) for _ in range(12))
        msk, ml, dd, oh1, oh2, A, pos, slotv = (rs(NT, NE) for _ in range(8))
        cnt, nblk, ends, starts, one32 = (rs(NE) for _ in range(5))
        capq = rs(NE, NT * P // CAP)
        cmp_ = rs(BLKPAD + 1, NE)
        blk_e = rs(BLKPAD + 1)
        cmp2, n_rounds = rs((BLKPAD + 1) // 2), rs(1)
        pair_f, over_f, token_f = rs(NBLK), rs(NBLK), rs(NBLK)
        assert at_r[0] <= 5120
        at_u = [5120]

        def us(n):
            at_u[0] += n
            return attn[:, at_u[0] - n:at_u[0]].bitcast(U32)

        slots_u = us(2 * NT)
        pair_u = us(2 * NT)
        table_u = us(64)
        empty_u = us(64)
        pair_all = us(64)
        token_all = us(64)
        token_col, pair_col = [us(1), us(1)], [us(1), us(1)]
        r_pe = steps("route_pe", "lg cum")
        r_act = steps("route_act", "ge ee")
        r_dve = steps("route_dve",
                      "lg gmax gs ge4 gsum gtop gq gq2 gidx msk0 msk1 ml m1 d1 q1 q1b i1 oh1 ml2 m2 d2 q2 q2b i2 oh2 "
                      "dm w0 w1a w1 w2 A cnt pos capq nblk one ends starts base slotv s1a s1 s2a s2 su1 su2 "
                      "pair empty cmp blk min tab cmp2 nr tabn pf p1 p2 p3 p4 token")
        s_route = sem("route_weights_loaded")
        s_bias = sem("group_bias_loaded")
        s_zero = sem("indices_cleared")
        s_hrow = sem("h_rows_stored")
        s_scat = [sem(f"indices_stored{i}") for i in range(2 * NT)]

        def route_pe(pe):
            r_pe.arm(pe)
            pe.wait_ge(s_route, 64)
            pe.wait_ge(n_dve["ffn"][f"ev{NT - 1}b"], n_dve["ffn"].after(0, f"ev{NT - 1}b"))
            pe.wait_ge(taken(LAST_OF["co"]), taken_count(LAST_OF["co"]))
            for t in range(NT):
                for c in range(KC):
                    mm = nc.tensor.matmul(bank[0][:, 36 * t:36 * t + 36], act_a[:, c, t * P:(t + 1) * P], w_route[:, c, :],
                                          start=c == 0, stop=c == KC - 1)
            mm.then_inc(r_pe.step("lg"), 1)
            pe.wait_ge(r_dve["A"], r_dve.after(0, "A"))
            for t in range(NT):
                for s in range(t + 1):
                    mm = nc.tensor.matmul(bank[1][:, NE * t:NE * t + NE], C("cum_p") if s == t else C("ones"), A[:, s, :],
                                          start=s == 0, stop=s == t)
            for s in range(NT):
                mm = nc.tensor.matmul(bank[1][:, NE * NT:NE * NT + NE], C("ones"), A[:, s, :], start=s == 0, stop=s == NT - 1)
            mm.then_inc(r_pe.step("cum"), 1)

        def route_act(act):
            r_act.arm(act)
            act.wait_ge(r_dve["gs"], r_dve.after(0, "gs"))
            nc.scalar.activation(g_e, g_s, ACT.Exp).then_inc(r_act.step("ge"), 1)
            act.wait_ge(r_dve["dm"], r_dve.after(0, "dm"))
            nc.scalar.activation(ee, ee, ACT.Exp).then_inc(r_act.step("ee"), 1)

        def route_dve(dve):
            r_dve.arm(dve)
            tt, ts, red = nc.vector.tensor_tensor, nc.vector.tensor_scalar, nc.vector.tensor_reduce
            stt = nc.vector.scalar_tensor_tensor

            def over(v, n):
                return v.unsqueeze(2).to_broadcast([P, NT, n])

            def row(v, n):
                return v.unsqueeze(1).to_broadcast([P, NT, n])

            dve.wait_ge(xs.act["o"], xs.act.after(NB - 1, "o"))
            dve.wait_ge(r_pe["lg"], r_pe.after(0, "lg"))
            tt(lg, bank[0][:, 0:36 * NT].rearrange("p (t n) -> p t n", t=NT), row(b_route, 36), ALU.add).then_inc(r_dve.step("lg"), 1)
            dve.wait_ge(r_dve["lg"], r_dve.after(0, "lg"))
            gl, el = lg[:, :, 0:4], lg[:, :, 4:36]
            red(gmax, gl, AX.X, ALU.max).then_inc(r_dve.step("gmax"), 1)
            dve.wait_ge(r_dve["gmax"], r_dve.after(0, "gmax"))
            tt(g_s, gl, over(gmax, 4), ALU.subtract).then_inc(r_dve.step("gs"), 1)
            dve.wait_ge(r_dve["gs"], r_dve.after(0, "gs"))
            dve.wait_ge(r_act["ge"], r_act.after(0, "ge"))
            red(gsum, g_e, AX.X, ALU.add).then_inc(r_dve.step("ge4"), 1)
            dve.wait_ge(r_dve["ge4"], r_dve.after(0, "ge4"))
            nc.vector.reciprocal(gsum, gsum).then_inc(r_dve.step("gsum"), 1)
            dve.wait_ge(r_dve["gsum"], r_dve.after(0, "gsum"))
            ts(g_q, g_s, 0.0, None, ALU.is_equal).then_inc(r_dve.step("gtop"), 1)
            dve.wait_ge(r_dve["gtop"], r_dve.after(0, "gtop"))
            ts(g_q, g_q, -100.0, 100.0, ALU.mult, ALU.add).then_inc(r_dve.step("gq"), 1)
            dve.wait_ge(r_dve["gq"], r_dve.after(0, "gq"))
            tt(g_q, g_q, row(C("iota8")[:, 0:4], 4), ALU.add).then_inc(r_dve.step("gq2"), 1)
            dve.wait_ge(r_dve["gq2"], r_dve.after(0, "gq2"))
            red(gidx, g_q, AX.X, ALU.min).then_inc(r_dve.step("gidx"), 1)
            dve.wait_ge(r_dve["gidx"], r_dve.after(0, "gidx"))
            tt(msk, row(C("group"), NE), over(gidx, NE), ALU.is_equal).then_inc(r_dve.step("msk0"), 1)
            dve.wait_ge(r_dve["msk0"], r_dve.after(0, "msk0"))
            ts(msk, msk, BIG, -BIG, ALU.mult, ALU.add).then_inc(r_dve.step("msk1"), 1)
            dve.wait_ge(r_dve["msk1"], r_dve.after(0, "msk1"))
            tt(ml, el, msk, ALU.add).then_inc(r_dve.step("ml"), 1)
            dve.wait_ge(r_dve["ml"], r_dve.after(0, "ml"))
            for k, m, i, oh in ((1, m1, i1, oh1), (2, m2, i2, oh2)):
                red(m, ml, AX.X, ALU.max).then_inc(r_dve.step(f"m{k}"), 1)
                dve.wait_ge(r_dve[f"m{k}"], r_dve.after(0, f"m{k}"))
                tt(dd, ml, over(m, NE), ALU.is_equal).then_inc(r_dve.step(f"d{k}"), 1)
                dve.wait_ge(r_dve[f"d{k}"], r_dve.after(0, f"d{k}"))
                ts(dd, dd, -100.0, 100.0, ALU.mult, ALU.add).then_inc(r_dve.step(f"q{k}"), 1)
                dve.wait_ge(r_dve[f"q{k}"], r_dve.after(0, f"q{k}"))
                tt(dd, dd, row(C("iota32"), NE), ALU.add).then_inc(r_dve.step(f"q{k}b"), 1)
                dve.wait_ge(r_dve[f"q{k}b"], r_dve.after(0, f"q{k}b"))
                red(i, dd, AX.X, ALU.min).then_inc(r_dve.step(f"i{k}"), 1)
                dve.wait_ge(r_dve[f"i{k}"], r_dve.after(0, f"i{k}"))
                tt(oh, row(C("iota32"), NE), over(i, NE), ALU.is_equal).then_inc(r_dve.step(f"oh{k}"), 1)
                dve.wait_ge(r_dve[f"oh{k}"], r_dve.after(0, f"oh{k}"))
                if k == 1:
                    stt(ml, oh, -BIG, ml, ALU.mult, ALU.add).then_inc(r_dve.step("ml2"), 1)
                    dve.wait_ge(r_dve["ml2"], r_dve.after(0, "ml2"))
            tt(ee, m2, m1, ALU.subtract).then_inc(r_dve.step("dm"), 1)
            dve.wait_ge(r_dve["dm"], r_dve.after(0, "dm"))
            dve.wait_ge(r_act["ee"], r_act.after(0, "ee"))
            ts(w1, ee, 1.0, None, ALU.add).then_inc(r_dve.step("w0"), 1)
            dve.wait_ge(r_dve["w0"], r_dve.after(0, "w0"))
            nc.vector.reciprocal(w1, w1).then_inc(r_dve.step("w1a"), 1)
            dve.wait_ge(r_dve["w1a"], r_dve.after(0, "w1a"))
            tt(w1, w1, gsum, ALU.mult).then_inc(r_dve.step("w1"), 1)
            dve.wait_ge(r_dve["w1"], r_dve.after(0, "w1"))
            tt(w2, w1, ee, ALU.mult).then_inc(r_dve.step("w2"), 1)
            dve.wait_ge(r_dve["w2"], r_dve.after(0, "w2"))
            tt(A, oh1, oh2, ALU.add).then_inc(r_dve.step("A"), 1)
            dve.wait_ge(r_dve["A"], r_dve.after(0, "A"))
            dve.wait_ge(r_pe["cum"], r_pe.after(0, "cum"))
            nc.vector.tensor_copy(cnt, bank[1][:, NE * NT:NE * NT + NE]).then_inc(r_dve.step("cnt"), 1)
            dve.wait_ge(r_dve["cnt"], r_dve.after(0, "cnt"))
            tt(pos, bank[1][:, 0:NE * NT].rearrange("p (t n) -> p t n", t=NT), A, ALU.subtract).then_inc(r_dve.step("pos"), 1)
            dve.wait_ge(r_dve["pos"], r_dve.after(0, "pos"))
            nc_ = NT * P // CAP
            tt(capq, cnt.unsqueeze(2).to_broadcast([P, NE, nc_]), C("capacities").unsqueeze(1).to_broadcast([P, NE, nc_]), ALU.is_gt).then_inc(r_dve.step("capq"), 1)
            dve.wait_ge(r_dve["capq"], r_dve.after(0, "capq"))
            red(nblk, capq, AX.X, ALU.add).then_inc(r_dve.step("nblk"), 1)
            dve.wait_ge(r_dve["nblk"], r_dve.after(0, "nblk"))
            nc.vector.memset(one32, 1.0).then_inc(r_dve.step("one"), 1)
            dve.wait_ge(r_dve["one"], r_dve.after(0, "one"))
            nc.vector.tensor_tensor_scan(ends, one32, nblk, 0.0, ALU.mult, ALU.add).then_inc(r_dve.step("ends"), 1)
            dve.wait_ge(r_dve["ends"], r_dve.after(0, "ends"))
            tt(starts, ends, nblk, ALU.subtract).then_inc(r_dve.step("starts"), 1)
            dve.wait_ge(r_dve["starts"], r_dve.after(0, "starts"))
            ts(starts, starts, float(CAP), None, ALU.mult).then_inc(r_dve.step("base"), 1)
            dve.wait_ge(r_dve["base"], r_dve.after(0, "base"))
            tt(slotv, pos, row(starts, NE), ALU.add).then_inc(r_dve.step("slotv"), 1)
            dve.wait_ge(r_dve["slotv"], r_dve.after(0, "slotv"))
            for k, oh, sl in ((1, oh1, sl1), (2, oh2, sl2)):
                tt(dd, oh, slotv, ALU.mult).then_inc(r_dve.step(f"s{k}a"), 1)
                dve.wait_ge(r_dve[f"s{k}a"], r_dve.after(0, f"s{k}a"))
                red(sl, dd, AX.X, ALU.add).then_inc(r_dve.step(f"s{k}"), 1)
                dve.wait_ge(r_dve[f"s{k}"], r_dve.after(0, f"s{k}"))
            nc.vector.tensor_copy(slots_u[:, 0:NT], sl1).then_inc(r_dve.step("su1"), 1)
            nc.vector.tensor_copy(slots_u[:, NT:2 * NT], sl2).then_inc(r_dve.step("su2"), 1)
            nc.vector.tensor_copy(pair_u, C("pair")).then_inc(r_dve.step("pair"), 1)
            nc.vector.tensor_copy(empty_u[:, 0:NBLK], C("empty")).then_inc(r_dve.step("empty"), 1)
            nb = BLKPAD + 1
            tt(cmp_, C("block").unsqueeze(2).to_broadcast([P, nb, NE]), ends.unsqueeze(1).to_broadcast([P, nb, NE]), ALU.is_ge).then_inc(r_dve.step("cmp"), 1)
            dve.wait_ge(r_dve["cmp"], r_dve.after(0, "cmp"))
            red(blk_e, cmp_, AX.X, ALU.add).then_inc(r_dve.step("blk"), 1)
            dve.wait_ge(r_dve["blk"], r_dve.after(0, "blk"))
            ts(blk_e, blk_e, float(NE - 1), None, ALU.min).then_inc(r_dve.step("min"), 1)
            dve.wait_ge(r_dve["min"], r_dve.after(0, "min"))
            nc.vector.tensor_copy(table_u[:, 1:1 + nb], blk_e).then_inc(r_dve.step("tab"), 1)
            dve.wait_ge(r_dve["tab"], r_dve.after(0, "tab"))
            tt(cmp2, ends[:, NE - 1:NE].to_broadcast([P, nb // 2]), C("block")[:, 0:nb:2], ALU.is_gt).then_inc(r_dve.step("cmp2"), 1)
            dve.wait_ge(r_dve["cmp2"], r_dve.after(0, "cmp2"))
            red(n_rounds, cmp2, AX.X, ALU.add).then_inc(r_dve.step("nr"), 1)
            dve.wait_ge(r_dve["nr"], r_dve.after(0, "nr"))
            nc.vector.tensor_copy(table_u[:, 0:1], n_rounds).then_inc(r_dve.step("tabn"), 1)

        def ffn_rows_pool(pool):
            s = n_pool["ffn"]
            pool.wait_ge(s_route, 64)
            pool.wait_ge(xs.act["o"], xs.act.after(NB - 1, "o"))
            for t in range(NT):
                pool.wait_ge(n_dve["ffn"][f"xn{t}"], n_dve["ffn"].after(0, f"xn{t}"))
                nc.gpsimd.tensor_tensor(h_row[:, t, :], scr[:, t % 2, :], gffn_row, ALU.mult).then_inc(s.step(f"g{t}"), 1)

        def route_pool(pool):
            pool.wait_ge(s_zero, 16)
            pool.wait_ge(r_dve["pair"], r_dve.after(0, "pair"))
            for i in range(2 * NT):
                pool.indirect_dma_start(a["slot_pair"], bass.IndirectOffsetOnAxis(slots_u[:, i:i + 1], 0), pair_u[:, i:i + 1], None)\
                    .then_inc(s_scat[i], 16)
            for i in range(2 * NT):
                pool.wait_ge(s_scat[i], 16)
            for k in range(2):
                half = slice(k * NBLK // 2, (k + 1) * NBLK // 2)
                pool.dma_start(pair_all[0:CAP, half], a["slot_pair"].rearrange("(b s) o -> s (b o)", s=CAP)[:, half],
                               allow_slow_non_contiguous=True).then_inc(s_y[k], 16)
            pool.wait_ge(s_hrow, 16 * NT)

        xg = [act_a[:, :, :].rearrange("p c t -> p (c t)")[:, 1024 * i:1024 * i + 1024] for i in range(2)]
        xgT = [act_b[:, 640 * i:640 * i + 640].rearrange("p (c s) -> p c s", c=KC) for i in range(2)]
        sgate = [act_b[:, 1280 + 160 * i:1440 + 160 * i] for i in range(2)]
        hT = [act_b[:, 1600 + 160 * i:1760 + 160 * i].rearrange("p (f s) -> p f s", f=2) for i in range(2)]
        yb = [act_b[:, 2048 + 1024 * i:3072 + 1024 * i] for i in range(2)]
        e_pe = steps("moe_pe", "tr0 tr1 gate up d0 d1")
        e_act = steps("moe_act", "x0 silu y0")
        e_dve = steps("moe_dve", "ix | x1 h pc y1")
        s_ew = [sem(f"expert_loaded{k}") for k in range(2)]
        s_xg = [sem(f"tokens_gathered{k}") for k in range(2)]
        s_y = [sem(f"pairs_loaded_rows_stored{k}") for k in range(2)]
        s_go = sem("indirect_dma_may_go")

        def rounds(eng):
            eng.wait_ge(r_dve["tabn"], r_dve.after(0, "tabn"))
            return eng.value_load(table_u[0:1, 0:1], min_val=1, max_val=(BLKPAD + 1) // 2)

        def moe_sync(sp):
            n = rounds(sp)
            with sp.Fori(0, n) as i:
                for k in range(2):
                    j = sp.snap(2 * i + k)
                    e = sp.value_load(table_u[0:1, bass.ds(j + 1, 1)], min_val=0, max_val=NE - 1)
                    sp.wait_ge(e_pe["d1"], e_pe.after(j - 2, "d1"))
                    w = W[:, k, :]
                    for m, name in enumerate(("w_gate", "w_up")):
                        sp.dma_start(w[:, 2048 * m:2048 * m + 2048].rearrange("p (c f) -> p c f", c=KC),
                                     a[name][0][bass.ds(e, 1)].rearrange("o (c p) f -> p (o c) f", p=P)).then_inc(s_ew[k], 16)
                    sp.dma_start(w[:, 4096:6144].rearrange("p (f d) -> p f d", f=2),
                                 a["w_down"][0][bass.ds(e, 1)].rearrange("o (f p) d -> p (o f) d", p=P)).then_inc(s_ew[k], 16)

        def moe_pool(pool):
            def gather(j, k):
                pool.wait_ge(e_pe["tr1"], e_pe.after(j - 2, "tr1"))
                pool.wait_ge(e_dve["ix"], e_dve.after(j, "ix"))
                pool.sem_inc(s_go, 1)
                pool.indirect_dma_start(xg[k][0:CAP, :], None, a["h_rows"], bass.IndirectOffsetOnAxis(token_col[k][0:CAP, :], 0))\
                    .then_inc(s_xg[k], 16)

            n = rounds(pool)
            for k in range(2):
                gather(k, k)
            with pool.Fori(0, n) as i:
                for k in range(2):
                    j = pool.snap(2 * i + k)
                    pool.wait_ge(e_act["y0"], e_act.after(j, "y0"))
                    pool.wait_ge(e_dve["y1"], e_dve.after(j, "y1"))
                    pool.sem_inc(s_go, 1)
                    pool.indirect_dma_start(a["pair_rows"], bass.IndirectOffsetOnAxis(pair_col[k][0:CAP, :], 0), yb[k][0:CAP, :], None)\
                        .then_inc(s_y[k], 16)
                    gather(j + 2, k)

        def moe_pe(pe):
            e_pe.arm(pe)
            n = rounds(pe)
            with pe.Fori(0, n) as i:
                for k in range(2):
                    j = pe.snap(2 * i + k)
                    pe.wait_ge(s_xg[k], i * 16 + 16)
                    for g, s, name in ((0, e_act, "x0"), (1, e_dve, "x1")):
                        pe.wait_ge(s[name], s.after(j - 1, name))
                        for c in range(4):
                            mm = nc.tensor.transpose(bank[g][:, c * CAP:(c + 1) * CAP], xg[k][0:CAP, (4 * g + c) * P:(4 * g + c + 1) * P],
                                                     ident[0:CAP, 0:CAP])
                        mm.then_inc(e_pe.step(f"tr{g}"), 1)
                    pe.wait_ge(e_act["x0"], e_act.after(j, "x0"))
                    pe.wait_ge(e_dve["x1"], e_dve.after(j, "x1"))
                    pe.wait_ge(e_dve["h"], e_dve.after(j - 1, "h"))
                    pe.wait_ge(s_ew[k], i * 48 + 48)
                    for m, name in enumerate(("gate", "up")):
                        w = W[:, k, 2048 * m:2048 * m + 2048].rearrange("p (c f) -> p c f", c=KC)
                        for f in range(2):
                            for c in range(KC):
                                mm = nc.tensor.matmul(bank[2 + m][:, CAP * f:CAP * f + CAP], w[:, c, f * P:(f + 1) * P], xgT[k][:, c, :],
                                                      start=c == 0, stop=c == KC - 1)
                        mm.then_inc(e_pe.step(name), 1)
                    pe.wait_ge(e_dve["h"], e_dve.after(j, "h"))
                    w = W[:, k, 4096:6144].rearrange("p (f d) -> p f d", f=2)
                    for g, s, name in ((0, e_act, "y0"), (1, e_dve, "y1")):
                        pe.wait_ge(s[name], s.after(j - 1, name))
                        for f in range(2):
                            mm = nc.tensor.matmul(bank[4 + g][0:CAP, :], hT[k][:, f, :], w[:, f, 512 * g:512 * g + 512], start=f == 0, stop=f == 1)
                        mm.then_inc(e_pe.step(f"d{g}"), 1)

        def moe_act(act):
            e_act.arm(act)
            n = rounds(act)
            with act.Fori(0, n) as i:
                for k in range(2):
                    j = act.snap(2 * i + k)
                    act.wait_ge(e_pe["tr0"], e_pe.after(j, "tr0"))
                    nc.scalar.copy(xgT[k][:, 0:4, :], bank[0][:, 0:4 * CAP].rearrange("p (c s) -> p c s", c=4)).then_inc(e_act.step("x0"), 1)
                    act.wait_ge(e_pe["gate"], e_pe.after(j, "gate"))
                    nc.scalar.activation(sgate[k], bank[2][:, 0:2 * CAP], ACT.Silu).then_inc(e_act.step("silu"), 1)
                    act.wait_ge(e_pe["d0"], e_pe.after(j, "d0"))
                    act.wait_ge(s_y[k], i * 16 + 16)
                    nc.scalar.copy(yb[k][0:CAP, 0:512], bank[4][0:CAP, :]).then_inc(e_act.step("y0"), 1)

        def moe_dve(dve):
            e_dve.arm(dve)
            n = rounds(dve)
            for k in range(2):
                dve.wait_ge(s_y[k], 16)
            rows = slice(0, CAP)
            ts = nc.vector.tensor_scalar
            pf, ov, tf = pair_f[rows], over_f[rows], token_f[rows]
            nc.vector.tensor_copy(pf, pair_all[rows, 0:NBLK]).then_inc(r_dve.step("pf"), 1)
            dve.wait_ge(r_dve["pf"], r_dve.after(0, "pf"))
            ts(ov, pf, float(NT * P), -float(NT * P), ALU.is_ge, ALU.mult).then_inc(r_dve.step("p1"), 1)
            dve.wait_ge(r_dve["p1"], r_dve.after(0, "p1"))
            nc.vector.tensor_tensor(tf, pf, ov, ALU.add).then_inc(r_dve.step("p2"), 1)
            dve.wait_ge(r_dve["p2"], r_dve.after(0, "p2"))
            ts(ov, pf, float(NPAIR), -float(NT * P), ALU.is_ge, ALU.mult).then_inc(r_dve.step("p3"), 1)
            dve.wait_ge(r_dve["p3"], r_dve.after(0, "p3"))
            nc.vector.tensor_tensor(tf, tf, ov, ALU.add).then_inc(r_dve.step("p4"), 1)
            dve.wait_ge(r_dve["p4"], r_dve.after(0, "p4"))
            nc.vector.tensor_copy(token_all[rows, 0:NBLK], tf).then_inc(r_dve.step("token"), 1)
            dve.wait_ge(r_dve["token"], r_dve.after(0, "token"))

            def columns(j, k):
                nc.vector.tensor_copy(token_col[k][rows, :], token_all[rows, bass.ds(j, 1)]).then_inc(e_dve.step("ix"), 1)

            for k in range(2):
                columns(k, k)
            with dve.Fori(0, n) as i:
                for k in range(2):
                    j = dve.snap(2 * i + k)
                    ahead = dve.snap(2 * i + (k + 2))
                    dve.wait_ge(e_pe["tr1"], e_pe.after(j, "tr1"))
                    nc.vector.tensor_copy(xgT[k][:, 4:8, :], bank[1][:, 0:4 * CAP].rearrange("p (c s) -> p c s", c=4)).then_inc(e_dve.step("x1"), 1)
                    columns(ahead, k)
                    dve.wait_ge(e_pe["up"], e_pe.after(j, "up"))
                    dve.wait_ge(e_act["silu"], e_act.after(j, "silu"))
                    nc.vector.tensor_tensor(hT[k][:, :, :].rearrange("p f s -> p (f s)"), bank[3][:, 0:2 * CAP], sgate[k], ALU.mult).then_inc(e_dve.step("h"), 1)
                    dve.wait_ge(s_y[k], i * 16 + 16)
                    nc.vector.tensor_copy(pair_col[k][rows, :], pair_all[rows, bass.ds(j, 1)]).then_inc(e_dve.step("pc"), 1)
                    dve.wait_ge(e_pe["d1"], e_pe.after(j, "d1"))
                    nc.vector.tensor_copy(yb[k][0:CAP, 512:1024], bank[5][0:CAP, :]).then_inc(e_dve.step("y1"), 1)

        Wf = W[:, :, :].rearrange("p a b -> p (a b)")
        back = [Wf[:, 1024 * i:1024 * i + 1024] for i in range(2 * NT)]
        gfin_row = Wf[:, 10240:11264]
        s_back = [sem(f"rows_back{i}") for i in range(2 * NT)]
        s_gfin = sem("g_final_loaded")
        f_dve = steps("final_dve", "x1 x2")
        f2_dve = steps("final_norm_dve", "xn y")
        f_act = steps("final_act", "sq")
        f_pool = steps("final_pool", "ms rn")
        s_store = [sem(f"y_stored{i}") for i in range(2)]

        def final_pool(pool):
            n = rounds(pool)
            for k in range(2):
                pool.wait_ge(s_y[k], n * 16 + 16)
            for k in range(2):
                pool.wait_ge(s_xg[k], n * 16 + 16)
            pool.wait_ge(e_pe["d1"], e_pe.after(2 * n - 1, "d1"))
            pool.sem_inc(s_go, 1)
            for i in range(2 * NT):
                pool.dma_start(back[i], a["pair_rows"][i * P:(i + 1) * P, :]).then_inc(s_back[i], 16)
            f_pool.arm(pool)
            pool.wait_ge(f_act["sq"], f_act.after(NT - 1, "sq"))
            nc.gpsimd.tensor_scalar(rstd[:, 0:NT], ss[:, 0:NT], 1.0 / D, EPS, ALU.mult, ALU.add).then_inc(f_pool.step("ms"), 1)
            pool.wait_ge(f_pool["ms"], f_pool.after(0, "ms"))
            nc.gpsimd.tensor_tensor(rstd[:, 0:NT], rstd[:, 0:NT], C("minus_half")[:, 0:NT], ALU.pow).then_inc(f_pool.step("rn"), 1)

        def final_dve(dve):
            f_dve.arm(dve)
            for t in range(NT):
                for k, w in ((0, w1), (1, w2)):
                    dve.wait_ge(s_back[t + NT * k], 16)
                    nc.vector.scalar_tensor_tensor(x[:, t, :], back[t + NT * k], w[:, t:t + 1], x[:, t, :], ALU.mult, ALU.add).then_inc(f_dve.step(f"x{k + 1}"), 1)
                    dve.wait_ge(f_dve[f"x{k + 1}"], f_dve.after(t, f"x{k + 1}"))
            f2_dve.arm(dve)
            dve.wait_ge(f_pool["rn"], f_pool.after(0, "rn"))
            dve.wait_ge(s_gfin, 16)
            for t in range(NT):
                if t >= 2:
                    dve.wait_ge(s_store[t % 2], 16 * (t // 2))
                nc.vector.tensor_scalar(scr[:, t % 2, :], x[:, t, :], rstd[:, t:t + 1], None, ALU.mult).then_inc(f2_dve.step("xn"), 1)
                dve.wait_ge(f2_dve["xn"], f2_dve.after(t, "xn"))
                nc.vector.tensor_tensor(scr[:, t % 2, :], scr[:, t % 2, :], gfin_row, ALU.mult).then_inc(f2_dve.step("y"), 1)

        def final_act(act):
            f_act.arm(act)
            for t in range(NT):
                act.wait_ge(f_dve["x2"], f_dve.after(t, "x2"))
                nc.scalar.activation(scr[:, 2, :], x[:, t, :], ACT.Square, accum_out=ss[:, t:t + 1]).then_inc(f_act.step("sq"), 1)
                act.wait_ge(f_act["sq"], f_act.after(t, "sq"))

        def final_sync(sp):
            n = rounds(sp)
            sp.wait_ge(e_pe["d1"], e_pe.after(2 * n - 1, "d1"))
            sp.dma_start(gfin_row, a["g_final"].partition_broadcast(P)).then_inc(s_gfin, 16)
            for t in range(NT):
                sp.wait_ge(f2_dve["y"], f2_dve.after(t, "y"))
                dst = a["y_prompt"][0][t * P:(t + 1) * P, :] if t < NTP else a["y_sample"].rearrange("b t d -> (b t) d")
                sp.dma_start(dst, scr[:, t % 2, :]).then_inc(s_store[t % 2], 16)
            sp.wait_ge(s_store[0], 16 * 3)
            sp.wait_ge(s_store[1], 16 * 2)

        def store(eng, dst, src):
            n_out[0] += 16
            eng.dma_start(dst, src).then_inc(s_out, 16)

        block = ctx.enter_context(nc.Block())

        w_in = a["w_in"][0]

        def cols(i):
            return slice(512 * i, 512 * i + 512)

        def rest_dst(job, b):
            what, ja, jb = job
            if what in ("mix", "co"):
                return [(x[:, ja, 512 * jb:512 * jb + 512], b[:, :], 1.0)]
            if what == "cq":
                n = 512 if jb == 0 else P
                return [(xq[:, ja, 512 * jb:512 * jb + n], b[:, 0:n], 1.0 / 16)]
            return [((mk_tok if what == "mk" else mv)[:, ja, 512 * jb:512 * jb + 512], b[:, :], 1.0)]

        @block.sync
        def _(sp):
            sp.dma_start(const[:, :], a["const"]).then_inc(s_const, 16)
            for t in range(NTP):
                sp.dma_start(x[:, t, :], a["x_prompt"][0][t * P:(t + 1) * P, :]).then_inc(s_x[t], 16)
            sp.dma_start(x[:, 4, :], a["x_sample"].rearrange("b t d -> (b t) d")).then_inc(s_x[4], 16)
            for i, n in enumerate(("g_mix", "g_mem", "g_cross", "g_ffn")):
                sp.dma_start(gains[:, i, :], a[n][0].rearrange("(c p) -> p c", p=P), allow_slow_non_contiguous=True).then_inc(s_gain, 16)
            load_weight(sp, "dq", w_in, cols(0))
            load_weight(sp, "dk", w_in, cols(1))
            sp.dma_start(hist, a["state_gdn_conv"][0].rearrange("b j c -> (b j) c")).then_inc(s_hist, 16)
            prep_sync_load(sp)
            load_weight(sp, "dv", w_in, cols(2))
            for i in range(3):
                load_weight(sp, f"conv{i}", w_in, cols(3 + i))
            load_weight(sp, "gz", w_in, slice(3080, 3592))
            for t in range(NT):
                for what, src, out in (("dk", dk_tok, "new_diff_k"), ("dv", dv, "new_diff_v")):
                    sp.wait_ge(taken(ORDER.index((what, t, 0))), taken_count(ORDER.index((what, t, 0))))
                    dst = (a[out + "_p"][0, 0].rearrange("t h c -> t (h c)")[t * P:(t + 1) * P] if t < NTP
                           else a[out + "_s"][0].rearrange("b t h c -> (b t) (h c)"))
                    store(sp, dst, src[:, t, :])
            sp.wait_ge(p_dve["tt2"], p_dve.after(0, "tt2"))
            store(sp, a["new_conv_p"][0, 0], tails_tok[0:3, :])
            store(sp, a["new_conv_s"][0].rearrange("b j c -> (b j) c"), tails_tok[3:27, :])
            streams_sync(sp, das, a["cache_diff_k"], a["cache_diff_v"])
            load_weight(sp, "mix0", a["w_out"][0], cols(0))
            load_weight(sp, "mix1", a["w_out"][0], cols(1))
            sp.wait_ge(das.pe["sc"], das.pe.after(NB - 1, "sc"))
            for h in range(H):
                sp.dma_start(states[:, h, :, :], a["state_gdn"][0].rearrange("b h k v -> h k b v")[h]).then_inc(s_state, 16)
            sp.wait_ge(gs_act["mix"], gs_act.after(0, "mix"))
            sp.wait_ge(gh_dve["s1"], gh_dve.after(H - 1, "s1"))
            for t in range(NTP):
                sp.dma_start(x[:, t, :], a["x_prompt"][0][t * P:(t + 1) * P, :]).then_inc(s_xback, 16)
            sp.dma_start(x[:, 4, :], a["x_sample"].rearrange("b t d -> (b t) d")).then_inc(s_xback, 16)
            store(sp, a["new_gdn_p"][0, 0].rearrange("h k v -> k h v"), h4(state))
            for h in range(H):
                store(sp, a["new_gdn_s"][0].rearrange("b h k v -> h k b v")[h], states[:, h, :, :])
            n1 = n_out[0]
            sp.wait_ge(s_out, n1)
            sp.dma_start(mem_rows[:, :, :], a["mem_prompt"][0].rearrange("(t p) d -> p t d", p=P)).then_inc(s_mem, 16)
            for i, n in enumerate(("w_ck", "w_cv", "w_cq")):
                for j in range(2):
                    load_weight(sp, f"{('mk', 'mv', 'cq')[i]}{j}", a[n][0], cols(j))
            sp.dma_start(gffn_row, a["g_ffn"][0].partition_broadcast(P)).then_inc(s_route, 16)
            w_r = a["w_rt"][0].rearrange("(c p) n -> p c n", p=P)
            w_g = a["w_grp"][0].rearrange("(c p) n -> p c n", p=P)
            sp.dma_start(w_route[:, :, 0:4], w_g).then_inc(s_route, 16)
            sp.dma_start(w_route[:, :, 4:36], w_r).then_inc(s_route, 16)
            sp.dma_start(b_route[:, 0:4], a["b_grp"][0].partition_broadcast(P)).then_inc(s_bias, 16)
            sp.dma_start(b_route[:, 4:36], a["b_rt"][0].partition_broadcast(P)).then_inc(s_route, 16)
            sp.wait_ge(s_bias, 16)
            all_taken(sp, LAST_OF["mv"])
            store(sp, a["new_mem_k_p"][0, 0].rearrange("(t p) h c -> p t (h c)", p=P), mk_tok)
            store(sp, a["new_mem_v_p"][0, 0].rearrange("(t p) h c -> p t (h c)", p=P), mv)
            streams_sync(sp, xs, a["cache_mem_k"], a["cache_mem_v"])
            load_weight(sp, "co0", a["w_co"][0], cols(0))
            load_weight(sp, "co1", a["w_co"][0], cols(1))
            for t in range(NT):
                sp.wait_ge(n_pool["ffn"][f"g{t}"], n_pool["ffn"].after(0, f"g{t}"))
                sp.dma_start(a["h_rows"][t * P:(t + 1) * P, :], h_row[:, t, :]).then_inc(s_hrow, 16)
            sp.wait_ge(r_dve["empty"], r_dve.after(0, "empty"))
            sp.dma_start(a["slot_pair"].rearrange("(p f) o -> p (f o)", p=CAP), empty_u[0:CAP, 0:NSLOT // CAP]).then_inc(s_zero, 16)
            moe_sync(sp)
            final_sync(sp)
            sp.wait_ge(s_out, n_out[0])

        @block.tensor
        def _(pe):
            prep_pe_a(pe)
            norm_pe(pe, "mix")
            pe.wait_ge(n_dve["mix"][f"ev{NT - 1}b"], n_dve["mix"].after(0, f"ev{NT - 1}b"))
            pe.wait_ge(s_small, N_SMALL)
            run_jobs(pe, ("dq", "dk", "dv", "conv", "gz", "gab"), act_a)
            prep_pe_b(pe)
            da_pe(pe)

            def ready(pe):
                pe.wait_ge(o_act["mix"], o_act.after(NTP - 1, "mix"))

            streams_pe(pe, das, ready)
            das_out_pe(pe)
            pe.wait_ge(t_act["mix"], t_act.after(0, "mix"))
            gdn_pe_prompt(pe)
            gdn_pe_sample(pe)
            pe.wait_ge(gs_act["mix"], gs_act.after(0, "mix"))
            run_jobs(pe, ("mix",), act_a)
            norm_pe(pe, "mem")
            pe.wait_ge(n_dve["mem"]["ev1b"], n_dve["mem"].after(0, "ev1b"))
            run_jobs(pe, ("mk", "mv"), mem_act)
            mem_turn_pe(pe)
            norm_pe(pe, "cross")
            pe.wait_ge(n_dve["cross"][f"ev{NT - 1}b"], n_dve["cross"].after(0, f"ev{NT - 1}b"))
            run_jobs(pe, ("cq",), act_a)
            xp_pe(pe)

            def attn_free(pe):
                pe.wait_ge(x_act["o0"], x_act.after(NTP - 1, "o0"))
                pe.wait_ge(x_dve["o1"], x_dve.after(NTP - 1, "o1"))

            streams_pe(pe, xs, attn_free)
            pe.wait_ge(xs.act["o"], xs.act.after(NB - 1, "o"))
            run_jobs(pe, ("co",), act_a)
            norm_pe(pe, "ffn")
            route_pe(pe)
            moe_pe(pe)

        @block.scalar
        def _(act):
            prep_act_a(act)
            act.wait_ge(s_const, 16)
            norm_act(act, "mix", x_tile, lambda t: (s_x[t], 16))
            take_jobs("act", act, ("dq", "dk", "dv", "conv", "gz", "gab"), project_dst)
            prep_act_b(act)
            act.wait_ge(n_dve["mix"][f"xn{NT - 1}"], n_dve["mix"].after(0, f"xn{NT - 1}"))
            da_act(act)

            def ready(act):
                act.wait_ge(s_out, 16 * (2 * NT + 2))
                act.wait_ge(d_pe["pv"], d_pe.after(UN - 1, "pv"))

            streams_act(act, das, ready)
            das_out_act(act)
            conv_act(act)
            act.wait_ge(c_act["silu"], c_act.after(0, "silu"))
            gdn_act(act)
            norm_act(act, "mem", lambda t: mem_rows[:, t, :], lambda t: (s_mem, 16))
            take_jobs("act", act, ("mk", "mv"), rest_dst)

            def x_sum(what, t):
                n = ORDER.index((what, t, 1))
                return taken(n), taken_count(n)

            norm_act(act, "cross", x_tile, lambda t: x_sum("mix", t))
            take_jobs("act", act, ("cq",), rest_dst)
            xp_act(act)
            streams_act(act, xs, lambda e: None)
            norm_act(act, "ffn", x_tile, lambda t: x_sum("co", t))
            route_act(act)
            moe_act(act)
            final_act(act)

        @block.vector
        def _(dve):
            prep_dve_a(dve)
            dve.wait_ge(s_gain, 64)
            norm_dve(dve, "mix", x_tile, gains[:, 0, :], act_a)
            take_jobs("dve", dve, ("dq", "dk", "dv", "conv", "gz", "gab"), project_dst)
            prep_dve_b(dve)
            da_dve(dve)

            def ready(dve):
                dve.wait_ge(d_pe["pv"], d_pe.after(UN - 1, "pv"))
                dve.wait_ge(s_out, 16 * (2 * NT + 2))

            streams_dve(dve, das, ready)
            t_dve.arm(dve)
            head_norm_dve(dve, t_dve, t_act, t_pool, 0, bank[6], gdn_g[:, 0:128])
            dve.wait_ge(t_pe["oT"], t_pe.after(0, "oT"))
            dve.wait_ge(c_act["silu"], c_act.after(0, "silu"))
            gdn_dve(dve)
            dve.wait_ge(s_xback, 16 * NT)
            take_jobs("dve", dve, ("mix",), rest_dst)
            norm_dve(dve, "mem", lambda t: mem_rows[:, t, :], gains[:, 1, :], mem_act)
            take_jobs("dve", dve, ("mk", "mv"), rest_dst)
            mem_turn_dve(dve)
            norm_dve(dve, "cross", x_tile, gains[:, 2, :], act_a)
            take_jobs("dve", dve, ("cq",), rest_dst)
            xp_dve(dve)
            streams_dve(dve, xs, lambda e: None)
            take_jobs("dve", dve, ("co",), rest_dst)
            norm_dve(dve, "ffn", x_tile, gains[:, 3, :], act_a)
            route_dve(dve)
            moe_dve(dve)
            final_dve(dve)

        @block.gpsimd
        def _(pool):
            prep_pool_a(pool)
            norm_pool(pool, "mix")
            da_pool(pool)
            t_pool.arm(pool)
            head_norm_pool(pool, t_pool, t_dve, 0)
            gdn_pool(pool)
            norm_pool(pool, "mem")
            norm_pool(pool, "cross")
            norm_pool(pool, "ffn")
            ffn_rows_pool(pool)
            route_pool(pool)
            moe_pool(pool)
            final_pool(pool)


SCRATCH = {"h_rows": ((NT * P, D), F32), "slot_pair": ((NSLOT, 1), U32), "pair_rows": ((NPAIR + 2 * CAP, D), F32)}

OUTPUTS = [
    ("y_prompt", (1, SEQ, D)), ("y_sample", (NB, TB, D)),
    ("new_diff_k_p", (1, 1, SEQ, H, 128)), ("new_diff_v_p", (1, 1, SEQ, H, 128)),
    ("new_conv_p", (1, 1, CONV - 1, 1536)), ("new_gdn_p", (1, 1, H, 128, 128)),
    ("new_mem_k_p", (1, 1, MEM, H, 256)), ("new_mem_v_p", (1, 1, MEM, H, 256)),
    ("new_diff_k_s", (1, NB, TB, H, 128)), ("new_diff_v_s", (1, NB, TB, H, 128)),
    ("new_conv_s", (1, NB, CONV - 1, 1536)), ("new_gdn_s", (1, NB, H, 128, 128)),
]


def kernel(**inputs):
    import numpy as _np
    import concourse.bacc as _bacc
    from concourse import mybir as _mybir
    from concourse.bass_utils import run_bass_kernel_spmd as _run

    nc = _bacc.Bacc("TRN2", target_bir_lowering=False, num_devices=1)
    arrays = {name: _np.ascontiguousarray(value) for name, value in inputs.items()}
    arrays["const"] = _np.concatenate([CONST[k] for k in CONST_AT], axis=1)
    aps = {}
    for name, value in arrays.items():
        aps[name] = nc.dram_tensor(name, value.shape, _mybir.dt.from_np(value.dtype), kind="ExternalInput").ap()
    for name, shape in OUTPUTS:
        aps[name] = nc.dram_tensor(name, shape, F32, kind="ExternalOutput").ap()
    for name, (shape, dt) in SCRATCH.items():
        aps[name] = nc.dram_tensor(name, shape, dt, kind="Internal").ap()
    build_encoder_step(nc, aps)
    r = _run(nc, [arrays], core_ids=[0])
    return tuple(r.results[0][name] for name, _ in OUTPUTS)
```

```python
from contextlib import ExitStack

import numpy as np

import concourse.bass as bass
from concourse import mybir

F32 = mybir.dt.float32
U32 = mybir.dt.uint32
ALU = mybir.AluOpType
ACT = mybir.ActivationFunctionType
AX = mybir.AxisListType

P = 128
D = 1024
KC = D // P
NT = 5
NTP = 4
SEQ = 512
NB = 8
TB = 16
PAST = 512
H = 4
MEM = 256
CONV = 4
NG, NE, TOPK = 4, 32, 2
EPG = NE // NG
FE = 256
CAP = 80
MAXBLK = (NT * P * TOPK) // CAP + NE
BLKPAD = MAXBLK + 1
NBLK = BLKPAD + 5
NPAIR = TOPK * NT * P
EPS = 1e-6
BIG = 1.0e30
LAM_INIT = 0.8 - 0.6
GW = 3 + SEQ + NB * (TB + 3)
GS = 3 + SEQ



def constant_columns():
    p = np.arange(P)[:, None]
    f = np.arange(P)[None, :]
    same = p // TB == f // TB
    cols = {}
    cols["ident"] = (p == f) * 1.0
    cols["ones"] = np.ones((P, P))
    cols["cum_p"] = (p <= f) * 1.0
    cols["cum_s"] = ((p <= f) & same) * 1.0
    cols["low_p"] = np.where(f < p, 0.0, -BIG)
    cols["low_s"] = np.where((f < p) & same, 0.0, -BIG)
    cols["up_p"] = np.where(f >= p, 0.0, -BIG)
    cols["up_s"] = np.where((f >= p) & same, 0.0, -BIG)
    cols["blk16"] = same * 1.0
    for s in (32, 64, 128):
        cols[f"lev{s}"] = ((p // s == f // s) & (p // (s // 2) > f // (s // 2))) * 1.0
    cols["stream_off"] = np.repeat(np.where(np.arange(NB)[:, None] == f // TB, 0.0, -BIG).reshape(1, -1), P, 0)
    cols["stream_row"] = (p // TB == np.arange(NB)[None, :]) * 1.0
    row = np.arange(P)
    h, m, q = row // 32, (row // 16) % 2, row % 16
    cols["pick"] = (h * 16 + q)[:, None] == np.arange(64)[None, :]
    cols["map0"] = (m == 0)[:, None]
    cols["map1"] = (m == 1)[:, None]
    cols["capacities"] = np.repeat(CAP * np.arange(NT * P // CAP)[None] * 1.0, P, 0)
    cols["minus_one"] = np.full((P, 1), -1.0)
    cols["eps"] = np.full((P, 1), EPS)
    cols["minus_half"] = np.full((P, 8), -0.5)
    cols["qk_scale"] = np.repeat(np.array([[P] * 4 + [1.0] * 4]), P, 0)
    cols["iota8"] = np.repeat(np.arange(8.0)[None], P, 0)
    cols["group"] = np.repeat((np.arange(NE) // EPG)[None] * 1.0, P, 0)
    cols["iota32"] = np.repeat(np.arange(NE)[None] * 1.0, P, 0)
    cols["block"] = np.repeat(np.arange(BLKPAD + 1)[None] * 1.0, P, 0)
    cols["pair"] = p + P * np.arange(TOPK * NT)[None, :] + 1
    cols["slot0"] = np.repeat(CAP * np.arange(NBLK)[None] * 1.0, P, 0)
    cols["iota_cap"] = np.repeat(np.arange(CAP)[None] * 1.0, P, 0)
    slot = np.arange(CAP)[:, None] + CAP * np.arange(NBLK)[None]
    cols["empty"] = np.zeros((P, NBLK))
    cols["empty"][:CAP] = (NPAIR + 1 + slot % (2 * CAP))
    return {k: np.asarray(v, np.float32) for k, v in cols.items()}


CONST = constant_columns()
CONST_AT, _at = {}, 0
for _k, _v in CONST.items():
    CONST_AT[_k] = (_at, _v.shape[1])
    _at += _v.shape[1]
NCONST = _at


class Steps:

    def __init__(self, sem, name, names):
        self.groups = []
        self.of = {}
        for i, group in enumerate(names.split("|")):
            group = group.split()
            self.groups.append([sem(f"{name}{i or ''}"), len(group), 0])
            for k, step in enumerate(group):
                assert step not in self.of
                self.of[step] = (i, k)

    def arm(self, eng):
        for sem, n, _ in self.groups:
            eng.sem_inc(sem, 2 * n)

    def __getitem__(self, name):
        return self.groups[self.of[name][0]][0]

    def after(self, it, name):
        i, k = self.of[name]
        n = self.groups[i][1]
        return it * n + (k + 1 + 2 * n)

    def step(self, name):
        i, k = self.of[name]
        group = self.groups[i]
        assert group[2] % group[1] == k, (name, k, group)
        group[2] += 1
        return group[0]




def weight_jobs():
    own = lambda what: [(what, t, 0) for t in range(NT)]
    wide = lambda what, n: [(what, m, c) for m in range(n) for c in range(2)]
    project = (
        [("dq", m, c) for m in range(4) for c in range(2)] + own("dk") + own("dv")
        + [("conv", m, c) for m in range(12) for c in range(2)] + own("gz") + [("gab", 0, 0)]
    )
    mix = [("mix", t, n) for n in range(2) for t in range(NT)]
    memory = [("mk", t, n) for n in range(2) for t in range(2)] + [("mv", t, n) for n in range(2) for t in range(2)]
    return {"project": project, "mix": mix, "memory": memory, "cq": wide("cq", KC),
            "co": [("co", t, n) for n in range(2) for t in range(NTP)] + [("co", NTP, n) for n in range(2)]}


JOBS = weight_jobs()
ORDER = [job for group in ("project", "mix", "memory", "cq", "co") for job in JOBS[group]]
JOB_BANK = [n % (2 if job[0] in ("conv", "gz", "gab") else 4) for n, job in enumerate(ORDER)]


def bank_before(n):
    return max((m for m in range(n) if JOB_BANK[m] == JOB_BANK[n]), default=None)




def evacuator(n):
    return "dve" if ORDER[n][0] in ("mix", "co") or n % 2 else "act"


TAKEN = {e: np.cumsum([evacuator(n) == e for n in range(len(ORDER))]).tolist() for e in ("act", "dve")}
FIRST_OF = {}
for _n, _job in enumerate(ORDER):
    FIRST_OF.setdefault(_job[0], _n)
LAST_OF = {job[0]: n for n, job in enumerate(ORDER)}

UNIT = {}
for _n, _u in enumerate(
    ["dq", "dk", "dv", "conv0", "conv1", "conv2", "gz"] + [f"da{b}" for b in range(NB)]
    + ["mix0", "mix1", "mk0", "mk1", "mv0", "mv1", "cq0", "cq1"] + [f"x{b}" for b in range(NB)]
):
    UNIT[_u] = _n
WSLOT = 6 * D


def unit_of(job):
    what, a, b = job
    if what == "conv":
        return UNIT[f"conv{a // 4}"]
    if what in ("mix", "mk", "mv"):
        return UNIT[f"{what}{b}"]
    if what == "cq":
        return UNIT[f"cq{a // 4}"]
    return None if what in ("gab", "co") else UNIT[what]


GDN_ACT = "stage sq0 sq1 EG eg D DT qT Mt M2 M2t M4 M4t M8 T0 T1 T2 w osq mix"
GDN_PE = ("tokqk tokv cum gcum chq chk kk kq Mt sq2 sq2t x1 sq4 sq4t x2 sq8 x3 "
          "T0 BX0 Y0 T1 BX1 Y1 T2 BX2 Y2 w vn o s oT")
GDN_DVE = ("gb gB gc S SD SU ss ssq qk0 qk1 kT vb be kbg kl ktail L0 L AT M B0 X0 X1 X2 X3 "
           "W0 Y0 B1 W1 Y1 B2 W2 Y2 qd vn sg s oss oms on og oz")
GDN_POOL = "rn orn"


def build_encoder_step(nc, a):
    ctx = ExitStack()
    with ctx:
        def sb(name, shape, dt=F32):
            return ctx.enter_context(nc.sbuf_tensor("sb_" + name, shape, dt))

        def sem(name):
            return ctx.enter_context(nc.semaphore(name))

        def steps(name, names):
            return Steps(sem, name, names)

        const = sb("const", [P, NCONST])
        x_buf = sb("x", [P, NT * D])
        x = x_buf[:, :].rearrange("p (t d) -> p t d", t=NT)
        act_a = sb("act_a", [P, KC, NT * P])
        act_b = sb("act_b", [P, KC * NT * P])
        attn = sb("attn", [P, 3 * NT * 512])
        conv = sb("conv", [P, 12 * GW])
        gz = sb("gz", [P, NT, 512])
        W = sb("W", [P, 2, WSLOT])
        scr = sb("scr", [P, 3, D])
        small = sb("small", [P, 768])
        gains = sb("gains", [P, 4, KC])
        gdn_g = sb("gdn_g", [P, 2 * 128])
        convw = sb("convw", [P, 12, CONV])
        w_gab = sb("w_gab", [P, KC, 8])

        def C(name, h=None):
            at, n = CONST_AT[name]
            v = const[:, at:at + n]
            return v if h is None else v.unsqueeze(1).to_broadcast([P, h, n])

        free = [0]

        def little(n):
            free[0] += n
            assert free[0] <= 768
            return small[:, free[0] - n:free[0]]

        ident = C("ident")
        dq = attn[:, 0:2560].rearrange("p (h t) -> p h t", h=H)
        dk = attn[:, 2560:5120].rearrange("p (h t) -> p h t", h=H)
        dv = attn[:, 5120:7680].rearrange("p (t c) -> p t c", t=NT)
        dk_tok = act_b[:, 0:2560].rearrange("p (t c) -> p t c", t=NT)
        cv = conv[:, :].rearrange("p (m c) -> p m c", m=12)
        bank = [ctx.enter_context(nc.psum_tensor(f"bank{i}", [P, 512], F32)) for i in range(8)]

        def quarters(b):
            return b[:, :].rearrange("p (h c) -> p h c", h=4)

        s_const = sem("const_loaded")
        s_gain = sem("gains_loaded")
        s_x = [sem(f"x_loaded{t}") for t in range(NT)]
        s_w = [sem(f"w_loaded{k}") for k in range(2)]
        s_kv = [sem(f"kv_loaded{k}") for k in range(2)]
        s_hist = sem("conv_history_loaded")
        s_job = sem("jobs_computed")
        s_taken = {"act": sem("jobs_taken_by_act"), "dve": sem("jobs_taken_by_dve")}
        s_out = sem("outputs_stored")
        n_out = [0]

        def taken(n):
            return s_taken[evacuator(n)]

        def taken_count(n):
            return TAKEN[evacuator(n)][n]

        def all_taken(eng, last):
            for e in ("act", "dve"):
                if TAKEN[e][last]:
                    eng.wait_ge(s_taken[e], TAKEN[e][last])

        NORMS = {"mix": NT, "mem": 2, "cross": NT, "ffn": NT}
        n_act = {k: steps(f"norm_{k}_act", " ".join(f"sq{t}" for t in range(n))) for k, n in NORMS.items()}
        n_pool = {k: steps(f"norm_{k}_pool", "ms rstd " + " ".join(f"g{t}" for t in range(n) if k == "ffn"))
                  for k, n in NORMS.items()}
        n_dve = {k: steps(f"norm_{k}_dve", " ".join(
            f"xn{t}" + ("" if t == 0 else f" ev{t - 1}a ev{t - 1}b") for t in range(n)) + f" ev{n - 1}a ev{n - 1}b")
            for k, n in NORMS.items()}
        n_pe = {k: steps(f"norm_{k}_pe", " ".join(f"tr{t}a tr{t}b" for t in range(n))) for k, n in NORMS.items()}
        ss = little(8)
        rstd = little(8)

        def norm_act(act, k, src, ready):
            s = n_act[k]
            s.arm(act)
            for t in range(NORMS[k]):
                act.wait_ge(*ready(t))
                nc.scalar.activation(scr[:, 2, :], src(t), ACT.Square, accum_out=ss[:, t:t + 1]).then_inc(s.step(f"sq{t}"), 1)
                act.wait_ge(s[f"sq{t}"], s.after(0, f"sq{t}"))

        def norm_pool(pool, k):
            s, n = n_pool[k], NORMS[k]
            s.arm(pool)
            pool.wait_ge(n_act[k][f"sq{n - 1}"], n_act[k].after(0, f"sq{n - 1}"))
            nc.gpsimd.tensor_scalar(rstd[:, 0:n], ss[:, 0:n], 1.0 / D, EPS, ALU.mult, ALU.add).then_inc(s.step("ms"), 1)
            pool.wait_ge(s["ms"], s.after(0, "ms"))
            nc.gpsimd.tensor_tensor(rstd[:, 0:n], rstd[:, 0:n], C("minus_half")[:, 0:n], ALU.pow).then_inc(s.step("rstd"), 1)

        def norm_dve(dve, k, src, gain, dst):
            s, n = n_dve[k], NORMS[k]
            s.arm(dve)
            dve.wait_ge(n_pool[k]["rstd"], n_pool[k].after(0, "rstd"))
            for t in range(n + 1):
                if t < n:
                    if t >= 2:
                        dve.wait_ge(n_pe[k][f"tr{t - 2}b"], n_pe[k].after(0, f"tr{t - 2}b"))
                        if k == "ffn":
                            dve.wait_ge(n_pool[k][f"g{t - 2}"], n_pool[k].after(0, f"g{t - 2}"))
                    nc.vector.tensor_scalar(scr[:, t % 2, :], src(t), rstd[:, t:t + 1], None, ALU.mult).then_inc(s.step(f"xn{t}"), 1)
                if t >= 1:
                    for i, ab in enumerate("ab"):
                        dve.wait_ge(n_pe[k][f"tr{t - 1}{ab}"], n_pe[k].after(0, f"tr{t - 1}{ab}"))
                        o = dst[:, 4 * i:4 * i + 4, (t - 1) * P:t * P]
                        g = gain[:, 4 * i:4 * i + 4].unsqueeze(2).to_broadcast([P, 4, P])
                        nc.vector.tensor_tensor(o, quarters(bank[4 + 2 * ((t - 1) % 2) + i]), g, ALU.mult).then_inc(s.step(f"ev{t - 1}{ab}"), 1)

        def norm_pe(pe, k):
            s = n_pe[k]
            s.arm(pe)
            for t in range(NORMS[k]):
                pe.wait_ge(n_dve[k][f"xn{t}"], n_dve[k].after(0, f"xn{t}"))
                for i, ab in enumerate("ab"):
                    if t >= 2:
                        pe.wait_ge(n_dve[k][f"ev{t - 2}{ab}"], n_dve[k].after(0, f"ev{t - 2}{ab}"))
                    for c in range(4):
                        q = 4 * i + c
                        mm = nc.tensor.transpose(quarters(bank[4 + 2 * (t % 2) + i])[:, c, :], scr[:, t % 2, q * P:(q + 1) * P], ident)
                    mm.then_inc(s.step(f"tr{t}{ab}"), 1)

        def x_tile(t):
            return x[:, t, :]

        def slot(n):
            return W[:, n % 2, 0:4096].rearrange("p (c n) -> p c n", c=KC)

        spare = [W[:, 0, 4096:], W[:, 1, 4096:]]
        s_co = [sem(f"w_co_loaded{n}") for n in range(2)]

        def co_chunk(n, c):
            return spare[c // 4][:, 512 * (c % 4):512 * (c % 4) + 512] if n == 0 else conv[:, 512 * c:512 * c + 512]

        def run_jobs(pe, names, src, between=None, only=None):
            at = -1
            for n, job in enumerate(ORDER):
                what, ja, jb = job
                if what not in names or (only is not None and n not in only):
                    continue
                at += 1
                unit = unit_of(job)
                if what == "co" and ja == NTP:
                    pe.wait_ge(xs_act["o"], xs_act.after(NB - 1, "o"))
                if what == "co" and ja == 0:
                    pe.wait_ge(s_co[jb], 16 * (2 - jb))
                first = n == 0 or unit_of(ORDER[n - 1]) != unit
                if unit is not None and first:
                    pe.wait_ge(s_w[unit % 2], 16 * W_COUNT[unit])
                m = bank_before(n)
                if m is not None:
                    pe.wait_ge(taken(m), taken_count(m))
                out = bank[JOB_BANK[n]]
                for c in range(KC):
                    if what in ("dq", "conv", "cq"):
                        cols = slice(0, 512) if jb == 0 else slice(512, 640)
                        m = ja % 4
                        mm = nc.tensor.matmul(out[:, 0:cols.stop - cols.start], slot(unit)[:, c, m * P:(m + 1) * P],
                                              src[:, c, cols], start=c == 0, stop=c == KC - 1)
                    elif what == "gab":
                        continue
                    else:
                        w = co_chunk(jb, c) if what == "co" else slot(unit)[:, c, :]
                        mm = nc.tensor.matmul(out[:, :], src[:, c, ja * P:(ja + 1) * P], w, start=c == 0, stop=c == KC - 1)
                        if c == KC - 1:
                            mm.then_inc(s_job, 1)
                    if between is not None:
                        between(at, c)
                if what == "gab":
                    for t in range(NT):
                        for c in range(KC):
                            mm = nc.tensor.matmul(out[:, 8 * t:8 * t + 8], src[:, c, t * P:(t + 1) * P], w_gab[:, c, :],
                                                  start=c == 0, stop=c == KC - 1)
                if what in ("dq", "conv", "cq", "gab"):
                    mm.then_inc(s_job, 1)

        gab = little(8 * NT)

        def take_jobs(me, eng, names, dst, between=None, only=None):
            at = -1
            for n, job in enumerate(ORDER):
                if job[0] not in names or evacuator(n) != me or (only is not None and n not in only):
                    continue
                at += 1
                if between is not None:
                    between(at)
                eng.wait_ge(s_job, n + 1)
                for i, (o, b, scale) in enumerate(dst(job, bank[JOB_BANK[n]])):
                    if job[0] in ("mix", "co"):
                        ins = nc.vector.tensor_tensor(o, b, o, ALU.add)
                    elif me == "act":
                        ins = nc.scalar.mul(o, b, scale) if scale != 1.0 else nc.scalar.copy(o, b)
                    elif scale != 1.0:
                        ins = nc.vector.tensor_scalar(o, b, scale, None, ALU.mult)
                    else:
                        ins = nc.vector.tensor_copy(o, b)
                ins.then_inc(s_taken[me], 1)

        def project_dst(job, b):
            what, ja, jb = job
            n = 512 if jb == 0 else P
            at = 512 * jb
            if what == "dq":
                return [(dq[:, ja, at:at + n], b[:, 0:n], 0.125)]
            if what == "conv":
                if jb == 0:
                    return [(cv[:, ja, 3:GS], b[:, :], 1.0)]
                return [(cv[:, ja, GS:GW].rearrange("p (b c) -> p b c", b=NB)[:, :, 3:],
                         b[:, 0:P].rearrange("p (b c) -> p b c", b=NB), 1.0)]
            if what == "gab":
                return [(gab, b[:, 0:8 * NT], 1.0)]
            return [({"dk": dk_tok, "dv": dv, "gz": gz}[what][:, ja, :], b[:, :], 1.0)]

        W_COUNT, _count = {}, [0, 0]
        for name, n in UNIT.items():
            if not (name[0:2] == "da" or name[0] == "x"):
                _count[n % 2] += 1
                W_COUNT[n] = _count[n % 2]

        LAST_JOB = {unit_of(job): n for n, job in enumerate(ORDER)}

        def load_weight(eng, name, src, cols):
            n = UNIT[name]
            b = n - 2 - UNIT["da0"]
            if 0 <= b < NB:
                eng.wait_ge(das_pe["pv"], das_pe.after(b, "pv"))
            if n - 2 in LAST_JOB:
                eng.wait_ge(s_job, LAST_JOB[n - 2] + 1)
            eng.dma_start(slot(n), src.rearrange("(c p) n -> p c n", p=P)[:, :, cols]).then_inc(s_w[n % 2], 16)

        lam4 = little(4 * 64)
        lamp = little(2)
        lame = little(2)
        nlam = little(1)
        row_sign = little(1)
        alog = little(4)
        dtb = little(4)
        nexp_a = little(4)
        glog = little(4 * NT)
        beta = little(4 * NT)
        tz, te = little(4 * NT), little(4 * NT)
        eps = C("eps")

        hist = act_b[0:NB * 3, 2560:4096]
        tails = act_b[:, 4096:4096 + 12 * 27].rearrange("p (m c) -> p m c", m=12)
        tails_tok = act_b[0:27, 2560:4096]

        p_dve = steps("prep_dve", "lam0 lam1 nlam sign sign2 gsub hist kT0 kT1 kT2 kT3 kT4 tt0 tt1 tt2 "
                                  "na z az sp0 sp1 g b1 b2")
        p_act = steps("prep_act", "lam ea e l eb")
        p_pe = steps("prep_pe", "hist kT0 kT1 kT2 kT3 kT4 tt0 tt1 tt2")
        p_pool = steps("prep_pool", "zero")
        s_small = sem("small_loaded")

        def prep_sync_load(sp):
            for i, n in enumerate(("lam_q1", "lam_k1", "lam_q2", "lam_k2")):
                sp.dma_start(lam4[:, 64 * i:64 * i + 64], a[n][0].partition_broadcast(P)).then_inc(s_small, 16)
            sp.dma_start(alog, a["a_log"][0].partition_broadcast(P)).then_inc(s_small, 16)
            sp.dma_start(dtb, a["dt_bias"][0].partition_broadcast(P)).then_inc(s_small, 16)
            sp.dma_start(gdn_g[:, 0:128], a["g_subln"][0].partition_broadcast(P)).then_inc(s_small, 16)
            sp.dma_start(gdn_g[:, 128:256], a["g_gdn_out"][0].partition_broadcast(P)).then_inc(s_small, 16)
            for m in range(CONV):
                sp.dma_start(convw[:, :, m], a["conv_w"][0][m].rearrange("(m p) -> p m", p=P),
                             allow_slow_non_contiguous=True).then_inc(s_small, 16)
            sp.dma_start(w_gab[:, :, :], a["w_in"][0].rearrange("(c p) n -> p c n", p=P)[:, :, 3072:3080]).then_inc(s_small, 16)

        N_SMALL = 16 * (4 + 2 + 2 + CONV + 1)

        def prep_pool_a(pool):
            p_pool.arm(pool)
            nc.gpsimd.memset(cv[:, :, 0:3], 0.0).then_inc(p_pool.step("zero"), 1)

        def prep_dve_a(dve):
            p_dve.arm(dve)
            dve.wait_ge(s_small, N_SMALL)
            dve.wait_ge(s_const, 16)
            l4 = lam4.rearrange("p (a b c) -> p a b c", a=2, b=2)
            nc.vector.tensor_tensor(l4[:, :, 0, :], l4[:, :, 0, :], l4[:, :, 1, :], ALU.mult).then_inc(p_dve.step("lam0"), 1)
            dve.wait_ge(p_dve["lam0"], p_dve.after(0, "lam0"))
            nc.vector.tensor_reduce(lamp, l4[:, :, 0, :], AX.X, ALU.add).then_inc(p_dve.step("lam1"), 1)
            dve.wait_ge(p_act["lam"], p_act.after(0, "lam"))
            nc.vector.scalar_tensor_tensor(nlam, lame[:, 1:2], -LAM_INIT, lame[:, 0:1], ALU.add, ALU.subtract).then_inc(p_dve.step("nlam"), 1)
            dve.wait_ge(p_dve["nlam"], p_dve.after(0, "nlam"))
            nc.vector.tensor_tensor(row_sign, C("map1"), nlam, ALU.mult).then_inc(p_dve.step("sign"), 1)
            dve.wait_ge(p_dve["sign"], p_dve.after(0, "sign"))
            nc.vector.tensor_tensor(row_sign, row_sign, C("map0"), ALU.add).then_inc(p_dve.step("sign2"), 1)
            nc.vector.tensor_scalar(gdn_g[:, 0:128], gdn_g[:, 0:128], 1.0 - LAM_INIT, None, ALU.mult).then_inc(p_dve.step("gsub"), 1)
            dve.wait_ge(p_pe["hist"], p_pe.after(0, "hist"))
            for b in range(NB):
                ins = nc.vector.tensor_copy(cv[:, :, GS + 19 * b:GS + 19 * b + 3],
                                            bank[7][:, 0:288].rearrange("p (m r) -> p m r", m=12)[:, :, 3 * b:3 * b + 3])
            ins.then_inc(p_dve.step("hist"), 1)

        def prep_act_a(act):
            p_act.arm(act)
            act.wait_ge(p_dve["lam1"], p_dve.after(0, "lam1"))
            nc.scalar.activation(lame, lamp, ACT.Exp).then_inc(p_act.step("lam"), 1)
            nc.scalar.activation(nexp_a, alog, ACT.Exp).then_inc(p_act.step("ea"), 1)

        def prep_pe_a(pe):
            p_pe.arm(pe)
            pe.wait_ge(s_const, 16)
            pe.wait_ge(s_hist, 16)
            for m in range(12):
                mm = nc.tensor.transpose(bank[7][:, 24 * m:24 * m + 24], hist[:, m * P:(m + 1) * P], ident[0:24, 0:24])
            mm.then_inc(p_pe.step("hist"), 1)

        def prep_pe_b(pe):
            for t in range(NT):
                pe.wait_ge(taken(ORDER.index(("dk", t, 0))), taken_count(ORDER.index(("dk", t, 0))))
                if t >= 2:
                    pe.wait_ge(p_dve[f"kT{t - 2}"], p_dve.after(0, f"kT{t - 2}"))
                else:
                    pe.wait_ge(n_dve["mix"][f"ev{NT - 1}b"], n_dve["mix"].after(0, f"ev{NT - 1}b"))
                for h in range(H):
                    mm = nc.tensor.transpose(quarters(bank[4 + t % 2])[:, h, :], dk_tok[:, t, h * P:(h + 1) * P], ident)
                mm.then_inc(p_pe.step(f"kT{t}"), 1)

        def tails_pe(pe):
            pe.wait_ge(c_pool["tail1"], c_pool.after(11, "tail1"))
            pe.wait_ge(d_act["aT"], d_act.after(UN - 1, "aT"))
            for g in range(3):
                if g == 2:
                    pe.wait_ge(p_dve["tt0"], p_dve.after(0, "tt0"))
                for i in range(4):
                    mm = nc.tensor.transpose(bank[4 + g % 2][0:27, i * P:(i + 1) * P], tails[:, 4 * g + i, :], ident)
                mm.then_inc(p_pe.step(f"tt{g}"), 1)

        def turn_k_dve(dve):
            for t in range(NT):
                dve.wait_ge(p_pe[f"kT{t}"], p_pe.after(0, f"kT{t}"))
                nc.vector.tensor_copy(dk[:, :, t * P:(t + 1) * P], quarters(bank[4 + t % 2])).then_inc(p_dve.step(f"kT{t}"), 1)

        def prep_dve_b(dve):
            for g in range(3):
                dve.wait_ge(p_pe[f"tt{g}"], p_pe.after(0, f"tt{g}"))
                nc.vector.tensor_copy(tails_tok[:, g * 512:(g + 1) * 512], bank[4 + g % 2][0:27, :]).then_inc(p_dve.step(f"tt{g}"), 1)
            dve.wait_ge(p_act["ea"], p_act.after(0, "ea"))
            nc.vector.tensor_scalar(nexp_a, nexp_a, -1.0, None, ALU.mult).then_inc(p_dve.step("na"), 1)
            dve.wait_ge(p_dve["na"], p_dve.after(0, "na"))
            dve.wait_ge(taken(LAST_OF["gab"]), taken_count(LAST_OF["gab"]))
            g3 = gab.rearrange("p (t c) -> p t c", t=NT)

            def wide(v):
                return v.unsqueeze(1).to_broadcast([P, NT, 4])

            v3 = lambda v: v.rearrange("p (t c) -> p t c", t=NT)
            nc.vector.tensor_tensor(v3(tz), g3[:, :, 0:4], wide(dtb), ALU.add).then_inc(p_dve.step("z"), 1)
            dve.wait_ge(p_dve["z"], p_dve.after(0, "z"))
            nc.vector.scalar_tensor_tensor(te, tz, -1.0, tz, ALU.mult, ALU.max).then_inc(p_dve.step("az"), 1)
            dve.wait_ge(p_act["l"], p_act.after(0, "l"))
            nc.vector.tensor_scalar(tz, tz, 0.0, None, ALU.max).then_inc(p_dve.step("sp0"), 1)
            dve.wait_ge(p_dve["sp0"], p_dve.after(0, "sp0"))
            nc.vector.tensor_tensor(tz, tz, te, ALU.add).then_inc(p_dve.step("sp1"), 1)
            dve.wait_ge(p_dve["sp1"], p_dve.after(0, "sp1"))
            nc.vector.tensor_tensor(v3(glog), v3(tz), wide(nexp_a), ALU.mult).then_inc(p_dve.step("g"), 1)
            dve.wait_ge(p_act["eb"], p_act.after(0, "eb"))
            nc.vector.tensor_scalar(beta, beta, 1.0, None, ALU.add).then_inc(p_dve.step("b1"), 1)
            dve.wait_ge(p_dve["b1"], p_dve.after(0, "b1"))
            nc.vector.reciprocal(beta, beta).then_inc(p_dve.step("b2"), 1)

        def prep_act_b(act):
            act.wait_ge(taken(LAST_OF["gab"]), taken_count(LAST_OF["gab"]))
            act.wait_ge(p_dve["az"], p_dve.after(0, "az"))
            nc.scalar.activation(te, te, ACT.Exp, scale=-1.0).then_inc(p_act.step("e"), 1)
            act.wait_ge(p_act["e"], p_act.after(0, "e"))
            nc.scalar.activation(te, te, ACT.Ln, bias=C("ones")[:, 0:1]).then_inc(p_act.step("l"), 1)
            nc.scalar.activation(beta.rearrange("p (t c) -> p t c", t=NT),
                                            gab.rearrange("p (t c) -> p t c", t=NT)[:, :, 4:8], ACT.Exp, scale=-1.0).then_inc(p_act.step("eb"), 1)

        NY = GW - 3
        c_mul = steps("conv_products", "m0 m1 m2 m3")
        c_pool = steps("conv_pool", "tail0 tail1 y1 y2 y3")
        c_act = steps("conv_silu", "silu0 silu3 silu6 silu9 gz")
        taps = scr[:, :, :].rearrange("p a b -> p (a b)")[:, 0:4 * NY].rearrange("p (j c) -> p j c", j=CONV)

        def conv_act_one(act, m):
            for jb in range(2):
                n = ORDER.index(("conv", m, jb))
                act.wait_ge(taken(n), taken_count(n))
            if m == 0:
                c_mul.arm(act)
                act.wait_ge(p_dve["hist"], p_dve.after(0, "hist"))
                act.wait_ge(p_pool["zero"], p_pool.after(0, "zero"))
                act.wait_ge(n_pe["mix"][f"tr{NT - 1}b"], n_pe["mix"].after(0, f"tr{NT - 1}b"))
            act.wait_ge(c_pool["y3"], c_pool.after(m - 1, "y3"))
            for j in range(CONV):
                nc.scalar.mul(taps[:, j, :], cv[:, m, j:j + NY], convw[:, m, j:j + 1]).then_inc(c_mul.step(f"m{j}"), 1)

        def conv_pool_one(pool, m):
            for jb in range(2):
                n = ORDER.index(("conv", m, jb))
                pool.wait_ge(taken(n), taken_count(n))
            nc.gpsimd.tensor_copy(tails[:, m, 0:3], cv[:, m, GS - 3:GS]).then_inc(c_pool.step("tail0"), 1)
            last3 = cv[:, m, GS:GW].rearrange("p (b c) -> p b c", b=NB)[:, :, TB:]
            nc.gpsimd.tensor_copy(tails[:, m, 3:27].rearrange("p (b c) -> p b c", b=NB), last3).then_inc(c_pool.step("tail1"), 1)
            pool.wait_ge(c_mul["m3"], c_mul.after(m, "m3"))
            nc.gpsimd.tensor_tensor(taps[:, 0, :], taps[:, 0, :], taps[:, 1, :], ALU.add).then_inc(c_pool.step("y1"), 1)
            nc.gpsimd.tensor_tensor(taps[:, 2, :], taps[:, 2, :], taps[:, 3, :], ALU.add).then_inc(c_pool.step("y2"), 1)
            pool.wait_ge(c_pool["y2"], c_pool.after(m, "y2"))
            nc.gpsimd.tensor_tensor(cv[:, m, 0:NY], taps[:, 0, :], taps[:, 2, :], ALU.add).then_inc(c_pool.step("y3"), 1)

        def gate_act(act):
            act.wait_ge(taken(LAST_OF["gz"]), taken_count(LAST_OF["gz"]))
            act.wait_ge(taken(LAST_OF["gz"] - 1), taken_count(LAST_OF["gz"] - 1))
            nc.scalar.activation(gz[:, :, :], gz[:, :, :], ACT.Silu).then_inc(c_act.step("gz"), 1)

        UN = NTP * H
        da_out = spare[0].rearrange("p (h t) -> p h t", h=H)
        moved = steps("da_outputs", "moved")
        d_pe = steps("da_pe", "sc | tr | pv")
        d_dve = steps("da_dve", "cut mx | r c2 a0 a")
        d_act = steps("da_act", "p0 p1 | aT")
        prob = [x_buf[:, 1024 * i:1024 * (i + 1)].rearrange("p (m k) -> p m k", m=2) for i in range(2)]
        aT = [x_buf[:, 2048 + 512 * i:2560 + 512 * i] for i in range(2)]
        osq, on = x_buf[:, 3072:3584], x_buf[:, 3584:4096]
        nmax = [little(2) for _ in range(2)]
        psum_p = [little(2) for _ in range(2)]
        pr = [little(2) for _ in range(2)]
        o_pe = steps("da_out_pe", "oT")
        o_act = steps("da_out_act", "sq mix")
        o_dve = steps("da_out_dve", "ss on og")
        o_pool = steps("da_out_pool", "ms rn")
        oss = little(4)

        def b4(v):
            return v.unsqueeze(2).to_broadcast([P, 4, P])

        def h4(v):
            return v.rearrange("p (h c) -> p h c", h=4)

        def beside(u):
            if u < 12:
                return [ORDER.index(("conv", u, jb)) for jb in range(2)]
            return [ORDER.index(("gz", u - 12, 0))] if u < 17 else [ORDER.index(("gab", 0, 0))] if u == 17 else []

        def da_pe(pe):
            d_pe.arm(pe)
            o_pe.arm(pe)
            for u in range(UN + 2):
                t, h = divmod(u, H)
                q = u % 2
                if u < UN:
                    if u == 0:
                        all_taken(pe, LAST_OF["dv"])
                        pe.wait_ge(p_dve["kT4"], p_dve.after(0, "kT4"))
                    else:
                        pe.wait_ge(d_act["p1"], d_act.after(u - 1, "p1"))
                    for m in range(2):
                        rows = slice(64 * m, 64 * m + 64)
                        mm = nc.tensor.matmul(bank[2 + m][:, 0:P * (t + 1)], dq[rows, h, t * P:(t + 1) * P],
                                              dk[rows, h, 0:P * (t + 1)], start=True, stop=True)
                    mm.then_inc(d_pe.step("sc"), 1)
                run_jobs(pe, ("conv", "gz", "gab"), act_a, None, beside(u)[:1])
                if 1 <= u and h == 0 and t >= 1:
                    pe.wait_ge(o_dve["og"], o_dve.after(t - 1, "og"))
                    for c in range(H):
                        mm = nc.tensor.transpose(quarters(bank[6 + (t - 1) % 2])[:, c, :], on[:, c * P:(c + 1) * P], ident)
                    mm.then_inc(o_pe.step("oT"), 1)
                if u < UN:
                    pe.wait_ge(d_dve["a"], d_dve.after(u, "a"))
                    for k in range(t + 1):
                        mm = nc.tensor.transpose(bank[4 + q][:, k * P:(k + 1) * P], prob[q][:, 0, k * P:(k + 1) * P], ident)
                    mm.then_inc(d_pe.step("tr"), 1)
                run_jobs(pe, ("conv", "gz", "gab"), act_a, None, beside(u)[1:])
                if u < UN:
                    pe.wait_ge(d_act["aT"], d_act.after(u, "aT"))
                    if h == 0 and t >= 2:
                        pe.wait_ge(o_act["mix"], o_act.after(t - 2, "mix"))
                    for k in range(t + 1):
                        mm = nc.tensor.matmul(bank[6 + t % 2][:, h * P:(h + 1) * P], aT[q][:, k * P:(k + 1) * P],
                                              dv[:, k, h * P:(h + 1) * P], start=k == 0, stop=k == t)
                    mm.then_inc(d_pe.step("pv"), 1)

        def da_dve(dve):
            d_dve.arm(dve)
            o_dve.arm(dve)
            for u in range(UN + 2):
                t, h = divmod(u, H)
                q = u % 2
                n = P * (t + 1)
                if u < UN:
                    dve.wait_ge(d_pe["sc"], d_pe.after(u, "sc"))
                    for m in range(2):
                        ins = nc.vector.memset(bank[2 + m][0:64, P * t + 64:P * t + 128], -BIG)
                    ins.then_inc(d_dve.step("cut"), 1)
                    dve.wait_ge(d_dve["cut"], d_dve.after(u, "cut"))
                    for m in range(2):
                        ins = nc.vector.tensor_reduce(nmax[q][:, m:m + 1], bank[2 + m][:, 0:n], AX.X, ALU.max, negate=True)
                    ins.then_inc(d_dve.step("mx"), 1)
                if h == 0 and t >= 1:
                    head_norm_dve(dve, o_dve, o_act, o_pool, t - 1, bank[6 + (t - 1) % 2], gdn_g[:, 0:128], osq, on)
                if u < UN:
                    dve.wait_ge(d_act["p1"], d_act.after(u, "p1"))
                    nc.vector.reciprocal(pr[q], psum_p[q]).then_inc(d_dve.step("r"), 1)
                    dve.wait_ge(d_dve["r"], d_dve.after(u, "r"))
                    nc.vector.tensor_tensor(pr[q][:, 1:2], pr[q][:, 1:2], nlam, ALU.mult).then_inc(d_dve.step("c2"), 1)
                    dve.wait_ge(d_dve["c2"], d_dve.after(u, "c2"))
                    nc.vector.tensor_scalar(prob[q][:, 0, 0:n], prob[q][:, 0, 0:n], pr[q][:, 0:1], None, ALU.mult).then_inc(d_dve.step("a0"), 1)
                    dve.wait_ge(d_dve["a0"], d_dve.after(u, "a0"))
                    nc.vector.scalar_tensor_tensor(prob[q][:, 0, 0:n], prob[q][:, 1, 0:n], pr[q][:, 1:2], prob[q][:, 0, 0:n],
                                                   ALU.mult, ALU.add).then_inc(d_dve.step("a"), 1)
                take_jobs("dve", dve, ("conv", "gz", "gab"), project_dst, None, beside(u))

        def head_norm_dve(dve, s, s_act, s_pool, t, b, gain, osq, on, part=None):
            if part != 1:
                dve.wait_ge(s_act["sq"], s_act.after(t, "sq"))
                nc.vector.tensor_reduce(oss, h4(osq), AX.X, ALU.add).then_inc(s.step("ss"), 1)
            if part != 0:
                dve.wait_ge(s_pool["rn"], s_pool.after(t, "rn"))
                nc.vector.tensor_tensor(h4(on), h4(b[:, :]), b4(oss), ALU.mult).then_inc(s.step("on"), 1)
                dve.wait_ge(s["on"], s.after(t, "on"))
                nc.vector.tensor_tensor(h4(on), h4(on), gain.unsqueeze(1).to_broadcast([P, 4, P]), ALU.mult).then_inc(s.step("og"), 1)

        def head_norm_pool(pool, s, s_dve, t):
            pool.wait_ge(s_dve["ss"], s_dve.after(t, "ss"))
            nc.gpsimd.tensor_scalar(oss, oss, 1.0 / P, EPS, ALU.mult, ALU.add).then_inc(s.step("ms"), 1)
            pool.wait_ge(s["ms"], s.after(t, "ms"))
            nc.gpsimd.tensor_tensor(oss, oss, C("minus_half")[:, 0:4], ALU.pow).then_inc(s.step("rn"), 1)

        def da_act(act):
            d_act.arm(act)
            o_act.arm(act)
            c_act.arm(act)
            for u in range(UN + 2):
                t, h = divmod(u, H)
                q = u % 2
                n = P * (t + 1)
                if u < UN:
                    act.wait_ge(d_dve["mx"], d_dve.after(u, "mx"))
                    if u >= 2:
                        act.wait_ge(d_pe["tr"], d_pe.after(u - 2, "tr"))
                    for m in range(2):
                        nc.scalar.activation(prob[q][:, m, 0:n], bank[2 + m][:, 0:n], ACT.Exp, bias=nmax[q][:, m:m + 1],
                                             accum_out=psum_p[q][:, m:m + 1]).then_inc(d_act.step(f"p{m}"), 1)
                if 1 <= u <= 12:
                    conv_act_one(act, u - 1)
                take_jobs("act", act, ("conv", "gz", "gab"), project_dst, None, beside(u)[:1])
                if h == 0 and t >= 1:
                    act.wait_ge(o_pe["oT"], o_pe.after(t - 1, "oT"))
                    nc.scalar.copy(da_out[:, :, (t - 1) * P:t * P], quarters(bank[6 + (t - 1) % 2])).then_inc(o_act.step("mix"), 1)
                if u < UN:
                    act.wait_ge(d_pe["tr"], d_pe.after(u, "tr"))
                    if u >= 2:
                        act.wait_ge(d_pe["pv"], d_pe.after(u - 2, "pv"))
                    nc.scalar.copy(aT[q][:, 0:n], bank[4 + q][:, 0:n]).then_inc(d_act.step("aT"), 1)
                take_jobs("act", act, ("conv", "gz", "gab"), project_dst, None, beside(u)[1:])
                if u < UN and h == H - 1:
                    act.wait_ge(d_pe["pv"], d_pe.after(u, "pv"))
                    nc.scalar.activation(osq, bank[6 + t % 2][:, :], ACT.Square).then_inc(o_act.step("sq"), 1)
                if u >= 4 and (u - 4) % 3 == 0 and u <= 13:
                    m = u - 4
                    act.wait_ge(c_pool["y3"], c_pool.after(m + 2, "y3"))
                    nc.scalar.activation(cv[:, m:m + 3, 0:NY], cv[:, m:m + 3, 0:NY], ACT.Silu).then_inc(c_act.step(f"silu{m}"), 1)
            act.wait_ge(s_job, len(JOBS["project"]))
            act.wait_ge(o_act["mix"], o_act.after(NTP - 1, "mix"))
            moved.arm(act)
            nc.scalar.copy(act_a[:, 0:4, 0:SEQ], da_out).then_inc(moved.step("moved"), 1)

        def da_pool(pool):
            o_pool.arm(pool)
            c_pool.arm(pool)
            pool.wait_ge(p_dve["hist"], p_dve.after(0, "hist"))
            pool.wait_ge(p_pool["zero"], p_pool.after(0, "zero"))
            for u in range(UN + 2):
                if u % H == 0 and u >= H:
                    head_norm_pool(pool, o_pool, o_dve, u // H - 1)
                if 1 <= u <= 12:
                    conv_pool_one(pool, u - 1)

        STAGES = 8
        sq_ = spare[1][:, 0:512].rearrange("p (h t) -> p h t", h=H)
        sk_ = spare[1][:, 512:1024].rearrange("p (h t) -> p h t", h=H)
        sv_ = spare[1][:, 1024:1536]
        s_aT = spare[1][:, 1536:1536 + 336]
        s_q = spare[0][:, 0:256].rearrange("p (c r) -> p c r", r=32)
        s_P, s_sn, s_cm = spare[0][:, 256:896], spare[0][:, 896:1024], spare[0][:, 1024:1088]
        s_o = spare[0][:, 1088:1344]
        s_KT = act_b[:, 0:2048]
        da_oT = act_b[:, 4608:5120].rearrange("p (h t) -> p h t", h=H)
        s_mx, s_sum = little(4), little(4)
        das_pe = steps("da_stream_pe", "f0 f1 f2 f3 sc pT pv oT")
        das_dve = steps("da_stream_dve", "q f1 f3 sn mx mx2 mxm sum r c cm pT")
        das_act = steps("da_stream_act", "f0 f2 p pn pv o")
        das_copy = steps("da_stream_sample", "zq za q k v")

        def kv_slot(first_unit, k, cross):
            w = W[:, (first_unit + k) % 2, 0:4096]
            n = 2 if cross else 4
            return (w[:, 0:2048].rearrange("p (m c) -> p m c", m=n), w[:, 2048:4096].rearrange("p (m c) -> p m c", m=n))

        def streams_sync(sp, first_unit, ck, cvv, s_pe):

            def one(b, k):
                if isinstance(b, int):
                    sp.wait_ge(s_job, LAST_JOB[first_unit + b - 2] + 1)
                else:
                    sp.wait_ge(s_pe["pv"], s_pe.after(b - 2, "pv"))
                kk, vv = kv_slot(first_unit, k, ck.shape[4] != 128)

                def src(c):
                    v = c[0][b] if isinstance(b, int) else c[0][bass.ds(b, 1)].rearrange("o t h c -> (o t) h c")
                    return v.rearrange("(t p) h c -> p t (h c)", p=P)

                sp.dma_start(kk, src(ck)).then_inc(s_kv[k], 16)
                sp.dma_start(vv, src(cvv)).then_inc(s_kv[k], 16)

            one(0, 0)
            one(1, 1)
            with sp.Fori(1, NB // 2) as i:
                one(sp.snap(2 * i), 0)
                one(sp.snap(2 * i + 1), 1)

        def das_pe_stage(pe, b, k, stage):
            kk, vv = kv_slot(UNIT["da0"], k, False)
            if stage < 4:
                f = stage
                if f == 0:
                    pe.wait_ge(s_kv[k], (b - k) * 16 + 32)
                    pe.wait_ge(das_act["pv"], das_act.after(b - 1, "pv"))
                elif f % 2:
                    pe.wait_ge(das_act[f"f{f - 1}"], das_act.after(b, f"f{f - 1}"))
                else:
                    pe.wait_ge(das_dve[f"f{f - 1}"], das_dve.after(b, f"f{f - 1}"))
                for i in range(4):
                    mm = nc.tensor.transpose(quarters(bank[6])[:, i, :], kk[:, i, f * P:(f + 1) * P], ident)
                mm.then_inc(das_pe.step(f"f{f}"), 1)
            elif stage == 4:
                pe.wait_ge(das_dve["f3"], das_dve.after(b, "f3"))
                pe.wait_ge(das_act["f2"], das_act.after(b, "f2"))
                pe.wait_ge(das_act["o"], das_act.after(b - 1, "o"))
                kt = s_KT.rearrange("p (h m) -> p h m", h=H)
                for h in range(H):
                    nc.tensor.matmul(bank[7][32 * h:32 * h + 32, :], s_q[:, h, :], kt[:, h, :], start=True, stop=True)
                for h in range(H):
                    mm = nc.tensor.matmul(bank[6][32 * h:32 * h + 32, 0:P], s_q[:, h, :], sk_[:, h, :], start=True, stop=True)
                mm.then_inc(das_pe.step("sc"), 1)
            elif stage == 5:
                pe.wait_ge(das_dve["cm"], das_dve.after(b, "cm"))
                for c in range(5):
                    mm = nc.tensor.matmul(bank[7][:, 64 * c:64 * c + 64], s_P[:, c * P:(c + 1) * P], s_cm, start=True, stop=True)
                mm.then_inc(das_pe.step("pT"), 1)
            elif stage == 6:
                pe.wait_ge(das_dve["pT"], das_dve.after(b, "pT"))
                for c in range(5):
                    for h in range(H):
                        v = vv[:, c, h * P:(h + 1) * P] if c < 4 else sv_[:, h * P:(h + 1) * P]
                        mm = nc.tensor.matmul(bank[6][32 * h:32 * h + 32, 0:P], s_aT[:, 64 * c + 16 * h:64 * c + 16 * h + 32], v,
                                              start=c == 0, stop=c == 4, skip_group_check=True)
                mm.then_inc(das_pe.step("pv"), 1)
            else:
                pe.wait_ge(das_act["pv"], das_act.after(b, "pv"))
                nc.tensor.transpose(bank[7][:, 0:P], s_o[:, 0:P], ident).then_inc(das_pe.step("oT"), 1)

        def das_act_stage(act, b, stage):
            if stage in (0, 2):
                act.wait_ge(das_pe[f"f{stage}"], das_pe.after(b, f"f{stage}"))
                nc.scalar.copy(s_KT[:, 512 * stage:512 * stage + 512], bank[6][:, :]).then_inc(das_act.step(f"f{stage}"), 1)
            elif stage == 4:
                act.wait_ge(das_dve["mxm"], das_dve.after(b, "mxm"))
                nc.scalar.activation(s_P[:, 0:512], bank[7][:, :], ACT.Exp, bias=s_mx[:, 0:1],
                                     accum_out=s_sum[:, 0:1]).then_inc(das_act.step("p"), 1)
                nc.scalar.activation(s_P[:, 512:640], s_sn, ACT.Exp, bias=s_mx[:, 0:1],
                                     accum_out=s_sum[:, 1:2]).then_inc(das_act.step("pn"), 1)
            elif stage == 6:
                act.wait_ge(das_pe["pv"], das_pe.after(b, "pv"))
                nc.scalar.copy(s_o[:, 0:P], bank[6][:, 0:P]).then_inc(das_act.step("pv"), 1)
            elif stage == 7:
                act.wait_ge(das_pe["oT"], das_pe.after(b, "oT"))
                nc.scalar.copy(da_oT[:, :, bass.ds(b * TB, TB)],
                               bank[7][:, 0:P].rearrange("p (h t) -> p h t", h=H)[:, :, 0:TB]).then_inc(das_act.step("o"), 1)

        def das_dve_stage(dve, b, stage):
            if stage == 0:
                dve.wait_ge(das_pe["sc"], das_pe.after(b - 1, "sc"))
                nc.vector.tensor_copy(s_q[0:64, 0:4, 0:16], sq_[0:64, :, bass.ds(b * TB, TB)])
                nc.vector.tensor_copy(s_q[64:128, 0:4, 16:32], sq_[64:128, :, bass.ds(b * TB, TB)]).then_inc(das_dve.step("q"), 1)
            elif stage in (1, 3):
                dve.wait_ge(das_pe[f"f{stage}"], das_pe.after(b, f"f{stage}"))
                nc.vector.tensor_copy(s_KT[:, 512 * stage:512 * stage + 512], bank[6][:, :]).then_inc(das_dve.step(f"f{stage}"), 1)
            elif stage == 4:
                dve.wait_ge(das_pe["sc"], das_pe.after(b, "sc"))
                w = C("stream_off")[:, bass.ds(b * P, P)]
                nc.vector.tensor_tensor(s_sn, bank[6][:, 0:P], w, ALU.add).then_inc(das_dve.step("sn"), 1)
                nc.vector.tensor_reduce(s_mx[:, 1:2], bank[7][:, :], AX.X, ALU.max).then_inc(das_dve.step("mx"), 1)
                dve.wait_ge(das_dve["mx"], das_dve.after(b, "mx"))
                nc.vector.tensor_reduce(s_mx[:, 2:3], s_sn, AX.X, ALU.max).then_inc(das_dve.step("mx2"), 1)
                dve.wait_ge(das_dve["mx2"], das_dve.after(b, "mx2"))
                nc.vector.scalar_tensor_tensor(s_mx[:, 0:1], s_mx[:, 1:2], s_mx[:, 2:3], C("minus_one"),
                                               ALU.max, ALU.mult).then_inc(das_dve.step("mxm"), 1)
            elif stage == 5:
                dve.wait_ge(das_act["pn"], das_act.after(b, "pn"))
                nc.vector.tensor_tensor(s_sum[:, 2:3], s_sum[:, 0:1], s_sum[:, 1:2], ALU.add).then_inc(das_dve.step("sum"), 1)
                dve.wait_ge(das_dve["sum"], das_dve.after(b, "sum"))
                nc.vector.reciprocal(s_sum[:, 3:4], s_sum[:, 2:3]).then_inc(das_dve.step("r"), 1)
                dve.wait_ge(das_dve["r"], das_dve.after(b, "r"))
                nc.vector.tensor_tensor(s_sum[:, 2:3], s_sum[:, 3:4], row_sign, ALU.mult).then_inc(das_dve.step("c"), 1)
                dve.wait_ge(das_dve["c"], das_dve.after(b, "c"))
                nc.vector.tensor_scalar(s_cm, C("pick"), s_sum[:, 2:3], None, ALU.mult).then_inc(das_dve.step("cm"), 1)
            elif stage == 6:
                dve.wait_ge(das_pe["pT"], das_pe.after(b, "pT"))
                nc.vector.tensor_copy(s_aT[:, 0:320], bank[7][:, 0:320]).then_inc(das_dve.step("pT"), 1)

        def das_start(dve):
            das_dve.arm(dve)
            das_copy.arm(dve)
            dve.wait_ge(moved["moved"], moved.after(0, "moved"))
            nc.vector.memset(s_q, 0.0).then_inc(das_copy.step("zq"), 1)
            nc.vector.memset(s_aT[:, 320:336], 0.0).then_inc(das_copy.step("za"), 1)
            nc.vector.tensor_copy(sq_, dq[:, :, SEQ:]).then_inc(das_copy.step("q"), 1)
            nc.vector.tensor_copy(sk_, dk[:, :, SEQ:]).then_inc(das_copy.step("k"), 1)
            nc.vector.tensor_copy(sv_, dv[:, 4, :]).then_inc(das_copy.step("v"), 1)
            dve.wait_ge(das_copy["v"], das_copy.after(0, "v"))

        t_pe = steps("da_s_pe", "turn oT")
        t_act = steps("da_s_act", "sq mix")
        t_dve = steps("da_s_dve", "ss on og")
        t_pool = steps("da_s_pool", "ms rn")

        t_on, t_sq = spare[0][:, 1344:1856], spare[1][:, 0:512]

        def das_out_pe(pe, i):
            if i == 0:
                t_pe.arm(pe)
                pe.wait_ge(das_act["o"], das_act.after(NB - 1, "o"))
                for h in range(H):
                    mm = nc.tensor.transpose(quarters(bank[6])[:, h, :], da_oT[:, h, :], ident)
                mm.then_inc(t_pe.step("turn"), 1)
            elif i == 4:
                pe.wait_ge(t_dve["og"], t_dve.after(0, "og"))
                for h in range(H):
                    mm = nc.tensor.transpose(quarters(bank[7])[:, h, :], t_on[:, h * P:(h + 1) * P], ident)
                mm.then_inc(t_pe.step("oT"), 1)

        def das_out_act(act, i):
            if i == 0:
                t_act.arm(act)
                act.wait_ge(t_pe["turn"], t_pe.after(0, "turn"))
                nc.scalar.activation(t_sq, bank[6][:, :], ACT.Square).then_inc(t_act.step("sq"), 1)
            elif i == 4:
                act.wait_ge(t_pe["oT"], t_pe.after(0, "oT"))
                nc.scalar.copy(act_a[:, 0:4, SEQ:], quarters(bank[7])).then_inc(t_act.step("mix"), 1)

        def das_out_dve(dve, i):
            if i == 1:
                t_dve.arm(dve)
                head_norm_dve(dve, t_dve, t_act, t_pool, 0, bank[6], gdn_g[:, 0:128], t_sq, t_on, 0)
            elif i == 3:
                head_norm_dve(dve, t_dve, t_act, t_pool, 0, bank[6], gdn_g[:, 0:128], t_sq, t_on, 1)

        g_act, g_pe, g_dve, g_pool = (steps("gdn_" + e, n) for e, n in
                                      (("act", GDN_ACT), ("pe", GDN_PE), ("dve", GDN_DVE), ("pool", GDN_POOL)))
        gs_act, gs_pe, gs_dve, gs_pool = (steps("gdn_s_" + e, n) for e, n in (
            ("act", "stage0 stage1 stage2 sq0 sq1 EG eg D DT qT Mt M2 M2t M4 M4t M8 w osq mix"),
            ("pe", "tokqk tokv cum gcum chq chk kk kq Mt sq2 sq2t x1 sq4 sq4t x2 sq8 x3 w oT"),
            ("dve", "gb gB gc S SD SU ss ssq qk0 qk1 kT vb be kbg kl ktail L0 L AT M X0 X1 X2 X3 qd oss oms on og oz"),
            ("pool", GDN_POOL)))
        gh_pe = steps("gdn_state_pe", "vn o s")
        gh_dve = steps("gdn_state_dve", "wM qM vn vM sg s0 s1")
        s_state = sem("states_loaded")

        stage = attn[:, 0:1536].rearrange("p (m t) -> p m t", m=12)
        qk_tok = attn[:, 1536:2560]
        qT, kT, vb, kbg, ktail, EG, SD, DT, S_, AT = (attn[:, 2560 + 512 * i:3072 + 512 * i] for i in range(10))
        gB, L, M, Mt, M2, M2t, X, Bm, T_, Wb = (x_buf[:, 512 * i:512 * i + 512] for i in range(10))
        scr_ = scr[:, :, :].rearrange("p a b -> p (a b)")
        wTn, qdT, vnew, gon, gsq = (scr_[:, 512 * i:512 * i + 512] for i in range(5))
        gsq2 = scr_[:, 2048:3072]
        state = act_b[:, 4096:4608]
        states = act_b[:, 0:4096].rearrange("p (h b v) -> p h b v", h=H, b=NB)
        wM = attn[:, 0:1024].rearrange("p (b t) -> p b t", b=NB)
        qM = qk_tok.rearrange("p (b t) -> p b t", b=NB)
        vM = x_buf[:, 1024:2048].rearrange("p (b t) -> p b t", b=NB)
        g_t, b_t, gc, eg, be, kl, goss = (little(4) for _ in range(7))
        rqk = little(8)

        def m4(name):
            return C(name, 4)

        def mul4(pe, out, lhs, rhs, start=True, stop=True):
            for h in range(H):
                mm = nc.tensor.matmul(quarters(out)[:, h, :], h4(lhs)[:, h, :], h4(rhs)[:, h, :], start=start, stop=stop)
            return mm

        def turn4(pe, out, src):
            for h in range(H):
                mm = nc.tensor.transpose(quarters(out)[:, h, :], h4(src)[:, h, :], ident)
            return mm

        def gdn_pe_tile(pe, t, sample, side):
            s, sa, sd = (gs_pe, gs_act, gs_dve) if sample else (g_pe, g_act, g_dve)
            cum = C("cum_s" if sample else "cum_p")
            pe.wait_ge(sa["stage2" if sample else "stage"], sa.after(t, "stage2" if sample else "stage"))
            pe.wait_ge(sd["s" if not sample else "oz"], sd.after(t - 1, "s" if not sample else "oz"))
            pe.wait_ge(sa["mix"], sa.after(t - 1, "mix"))
            for i in range(8):
                mm = nc.tensor.transpose(quarters(bank[i // 4])[:, i % 4, :], stage[:, i, :], ident)
            mm.then_inc(s.step("tokqk"), 1)
            for i in range(4):
                mm = nc.tensor.transpose(quarters(bank[2])[:, i, :], stage[:, 8 + i, :], ident)
            mm.then_inc(s.step("tokv"), 1)
            side(0)
            pe.wait_ge(sd["gB"], sd.after(t, "gB"))
            nc.tensor.matmul(bank[3][:, 0:4], cum, g_t, start=True, stop=True).then_inc(s.step("cum"), 1)
            for h in range(H):
                mm = nc.tensor.matmul(quarters(bank[4])[:, h, :], h4(gB)[:, h, :], cum, start=True, stop=True)
            mm.then_inc(s.step("gcum"), 1)
            side(1)
            pe.wait_ge(sd["qk1"], sd.after(t, "qk1"))
            turn4(pe, bank[0], qk_tok[:, 0:512]).then_inc(s.step("chq"), 1)
            turn4(pe, bank[1], qk_tok[:, 512:1024]).then_inc(s.step("chk"), 1)
            side(2)
            pe.wait_ge(sd["kT"], sd.after(t, "kT"))
            pe.wait_ge(sd["S"], sd.after(t, "S"))
            pe.wait_ge(sa["qT"], sa.after(t, "qT"))
            mul4(pe, bank[3], kT, kT).then_inc(s.step("kk"), 1)
            mul4(pe, bank[4], kT, qT).then_inc(s.step("kq"), 1)
            side(3)
            pe.wait_ge(sd["M"], sd.after(t, "M"))
            turn4(pe, bank[5], M).then_inc(s.step("Mt"), 1)
            side(4)
            pe.wait_ge(sa["Mt"], sa.after(t, "Mt"))
            mul4(pe, bank[0], Mt, M).then_inc(s.step("sq2"), 1)
            mul4(pe, bank[1], M, Mt).then_inc(s.step("sq2t"), 1)
            side(5)
            pe.wait_ge(sd["X0"], sd.after(t, "X0"))
            pe.wait_ge(sa["M2t"], sa.after(t, "M2t"))
            mul4(pe, bank[5], M2, X).then_inc(s.step("x1"), 1)
            mul4(pe, bank[0], M2t, M2).then_inc(s.step("sq4"), 1)
            mul4(pe, bank[1], M2, M2t).then_inc(s.step("sq4t"), 1)
            side(6)
            pe.wait_ge(sd["X1"], sd.after(t, "X1"))
            pe.wait_ge(sa["M4t"], sa.after(t, "M4t"))
            mul4(pe, bank[5], M, X).then_inc(s.step("x2"), 1)
            mul4(pe, bank[0], Mt, M).then_inc(s.step("sq8"), 1)
            side(7)
            pe.wait_ge(sd["X2"], sd.after(t, "X2"))
            pe.wait_ge(sa["M8"], sa.after(t, "M8"))
            mul4(pe, bank[5], M2, X).then_inc(s.step("x3"), 1)
            side(8)
            if not sample:
                for l in range(3):
                    pe.wait_ge(sd[f"B{l}"], sd.after(t, f"B{l}"))
                    if l == 0:
                        pe.wait_ge(sd["X3"], sd.after(t, "X3"))
                    turn4(pe, bank[0], X).then_inc(s.step(f"T{l}"), 1)
                    mul4(pe, bank[1], Bm, X).then_inc(s.step(f"BX{l}"), 1)
                    side(9 + 2 * l)
                    pe.wait_ge(sa[f"T{l}"], sa.after(t, f"T{l}"))
                    pe.wait_ge(sd[f"W{l}"], sd.after(t, f"W{l}"))
                    mul4(pe, bank[5], T_, Wb).then_inc(s.step(f"Y{l}"), 1)
                    side(10 + 2 * l)
            pe.wait_ge(sd["X3" if sample else "Y2"], sd.after(t, "X3" if sample else "Y2"))
            pe.wait_ge(sa["M8"], sa.after(t, "M8"))
            mul4(pe, bank[0], kbg, X).then_inc(s.step("w"), 1)
            side(15)

        def gdn_pe_prompt(pe):
            g_pe.arm(pe)
            das_pe.arm(pe)

            def tile(t):
                gdn_pe_tile(pe, t, False, lambda i: das_pe_stage(pe, 2 * t + i // STAGES, i // STAGES, i % STAGES))
                pe.wait_ge(g_act["w"], g_act.after(t, "w"))
                mm = None
                for h in range(H):
                    nc.tensor.matmul(quarters(bank[1])[:, h, :], h4(X)[:, h, :], h4(vb)[:, h, :], start=True, stop=False)
                    mm = nc.tensor.matmul(quarters(bank[1])[:, h, :], h4(wTn)[:, h, :], h4(state)[:, h, :], start=False, stop=True)
                mm.then_inc(g_pe.step("vn"), 1)
                pe.wait_ge(g_dve["vn"], g_dve.after(t, "vn"))
                for h in range(H):
                    nc.tensor.matmul(quarters(bank[2])[:, h, :], h4(qdT)[:, h, :], h4(state)[:, h, :], start=True, stop=False)
                    mm = nc.tensor.matmul(quarters(bank[2])[:, h, :], h4(AT)[:, h, :], h4(vnew)[:, h, :], start=False, stop=True)
                mm.then_inc(g_pe.step("o"), 1)
                mul4(pe, bank[3], ktail, vnew).then_inc(g_pe.step("s"), 1)
                pe.wait_ge(g_dve["oz"], g_dve.after(t, "oz"))
                turn4(pe, bank[4], gon).then_inc(g_pe.step("oT"), 1)

            with pe.Fori(0, NTP) as t:
                tile(t)

        def gdn_pe_sample(pe):
            gs_pe.arm(pe)
            gh_pe.arm(pe)
            pe.wait_ge(g_act["mix"], g_act.after(NTP - 1, "mix"))
            gdn_pe_tile(pe, 0, True, lambda i: das_out_pe(pe, i))
            pe.wait_ge(s_state, 16 * H)
            for h in range(H):
                pe.wait_ge(gh_dve["qM"], gh_dve.after(h, "qM"))
                nc.tensor.matmul(quarters(bank[1])[:, h, :], h4(X)[:, h, :], h4(vb)[:, h, :], start=True, stop=False)
                for b in range(NB):
                    mm = nc.tensor.matmul(quarters(bank[1])[:, h, :], wM[:, b, :], states[:, h, b, :], start=False, stop=b == NB - 1)
                mm.then_inc(gh_pe.step("vn"), 1)
                pe.wait_ge(gh_dve["vM"], gh_dve.after(h, "vM"))
                for b in range(NB):
                    nc.tensor.matmul(quarters(bank[2])[:, h, :], qM[:, b, :], states[:, h, b, :], start=b == 0, stop=False)
                mm = nc.tensor.matmul(quarters(bank[2])[:, h, :], h4(AT)[:, h, :], h4(vnew)[:, h, :], start=False, stop=True)
                mm.then_inc(gh_pe.step("o"), 1)
                pe.wait_ge(gh_dve["s1"], gh_dve.after(h - 1, "s1"))
                for i in range(2):
                    mm = nc.tensor.matmul(bank[3 + i][:, :], h4(ktail)[:, h, :], vM[:, 4 * i:4 * i + 4, :], start=True, stop=True)
                mm.then_inc(gh_pe.step("s"), 1)
            pe.wait_ge(gs_dve["oz"], gs_dve.after(0, "oz"))
            turn4(pe, bank[5], gon).then_inc(gs_pe.step("oT"), 1)

        def tile_cols(t):
            return bass.ds(t * P, P) if not isinstance(t, int) else slice(t * P, t * P + P)

        def gdn_act_tile(act, t, sample, side):
            s, sp_, sd, spo = (gs_act, gs_pe, gs_dve, gs_pool) if sample else (g_act, g_pe, g_dve, g_pool)
            if sample:
                for i in range(3):
                    src = cv[:, 4 * i:4 * i + 4, GS:GW].rearrange("p m (b c) -> p m b c", b=NB)[:, :, :, 0:TB]
                    nc.scalar.copy(stage[:, 4 * i:4 * i + 4, :].rearrange("p m (b c) -> p m b c", b=NB), src).then_inc(s.step(f"stage{i}"), 1)
            else:
                act.wait_ge(sp_["tokv"], sp_.after(t - 1, "tokv"))
                nc.scalar.copy(stage[:, :, :], cv[:, :, tile_cols(t)]).then_inc(s.step("stage"), 1)
            act.wait_ge(sp_["tokqk"], sp_.after(t, "tokqk"))
            nc.scalar.activation(gsq2[:, 0:512], bank[0][:, :], ACT.Square).then_inc(s.step("sq0"), 1)
            nc.scalar.activation(gsq2[:, 512:1024], bank[1][:, :], ACT.Square).then_inc(s.step("sq1"), 1)
            side(0)
            act.wait_ge(sp_["gcum"], sp_.after(t, "gcum"))
            nc.scalar.activation(EG, bank[4][:, :], ACT.Exp).then_inc(s.step("EG"), 1)
            act.wait_ge(sd["gc"], sd.after(t, "gc"))
            nc.scalar.activation(eg, gc, ACT.Exp).then_inc(s.step("eg"), 1)
            act.wait_ge(sd["SU"], sd.after(t, "SU"))
            nc.scalar.activation(SD, SD, ACT.Exp).then_inc(s.step("D"), 1)
            nc.scalar.activation(DT, DT, ACT.Exp).then_inc(s.step("DT"), 1)
            side(1)
            act.wait_ge(sp_["chq"], sp_.after(t, "chq"))
            nc.scalar.copy(qT, bank[0][:, :]).then_inc(s.step("qT"), 1)
            side(2)
            side(3)
            act.wait_ge(sp_["Mt"], sp_.after(t, "Mt"))
            nc.scalar.copy(Mt, bank[5][:, :]).then_inc(s.step("Mt"), 1)
            side(4)
            for n in ("sq2", "sq4"):
                act.wait_ge(sp_[n], sp_.after(t, n))
                nc.scalar.copy(M2 if n == "sq2" else M, bank[0][:, :]).then_inc(s.step("M2" if n == "sq2" else "M4"), 1)
                act.wait_ge(sp_[n + "t"], sp_.after(t, n + "t"))
                nc.scalar.copy(M2t if n == "sq2" else Mt, bank[1][:, :]).then_inc(s.step("M2t" if n == "sq2" else "M4t"), 1)
                side(5 if n == "sq2" else 6)
            act.wait_ge(sp_["sq8"], sp_.after(t, "sq8"))
            nc.scalar.copy(M2, bank[0][:, :]).then_inc(s.step("M8"), 1)
            side(7)
            side(8)
            if not sample:
                for l in range(3):
                    act.wait_ge(sp_[f"T{l}"], sp_.after(t, f"T{l}"))
                    nc.scalar.copy(T_, bank[0][:, :]).then_inc(s.step(f"T{l}"), 1)
                    side(9 + 2 * l)
                    side(10 + 2 * l)
            act.wait_ge(sp_["w"], sp_.after(t, "w"))
            nc.scalar.copy(wTn, bank[0][:, :]).then_inc(s.step("w"), 1)
            side(15)
            if sample:
                act.wait_ge(gh_pe["o"], gh_pe.after(H - 1, "o"))
            else:
                act.wait_ge(sp_["o"], sp_.after(t, "o"))
            nc.scalar.activation(gsq, bank[2][:, :], ACT.Square).then_inc(s.step("osq"), 1)
            act.wait_ge(sp_["oT"], sp_.after(t, "oT"))
            dst = act_a[:, 4:8, SEQ:] if sample else act_a[:, 4:8, tile_cols(t)]
            nc.scalar.copy(dst, quarters(bank[5 if sample else 4])).then_inc(s.step("mix"), 1)

        def gdn_act(act):
            g_act.arm(act)
            das_act.arm(act)
            gs_act.arm(act)
            with act.Fori(0, NTP) as t:
                gdn_act_tile(act, t, False, lambda i: das_act_stage(act, 2 * t + i // STAGES, i % STAGES))
            gdn_act_tile(act, 0, True, lambda i: das_out_act(act, i))

        def gdn_pool(pool):
            for s, sd, n in ((g_pool, g_dve, NTP), (gs_pool, gs_dve, 1)):
                s.arm(pool)

                def tile(t):
                    pool.wait_ge(sd["ssq"], sd.after(t, "ssq"))
                    nc.gpsimd.tensor_tensor(rqk, rqk, C("minus_half"), ALU.pow).then_inc(s.step("rn"), 1)
                    if n == 1:
                        t_pool.arm(pool)
                        head_norm_pool(pool, t_pool, t_dve, 0)
                    pool.wait_ge(sd["oms"], sd.after(t, "oms"))
                    nc.gpsimd.tensor_tensor(goss, goss, C("minus_half")[:, 0:4], ALU.pow).then_inc(s.step("orn"), 1)

                if n == 1:
                    tile(0)
                else:
                    with pool.Fori(0, n) as t:
                        tile(t)

        def gdn_dve_tile(dve, t, sample, side):
            s, sp_, sa, spo = (gs_dve, gs_pe, gs_act, gs_pool) if sample else (g_dve, g_pe, g_act, g_pool)
            sfx = "_s" if sample else "_p"
            tt = nc.vector.tensor_tensor
            gcols = slice(4 * (NT - 1), 4 * NT) if sample else bass.ds(t * 4, 4)
            nc.vector.tensor_copy(b_t, beta[:, gcols])
            nc.vector.tensor_copy(g_t, glog[:, gcols]).then_inc(s.step("gb"), 1)
            dve.wait_ge(s["gb"], s.after(t, "gb"))
            dve.wait_ge(sp_["gcum"], sp_.after(t - 1, "gcum"))
            nc.vector.tensor_copy(h4(gB), b4(g_t)).then_inc(s.step("gB"), 1)
            side(0)
            dve.wait_ge(sp_["gcum"], sp_.after(t, "gcum"))
            nc.vector.tensor_copy(gc, bank[3][:, 0:4]).then_inc(s.step("gc"), 1)
            dve.wait_ge(s["gc"], s.after(t, "gc"))
            dve.wait_ge(sa["eg"], sa.after(t, "eg"))
            tt(h4(S_), quarters(bank[4]), b4(gc), ALU.subtract).then_inc(s.step("S"), 1)
            dve.wait_ge(s["S"], s.after(t, "S"))
            tt(h4(SD), m4("low" + sfx), h4(S_), ALU.subtract).then_inc(s.step("SD"), 1)
            tt(h4(DT), m4("up" + sfx), h4(S_), ALU.add).then_inc(s.step("SU"), 1)
            dve.wait_ge(sa["sq1"], sa.after(t, "sq1"))
            nc.vector.tensor_reduce(rqk, gsq2.rearrange("p (h c) -> p h c", h=8), AX.X, ALU.add).then_inc(s.step("ss"), 1)
            dve.wait_ge(s["ss"], s.after(t, "ss"))
            nc.vector.scalar_tensor_tensor(rqk, rqk, EPS, C("qk_scale"), ALU.add, ALU.mult).then_inc(s.step("ssq"), 1)
            side(1)
            dve.wait_ge(spo["rn"], spo.after(t, "rn"))
            tt(h4(qk_tok[:, 0:512]), quarters(bank[0]), b4(rqk[:, 0:4]), ALU.mult).then_inc(s.step("qk0"), 1)
            tt(h4(qk_tok[:, 512:1024]), quarters(bank[1]), b4(rqk[:, 4:8]), ALU.mult).then_inc(s.step("qk1"), 1)
            dve.wait_ge(sp_["chk"], sp_.after(t, "chk"))
            nc.vector.tensor_copy(kT, bank[1][:, :]).then_inc(s.step("kT"), 1)
            side(2)
            tt(h4(vb), quarters(bank[2]), b4(b_t), ALU.mult).then_inc(s.step("vb"), 1)
            nc.vector.scalar_tensor_tensor(be, b_t, -1.0, eg, ALU.mult, ALU.mult).then_inc(s.step("be"), 1)
            dve.wait_ge(s["be"], s.after(t, "be"))
            tt(h4(kbg), h4(qk_tok[:, 512:1024]), b4(be), ALU.mult).then_inc(s.step("kbg"), 1)
            dve.wait_ge(sa["DT"], sa.after(t, "DT"))
            if sample:
                last = h4(DT)[:, :, TB - 1:P:TB]
                nc.vector.tensor_reduce(kl, last, AX.X, ALU.add).then_inc(s.step("kl"), 1)
                dve.wait_ge(s["kl"], s.after(t, "kl"))
            else:
                nc.vector.tensor_copy(kl, h4(DT)[:, :, P - 1]).then_inc(s.step("kl"), 1)
                dve.wait_ge(s["kl"], s.after(t, "kl"))
            tt(h4(ktail), h4(qk_tok[:, 512:1024]), b4(kl), ALU.mult).then_inc(s.step("ktail"), 1)
            dve.wait_ge(sp_["kk"], sp_.after(t, "kk"))
            tt(h4(L), quarters(bank[3]), h4(SD), ALU.mult).then_inc(s.step("L0"), 1)
            dve.wait_ge(s["L0"], s.after(t, "L0"))
            tt(h4(L), h4(L), b4(b_t), ALU.mult).then_inc(s.step("L"), 1)
            dve.wait_ge(s["L"], s.after(t, "L"))
            dve.wait_ge(sp_["kq"], sp_.after(t, "kq"))
            tt(h4(AT), quarters(bank[4]), h4(DT), ALU.mult).then_inc(s.step("AT"), 1)
            tt(h4(M), h4(L), m4("blk16"), ALU.mult).then_inc(s.step("M"), 1)
            if not sample:
                tt(h4(Bm), h4(L), m4("lev32"), ALU.mult).then_inc(s.step("B0"), 1)
            side(3)
            dve.wait_ge(sp_["Mt"], sp_.after(t, "Mt"))
            dve.wait_ge(sa["Mt"], sa.after(t, "Mt"))
            tt(h4(X), m4("ident"), quarters(bank[5]), ALU.subtract).then_inc(s.step("X0"), 1)
            side(4)
            side(5)
            for i in (1, 2, 3):
                dve.wait_ge(sp_[f"x{i}"], sp_.after(t, f"x{i}"))
                tt(h4(X), h4(X), quarters(bank[5]), ALU.add).then_inc(s.step(f"X{i}"), 1)
                side(5 + i)
            if not sample:
                for l in range(3):
                    if l:
                        dve.wait_ge(sp_[f"BX{l - 1}"], sp_.after(t, f"BX{l - 1}"))
                        tt(h4(Bm), h4(L), m4(f"lev{32 << l}"), ALU.mult).then_inc(s.step(f"B{l}"), 1)
                    dve.wait_ge(sp_[f"BX{l}"], sp_.after(t, f"BX{l}"))
                    nc.vector.tensor_copy(Wb, bank[1][:, :]).then_inc(s.step(f"W{l}"), 1)
                    side(9 + 2 * l)
                    dve.wait_ge(sp_[f"Y{l}"], sp_.after(t, f"Y{l}"))
                    tt(h4(X), h4(X), quarters(bank[5]), ALU.subtract).then_inc(s.step(f"Y{l}"), 1)
                    side(10 + 2 * l)
            dve.wait_ge(sa["qT"], sa.after(t, "qT"))
            tt(qdT, qT, EG, ALU.mult).then_inc(s.step("qd"), 1)
            side(15)
            if not sample:
                dve.wait_ge(sp_["vn"], sp_.after(t, "vn"))
                nc.vector.tensor_copy(vnew, bank[1][:, :]).then_inc(s.step("vn"), 1)
                dve.wait_ge(sp_["o"], sp_.after(t, "o"))
                tt(h4(state), h4(state), b4(h4(EG)[:, :, P - 1]), ALU.mult).then_inc(s.step("sg"), 1)
                dve.wait_ge(s["sg"], s.after(t, "sg"))
                dve.wait_ge(sp_["s"], sp_.after(t, "s"))
                tt(state, state, bank[3][:, :], ALU.add).then_inc(s.step("s"), 1)
            else:
                gdn_dve_states(dve)
            dve.wait_ge(sa["osq"], sa.after(t, "osq"))
            nc.vector.tensor_reduce(goss, h4(gsq), AX.X, ALU.add).then_inc(s.step("oss"), 1)
            dve.wait_ge(s["oss"], s.after(t, "oss"))
            nc.vector.tensor_scalar(goss, goss, 1.0 / P, EPS, ALU.mult, ALU.add).then_inc(s.step("oms"), 1)
            dve.wait_ge(spo["orn"], spo.after(t, "orn"))
            tt(h4(gon), quarters(bank[2]), b4(goss), ALU.mult).then_inc(s.step("on"), 1)
            dve.wait_ge(s["on"], s.after(t, "on"))
            tt(h4(gon), h4(gon), gdn_g[:, 128:256].unsqueeze(1).to_broadcast([P, 4, P]), ALU.mult).then_inc(s.step("og"), 1)
            dve.wait_ge(s["og"], s.after(t, "og"))
            gate = gz[:, NT - 1, :] if sample else gz[:, bass.ds(t, 1), :].rearrange("p o c -> p (o c)")
            tt(gon, gon, gate, ALU.mult).then_inc(s.step("oz"), 1)

        def gdn_dve_states(dve):
            gh_dve.arm(dve)
            tt = nc.vector.tensor_tensor
            dve.wait_ge(gs_dve["qd"], gs_dve.after(0, "qd"))
            dve.wait_ge(gs_act["w"], gs_act.after(0, "w"))
            dve.wait_ge(s_state, 16 * H)
            off = C("stream_off").rearrange("p (b t) -> p b t", b=NB)
            for h in range(H):
                def over(v):
                    return h4(v)[:, h, :].unsqueeze(1).to_broadcast([P, NB, P])

                dve.wait_ge(gh_pe["vn"], gh_pe.after(h - 1, "vn"))
                nc.vector.scalar_tensor_tensor(wM, off, 0.0, over(wTn), ALU.is_equal, ALU.mult).then_inc(gh_dve.step("wM"), 1)
                dve.wait_ge(gh_pe["o"], gh_pe.after(h - 1, "o"))
                nc.vector.scalar_tensor_tensor(qM, off, 0.0, over(qdT), ALU.is_equal, ALU.mult).then_inc(gh_dve.step("qM"), 1)
                dve.wait_ge(gh_pe["vn"], gh_pe.after(h, "vn"))
                nc.vector.tensor_copy(h4(vnew)[:, h, :], quarters(bank[1])[:, h, :]).then_inc(gh_dve.step("vn"), 1)
                dve.wait_ge(gh_dve["vn"], gh_dve.after(h, "vn"))
                dve.wait_ge(gh_pe["s"], gh_pe.after(h - 1, "s"))
                tt(vM, over(vnew), C("stream_row").unsqueeze(2).to_broadcast([P, NB, P]), ALU.mult).then_inc(gh_dve.step("vM"), 1)
                dve.wait_ge(gh_pe["o"], gh_pe.after(h, "o"))
                last = h4(EG)[:, h, TB - 1:P:TB].unsqueeze(2).to_broadcast([P, NB, P])
                tt(states[:, h, :, :], states[:, h, :, :], last, ALU.mult).then_inc(gh_dve.step("sg"), 1)
                dve.wait_ge(gh_dve["sg"], gh_dve.after(h, "sg"))
                dve.wait_ge(gh_pe["s"], gh_pe.after(h, "s"))
                for i in range(2):
                    o = states[:, h, 4 * i:4 * i + 4, :]
                    tt(o, o, quarters(bank[3 + i]), ALU.add).then_inc(gh_dve.step(f"s{i}"), 1)

        def gdn_dve(dve):
            g_dve.arm(dve)
            gs_dve.arm(dve)
            g0.arm(dve)
            nc.vector.memset(state, 0.0).then_inc(g0.step("state"), 1)
            dve.wait_ge(g0["state"], g0.after(0, "state"))
            with dve.Fori(0, NTP) as t:
                gdn_dve_tile(dve, t, False, lambda i: das_dve_stage(dve, 2 * t + i // STAGES, i % STAGES))
            gdn_dve_tile(dve, 0, True, lambda i: das_out_dve(dve, i))

        g0 = steps("gdn_state_zero", "state")

        mem_rows = act_b[:, 2048:4096].rearrange("p (t d) -> p t d", t=2)
        mem_act = act_b[:, 0:2048].rearrange("p (c t) -> p c t", c=KC)
        mk_tok = conv[:, 0:2048].rearrange("p (t d) -> p t d", t=2)
        mkT = conv[:, 2048:4096].rearrange("p (c m) -> p c m", c=KC)
        mv = conv[:, 4096:6144].rearrange("p (t d) -> p t d", t=2)
        m_pe = steps("mem_pe", "t0 t1 t2 t3")
        m_dve = steps("mem_dve", "t0 t1 t2 t3")
        s_mem = sem("memory_rows_loaded")
        s_xback = sem("x_reloaded")

        def mem_turn_pe(pe):
            m_pe.arm(pe)
            all_taken(pe, LAST_OF["mk"])
            for g in range(4):
                pe.wait_ge(n_dve["mem"]["ev1b"], n_dve["mem"].after(0, "ev1b"))
                if g >= 2:
                    pe.wait_ge(m_dve[f"t{g - 2}"], m_dve.after(0, f"t{g - 2}"))
                for i in range(4):
                    c, m = 2 * g + i // 2, i % 2
                    mm = nc.tensor.transpose(quarters(bank[4 + g % 2])[:, i, :], mk_tok[:, m, c * P:(c + 1) * P], ident)
                mm.then_inc(m_pe.step(f"t{g}"), 1)

        def mem_turn_dve(dve):
            m_dve.arm(dve)
            for g in range(4):
                dve.wait_ge(m_pe[f"t{g}"], m_pe.after(0, f"t{g}"))
                nc.vector.tensor_copy(mkT[:, 2 * g:2 * g + 2, :].rearrange("p a b -> p (a b)"), bank[4 + g % 2][:, :]).then_inc(m_dve.step(f"t{g}"), 1)

        xq = act_b[:, :].rearrange("p (c t) -> p c t", c=KC)
        x_pe = steps("xp_pe", "sc | tr0 tr1 pv0 pv1")
        x_dve = steps("xp_dve", "m0 m1 | r pn T1 o1")
        x_act = steps("xp_act", "p0 p1 p2 p3 | T0 o0")
        xP = [gz[:, 2 * i:2 * i + 2, :].rearrange("p a b -> p (a b)") for i in range(2)]
        xPT = [scr[:, i, :] for i in range(2)]
        xmx = [little(4) for _ in range(2)]
        xsum = [little(4) for _ in range(2)]

        def xp_pe(pe):
            x_pe.arm(pe)
            all_taken(pe, LAST_OF["cq"])
            pe.wait_ge(m_dve["t3"], m_dve.after(0, "t3"))
            pe.wait_ge(n_dve["cross"][f"ev{NT - 1}b"], n_dve["cross"].after(0, f"ev{NT - 1}b"))
            for u in range(NTP + 1):
                if u < NTP:
                    pe.wait_ge(x_act["p3"], x_act.after(u - 2, "p3"))
                    for h in range(H):
                        for c in range(2):
                            mm = nc.tensor.matmul(bank[2 * (u % 2) + h // 2][:, MEM * (h % 2):MEM * (h % 2) + MEM],
                                                  xq[:, 2 * h + c, u * P:(u + 1) * P], mkT[:, 2 * h + c, :], start=c == 0, stop=c == 1)
                    mm.then_inc(x_pe.step("sc"), 1)
                if u >= 1:
                    v = u - 1
                    pe.wait_ge(x_dve["pn"], x_dve.after(v, "pn"))
                    for g, s in ((0, x_act), (1, x_dve)):
                        pe.wait_ge(s[f"T{g}"], s.after(v - 1, f"T{g}"))
                        for i in range(4):
                            q = 4 * g + i
                            mm = nc.tensor.transpose(quarters(bank[4 + g])[:, i, :], xP[v % 2][:, q * P:(q + 1) * P], ident)
                        mm.then_inc(x_pe.step(f"tr{g}"), 1)
                    pe.wait_ge(x_act["T0"], x_act.after(v, "T0"))
                    pe.wait_ge(x_dve["T1"], x_dve.after(v, "T1"))
                    for g, s in ((0, x_act), (1, x_dve)):
                        pe.wait_ge(s[f"o{g}"], s.after(v - 1, f"o{g}"))
                        for i in range(4):
                            q = 4 * g + i
                            for m in range(2):
                                mm = nc.tensor.matmul(quarters(bank[6 + g])[:, i, :], mv[:, m, q * P:(q + 1) * P],
                                                      xPT[v % 2][:, (2 * (q // 2) + m) * P:(2 * (q // 2) + m + 1) * P], start=m == 0, stop=m == 1)
                        mm.then_inc(x_pe.step(f"pv{g}"), 1)

        def xp_dve(dve):
            x_dve.arm(dve)
            for u in range(NTP + 1):
                if u < NTP:
                    dve.wait_ge(x_pe["sc"], x_pe.after(u, "sc"))
                    for g in range(2):
                        ins = nc.vector.tensor_reduce(xmx[u % 2][:, 2 * g:2 * g + 2],
                                                      bank[2 * (u % 2) + g][:, :].rearrange("p (h m) -> p h m", h=2), AX.X, ALU.max, negate=True)
                        ins.then_inc(x_dve.step(f"m{g}"), 1)
                if u >= 1:
                    v = u - 1
                    dve.wait_ge(x_act["p3"], x_act.after(v, "p3"))
                    nc.vector.reciprocal(xsum[v % 2], xsum[v % 2]).then_inc(x_dve.step("r"), 1)
                    dve.wait_ge(x_dve["r"], x_dve.after(v, "r"))
                    pp = xP[v % 2].rearrange("p (h m) -> p h m", h=H)
                    nc.vector.tensor_tensor(pp, pp, xsum[v % 2].unsqueeze(2).to_broadcast([P, H, MEM]), ALU.mult).then_inc(x_dve.step("pn"), 1)
                    dve.wait_ge(x_pe["tr1"], x_pe.after(v, "tr1"))
                    nc.vector.tensor_copy(xPT[v % 2][:, 512:1024], bank[5][:, :]).then_inc(x_dve.step("T1"), 1)
                    dve.wait_ge(x_pe["pv1"], x_pe.after(v, "pv1"))
                    nc.vector.tensor_copy(act_a[:, 4:8, v * P:(v + 1) * P], quarters(bank[7])).then_inc(x_dve.step("o1"), 1)

        def xp_act(act):
            x_act.arm(act)
            for u in range(NTP + 1):
                if u < NTP:
                    q = u % 2
                    act.wait_ge(x_dve["m1"], x_dve.after(u, "m1"))
                    act.wait_ge(x_pe["tr1"], x_pe.after(u - 2, "tr1"))
                    for h in range(H):
                        c = slice(MEM * (h % 2), MEM * (h % 2) + MEM)
                        nc.scalar.activation(xP[q][:, MEM * h:MEM * h + MEM], bank[2 * q + h // 2][:, c], ACT.Exp,
                                                        bias=xmx[q][:, h:h + 1], accum_out=xsum[q][:, h:h + 1]).then_inc(x_act.step(f"p{h}"), 1)
                if u >= 1:
                    v = u - 1
                    act.wait_ge(x_pe["tr0"], x_pe.after(v, "tr0"))
                    nc.scalar.copy(xPT[v % 2][:, 0:512], bank[4][:, :]).then_inc(x_act.step("T0"), 1)
                    act.wait_ge(x_pe["pv0"], x_pe.after(v, "pv0"))
                    nc.scalar.copy(act_a[:, 0:4, v * P:(v + 1) * P], quarters(bank[6])).then_inc(x_act.step("o0"), 1)

        xs_pe = steps("x_stream_pe", "f0 f1 f2 f3 sc pT pv oT")
        xs_dve = steps("x_stream_dve", "q f1 f3 mx r pn pT")
        xs_act = steps("x_stream_act", "f0 f2 p pv o")
        xs_zero = steps("x_stream_zero", "q")
        c_KT = attn[:, 0:2048].rearrange("p (c m) -> p c m", c=KC)
        c_q = attn[:, 2048:2304].rearrange("p (c r) -> p c r", r=32)
        c_P, c_aT, c_o = (attn[:, 2304 + MEM * i:2304 + MEM * (i + 1)] for i in range(3))
        c_mx, c_sum = little(1), little(1)

        def xs_pe_stage(pe, b, k, stage):
            kk, vv = kv_slot(UNIT["x0"], k, True)
            if stage < 4:
                f = stage
                if f == 0:
                    pe.wait_ge(s_kv[k], (b - k) * 16 + 32 + 32 * (NB // 2))
                    pe.wait_ge(xs_act["o"], xs_act.after(b - 1, "o"))
                elif f % 2:
                    pe.wait_ge(xs_act[f"f{f - 1}"], xs_act.after(b, f"f{f - 1}"))
                else:
                    pe.wait_ge(xs_dve[f"f{f - 1}"], xs_dve.after(b, f"f{f - 1}"))
                for i in range(4):
                    src = kk[:, i % 2, (2 * f + i // 2) * P:(2 * f + i // 2 + 1) * P]
                    mm = nc.tensor.transpose(quarters(bank[6])[:, i, :], src, ident)
                mm.then_inc(xs_pe.step(f"f{f}"), 1)
            elif stage == 4:
                pe.wait_ge(xs_dve["f3"], xs_dve.after(b, "f3"))
                pe.wait_ge(xs_act["f2"], xs_act.after(b, "f2"))
                for c in range(2):
                    for h in range(H):
                        mm = nc.tensor.matmul(bank[7][32 * h:32 * h + 32, 0:MEM], c_q[:, 2 * h + c, :], c_KT[:, 2 * h + c, :],
                                              start=c == 0, stop=c == 1, skip_group_check=True)
                mm.then_inc(xs_pe.step("sc"), 1)
            elif stage == 5:
                pe.wait_ge(xs_dve["pn"], xs_dve.after(b, "pn"))
                for m in range(2):
                    mm = nc.tensor.transpose(bank[6][:, m * P:(m + 1) * P], c_P[:, m * P:(m + 1) * P], ident)
                mm.then_inc(xs_pe.step("pT"), 1)
            elif stage == 6:
                pe.wait_ge(xs_dve["pT"], xs_dve.after(b, "pT"))
                for m in range(2):
                    for h in range(H):
                        mm = nc.tensor.matmul(bank[7][32 * h:32 * h + 32, 0:MEM], c_aT[:, m * P + 32 * h:m * P + 32 * h + 32],
                                              vv[:, m, MEM * h:MEM * h + MEM], start=m == 0, stop=m == 1, skip_group_check=True)
                mm.then_inc(xs_pe.step("pv"), 1)
            else:
                pe.wait_ge(xs_act["pv"], xs_act.after(b, "pv"))
                for e in range(2):
                    mm = nc.tensor.transpose(bank[6][:, e * P:(e + 1) * P], c_o[:, e * P:(e + 1) * P], ident)
                mm.then_inc(xs_pe.step("oT"), 1)

        def xs_act_stage(act, b, stage):
            if stage in (0, 2):
                act.wait_ge(xs_pe[f"f{stage}"], xs_pe.after(b, f"f{stage}"))
                nc.scalar.copy(c_KT[:, 2 * stage:2 * stage + 2, :],
                               bank[6][:, :].rearrange("p (c m) -> p c m", c=2)).then_inc(xs_act.step(f"f{stage}"), 1)
            elif stage == 4:
                act.wait_ge(xs_dve["mx"], xs_dve.after(b, "mx"))
                nc.scalar.activation(c_P, bank[7][:, 0:MEM], ACT.Exp, bias=c_mx, accum_out=c_sum).then_inc(xs_act.step("p"), 1)
            elif stage == 6:
                act.wait_ge(xs_pe["pv"], xs_pe.after(b, "pv"))
                nc.scalar.copy(c_o, bank[7][:, 0:MEM]).then_inc(xs_act.step("pv"), 1)
            elif stage == 7:
                act.wait_ge(xs_pe["oT"], xs_pe.after(b, "oT"))
                src = bank[6][:, 0:2 * P].rearrange("p (e h t) -> p e h t", e=2, h=H)
                dst = act_a[:, :, SEQ + b * TB:SEQ + (b + 1) * TB].rearrange("p (h e) t -> p e h t", h=H)
                for e in range(2):
                    ins = nc.scalar.copy(dst[:, e, :, :], src[:, e, :, 0:TB])
                ins.then_inc(xs_act.step("o"), 1)

        def xs_dve_stage(dve, b, stage):
            if stage == 0:
                dve.wait_ge(xs_pe["sc"], xs_pe.after(b - 1, "sc"))
                nc.vector.tensor_copy(c_q[:, :, 0:TB], xq[:, :, SEQ + b * TB:SEQ + (b + 1) * TB]).then_inc(xs_dve.step("q"), 1)
            elif stage in (1, 3):
                dve.wait_ge(xs_pe[f"f{stage}"], xs_pe.after(b, f"f{stage}"))
                nc.vector.tensor_copy(c_KT[:, 2 * stage:2 * stage + 2, :],
                                      bank[6][:, :].rearrange("p (c m) -> p c m", c=2)).then_inc(xs_dve.step(f"f{stage}"), 1)
            elif stage == 4:
                dve.wait_ge(xs_pe["sc"], xs_pe.after(b, "sc"))
                nc.vector.tensor_reduce(c_mx, bank[7][:, 0:MEM], AX.X, ALU.max, negate=True).then_inc(xs_dve.step("mx"), 1)
            elif stage == 5:
                dve.wait_ge(xs_act["p"], xs_act.after(b, "p"))
                nc.vector.reciprocal(c_sum, c_sum).then_inc(xs_dve.step("r"), 1)
                dve.wait_ge(xs_dve["r"], xs_dve.after(b, "r"))
                nc.vector.tensor_scalar(c_P, c_P, c_sum, None, ALU.mult).then_inc(xs_dve.step("pn"), 1)
            elif stage == 6:
                dve.wait_ge(xs_pe["pT"], xs_pe.after(b, "pT"))
                nc.vector.tensor_copy(c_aT, bank[6][:, 0:MEM]).then_inc(xs_dve.step("pT"), 1)

        h_row = conv[:, 0:5 * D].rearrange("p (t d) -> p t d", t=NT)
        gffn_row = conv[:, 6144:7168]
        w_route = conv[:, 7168:7168 + 36 * KC].rearrange("p (c n) -> p c n", c=KC)
        b_route = conv[:, 7456:7492]
        at_r = [0]

        def rs(*shape):
            n = int(np.prod(shape))
            at_r[0] += n
            v = attn[:, at_r[0] - n:at_r[0]]
            if len(shape) == 2:
                v = v.rearrange("p (a b) -> p a b", a=shape[0])
            return v

        lg = rs(NT, 36)
        g_s, g_e, g_q = rs(NT, 4), rs(NT, 4), rs(NT, 4)
        gmax, gsum, gidx, m1, m2, i1, i2, ee, w1, w2 = (rs(NT) for _ in range(10))
        sl12, place = rs(2 * NT), rs(2 * NT)
        sl1, sl2 = sl12[:, 0:NT], sl12[:, NT:]
        msk, ml, dd, oh1, oh2, A, pos, slotv = (rs(NT, NE) for _ in range(8))
        cnt, nblk, ends, starts, one32 = (rs(NE) for _ in range(5))
        capq = rs(NE, NT * P // CAP)
        cmp_ = rs(BLKPAD + 1, NE)
        blk_e = rs(BLKPAD + 1)
        cmp2, n_rounds = rs((BLKPAD + 1) // 2), rs(1)
        pair_f, over_f, token_f = rs(NBLK), rs(NBLK), rs(NBLK)
        in_block, off = rs(2 * NT, NBLK), rs(2 * NT, NBLK)
        at_place = cmp_.rearrange("p a b -> p (a b)")[:, 0:2 * NT * CAP].rearrange("p (a b) -> p a b", b=CAP)
        assert at_r[0] <= 5120
        at_u = [5120]

        def us(n):
            at_u[0] += n
            return attn[:, at_u[0] - n:at_u[0]].bitcast(U32)

        table_u = us(64)
        pair_all = us(64)
        token_all = us(64)
        token_col, pair_col = [us(1), us(1)], [us(1), us(1)]
        r_pe = steps("route_pe", "lg cum table")
        r_act = steps("route_act", "ge ee")
        r_dve = steps("route_dve",
                      "lg gmax gs ge4 gsum gtop gq gq2 gidx msk0 msk1 ml m1 d1 q1 q1b i1 oh1 ml2 m2 d2 q2 q2b i2 oh2 "
                      "dm w0 w1a w1 w2 A cnt pos capq nblk one ends "
                      "cmp blk min tab cmp2 nr tabn starts base slotv s1a s1 s2a s2 off ib0 ib off2 place ap pairs "
                      "e0 e1 pf pu p1 p2 p3 p4 token")
        s_route = sem("route_weights_loaded")
        s_bias = sem("group_bias_loaded")
        s_rows = [sem(f"rows_stored{k}") for k in range(2)]
        H_ROWS = [16 * len(range(k, NT, 2)) for k in range(2)]

        def route_pe(pe):
            r_pe.arm(pe)
            pe.wait_ge(s_route, 64)
            pe.wait_ge(n_dve["ffn"][f"ev{NT - 1}b"], n_dve["ffn"].after(0, f"ev{NT - 1}b"))
            pe.wait_ge(taken(LAST_OF["co"]), taken_count(LAST_OF["co"]))
            for t in range(NT):
                for c in range(KC):
                    mm = nc.tensor.matmul(bank[0][:, 36 * t:36 * t + 36], act_a[:, c, t * P:(t + 1) * P], w_route[:, c, :],
                                          start=c == 0, stop=c == KC - 1)
            mm.then_inc(r_pe.step("lg"), 1)
            pe.wait_ge(r_dve["A"], r_dve.after(0, "A"))
            for t in range(NT):
                for s in range(t + 1):
                    mm = nc.tensor.matmul(bank[1][:, NE * t:NE * t + NE], C("cum_p") if s == t else C("ones"), A[:, s, :],
                                          start=s == 0, stop=s == t)
            for s in range(NT):
                mm = nc.tensor.matmul(bank[1][:, NE * NT:NE * NT + NE], C("ones"), A[:, s, :], start=s == 0, stop=s == NT - 1)
            mm.then_inc(r_pe.step("cum"), 1)
            pe.wait_ge(r_dve["pairs"], r_dve.after(0, "pairs"))
            for i in range(2 * NT):
                mm = nc.tensor.matmul(bank[2][0:CAP, 0:NBLK], at_place[:, i, :], in_block[:, i, :], start=i == 0, stop=i == 2 * NT - 1)
            mm.then_inc(r_pe.step("table"), 1)

        def route_act(act):
            r_act.arm(act)
            act.wait_ge(r_dve["gs"], r_dve.after(0, "gs"))
            nc.scalar.activation(g_e, g_s, ACT.Exp).then_inc(r_act.step("ge"), 1)
            act.wait_ge(r_dve["dm"], r_dve.after(0, "dm"))
            nc.scalar.activation(ee, ee, ACT.Exp).then_inc(r_act.step("ee"), 1)

        def route_dve(dve):
            r_dve.arm(dve)
            tt, ts, red = nc.vector.tensor_tensor, nc.vector.tensor_scalar, nc.vector.tensor_reduce
            stt = nc.vector.scalar_tensor_tensor

            def over(v, n):
                return v.unsqueeze(2).to_broadcast([P, NT, n])

            def row(v, n):
                return v.unsqueeze(1).to_broadcast([P, NT, n])

            dve.wait_ge(xs_act["o"], xs_act.after(NB - 1, "o"))
            dve.wait_ge(r_pe["lg"], r_pe.after(0, "lg"))
            tt(lg, bank[0][:, 0:36 * NT].rearrange("p (t n) -> p t n", t=NT), row(b_route, 36), ALU.add).then_inc(r_dve.step("lg"), 1)
            dve.wait_ge(r_dve["lg"], r_dve.after(0, "lg"))
            gl, el = lg[:, :, 0:4], lg[:, :, 4:36]
            red(gmax, gl, AX.X, ALU.max).then_inc(r_dve.step("gmax"), 1)
            dve.wait_ge(r_dve["gmax"], r_dve.after(0, "gmax"))
            tt(g_s, gl, over(gmax, 4), ALU.subtract).then_inc(r_dve.step("gs"), 1)
            dve.wait_ge(r_dve["gs"], r_dve.after(0, "gs"))
            dve.wait_ge(r_act["ge"], r_act.after(0, "ge"))
            red(gsum, g_e, AX.X, ALU.add).then_inc(r_dve.step("ge4"), 1)
            dve.wait_ge(r_dve["ge4"], r_dve.after(0, "ge4"))
            nc.vector.reciprocal(gsum, gsum).then_inc(r_dve.step("gsum"), 1)
            dve.wait_ge(r_dve["gsum"], r_dve.after(0, "gsum"))
            ts(g_q, g_s, 0.0, None, ALU.is_equal).then_inc(r_dve.step("gtop"), 1)
            dve.wait_ge(r_dve["gtop"], r_dve.after(0, "gtop"))
            ts(g_q, g_q, -100.0, 100.0, ALU.mult, ALU.add).then_inc(r_dve.step("gq"), 1)
            dve.wait_ge(r_dve["gq"], r_dve.after(0, "gq"))
            tt(g_q, g_q, row(C("iota8")[:, 0:4], 4), ALU.add).then_inc(r_dve.step("gq2"), 1)
            dve.wait_ge(r_dve["gq2"], r_dve.after(0, "gq2"))
            red(gidx, g_q, AX.X, ALU.min).then_inc(r_dve.step("gidx"), 1)
            dve.wait_ge(r_dve["gidx"], r_dve.after(0, "gidx"))
            tt(msk, row(C("group"), NE), over(gidx, NE), ALU.is_equal).then_inc(r_dve.step("msk0"), 1)
            dve.wait_ge(r_dve["msk0"], r_dve.after(0, "msk0"))
            ts(msk, msk, BIG, -BIG, ALU.mult, ALU.add).then_inc(r_dve.step("msk1"), 1)
            dve.wait_ge(r_dve["msk1"], r_dve.after(0, "msk1"))
            tt(ml, el, msk, ALU.add).then_inc(r_dve.step("ml"), 1)
            dve.wait_ge(r_dve["ml"], r_dve.after(0, "ml"))
            for k, m, i, oh in ((1, m1, i1, oh1), (2, m2, i2, oh2)):
                red(m, ml, AX.X, ALU.max).then_inc(r_dve.step(f"m{k}"), 1)
                dve.wait_ge(r_dve[f"m{k}"], r_dve.after(0, f"m{k}"))
                tt(dd, ml, over(m, NE), ALU.is_equal).then_inc(r_dve.step(f"d{k}"), 1)
                dve.wait_ge(r_dve[f"d{k}"], r_dve.after(0, f"d{k}"))
                ts(dd, dd, -100.0, 100.0, ALU.mult, ALU.add).then_inc(r_dve.step(f"q{k}"), 1)
                dve.wait_ge(r_dve[f"q{k}"], r_dve.after(0, f"q{k}"))
                tt(dd, dd, row(C("iota32"), NE), ALU.add).then_inc(r_dve.step(f"q{k}b"), 1)
                dve.wait_ge(r_dve[f"q{k}b"], r_dve.after(0, f"q{k}b"))
                red(i, dd, AX.X, ALU.min).then_inc(r_dve.step(f"i{k}"), 1)
                dve.wait_ge(r_dve[f"i{k}"], r_dve.after(0, f"i{k}"))
                tt(oh, row(C("iota32"), NE), over(i, NE), ALU.is_equal).then_inc(r_dve.step(f"oh{k}"), 1)
                dve.wait_ge(r_dve[f"oh{k}"], r_dve.after(0, f"oh{k}"))
                if k == 1:
                    stt(ml, oh, -BIG, ml, ALU.mult, ALU.add).then_inc(r_dve.step("ml2"), 1)
                    dve.wait_ge(r_dve["ml2"], r_dve.after(0, "ml2"))
            tt(ee, m2, m1, ALU.subtract).then_inc(r_dve.step("dm"), 1)
            dve.wait_ge(r_dve["dm"], r_dve.after(0, "dm"))
            dve.wait_ge(r_act["ee"], r_act.after(0, "ee"))
            ts(w1, ee, 1.0, None, ALU.add).then_inc(r_dve.step("w0"), 1)
            dve.wait_ge(r_dve["w0"], r_dve.after(0, "w0"))
            nc.vector.reciprocal(w1, w1).then_inc(r_dve.step("w1a"), 1)
            dve.wait_ge(r_dve["w1a"], r_dve.after(0, "w1a"))
            tt(w1, w1, gsum, ALU.mult).then_inc(r_dve.step("w1"), 1)
            dve.wait_ge(r_dve["w1"], r_dve.after(0, "w1"))
            tt(w2, w1, ee, ALU.mult).then_inc(r_dve.step("w2"), 1)
            dve.wait_ge(r_dve["w2"], r_dve.after(0, "w2"))
            tt(A, oh1, oh2, ALU.add).then_inc(r_dve.step("A"), 1)
            dve.wait_ge(r_dve["A"], r_dve.after(0, "A"))
            dve.wait_ge(r_pe["cum"], r_pe.after(0, "cum"))
            nc.vector.tensor_copy(cnt, bank[1][:, NE * NT:NE * NT + NE]).then_inc(r_dve.step("cnt"), 1)
            dve.wait_ge(r_dve["cnt"], r_dve.after(0, "cnt"))
            tt(pos, bank[1][:, 0:NE * NT].rearrange("p (t n) -> p t n", t=NT), A, ALU.subtract).then_inc(r_dve.step("pos"), 1)
            dve.wait_ge(r_dve["pos"], r_dve.after(0, "pos"))
            nc_ = NT * P // CAP
            tt(capq, cnt.unsqueeze(2).to_broadcast([P, NE, nc_]), C("capacities").unsqueeze(1).to_broadcast([P, NE, nc_]), ALU.is_gt).then_inc(r_dve.step("capq"), 1)
            dve.wait_ge(r_dve["capq"], r_dve.after(0, "capq"))
            red(nblk, capq, AX.X, ALU.add).then_inc(r_dve.step("nblk"), 1)
            dve.wait_ge(r_dve["nblk"], r_dve.after(0, "nblk"))
            nc.vector.memset(one32, 1.0).then_inc(r_dve.step("one"), 1)
            dve.wait_ge(r_dve["one"], r_dve.after(0, "one"))
            nc.vector.tensor_tensor_scan(ends, one32, nblk, 0.0, ALU.mult, ALU.add).then_inc(r_dve.step("ends"), 1)
            dve.wait_ge(r_dve["ends"], r_dve.after(0, "ends"))
            nb = BLKPAD + 1
            tt(cmp_, C("block").unsqueeze(2).to_broadcast([P, nb, NE]), ends.unsqueeze(1).to_broadcast([P, nb, NE]), ALU.is_ge).then_inc(r_dve.step("cmp"), 1)
            dve.wait_ge(r_dve["cmp"], r_dve.after(0, "cmp"))
            red(blk_e, cmp_, AX.X, ALU.add).then_inc(r_dve.step("blk"), 1)
            dve.wait_ge(r_dve["blk"], r_dve.after(0, "blk"))
            ts(blk_e, blk_e, float(NE - 1), None, ALU.min).then_inc(r_dve.step("min"), 1)
            dve.wait_ge(r_dve["min"], r_dve.after(0, "min"))
            nc.vector.tensor_copy(table_u[:, 1:1 + nb], blk_e).then_inc(r_dve.step("tab"), 1)
            dve.wait_ge(r_dve["tab"], r_dve.after(0, "tab"))
            tt(cmp2, ends[:, NE - 1:NE].to_broadcast([P, nb // 2]), C("block")[:, 0:nb:2], ALU.is_gt).then_inc(r_dve.step("cmp2"), 1)
            dve.wait_ge(r_dve["cmp2"], r_dve.after(0, "cmp2"))
            red(n_rounds, cmp2, AX.X, ALU.add).then_inc(r_dve.step("nr"), 1)
            dve.wait_ge(r_dve["nr"], r_dve.after(0, "nr"))
            nc.vector.tensor_copy(table_u[:, 0:1], n_rounds).then_inc(r_dve.step("tabn"), 1)
            tt(starts, ends, nblk, ALU.subtract).then_inc(r_dve.step("starts"), 1)
            dve.wait_ge(r_dve["starts"], r_dve.after(0, "starts"))
            ts(starts, starts, float(CAP), None, ALU.mult).then_inc(r_dve.step("base"), 1)
            dve.wait_ge(r_dve["base"], r_dve.after(0, "base"))
            tt(slotv, pos, row(starts, NE), ALU.add).then_inc(r_dve.step("slotv"), 1)
            dve.wait_ge(r_dve["slotv"], r_dve.after(0, "slotv"))
            for k, oh, sl in ((1, oh1, sl1), (2, oh2, sl2)):
                tt(dd, oh, slotv, ALU.mult).then_inc(r_dve.step(f"s{k}a"), 1)
                dve.wait_ge(r_dve[f"s{k}a"], r_dve.after(0, f"s{k}a"))
                red(sl, dd, AX.X, ALU.add).then_inc(r_dve.step(f"s{k}"), 1)
                dve.wait_ge(r_dve[f"s{k}"], r_dve.after(0, f"s{k}"))
            tt(off, sl12.unsqueeze(2).to_broadcast([P, 2 * NT, NBLK]), C("slot0").unsqueeze(1).to_broadcast([P, 2 * NT, NBLK]),
               ALU.subtract).then_inc(r_dve.step("off"), 1)
            dve.wait_ge(r_dve["off"], r_dve.after(0, "off"))
            ts(in_block, off, 0.0, None, ALU.is_ge).then_inc(r_dve.step("ib0"), 1)
            dve.wait_ge(r_dve["ib0"], r_dve.after(0, "ib0"))
            stt(in_block, off, float(CAP), in_block, ALU.is_lt, ALU.mult).then_inc(r_dve.step("ib"), 1)
            dve.wait_ge(r_dve["ib"], r_dve.after(0, "ib"))
            tt(off, off, in_block, ALU.mult).then_inc(r_dve.step("off2"), 1)
            dve.wait_ge(r_dve["off2"], r_dve.after(0, "off2"))
            red(place, off, AX.X, ALU.add).then_inc(r_dve.step("place"), 1)
            dve.wait_ge(r_dve["place"], r_dve.after(0, "place"))
            tt(at_place, C("iota_cap").unsqueeze(1).to_broadcast([P, 2 * NT, CAP]), place.unsqueeze(2).to_broadcast([P, 2 * NT, CAP]),
               ALU.is_equal).then_inc(r_dve.step("ap"), 1)
            tt(in_block, in_block, C("pair").unsqueeze(2).to_broadcast([P, 2 * NT, NBLK]), ALU.mult).then_inc(r_dve.step("pairs"), 1)
            r_ = slice(0, CAP)
            pf, ov, tf, table = pair_f[r_], over_f[r_], token_f[r_], bank[2][r_, 0:NBLK]
            dve.wait_ge(r_pe["table"], r_pe.after(0, "table"))
            ts(ov, table, 0.0, None, ALU.is_equal).then_inc(r_dve.step("e0"), 1)
            dve.wait_ge(r_dve["e0"], r_dve.after(0, "e0"))
            tt(ov, ov, C("empty")[r_], ALU.mult).then_inc(r_dve.step("e1"), 1)
            dve.wait_ge(r_dve["e1"], r_dve.after(0, "e1"))
            stt(pf, table, -1.0, ov, ALU.add, ALU.add).then_inc(r_dve.step("pf"), 1)
            dve.wait_ge(r_dve["pf"], r_dve.after(0, "pf"))
            nc.vector.tensor_copy(pair_all[r_, 0:NBLK], pf).then_inc(r_dve.step("pu"), 1)
            ts(ov, pf, float(NT * P), -float(NT * P), ALU.is_ge, ALU.mult).then_inc(r_dve.step("p1"), 1)
            dve.wait_ge(r_dve["p1"], r_dve.after(0, "p1"))
            tt(tf, pf, ov, ALU.add).then_inc(r_dve.step("p2"), 1)
            dve.wait_ge(r_dve["p2"], r_dve.after(0, "p2"))
            ts(ov, pf, float(NPAIR), -float(NT * P), ALU.is_ge, ALU.mult).then_inc(r_dve.step("p3"), 1)
            dve.wait_ge(r_dve["p3"], r_dve.after(0, "p3"))
            tt(tf, tf, ov, ALU.add).then_inc(r_dve.step("p4"), 1)
            dve.wait_ge(r_dve["p4"], r_dve.after(0, "p4"))
            nc.vector.tensor_copy(token_all[r_, 0:NBLK], tf).then_inc(r_dve.step("token"), 1)
            dve.wait_ge(r_dve["token"], r_dve.after(0, "token"))

        def ffn_rows_pool(pool):
            s = n_pool["ffn"]
            pool.wait_ge(s_route, 64)
            pool.wait_ge(xs_act["o"], xs_act.after(NB - 1, "o"))
            for t in range(NT):
                pool.wait_ge(n_dve["ffn"][f"xn{t}"], n_dve["ffn"].after(0, f"xn{t}"))
                nc.gpsimd.tensor_tensor(h_row[:, t, :], scr[:, t % 2, :], gffn_row, ALU.mult).then_inc(s.step(f"g{t}"), 1)
            for t in range(NT):
                pool.wait_ge(s[f"g{t}"], s.after(0, f"g{t}"))
                pool.dma_start(a["h_rows"][t * P:(t + 1) * P, :], h_row[:, t, :]).then_inc(s_rows[t % 2], 16)
            for k in range(2):
                pool.wait_ge(s_rows[k], H_ROWS[k])

        xg = [act_a[:, :, :].rearrange("p c t -> p (c t)")[:, 1024 * i:1024 * i + 1024] for i in range(2)]
        xgT = [act_b[:, 640 * i:640 * i + 640].rearrange("p (c s) -> p c s", c=KC) for i in range(2)]
        sgate = [act_b[:, 1280 + 160 * i:1440 + 160 * i] for i in range(2)]
        hT = [act_b[:, 1600 + 160 * i:1760 + 160 * i].rearrange("p (f s) -> p f s", f=2) for i in range(2)]
        yb = [act_b[:, 2048 + 1024 * i:3072 + 1024 * i] for i in range(2)]
        e_pe = steps("moe_pe", "tr0 tr1 | gate up d0 d1")
        e_act = steps("moe_act", "x0 | silu y0")
        e_dve = steps("moe_dve", "x1 | ix | h pc y1")
        s_ew = [sem(f"expert_loaded{k}") for k in range(2)]
        s_xg = [sem(f"tokens_gathered{k}") for k in range(2)]
        s_go = sem("indirect_dma_may_go")

        def rounds(eng):
            eng.wait_ge(r_dve["tabn"], r_dve.after(0, "tabn"))
            return eng.value_load(table_u[0:1, 0:1], min_val=1, max_val=(BLKPAD + 1) // 2)

        def moe_sync(sp):
            n = rounds(sp)
            with sp.Fori(0, n) as i:
                for k in range(2):
                    j = sp.snap(2 * i + k)
                    e = sp.value_load(table_u[0:1, bass.ds(j + 1, 1)], min_val=0, max_val=NE - 1)
                    sp.wait_ge(e_pe["d1"], e_pe.after(j - 2, "d1"))
                    w = W[:, k, :]
                    for m, name in enumerate(("w_gate", "w_up")):
                        sp.dma_start(w[:, 2048 * m:2048 * m + 2048].rearrange("p (c f) -> p c f", c=KC),
                                     a[name][0][bass.ds(e, 1)].rearrange("o (c p) f -> p (o c) f", p=P)).then_inc(s_ew[k], 16)
                    sp.dma_start(w[:, 4096:6144].rearrange("p (f d) -> p f d", f=2),
                                 a["w_down"][0][bass.ds(e, 1)].rearrange("o (f p) d -> p (o f) d", p=P)).then_inc(s_ew[k], 16)

        def moe_pool(pool):
            def gather(j, k):
                pool.wait_ge(e_pe["tr1"], e_pe.after(j - 2, "tr1"))
                pool.wait_ge(e_dve["ix"], e_dve.after(j, "ix"))
                pool.sem_inc(s_go, 1)
                pool.indirect_dma_start(xg[k][0:CAP, :], None, a["h_rows"], bass.IndirectOffsetOnAxis(token_col[k][0:CAP, :], 0))\
                    .then_inc(s_xg[k], 16)

            n = rounds(pool)
            for k in range(2):
                gather(k, k)
            with pool.Fori(0, n) as i:
                for k in range(2):
                    j = pool.snap(2 * i + k)
                    gather(j + 2, k)
                    pool.wait_ge(e_act["y0"], e_act.after(j, "y0"))
                    pool.wait_ge(e_dve["y1"], e_dve.after(j, "y1"))
                    pool.sem_inc(s_go, 1)
                    pool.indirect_dma_start(a["pair_rows"], bass.IndirectOffsetOnAxis(pair_col[k][0:CAP, :], 0), yb[k][0:CAP, :], None)\
                        .then_inc(s_rows[k], 16)

        def moe_pe(pe):
            e_pe.arm(pe)
            n = rounds(pe)

            def turn(j, k, count):
                pe.wait_ge(s_xg[k], count)
                for g, s, name in ((0, e_act, "x0"), (1, e_dve, "x1")):
                    pe.wait_ge(s[name], s.after(j - 1, name))
                    for c in range(4):
                        mm = nc.tensor.transpose(bank[g][:, c * CAP:(c + 1) * CAP], xg[k][0:CAP, (4 * g + c) * P:(4 * g + c + 1) * P],
                                                 ident[0:CAP, 0:CAP])
                    mm.then_inc(e_pe.step(f"tr{g}"), 1)

            turn(0, 0, 16)
            with pe.Fori(0, n) as i:
                for k in range(2):
                    j = pe.snap(2 * i + k)
                    pe.wait_ge(e_act["x0"], e_act.after(j, "x0"))
                    pe.wait_ge(e_dve["x1"], e_dve.after(j, "x1"))
                    pe.wait_ge(e_dve["h"], e_dve.after(j - 1, "h"))
                    pe.wait_ge(s_ew[k], i * 48 + 48)
                    for m, name in enumerate(("gate", "up")):
                        w = W[:, k, 2048 * m:2048 * m + 2048].rearrange("p (c f) -> p c f", c=KC)
                        for f in range(2):
                            for c in range(KC):
                                mm = nc.tensor.matmul(bank[2 + m][:, CAP * f:CAP * f + CAP], w[:, c, f * P:(f + 1) * P], xgT[k][:, c, :],
                                                      start=c == 0, stop=c == KC - 1)
                        mm.then_inc(e_pe.step(name), 1)
                    turn(j + 1, 1 - k, i * 16 + 16 + 16 * k)
                    pe.wait_ge(e_dve["h"], e_dve.after(j, "h"))
                    w = W[:, k, 4096:6144].rearrange("p (f d) -> p f d", f=2)
                    for g, s, name in ((0, e_act, "y0"), (1, e_dve, "y1")):
                        pe.wait_ge(s[name], s.after(j - 1, name))
                        for f in range(2):
                            mm = nc.tensor.matmul(bank[4 + g][0:CAP, :], hT[k][:, f, :], w[:, f, 512 * g:512 * g + 512], start=f == 0, stop=f == 1)
                        mm.then_inc(e_pe.step(f"d{g}"), 1)

        def moe_act(act):
            e_act.arm(act)
            n = rounds(act)

            def turned(j, k):
                act.wait_ge(e_pe["tr0"], e_pe.after(j, "tr0"))
                nc.scalar.copy(xgT[k][:, 0:4, :], bank[0][:, 0:4 * CAP].rearrange("p (c s) -> p c s", c=4)).then_inc(e_act.step("x0"), 1)

            turned(0, 0)
            with act.Fori(0, n) as i:
                for k in range(2):
                    j = act.snap(2 * i + k)
                    act.wait_ge(e_pe["gate"], e_pe.after(j, "gate"))
                    nc.scalar.activation(sgate[k], bank[2][:, 0:2 * CAP], ACT.Silu).then_inc(e_act.step("silu"), 1)
                    turned(j + 1, 1 - k)
                    act.wait_ge(e_pe["d0"], e_pe.after(j, "d0"))
                    act.wait_ge(s_rows[k], i * 16 + H_ROWS[k])
                    nc.scalar.copy(yb[k][0:CAP, 0:512], bank[4][0:CAP, :]).then_inc(e_act.step("y0"), 1)

        def moe_dve(dve):
            e_dve.arm(dve)
            n = rounds(dve)
            rows = slice(0, CAP)

            def columns(j, k):
                nc.vector.tensor_copy(token_col[k][rows, :], token_all[rows, bass.ds(j, 1)]).then_inc(e_dve.step("ix"), 1)

            def turned(j, k, j2):
                dve.wait_ge(e_pe["tr1"], e_pe.after(j, "tr1"))
                nc.vector.tensor_copy(xgT[k][:, 4:8, :], bank[1][:, 0:4 * CAP].rearrange("p (c s) -> p c s", c=4)).then_inc(e_dve.step("x1"), 1)
                columns(j2, k)

            for k in range(2):
                columns(k, k)
            turned(0, 0, 2)
            with dve.Fori(0, n) as i:
                for k in range(2):
                    j = dve.snap(2 * i + k)
                    ahead = dve.snap(2 * i + (k + 3))
                    dve.wait_ge(e_pe["up"], e_pe.after(j, "up"))
                    dve.wait_ge(e_act["silu"], e_act.after(j, "silu"))
                    nc.vector.tensor_tensor(hT[k][:, :, :].rearrange("p f s -> p (f s)"), bank[3][:, 0:2 * CAP], sgate[k], ALU.mult).then_inc(e_dve.step("h"), 1)
                    turned(j + 1, 1 - k, ahead)
                    dve.wait_ge(s_rows[k], i * 16 + H_ROWS[k])
                    nc.vector.tensor_copy(pair_col[k][rows, :], pair_all[rows, bass.ds(j, 1)]).then_inc(e_dve.step("pc"), 1)
                    dve.wait_ge(e_pe["d1"], e_pe.after(j, "d1"))
                    nc.vector.tensor_copy(yb[k][0:CAP, 512:1024], bank[5][0:CAP, :]).then_inc(e_dve.step("y1"), 1)

        Wf = W[:, :, :].rearrange("p a b -> p (a b)")
        back = [Wf[:, 1024 * i:1024 * i + 1024] for i in range(2 * NT)]
        gfin_row = Wf[:, 10240:11264]
        s_back = [sem(f"rows_back{i}") for i in range(2 * NT)]
        s_gfin = sem("g_final_loaded")
        f_dve = steps("final_dve", "x1 x2")
        f2_dve = steps("final_norm_dve", "xn y")
        f_act = steps("final_act", "sq")
        f_pool = steps("final_pool", "ms rn")
        s_store = [sem(f"y_stored{i}") for i in range(2)]

        def final_pool(pool):
            n = rounds(pool)
            for k in range(2):
                pool.wait_ge(s_rows[k], n * 16 + H_ROWS[k])
            for k in range(2):
                pool.wait_ge(s_xg[k], n * 16 + 16)
            pool.wait_ge(e_pe["d1"], e_pe.after(2 * n - 1, "d1"))
            pool.sem_inc(s_go, 1)
            for i in range(2 * NT):
                pool.dma_start(back[i], a["pair_rows"][i * P:(i + 1) * P, :]).then_inc(s_back[i], 16)
            f_pool.arm(pool)
            pool.wait_ge(f_act["sq"], f_act.after(NT - 1, "sq"))
            nc.gpsimd.tensor_scalar(rstd[:, 0:NT], ss[:, 0:NT], 1.0 / D, EPS, ALU.mult, ALU.add).then_inc(f_pool.step("ms"), 1)
            pool.wait_ge(f_pool["ms"], f_pool.after(0, "ms"))
            nc.gpsimd.tensor_tensor(rstd[:, 0:NT], rstd[:, 0:NT], C("minus_half")[:, 0:NT], ALU.pow).then_inc(f_pool.step("rn"), 1)

        def final_dve(dve):
            f_dve.arm(dve)
            for t in range(NT):
                for k, w in ((0, w1), (1, w2)):
                    dve.wait_ge(s_back[t + NT * k], 16)
                    nc.vector.scalar_tensor_tensor(x[:, t, :], back[t + NT * k], w[:, t:t + 1], x[:, t, :], ALU.mult, ALU.add).then_inc(f_dve.step(f"x{k + 1}"), 1)
                    dve.wait_ge(f_dve[f"x{k + 1}"], f_dve.after(t, f"x{k + 1}"))
            f2_dve.arm(dve)
            dve.wait_ge(f_pool["rn"], f_pool.after(0, "rn"))
            dve.wait_ge(s_gfin, 16)
            for t in range(NT):
                if t >= 2:
                    dve.wait_ge(s_store[t % 2], 16 * (t // 2))
                nc.vector.tensor_scalar(scr[:, t % 2, :], x[:, t, :], rstd[:, t:t + 1], None, ALU.mult).then_inc(f2_dve.step("xn"), 1)
                dve.wait_ge(f2_dve["xn"], f2_dve.after(t, "xn"))
                nc.vector.tensor_tensor(scr[:, t % 2, :], scr[:, t % 2, :], gfin_row, ALU.mult).then_inc(f2_dve.step("y"), 1)

        def final_act(act):
            f_act.arm(act)
            for t in range(NT):
                act.wait_ge(f_dve["x2"], f_dve.after(t, "x2"))
                nc.scalar.activation(scr[:, 2, :], x[:, t, :], ACT.Square, accum_out=ss[:, t:t + 1]).then_inc(f_act.step("sq"), 1)
                act.wait_ge(f_act["sq"], f_act.after(t, "sq"))

        def final_sync(sp):
            n = rounds(sp)
            sp.wait_ge(e_pe["d1"], e_pe.after(2 * n - 1, "d1"))
            sp.dma_start(gfin_row, a["g_final"].partition_broadcast(P)).then_inc(s_gfin, 16)
            for t in range(NT):
                sp.wait_ge(f2_dve["y"], f2_dve.after(t, "y"))
                dst = a["y_prompt"][0][t * P:(t + 1) * P, :] if t < NTP else a["y_sample"].rearrange("b t d -> (b t) d")
                sp.dma_start(dst, scr[:, t % 2, :]).then_inc(s_store[t % 2], 16)
            sp.wait_ge(s_store[0], 16 * 3)
            sp.wait_ge(s_store[1], 16 * 2)

        def store(eng, dst, src):
            n_out[0] += 16
            eng.dma_start(dst, src).then_inc(s_out, 16)

        block = ctx.enter_context(nc.Block())

        w_in = a["w_in"][0]

        def cols(i):
            return slice(512 * i, 512 * i + 512)

        def rest_dst(job, b):
            what, ja, jb = job
            if what in ("mix", "co"):
                return [(x[:, ja, 512 * jb:512 * jb + 512], b[:, :], 1.0)]
            if what == "cq":
                n = 512 if jb == 0 else P
                return [(xq[:, ja, 512 * jb:512 * jb + n], b[:, 0:n], 1.0 / 16)]
            return [((mk_tok if what == "mk" else mv)[:, ja, 512 * jb:512 * jb + 512], b[:, :], 1.0)]

        @block.sync
        def _(sp):
            sp.dma_start(const[:, :], a["const"]).then_inc(s_const, 16)
            for t in range(NTP):
                sp.dma_start(x[:, t, :], a["x_prompt"][0][t * P:(t + 1) * P, :]).then_inc(s_x[t], 16)
            sp.dma_start(x[:, 4, :], a["x_sample"].rearrange("b t d -> (b t) d")).then_inc(s_x[4], 16)
            for i, n in enumerate(("g_mix", "g_mem", "g_cross", "g_ffn")):
                sp.dma_start(gains[:, i, :], a[n][0].rearrange("(c p) -> p c", p=P), allow_slow_non_contiguous=True).then_inc(s_gain, 16)
            load_weight(sp, "dq", w_in, cols(0))
            load_weight(sp, "dk", w_in, cols(1))
            sp.dma_start(hist, a["state_gdn_conv"][0].rearrange("b j c -> (b j) c")).then_inc(s_hist, 16)
            prep_sync_load(sp)
            load_weight(sp, "dv", w_in, cols(2))
            for i in range(3):
                load_weight(sp, f"conv{i}", w_in, cols(3 + i))
            load_weight(sp, "gz", w_in, slice(3080, 3592))
            for t in range(NT):
                for what, src, out in (("dk", dk_tok, "new_diff_k"), ("dv", dv, "new_diff_v")):
                    sp.wait_ge(taken(ORDER.index((what, t, 0))), taken_count(ORDER.index((what, t, 0))))
                    dst = (a[out + "_p"][0, 0].rearrange("t h c -> t (h c)")[t * P:(t + 1) * P] if t < NTP
                           else a[out + "_s"][0].rearrange("b t h c -> (b t) (h c)"))
                    store(sp, dst, src[:, t, :])
            sp.wait_ge(p_dve["tt2"], p_dve.after(0, "tt2"))
            store(sp, a["new_conv_p"][0, 0], tails_tok[0:3, :])
            store(sp, a["new_conv_s"][0].rearrange("b j c -> (b j) c"), tails_tok[3:27, :])
            streams_sync(sp, UNIT["da0"], a["cache_diff_k"], a["cache_diff_v"], das_pe)
            load_weight(sp, "mix0", a["w_out"][0], cols(0))
            load_weight(sp, "mix1", a["w_out"][0], cols(1))
            sp.wait_ge(das_pe["sc"], das_pe.after(NB - 1, "sc"))
            for h in range(H):
                sp.dma_start(states[:, h, :, :], a["state_gdn"][0].rearrange("b h k v -> h k b v")[h]).then_inc(s_state, 16)
            sp.wait_ge(gs_act["mix"], gs_act.after(0, "mix"))
            sp.wait_ge(gh_dve["s1"], gh_dve.after(H - 1, "s1"))
            for t in range(NTP):
                sp.dma_start(x[:, t, :], a["x_prompt"][0][t * P:(t + 1) * P, :]).then_inc(s_xback, 16)
            sp.dma_start(x[:, 4, :], a["x_sample"].rearrange("b t d -> (b t) d")).then_inc(s_xback, 16)
            store(sp, a["new_gdn_p"][0, 0].rearrange("h k v -> k h v"), h4(state))
            for h in range(H):
                store(sp, a["new_gdn_s"][0].rearrange("b h k v -> h k b v")[h], states[:, h, :, :])
            n1 = n_out[0]
            sp.wait_ge(s_out, n1)
            sp.dma_start(mem_rows[:, :, :], a["mem_prompt"][0].rearrange("(t p) d -> p t d", p=P)).then_inc(s_mem, 16)
            for i, n in enumerate(("w_ck", "w_cv", "w_cq")):
                for j in range(2):
                    load_weight(sp, f"{('mk', 'mv', 'cq')[i]}{j}", a[n][0], cols(j))
            sp.dma_start(gffn_row, a["g_ffn"][0].partition_broadcast(P)).then_inc(s_route, 16)
            w_r = a["w_rt"][0].rearrange("(c p) n -> p c n", p=P)
            w_g = a["w_grp"][0].rearrange("(c p) n -> p c n", p=P)
            sp.dma_start(w_route[:, :, 0:4], w_g).then_inc(s_route, 16)
            sp.dma_start(w_route[:, :, 4:36], w_r).then_inc(s_route, 16)
            sp.dma_start(b_route[:, 0:4], a["b_grp"][0].partition_broadcast(P)).then_inc(s_bias, 16)
            sp.dma_start(b_route[:, 4:36], a["b_rt"][0].partition_broadcast(P)).then_inc(s_route, 16)
            sp.wait_ge(s_bias, 16)
            all_taken(sp, LAST_OF["mv"])
            store(sp, a["new_mem_k_p"][0, 0].rearrange("(t p) h c -> p t (h c)", p=P), mk_tok)
            store(sp, a["new_mem_v_p"][0, 0].rearrange("(t p) h c -> p t (h c)", p=P), mv)
            w_co = a["w_co"][0].rearrange("(c p) n -> p c n", p=P)
            for i in range(2):
                sp.dma_start(spare[i].rearrange("p (c n) -> p c n", n=512), w_co[:, 4 * i:4 * i + 4, cols(0)]).then_inc(s_co[0], 16)
            sp.wait_ge(x_dve["o1"], x_dve.after(NTP - 1, "o1"))
            sp.wait_ge(x_pe["pv1"], x_pe.after(NTP - 1, "pv1"))
            sp.wait_ge(s_out, n_out[0])
            sp.dma_start(conv[:, 0:4096].rearrange("p (c n) -> p c n", n=512), w_co[:, :, cols(1)]).then_inc(s_co[1], 16)
            streams_sync(sp, UNIT["x0"], a["cache_mem_k"], a["cache_mem_v"], xs_pe)
            moe_sync(sp)
            final_sync(sp)
            sp.wait_ge(s_out, n_out[0])

        @block.tensor
        def _(pe):
            prep_pe_a(pe)
            norm_pe(pe, "mix")
            pe.wait_ge(n_dve["mix"][f"ev{NT - 1}b"], n_dve["mix"].after(0, f"ev{NT - 1}b"))
            pe.wait_ge(s_small, N_SMALL)
            run_jobs(pe, ("dq", "dk", "dv"), act_a)
            prep_pe_b(pe)
            da_pe(pe)
            tails_pe(pe)

            pe.wait_ge(o_act["mix"], o_act.after(NTP - 1, "mix"))
            pe.wait_ge(das_copy["v"], das_copy.after(0, "v"))
            gdn_pe_prompt(pe)
            gdn_pe_sample(pe)
            pe.wait_ge(gs_act["mix"], gs_act.after(0, "mix"))
            run_jobs(pe, ("mix",), act_a)
            norm_pe(pe, "mem")
            pe.wait_ge(n_dve["mem"]["ev1b"], n_dve["mem"].after(0, "ev1b"))
            run_jobs(pe, ("mk", "mv"), mem_act)
            mem_turn_pe(pe)
            norm_pe(pe, "cross")
            pe.wait_ge(n_dve["cross"][f"ev{NT - 1}b"], n_dve["cross"].after(0, f"ev{NT - 1}b"))
            run_jobs(pe, ("cq",), act_a)
            xp_pe(pe)
            pe.wait_ge(x_act["o0"], x_act.after(NTP - 1, "o0"))
            pe.wait_ge(x_dve["o1"], x_dve.after(NTP - 1, "o1"))
            xs_pe.arm(pe)

            def stream(job, c):
                if job < NB:
                    xs_pe_stage(pe, job, job % 2, c)

            run_jobs(pe, ("co",), act_a, stream)
            norm_pe(pe, "ffn")
            route_pe(pe)
            moe_pe(pe)

        @block.scalar
        def _(act):
            prep_act_a(act)
            act.wait_ge(s_const, 16)
            norm_act(act, "mix", x_tile, lambda t: (s_x[t], 16))
            take_jobs("act", act, ("dq", "dk", "dv"), project_dst)
            act.wait_ge(n_dve["mix"][f"xn{NT - 1}"], n_dve["mix"].after(0, f"xn{NT - 1}"))
            da_act(act)
            prep_act_b(act)
            act.wait_ge(s_out, 16 * (2 * NT + 2))
            act.wait_ge(d_pe["pv"], d_pe.after(UN - 1, "pv"))
            act.wait_ge(o_pe["oT"], o_pe.after(NTP - 1, "oT"))
            act.wait_ge(das_copy["v"], das_copy.after(0, "v"))
            gate_act(act)
            act.wait_ge(c_act["gz"], c_act.after(0, "gz"))
            gdn_act(act)
            norm_act(act, "mem", lambda t: mem_rows[:, t, :], lambda t: (s_mem, 16))
            take_jobs("act", act, ("mk", "mv"), rest_dst)

            def x_sum(what, t):
                n = ORDER.index((what, t, 1))
                return taken(n), taken_count(n)

            norm_act(act, "cross", x_tile, lambda t: x_sum("mix", t))
            take_jobs("act", act, ("cq",), rest_dst)
            xp_act(act)
            xs_act.arm(act)
            for b in range(NB):
                for stage in range(STAGES):
                    xs_act_stage(act, b, stage)
            norm_act(act, "ffn", x_tile, lambda t: x_sum("co", t))
            route_act(act)
            moe_act(act)
            final_act(act)

        @block.vector
        def _(dve):
            prep_dve_a(dve)
            dve.wait_ge(s_gain, 64)
            norm_dve(dve, "mix", x_tile, gains[:, 0, :], act_a)
            take_jobs("dve", dve, ("dq", "dk", "dv"), project_dst)
            turn_k_dve(dve)
            da_dve(dve)
            das_start(dve)
            prep_dve_b(dve)
            dve.wait_ge(d_pe["pv"], d_pe.after(UN - 1, "pv"))
            dve.wait_ge(o_pe["oT"], o_pe.after(NTP - 1, "oT"))
            dve.wait_ge(s_out, 16 * (2 * NT + 2))
            dve.wait_ge(c_act["gz"], c_act.after(0, "gz"))
            gdn_dve(dve)
            dve.wait_ge(s_xback, 16 * NT)
            take_jobs("dve", dve, ("mix",), rest_dst)
            norm_dve(dve, "mem", lambda t: mem_rows[:, t, :], gains[:, 1, :], mem_act)
            take_jobs("dve", dve, ("mk", "mv"), rest_dst)
            mem_turn_dve(dve)
            norm_dve(dve, "cross", x_tile, gains[:, 2, :], act_a)
            take_jobs("dve", dve, ("cq",), rest_dst)
            xp_dve(dve)
            xs_dve.arm(dve)
            xs_zero.arm(dve)
            nc.vector.memset(c_q, 0.0).then_inc(xs_zero.step("q"), 1)
            dve.wait_ge(xs_zero["q"], xs_zero.after(0, "q"))

            def stream(job):
                if job < NB:
                    for stage in range(STAGES):
                        xs_dve_stage(dve, job, stage)

            take_jobs("dve", dve, ("co",), rest_dst, stream)
            norm_dve(dve, "ffn", x_tile, gains[:, 3, :], act_a)
            route_dve(dve)
            moe_dve(dve)
            final_dve(dve)

        @block.gpsimd
        def _(pool):
            prep_pool_a(pool)
            norm_pool(pool, "mix")
            da_pool(pool)
            gdn_pool(pool)
            norm_pool(pool, "mem")
            norm_pool(pool, "cross")
            norm_pool(pool, "ffn")
            ffn_rows_pool(pool)
            moe_pool(pool)
            final_pool(pool)


SCRATCH = {"h_rows": ((NT * P, D), F32), "pair_rows": ((NPAIR + 2 * CAP, D), F32)}

OUTPUTS = [
    ("y_prompt", (1, SEQ, D)), ("y_sample", (NB, TB, D)),
    ("new_diff_k_p", (1, 1, SEQ, H, 128)), ("new_diff_v_p", (1, 1, SEQ, H, 128)),
    ("new_conv_p", (1, 1, CONV - 1, 1536)), ("new_gdn_p", (1, 1, H, 128, 128)),
    ("new_mem_k_p", (1, 1, MEM, H, 256)), ("new_mem_v_p", (1, 1, MEM, H, 256)),
    ("new_diff_k_s", (1, NB, TB, H, 128)), ("new_diff_v_s", (1, NB, TB, H, 128)),
    ("new_conv_s", (1, NB, CONV - 1, 1536)), ("new_gdn_s", (1, NB, H, 128, 128)),
]


def kernel(**inputs):
    import numpy as _np
    import concourse.bacc as _bacc
    from concourse import mybir as _mybir
    from concourse.bass_utils import run_bass_kernel_spmd as _run

    nc = _bacc.Bacc("TRN2", target_bir_lowering=False, num_devices=1)
    arrays = {name: _np.ascontiguousarray(value) for name, value in inputs.items()}
    arrays["const"] = _np.concatenate([CONST[k] for k in CONST_AT], axis=1)
    aps = {}
    for name, value in arrays.items():
        aps[name] = nc.dram_tensor(name, value.shape, _mybir.dt.from_np(value.dtype), kind="ExternalInput").ap()
    for name, shape in OUTPUTS:
        aps[name] = nc.dram_tensor(name, shape, F32, kind="ExternalOutput").ap()
    for name, (shape, dt) in SCRATCH.items():
        aps[name] = nc.dram_tensor(name, shape, dt, kind="Internal").ap()
    build_encoder_step(nc, aps)
    r = _run(nc, [arrays], core_ids=[0])
    return tuple(r.results[0][name] for name, _ in OUTPUTS)
```

```python
from contextlib import ExitStack

import numpy as np

import concourse.bass as bass
from concourse import mybir

F32 = mybir.dt.float32
U32 = mybir.dt.uint32
ALU = mybir.AluOpType
ACT = mybir.ActivationFunctionType
AX = mybir.AxisListType

P = 128
D = 1024
KC = D // P
NT = 5
NTP = 4
SEQ = 512
NB = 8
TB = 16
H = 4
MEM = 256
CONV = 4
NG, NE, TOPK = 4, 32, 2
EPG = NE // NG
CAP = 80
MAXBLK = (NT * P * TOPK) // CAP + NE
BLKPAD = MAXBLK + 1
NBLK = BLKPAD + 5
NPAIR = TOPK * NT * P
EPS = 1e-6
BIG = 1.0e30
LAM_INIT = 0.8 - 0.6
GW = 3 + SEQ + NB * (TB + 3)
GS = 3 + SEQ



def constant_columns():
    p = np.arange(P)[:, None]
    f = np.arange(P)[None, :]
    same = p // TB == f // TB
    cols = {}
    cols["ident"] = (p == f) * 1.0
    cols["minus_half"] = np.full((P, 8), -0.5)
    cols["ones"] = np.ones((P, P))
    cols["cum_p"] = (p <= f) * 1.0
    cols["cum_s"] = ((p <= f) & same) * 1.0
    cols["low_p"] = np.where(f < p, 0.0, -BIG)
    cols["low_s"] = np.where((f < p) & same, 0.0, -BIG)
    cols["up_p"] = np.where(f >= p, 0.0, -BIG)
    cols["up_s"] = np.where((f >= p) & same, 0.0, -BIG)
    cols["blk16"] = same * 1.0
    for s in (32, 64, 128):
        cols[f"lev{s}"] = ((p // s == f // s) & (p // (s // 2) > f // (s // 2))) * 1.0
    cols["stream_off"] = np.repeat(np.where(np.arange(NB)[:, None] == f // TB, 0.0, -BIG).reshape(1, -1), P, 0)
    cols["stream_row"] = (p // TB == np.arange(NB)[None, :]) * 1.0
    row = np.arange(P)
    h, m, q = row // 32, (row // 16) % 2, row % 16
    cols["pick"] = (h * 16 + q)[:, None] == np.arange(64)[None, :]
    cols["map0"] = (m == 0)[:, None]
    cols["map1"] = (m == 1)[:, None]
    cols["capacities"] = np.repeat(CAP * np.arange(NT * P // CAP)[None] * 1.0, P, 0)
    cols["minus_one"] = np.full((P, 1), -1.0)
    cols["qk_scale"] = np.repeat(np.array([[P] * 4 + [1.0] * 4]), P, 0)
    cols["iota8"] = np.repeat(np.arange(8.0)[None], P, 0)
    cols["group"] = np.repeat((np.arange(NE) // EPG)[None] * 1.0, P, 0)
    cols["iota32"] = np.repeat(np.arange(NE)[None] * 1.0, P, 0)
    cols["block"] = np.repeat(np.arange(BLKPAD + 1)[None] * 1.0, P, 0)
    cols["pair"] = p + P * np.arange(TOPK * NT)[None, :] + 1
    cols["slot0"] = np.repeat(CAP * np.arange(NBLK)[None] * 1.0, P, 0)
    cols["iota_cap"] = np.repeat(np.arange(CAP)[None] * 1.0, P, 0)
    slot = np.arange(CAP)[:, None] + CAP * np.arange(NBLK)[None]
    cols["empty"] = np.zeros((P, NBLK))
    cols["empty"][:CAP] = (NPAIR + 1 + slot % (2 * CAP))
    return {k: np.asarray(v, np.float32) for k, v in cols.items()}


CONST = constant_columns()
CONST_AT, _at = {}, 0
for _k, _v in CONST.items():
    CONST_AT[_k] = (_at, _v.shape[1])
    _at += _v.shape[1]
NCONST = _at


class Steps:

    def __init__(self, sem, name, names):
        self.groups = []
        self.of = {}
        for i, group in enumerate(names.split("|")):
            group = group.split()
            self.groups.append([sem(f"{name}{i or ''}"), len(group), 0])
            for k, step in enumerate(group):
                assert step not in self.of
                self.of[step] = (i, k)

    def arm(self, eng):
        for sem, n, _ in self.groups:
            eng.sem_inc(sem, 2 * n)

    def __getitem__(self, name):
        return self.groups[self.of[name][0]][0]

    def after(self, it, name):
        i, k = self.of[name]
        n = self.groups[i][1]
        return it * n + (k + 1 + 2 * n)

    def step(self, name):
        i, k = self.of[name]
        group = self.groups[i]
        assert group[2] % group[1] == k, (name, k, group)
        group[2] += 1
        return group[0]




def weight_jobs():
    own = lambda what: [(what, t, 0) for t in range(NT)]
    wide = lambda what, n: [(what, m, c) for m in range(n) for c in range(2)]
    project = (
        [("dq", m, c) for m in range(4) for c in range(2)] + own("dk") + own("dv")
        + [("conv", m, c) for m in range(12) for c in range(2)] + [("gab", 0, c) for c in range(2)] + own("gz")
    )
    mix = [("mix", t, n) for n in range(2) for t in range(NTP)] + [("mix", NTP, n) for n in range(2)]
    memory = [("mk", t, n) for n in range(2) for t in range(2)] + [("mv", t, n) for n in range(2) for t in range(2)]
    return {"project": project, "mix": mix, "memory": memory, "cq": wide("cq", KC),
            "co": [("co", t, n) for n in range(2) for t in range(NTP)] + [("co", NTP, n) for n in range(2)]}


JOBS = weight_jobs()
ORDER = [job for group in ("project", "mix", "memory", "cq", "co") for job in JOBS[group]]
JOB_BANK = [7 if job[0] == "mix" and job[1] < NTP else n % (2 if job[0] in ("conv", "gz", "gab") else 4)
            for n, job in enumerate(ORDER)]


def bank_before(n):
    return max((m for m in range(n) if JOB_BANK[m] == JOB_BANK[n]), default=None)



def evacuator(n):
    if ORDER[n][0] == "mix":
        return "act" if ORDER[n][1] < NTP else "dve"
    return "dve" if ORDER[n][0] == "co" or n % 2 else "act"


TAKEN = {e: np.cumsum([evacuator(n) == e for n in range(len(ORDER))]).tolist() for e in ("act", "dve")}
MIX_JOBS = [n for n, job in enumerate(ORDER) if job[0] == "mix" and job[1] < NTP]
MEM_JOBS = [n for n, job in enumerate(ORDER) if job[0] in ("mk", "mv")]
CO_JOBS = [n for n, job in enumerate(ORDER) if job[0] == "co"]
LAST_OF = {job[0]: n for n, job in enumerate(ORDER)}

UNIT = {}
for _n, _u in enumerate(
    ["dq", "dk", "dv", "conv0", "conv1", "conv2", "gz"] + [f"da{b}" for b in range(NB)]
    + ["mix0", "mix1", "mk0", "mk1", "mv0", "mv1", "cq0", "cq1"] + [f"x{b}" for b in range(NB)]
):
    UNIT[_u] = _n
WSLOT = 6 * D


def unit_of(job):
    what, a, b = job
    if what == "conv":
        return UNIT[f"conv{a // 4}"]
    if what in ("mix", "mk", "mv"):
        return UNIT[f"{what}{b}"]
    if what == "cq":
        return UNIT[f"cq{a // 4}"]
    return None if what in ("gab", "co") else UNIT[what]


GDN_ACT = "sq0 sq1 EG eg qT D DT Mt M2 M2t M4 M4t M8 T0 T1 T2 w osq | mix"
GDN_PE = ("tokqk cum gcum chq chk kk kq Mt tokv sq2 sq2t x1 sq4 sq4t x2 sq8 x3 "
          "T0 BX0 Y0 T1 BX1 Y1 T2 BX2 Y2 w vn o s | oT")
GDN_DVE = ("gb gB ss ssq gc S qk0 qk1 SD SU kT SDb L M X0 vb be kbg X1 kl ktail X2 AT B0 X3 "
           "W0 Y0 B1 W1 Y1 B2 W2 Y2 qd vn sg s | oss oms on og oz")
GDN_POOL = "rn | orn"


def build_encoder_step(nc, a):
    ctx = ExitStack()
    with ctx:
        def sb(name, shape, dt=F32):
            return ctx.enter_context(nc.sbuf_tensor("sb_" + name, shape, dt))

        def sem(name):
            return ctx.enter_context(nc.semaphore(name))

        def steps(name, names):
            return Steps(sem, name, names)

        const = sb("const", [P, NCONST])
        x_buf = sb("x", [P, NT * D])
        x = x_buf[:, :].rearrange("p (t d) -> p t d", t=NT)
        act_a = sb("act_a", [P, KC, NT * P])
        act_b = sb("act_b", [P, KC * NT * P])
        attn = sb("attn", [P, 3 * NT * 512])
        conv = sb("conv", [P, 12 * GW])
        gz = sb("gz", [P, NT, 512])
        W = sb("W", [P, 2, WSLOT])
        scr = sb("scr", [P, 3, D])
        small = sb("small", [P, 768])
        gains = sb("gains", [P, 4, KC])
        gdn_g = sb("gdn_g", [P, 2 * 128])
        convw = sb("convw", [P, 12, CONV])
        w_gab = sb("w_gab", [P, KC, 8])

        def C(name, h=None):
            at, n = CONST_AT[name]
            v = const[:, at:at + n]
            return v if h is None else v.unsqueeze(1).to_broadcast([P, h, n])

        free = [0]

        def little(n):
            free[0] += n
            assert free[0] <= 768
            return small[:, free[0] - n:free[0]]

        ident = C("ident")
        dq = attn[:, 0:2560].rearrange("p (h t) -> p h t", h=H)
        dk = attn[:, 2560:5120].rearrange("p (h t) -> p h t", h=H)
        dv = attn[:, 5120:7680].rearrange("p (t c) -> p t c", t=NT)
        dk_tok = act_b[:, 0:2560].rearrange("p (t c) -> p t c", t=NT)
        cv = conv[:, :].rearrange("p (m c) -> p m c", m=12)
        bank = [ctx.enter_context(nc.psum_tensor(f"bank{i}", [P, 512], F32)) for i in range(8)]

        def quarters(b):
            return b[:, :].rearrange("p (h c) -> p h c", h=4)

        s_ident = sem("identity_loaded")
        s_const = sem("const_loaded")
        s_gain = sem("gains_loaded")
        s_x = [sem(f"x_loaded{t}") for t in range(NT)]
        s_w = [sem(f"w_loaded{k}") for k in range(2)]
        s_kv = [sem(f"kv_loaded{k}") for k in range(2)]
        s_hist = sem("conv_history_loaded")
        s_job = sem("jobs_computed")
        s_taken = {"act": sem("jobs_taken_by_act"), "dve": sem("jobs_taken_by_dve")}
        s_out = sem("outputs_stored")
        s_tails = sem("conv_history_stored")
        n_out = [0]

        def taken(n):
            return s_taken[evacuator(n)]

        def taken_count(n):
            return TAKEN[evacuator(n)][n]

        def all_taken(eng, last):
            for e in ("act", "dve"):
                if TAKEN[e][last]:
                    eng.wait_ge(s_taken[e], TAKEN[e][last])

        NORMS = {"mix": NT, "mem": 2, "cross": NT, "ffn": NT}
        n_act = {k: steps(f"norm_{k}_act", " ".join(f"sq{t}" for t in range(n))) for k, n in NORMS.items()}
        n_pool = {k: steps(f"norm_{k}_pool", " ".join(
            f"ms{t} rn{t}" + (f" g{t - 1}" if k == "ffn" and t >= 1 else "") for t in range(n)) + (f" g{n - 1}" if k == "ffn" else ""))
            for k, n in NORMS.items()}
        n_dve = {k: steps(f"norm_{k}_dve", " ".join(
            f"xn{t}" + ("" if t == 0 else f" ev{t - 1}a ev{t - 1}b") for t in range(n)) + f" ev{n - 1}a ev{n - 1}b"
            if k != "mem" else "xn0 xn1 ev0a ev0b ev1a ev1b") for k, n in NORMS.items()}
        n_pe = {k: steps(f"norm_{k}_pe", " ".join(f"tr{t}a tr{t}b" for t in range(n))) for k, n in NORMS.items()}
        ssq = {k: little(n) for k, n in NORMS.items()}
        rstd = {k: little(n) for k, n in NORMS.items()}

        def norm_act_tile(act, k, t, src, sem_, value):
            s = n_act[k]
            if t == 0:
                s.arm(act)
            act.wait_ge(sem_, value)
            if t:
                act.wait_ge(s[f"sq{t - 1}"], s.after(0, f"sq{t - 1}"))
            elif k == "cross":
                act.wait_ge(n_act["mem"]["sq1"], n_act["mem"].after(0, "sq1"))
            nc.scalar.activation(scr[:, 2, :], src, ACT.Square, accum_out=ssq[k][:, t:t + 1]).then_inc(s.step(f"sq{t}"), 1)

        def norm_pool_tile(pool, k, t):
            s = n_pool[k]
            if t == 0:
                s.arm(pool)
            pool.wait_ge(n_act[k][f"sq{t}"], n_act[k].after(0, f"sq{t}"))
            c = slice(t, t + 1)
            nc.gpsimd.tensor_scalar(rstd[k][:, c], ssq[k][:, c], 1.0 / D, EPS, ALU.mult, ALU.add).then_inc(s.step(f"ms{t}"), 1)
            pool.wait_ge(s[f"ms{t}"], s.after(0, f"ms{t}"))
            nc.gpsimd.tensor_tensor(rstd[k][:, c], rstd[k][:, c], C("minus_half")[:, 0:1], ALU.pow).then_inc(s.step(f"rn{t}"), 1)

        def norm_dve_rows(dve, k, t, src):
            s = n_dve[k]
            if t == 0:
                s.arm(dve)
            dve.wait_ge(n_pool[k][f"rn{t}"], n_pool[k].after(0, f"rn{t}"))
            if t >= 2:
                dve.wait_ge(n_pe[k][f"tr{t - 2}b"], n_pe[k].after(0, f"tr{t - 2}b"))
                if k == "ffn":
                    dve.wait_ge(n_pool[k][f"g{t - 2}"], n_pool[k].after(0, f"g{t - 2}"))
            elif k == "cross":
                dve.wait_ge(n_pe["mem"]["tr1b"], n_pe["mem"].after(0, "tr1b"))
            nc.vector.tensor_scalar(scr[:, t % 2, :], src, rstd[k][:, t:t + 1], None, ALU.mult).then_inc(s.step(f"xn{t}"), 1)

        def norm_dve_out(dve, k, t, gain, dst):
            for i, ab in enumerate("ab"):
                dve.wait_ge(n_pe[k][f"tr{t}{ab}"], n_pe[k].after(0, f"tr{t}{ab}"))
                o = dst[:, 4 * i:4 * i + 4, t * P:(t + 1) * P]
                g = gain[:, 4 * i:4 * i + 4].unsqueeze(2).to_broadcast([P, 4, P])
                nc.vector.tensor_tensor(o, quarters(bank[4 + 2 * (t % 2) + i]), g, ALU.mult).then_inc(n_dve[k].step(f"ev{t}{ab}"), 1)

        def norm_pe_tile(pe, k, t):
            s = n_pe[k]
            if t == 0:
                s.arm(pe)
            pe.wait_ge(n_dve[k][f"xn{t}"], n_dve[k].after(0, f"xn{t}"))
            for i, ab in enumerate("ab"):
                if t >= 2:
                    pe.wait_ge(n_dve[k][f"ev{t - 2}{ab}"], n_dve[k].after(0, f"ev{t - 2}{ab}"))
                elif k == "cross":
                    pe.wait_ge(n_dve["mem"]["ev1b"], n_dve["mem"].after(0, "ev1b"))
                for c in range(4):
                    q = 4 * i + c
                    mm = nc.tensor.transpose(quarters(bank[4 + 2 * (t % 2) + i])[:, c, :], scr[:, t % 2, q * P:(q + 1) * P], ident)
                mm.then_inc(s.step(f"tr{t}{ab}"), 1)

        def norm_dve(dve, k, src, gain, dst):
            for t in range(NORMS[k] + 1):
                if t < NORMS[k]:
                    norm_dve_rows(dve, k, t, src(t))
                if t >= 1:
                    norm_dve_out(dve, k, t - 1, gain, dst)

        def x_tile(t):
            return x[:, t, :]

        def slot(n):
            return W[:, n % 2, 0:4096].rearrange("p (c n) -> p c n", c=KC)

        spare = [W[:, 0, 4096:], W[:, 1, 4096:]]
        s_co = [sem(f"w_co_loaded{n}") for n in range(2)]

        def co_chunk(n, c):
            return spare[c // 4][:, 512 * (c % 4):512 * (c % 4) + 512] if n == 0 else conv[:, 512 * c:512 * c + 512]

        def run_jobs(pe, names, src, between=None, only=None, chunks=range(KC)):
            at = -1
            for n, job in enumerate(ORDER):
                what, ja, jb = job
                if what not in names or (only is not None and n not in only):
                    continue
                at += 1
                unit = unit_of(job)
                if what == "co" and ja == NTP:
                    pe.wait_ge(xs_act["o"], xs_act.after(NB - 1, "o"))
                if what == "co" and ja == 0:
                    pe.wait_ge(s_co[jb], 16 * (2 - jb))
                first = n == 0 or unit_of(ORDER[n - 1]) != unit
                if unit is not None and first and chunks[0] == 0:
                    pe.wait_ge(s_w[unit % 2], 16 * W_COUNT[unit])
                m = bank_before(n)
                if m is not None and chunks[0] == 0:
                    pe.wait_ge(taken(m), taken_count(m))
                out = bank[JOB_BANK[n]]
                for c in chunks:
                    if what == "gab":
                        cols = slice(0, 512) if jb == 0 else slice(512, 640)
                        mm = nc.tensor.matmul(out[0:8, 0:cols.stop - cols.start], w_gab[:, c, :], src[:, c, cols],
                                              start=c == 0, stop=c == KC - 1)
                    elif what in ("dq", "conv", "cq"):
                        cols = slice(0, 512) if jb == 0 else slice(512, 640)
                        m = ja % 4
                        mm = nc.tensor.matmul(out[:, 0:cols.stop - cols.start], slot(unit)[:, c, m * P:(m + 1) * P],
                                              src[:, c, cols], start=c == 0, stop=c == KC - 1)
                    else:
                        w = co_chunk(jb, c) if what == "co" else slot(unit)[:, c, :]
                        mm = nc.tensor.matmul(out[:, :], src[:, c, ja * P:(ja + 1) * P], w, start=c == 0, stop=c == KC - 1)
                        if c == KC - 1:
                            mm.then_inc(s_job, 1)
                    if between is not None:
                        between(at, c)
                if what in ("dq", "conv", "cq", "gab"):
                    mm.then_inc(s_job, 1)

        gabT = act_b[0:8, 4480:4480 + NT * P]
        gab = bank[3][:, 0:8 * NT]

        def take_jobs(me, eng, names, dst, between=None, only=None):
            at = -1
            for n, job in enumerate(ORDER):
                if job[0] not in names or evacuator(n) != me or (only is not None and n not in only):
                    continue
                at += 1
                if between is not None:
                    between(at)
                eng.wait_ge(s_job, n + 1)
                for i, (o, b, scale) in enumerate(dst(job, bank[JOB_BANK[n]])):
                    if me == "dve" and job[0] in ("mix", "co"):
                        ins = nc.vector.tensor_tensor(o, b, o, ALU.add)
                    elif me == "act":
                        ins = nc.scalar.mul(o, b, scale) if scale != 1.0 else nc.scalar.copy(o, b)
                    elif scale != 1.0:
                        ins = nc.vector.tensor_scalar(o, b, scale, None, ALU.mult)
                    else:
                        ins = nc.vector.tensor_copy(o, b)
                ins.then_inc(s_taken[me], 1)

        def project_dst(job, b):
            what, ja, jb = job
            n = 512 if jb == 0 else P
            at = 512 * jb
            if what == "dq":
                return [(dq[:, ja, at:at + n], b[:, 0:n], 0.125)]
            if what == "conv":
                if jb == 0:
                    return [(cv[:, ja, 3:GS], b[:, :], 1.0)]
                return [(cv[:, ja, GS:GW].rearrange("p (b c) -> p b c", b=NB)[:, :, 3:],
                         b[:, 0:P].rearrange("p (b c) -> p b c", b=NB), 1.0)]
            if what == "gab":
                return [(gabT[:, at:at + n], b[0:8, 0:n], 1.0)]
            return [({"dk": dk_tok, "dv": dv, "gz": gz}[what][:, ja, :], b[:, :], 1.0)]

        W_COUNT, _count = {}, [0, 0]
        for name, n in UNIT.items():
            if not (name[0:2] == "da" or name[0] == "x"):
                _count[n % 2] += 1
                W_COUNT[n] = _count[n % 2]

        LAST_JOB = {unit_of(job): n for n, job in enumerate(ORDER)}

        def load_weight(eng, name, src, cols):
            n = UNIT[name]
            b = n - 2 - UNIT["da0"]
            if 0 <= b < NB:
                eng.wait_ge(das_pe["pv"], das_pe.after(b, "pv"))
            if n - 2 in LAST_JOB:
                eng.wait_ge(s_job, LAST_JOB[n - 2] + 1)
            eng.dma_start(slot(n), src.rearrange("(c p) n -> p c n", p=P)[:, :, cols]).then_inc(s_w[n % 2], 16)

        lam4 = little(4 * 64)
        lamp = little(2)
        lame = little(2)
        nlam = little(1)
        row_sign = little(1)
        alog = little(4)
        dtb = little(4)
        nexp_a = little(4)
        glog = little(4 * NT)
        beta = little(4 * NT)
        tz, te = little(4 * NT), little(4 * NT)

        hist = act_b[0:NB * 3, 2560:4096]
        tails = act_b[:, 4096:4096 + 12 * 27].rearrange("p (m c) -> p m c", m=12)
        tails_tok = act_b[0:27, 2560:4096]

        p_dve = steps("prep_dve", "lam0 lam1 nlam sign sign2 gsub hist kT0 kT1 kT2 kT3 kT4 na z az "
                                  "tt0 tt1 tt2 sp0 sp1 g b1 b2")
        p_act = steps("prep_act", "lam ea e l eb")
        p_pe = steps("prep_pe", "hist kT0 kT1 kT2 kT3 kT4 gab tt0 tt1 tt2")
        p_pool = steps("prep_pool", "zero")
        s_small = sem("small_loaded")

        def prep_sync_load(sp):
            for i, n in enumerate(("lam_q1", "lam_k1", "lam_q2", "lam_k2")):
                sp.dma_start(lam4[:, 64 * i:64 * i + 64], a[n][0].partition_broadcast(P)).then_inc(s_small, 16)
            sp.dma_start(alog, a["a_log"][0].partition_broadcast(P)).then_inc(s_small, 16)
            sp.dma_start(dtb, a["dt_bias"][0].partition_broadcast(P)).then_inc(s_small, 16)
            sp.dma_start(gdn_g[:, 0:128], a["g_subln"][0].partition_broadcast(P)).then_inc(s_small, 16)
            sp.dma_start(gdn_g[:, 128:256], a["g_gdn_out"][0].partition_broadcast(P)).then_inc(s_small, 16)
            for m in range(CONV):
                sp.dma_start(convw[:, :, m], a["conv_w"][0][m].rearrange("(m p) -> p m", p=P),
                             allow_slow_non_contiguous=True).then_inc(s_small, 16)
            sp.dma_start(w_gab[:, :, :], a["w_in"][0].rearrange("(c p) n -> p c n", p=P)[:, :, 3072:3080]).then_inc(s_small, 16)

        N_SMALL = 16 * (4 + 2 + 2 + CONV + 1)

        def prep_pool_a(pool):
            p_pool.arm(pool)
            nc.gpsimd.memset(cv[:, :, 0:3], 0.0).then_inc(p_pool.step("zero"), 1)

        def prep_dve_a(dve):
            p_dve.arm(dve)
            dve.wait_ge(s_small, N_SMALL)
            dve.wait_ge(s_const, 16)
            l4 = lam4.rearrange("p (a b c) -> p a b c", a=2, b=2)
            nc.vector.tensor_tensor(l4[:, :, 0, :], l4[:, :, 0, :], l4[:, :, 1, :], ALU.mult).then_inc(p_dve.step("lam0"), 1)
            dve.wait_ge(p_dve["lam0"], p_dve.after(0, "lam0"))
            nc.vector.tensor_reduce(lamp, l4[:, :, 0, :], AX.X, ALU.add).then_inc(p_dve.step("lam1"), 1)
            dve.wait_ge(p_act["lam"], p_act.after(0, "lam"))
            nc.vector.scalar_tensor_tensor(nlam, lame[:, 1:2], -LAM_INIT, lame[:, 0:1], ALU.add, ALU.subtract).then_inc(p_dve.step("nlam"), 1)
            dve.wait_ge(p_dve["nlam"], p_dve.after(0, "nlam"))
            nc.vector.tensor_tensor(row_sign, C("map1"), nlam, ALU.mult).then_inc(p_dve.step("sign"), 1)
            dve.wait_ge(p_dve["sign"], p_dve.after(0, "sign"))
            nc.vector.tensor_tensor(row_sign, row_sign, C("map0"), ALU.add).then_inc(p_dve.step("sign2"), 1)
            nc.vector.tensor_scalar(gdn_g[:, 0:128], gdn_g[:, 0:128], 1.0 - LAM_INIT, None, ALU.mult).then_inc(p_dve.step("gsub"), 1)
            dve.wait_ge(p_pe["hist"], p_pe.after(0, "hist"))
            for b in range(NB):
                ins = nc.vector.tensor_copy(cv[:, :, GS + 19 * b:GS + 19 * b + 3],
                                            bank[7][:, 0:288].rearrange("p (m r) -> p m r", m=12)[:, :, 3 * b:3 * b + 3])
            ins.then_inc(p_dve.step("hist"), 1)

        def prep_act_a(act):
            p_act.arm(act)
            act.wait_ge(p_dve["lam1"], p_dve.after(0, "lam1"))
            nc.scalar.activation(lame, lamp, ACT.Exp).then_inc(p_act.step("lam"), 1)
            nc.scalar.activation(nexp_a, alog, ACT.Exp).then_inc(p_act.step("ea"), 1)

        def prep_pe_a(pe):
            p_pe.arm(pe)
            pe.wait_ge(s_const, 16)
            pe.wait_ge(s_hist, 16)
            pe.wait_ge(n_dve["mix"][f"ev{NT - 1}b"], n_dve["mix"].after(0, f"ev{NT - 1}b"))
            for m in range(12):
                mm = nc.tensor.transpose(bank[7][:, 24 * m:24 * m + 24], hist[:, m * P:(m + 1) * P], ident[0:24, 0:24])
            mm.then_inc(p_pe.step("hist"), 1)

        def prep_pe_b(pe):
            for t in range(NT):
                pe.wait_ge(taken(ORDER.index(("dk", t, 0))), taken_count(ORDER.index(("dk", t, 0))))
                if t >= 2:
                    pe.wait_ge(p_dve[f"kT{t - 2}"], p_dve.after(0, f"kT{t - 2}"))
                else:
                    pe.wait_ge(n_dve["mix"][f"ev{NT - 1}b"], n_dve["mix"].after(0, f"ev{NT - 1}b"))
                for h in range(H):
                    mm = nc.tensor.transpose(quarters(bank[4 + t % 2])[:, h, :], dk_tok[:, t, h * P:(h + 1) * P], ident)
                mm.then_inc(p_pe.step(f"kT{t}"), 1)

        def tails_pe(pe):
            pe.wait_ge(d_act["p1"], d_act.after(UN - 1, "p1"))
            all_taken(pe, LAST_OF["gab"])
            for t in range(NT):
                mm = nc.tensor.transpose(gab[:, 8 * t:8 * t + 8], gabT[:, t * P:(t + 1) * P], ident[0:8, 0:8])
            mm.then_inc(p_pe.step("gab"), 1)
            pe.wait_ge(c_pool["tail1"], c_pool.after(11, "tail1"))
            pe.wait_ge(d_act["aT"], d_act.after(UN - 1, "aT"))
            for g in range(3):
                if g == 2:
                    pe.wait_ge(p_dve["tt0"], p_dve.after(0, "tt0"))
                for i in range(4):
                    mm = nc.tensor.transpose(bank[4 + g % 2][0:27, i * P:(i + 1) * P], tails[:, 4 * g + i, :], ident)
                mm.then_inc(p_pe.step(f"tt{g}"), 1)

        def turn_k_dve(dve):
            for t in range(NT):
                dve.wait_ge(p_pe[f"kT{t}"], p_pe.after(0, f"kT{t}"))
                nc.vector.tensor_copy(dk[:, :, t * P:(t + 1) * P], quarters(bank[4 + t % 2])).then_inc(p_dve.step(f"kT{t}"), 1)

        def prep_dve_b(dve):
            dve.wait_ge(p_act["ea"], p_act.after(0, "ea"))
            nc.vector.tensor_scalar(nexp_a, nexp_a, -1.0, None, ALU.mult).then_inc(p_dve.step("na"), 1)
            dve.wait_ge(p_dve["na"], p_dve.after(0, "na"))
            dve.wait_ge(p_pe["gab"], p_pe.after(0, "gab"))
            g3 = gab.rearrange("p (t c) -> p t c", t=NT)

            def wide(v):
                return v.unsqueeze(1).to_broadcast([P, NT, 4])

            v3 = lambda v: v.rearrange("p (t c) -> p t c", t=NT)
            nc.vector.tensor_tensor(v3(tz), g3[:, :, 0:4], wide(dtb), ALU.add).then_inc(p_dve.step("z"), 1)
            dve.wait_ge(p_dve["z"], p_dve.after(0, "z"))
            nc.vector.scalar_tensor_tensor(te, tz, -1.0, tz, ALU.mult, ALU.max).then_inc(p_dve.step("az"), 1)
            for g in range(3):
                dve.wait_ge(p_pe[f"tt{g}"], p_pe.after(0, f"tt{g}"))
                nc.vector.tensor_copy(tails_tok[:, g * 512:(g + 1) * 512], bank[4 + g % 2][0:27, :]).then_inc(p_dve.step(f"tt{g}"), 1)
            dve.wait_ge(p_act["l"], p_act.after(0, "l"))
            nc.vector.tensor_scalar(tz, tz, 0.0, None, ALU.max).then_inc(p_dve.step("sp0"), 1)
            dve.wait_ge(p_dve["sp0"], p_dve.after(0, "sp0"))
            nc.vector.tensor_tensor(tz, tz, te, ALU.add).then_inc(p_dve.step("sp1"), 1)
            dve.wait_ge(p_dve["sp1"], p_dve.after(0, "sp1"))
            nc.vector.tensor_tensor(v3(glog), v3(tz), wide(nexp_a), ALU.mult).then_inc(p_dve.step("g"), 1)
            dve.wait_ge(p_act["eb"], p_act.after(0, "eb"))
            nc.vector.tensor_scalar(beta, beta, 1.0, None, ALU.add).then_inc(p_dve.step("b1"), 1)
            dve.wait_ge(p_dve["b1"], p_dve.after(0, "b1"))
            nc.vector.reciprocal(beta, beta).then_inc(p_dve.step("b2"), 1)

        def prep_act_b(act):
            act.wait_ge(p_pe["gab"], p_pe.after(0, "gab"))
            act.wait_ge(p_dve["az"], p_dve.after(0, "az"))
            nc.scalar.activation(te, te, ACT.Exp, scale=-1.0).then_inc(p_act.step("e"), 1)
            act.wait_ge(p_act["e"], p_act.after(0, "e"))
            nc.scalar.activation(te, te, ACT.Ln, bias=C("ones")[:, 0:1]).then_inc(p_act.step("l"), 1)
            nc.scalar.activation(beta.rearrange("p (t c) -> p t c", t=NT),
                                            gab.rearrange("p (t c) -> p t c", t=NT)[:, :, 4:8], ACT.Exp, scale=-1.0).then_inc(p_act.step("eb"), 1)

        NY = GW - 3
        c_mul = steps("conv_products", "m0 m1 m2 m3")
        c_pool = steps("conv_pool", "tail0 tail1 y1 y2 y3")
        c_act = steps("conv_silu", "silu0 silu3 silu6 silu9 gz")
        taps = scr[:, :, :].rearrange("p a b -> p (a b)")[:, 0:4 * NY].rearrange("p (j c) -> p j c", j=CONV)

        def conv_act_one(act, m):
            for jb in range(2):
                n = ORDER.index(("conv", m, jb))
                act.wait_ge(taken(n), taken_count(n))
            if m == 0:
                c_mul.arm(act)
                act.wait_ge(p_dve["hist"], p_dve.after(0, "hist"))
                act.wait_ge(p_pool["zero"], p_pool.after(0, "zero"))
                act.wait_ge(n_pe["mix"][f"tr{NT - 1}b"], n_pe["mix"].after(0, f"tr{NT - 1}b"))
            act.wait_ge(c_pool["y3"], c_pool.after(m - 1, "y3"))
            for j in range(CONV):
                nc.scalar.mul(taps[:, j, :], cv[:, m, j:j + NY], convw[:, m, j:j + 1]).then_inc(c_mul.step(f"m{j}"), 1)

        def conv_pool_one(pool, m):
            for jb in range(2):
                n = ORDER.index(("conv", m, jb))
                pool.wait_ge(taken(n), taken_count(n))
            nc.gpsimd.tensor_copy(tails[:, m, 0:3], cv[:, m, GS - 3:GS]).then_inc(c_pool.step("tail0"), 1)
            last3 = cv[:, m, GS:GW].rearrange("p (b c) -> p b c", b=NB)[:, :, TB:]
            nc.gpsimd.tensor_copy(tails[:, m, 3:27].rearrange("p (b c) -> p b c", b=NB), last3).then_inc(c_pool.step("tail1"), 1)
            pool.wait_ge(c_mul["m3"], c_mul.after(m, "m3"))
            nc.gpsimd.tensor_tensor(taps[:, 0, :], taps[:, 0, :], taps[:, 1, :], ALU.add).then_inc(c_pool.step("y1"), 1)
            nc.gpsimd.tensor_tensor(taps[:, 2, :], taps[:, 2, :], taps[:, 3, :], ALU.add).then_inc(c_pool.step("y2"), 1)
            pool.wait_ge(c_pool["y2"], c_pool.after(m, "y2"))
            nc.gpsimd.tensor_tensor(cv[:, m, 0:NY], taps[:, 0, :], taps[:, 2, :], ALU.add).then_inc(c_pool.step("y3"), 1)

        def gate_act(act):
            act.wait_ge(taken(LAST_OF["gz"]), taken_count(LAST_OF["gz"]))
            act.wait_ge(taken(LAST_OF["gz"] - 1), taken_count(LAST_OF["gz"] - 1))
            nc.scalar.activation(gz[:, :, :], gz[:, :, :], ACT.Silu).then_inc(c_act.step("gz"), 1)

        UN = NTP * H
        da_out = spare[0].rearrange("p (h t) -> p h t", h=H)
        moved = steps("da_outputs", "moved")
        d_pe = steps("da_pe", "sc | tr | pv")
        d_dve = steps("da_dve", "cut mx | r c2 a0 a")
        d_act = steps("da_act", "p0 p1 | aT")
        prob = [x_buf[:, 1024 * i:1024 * (i + 1)].rearrange("p (m k) -> p m k", m=2) for i in range(2)]
        aT = [x_buf[:, 2048 + 512 * i:2560 + 512 * i] for i in range(2)]
        osq, on = x_buf[:, 3072:3584], x_buf[:, 3584:4096]
        nmax = [little(2) for _ in range(2)]
        psum_p = [little(2) for _ in range(2)]
        pr = [little(2) for _ in range(2)]
        o_pe = steps("da_out_pe", "oT")
        o_act = steps("da_out_act", "sq mix")
        o_dve = steps("da_out_dve", "ss on og")
        o_pool = steps("da_out_pool", "ms rn")
        oss = little(4)

        def b4(v):
            return v.unsqueeze(2).to_broadcast([P, 4, P])

        def h4(v):
            return v.rearrange("p (h c) -> p h c", h=4)

        def beside(u):
            if u < 12:
                return [ORDER.index(("conv", u, jb)) for jb in range(2)]
            return [ORDER.index(("gab", 0, c)) for c in range(2)] if u == 12 else [ORDER.index(("gz", u - 13, 0))]

        def da_pe(pe):
            d_pe.arm(pe)
            o_pe.arm(pe)
            for u in range(UN + 2):
                t, h = divmod(u, H)
                q = u % 2
                if u < UN:
                    if u == 0:
                        all_taken(pe, LAST_OF["dv"])
                        pe.wait_ge(p_dve["kT4"], p_dve.after(0, "kT4"))
                    else:
                        pe.wait_ge(d_act["p1"], d_act.after(u - 1, "p1"))
                    for m in range(2):
                        rows = slice(64 * m, 64 * m + 64)
                        mm = nc.tensor.matmul(bank[2 + m][:, 0:P * (t + 1)], dq[rows, h, t * P:(t + 1) * P],
                                              dk[rows, h, 0:P * (t + 1)], start=True, stop=True)
                    mm.then_inc(d_pe.step("sc"), 1)
                run_jobs(pe, ("conv", "gz", "gab"), act_a, None, beside(u)[:1])
                if 1 <= u and h == 0 and t >= 1:
                    pe.wait_ge(o_dve["og"], o_dve.after(t - 1, "og"))
                    for c in range(H):
                        mm = nc.tensor.transpose(quarters(bank[6 + (t - 1) % 2])[:, c, :], on[:, c * P:(c + 1) * P], ident)
                    mm.then_inc(o_pe.step("oT"), 1)
                if u < UN:
                    pe.wait_ge(d_dve["a"], d_dve.after(u, "a"))
                    for k in range(t + 1):
                        mm = nc.tensor.transpose(bank[4 + q][:, k * P:(k + 1) * P], prob[q][:, 0, k * P:(k + 1) * P], ident)
                    mm.then_inc(d_pe.step("tr"), 1)
                run_jobs(pe, ("conv", "gz", "gab"), act_a, None, beside(u)[1:])
                if u < UN:
                    pe.wait_ge(d_act["aT"], d_act.after(u, "aT"))
                    if h == 0 and t >= 2:
                        pe.wait_ge(o_act["mix"], o_act.after(t - 2, "mix"))
                    for k in range(t + 1):
                        mm = nc.tensor.matmul(bank[6 + t % 2][:, h * P:(h + 1) * P], aT[q][:, k * P:(k + 1) * P],
                                              dv[:, k, h * P:(h + 1) * P], start=k == 0, stop=k == t)
                    mm.then_inc(d_pe.step("pv"), 1)

        def da_dve(dve):
            d_dve.arm(dve)
            o_dve.arm(dve)
            for u in range(UN + 2):
                t, h = divmod(u, H)
                q = u % 2
                n = P * (t + 1)
                if u < UN:
                    dve.wait_ge(d_pe["sc"], d_pe.after(u, "sc"))
                    for m in range(2):
                        ins = nc.vector.memset(bank[2 + m][0:64, P * t + 64:P * t + 128], -BIG)
                    ins.then_inc(d_dve.step("cut"), 1)
                    dve.wait_ge(d_dve["cut"], d_dve.after(u, "cut"))
                    for m in range(2):
                        ins = nc.vector.tensor_reduce(nmax[q][:, m:m + 1], bank[2 + m][:, 0:n], AX.X, ALU.max, negate=True)
                    ins.then_inc(d_dve.step("mx"), 1)
                if h == 0 and t >= 1:
                    head_norm_dve(dve, o_dve, o_act, o_pool, t - 1, bank[6 + (t - 1) % 2], gdn_g[:, 0:128], osq, on)
                if u < UN:
                    dve.wait_ge(d_act["p1"], d_act.after(u, "p1"))
                    nc.vector.reciprocal(pr[q], psum_p[q]).then_inc(d_dve.step("r"), 1)
                    dve.wait_ge(d_dve["r"], d_dve.after(u, "r"))
                    nc.vector.tensor_tensor(pr[q][:, 1:2], pr[q][:, 1:2], nlam, ALU.mult).then_inc(d_dve.step("c2"), 1)
                    dve.wait_ge(d_dve["c2"], d_dve.after(u, "c2"))
                    nc.vector.tensor_scalar(prob[q][:, 0, 0:n], prob[q][:, 0, 0:n], pr[q][:, 0:1], None, ALU.mult).then_inc(d_dve.step("a0"), 1)
                    dve.wait_ge(d_dve["a0"], d_dve.after(u, "a0"))
                    nc.vector.scalar_tensor_tensor(prob[q][:, 0, 0:n], prob[q][:, 1, 0:n], pr[q][:, 1:2], prob[q][:, 0, 0:n],
                                                   ALU.mult, ALU.add).then_inc(d_dve.step("a"), 1)
                take_jobs("dve", dve, ("conv", "gz", "gab"), project_dst, None, beside(u))

        def head_norm_dve(dve, s, s_act, s_pool, t, b, gain, osq, on, part=None):
            if part != 1:
                dve.wait_ge(s_act["sq"], s_act.after(t, "sq"))
                nc.vector.tensor_reduce(oss, h4(osq), AX.X, ALU.add).then_inc(s.step("ss"), 1)
            if part != 0:
                dve.wait_ge(s_pool["rn"], s_pool.after(t, "rn"))
                nc.vector.tensor_tensor(h4(on), h4(b[:, :]), b4(oss), ALU.mult).then_inc(s.step("on"), 1)
                dve.wait_ge(s["on"], s.after(t, "on"))
                nc.vector.tensor_tensor(h4(on), h4(on), gain.unsqueeze(1).to_broadcast([P, 4, P]), ALU.mult).then_inc(s.step("og"), 1)

        def head_norm_pool(pool, s, s_dve, t):
            pool.wait_ge(s_dve["ss"], s_dve.after(t, "ss"))
            nc.gpsimd.tensor_scalar(oss, oss, 1.0 / P, EPS, ALU.mult, ALU.add).then_inc(s.step("ms"), 1)
            pool.wait_ge(s["ms"], s.after(t, "ms"))
            nc.gpsimd.tensor_tensor(oss, oss, C("minus_half")[:, 0:4], ALU.pow).then_inc(s.step("rn"), 1)

        def da_act(act):
            d_act.arm(act)
            o_act.arm(act)
            c_act.arm(act)
            for u in range(UN + 2):
                t, h = divmod(u, H)
                q = u % 2
                n = P * (t + 1)
                if u < UN:
                    act.wait_ge(d_dve["mx"], d_dve.after(u, "mx"))
                    if u >= 2:
                        act.wait_ge(d_pe["tr"], d_pe.after(u - 2, "tr"))
                    for m in range(2):
                        nc.scalar.activation(prob[q][:, m, 0:n], bank[2 + m][:, 0:n], ACT.Exp, bias=nmax[q][:, m:m + 1],
                                             accum_out=psum_p[q][:, m:m + 1]).then_inc(d_act.step(f"p{m}"), 1)
                if 1 <= u <= 12:
                    conv_act_one(act, u - 1)
                take_jobs("act", act, ("conv", "gz", "gab"), project_dst, None, beside(u)[:1])
                if h == 0 and t >= 1:
                    act.wait_ge(o_pe["oT"], o_pe.after(t - 1, "oT"))
                    nc.scalar.copy(da_out[:, :, (t - 1) * P:t * P], quarters(bank[6 + (t - 1) % 2])).then_inc(o_act.step("mix"), 1)
                if u < UN:
                    act.wait_ge(d_pe["tr"], d_pe.after(u, "tr"))
                    if u >= 2:
                        act.wait_ge(d_pe["pv"], d_pe.after(u - 2, "pv"))
                    nc.scalar.copy(aT[q][:, 0:n], bank[4 + q][:, 0:n]).then_inc(d_act.step("aT"), 1)
                take_jobs("act", act, ("conv", "gz", "gab"), project_dst, None, beside(u)[1:])
                if u < UN and h == H - 1:
                    act.wait_ge(d_pe["pv"], d_pe.after(u, "pv"))
                    nc.scalar.activation(osq, bank[6 + t % 2][:, :], ACT.Square).then_inc(o_act.step("sq"), 1)
                if u >= 4 and (u - 4) % 3 == 0 and u <= 13:
                    m = u - 4
                    act.wait_ge(c_pool["y3"], c_pool.after(m + 2, "y3"))
                    nc.scalar.activation(cv[:, m:m + 3, 0:NY], cv[:, m:m + 3, 0:NY], ACT.Silu).then_inc(c_act.step(f"silu{m}"), 1)
            gate_act(act)
            act.wait_ge(s_job, len(JOBS["project"]))
            act.wait_ge(o_act["mix"], o_act.after(NTP - 1, "mix"))
            moved.arm(act)
            nc.scalar.copy(act_a[:, 0:4, 0:SEQ], da_out).then_inc(moved.step("moved"), 1)

        def da_pool(pool):
            o_pool.arm(pool)
            c_pool.arm(pool)
            pool.wait_ge(p_dve["hist"], p_dve.after(0, "hist"))
            pool.wait_ge(p_pool["zero"], p_pool.after(0, "zero"))
            for u in range(UN + 2):
                if u % H == 0 and u >= H:
                    head_norm_pool(pool, o_pool, o_dve, u // H - 1)
                if 1 <= u <= 12:
                    conv_pool_one(pool, u - 1)

        STAGES = 8
        sq_ = spare[1][:, 0:512].rearrange("p (h t) -> p h t", h=H)
        sk_ = spare[1][:, 512:1024].rearrange("p (h t) -> p h t", h=H)
        sv_ = spare[1][:, 1024:1536]
        s_aT = spare[1][:, 1536:1536 + 336]
        s_q = spare[0][:, 0:256].rearrange("p (c r) -> p c r", r=32)
        s_P, s_sn, s_cm = spare[0][:, 256:896], spare[0][:, 896:1024], spare[0][:, 1024:1088]
        s_o = spare[0][:, 1088:1344]
        s_KT = act_b[:, 0:2048]
        da_oT = act_b[:, 4608:5120].rearrange("p (h t) -> p h t", h=H)
        s_mx, s_sum = little(4), little(4)
        das_pe = steps("da_stream_pe", "f0 f1 f2 f3 sc pT pv oT")
        das_dve = steps("da_stream_dve", "q f1 f3 sn mx mx2 mxm sum r c cm pT")
        das_act = steps("da_stream_act", "f0 f2 p pn pv o")
        das_copy = steps("da_stream_sample", "q k v zq za")

        def kv_slot(first_unit, k, cross):
            w = W[:, (first_unit + k) % 2, 0:4096]
            n = 2 if cross else 4
            return (w[:, 0:2048].rearrange("p (m c) -> p m c", m=n), w[:, 2048:4096].rearrange("p (m c) -> p m c", m=n))

        def streams_sync(sp, first_unit, ck, cvv, s_pe):

            def one(b, k):
                if isinstance(b, int):
                    sp.wait_ge(s_job, LAST_JOB[first_unit + b - 2] + 1)
                else:
                    sp.wait_ge(s_pe["pv"], s_pe.after(b - 2, "pv"))
                kk, vv = kv_slot(first_unit, k, ck.shape[4] != 128)

                def src(c):
                    v = c[0][b] if isinstance(b, int) else c[0][bass.ds(b, 1)].rearrange("o t h c -> (o t) h c")
                    return v.rearrange("(t p) h c -> p t (h c)", p=P)

                sp.dma_start(kk, src(ck)).then_inc(s_kv[k], 16)
                sp.dma_start(vv, src(cvv)).then_inc(s_kv[k], 16)

            one(0, 0)
            one(1, 1)
            with sp.Fori(1, NB // 2) as i:
                one(sp.snap(2 * i), 0)
                one(sp.snap(2 * i + 1), 1)

        def das_pe_stage(pe, b, k, stage):
            kk, vv = kv_slot(UNIT["da0"], k, False)
            if stage < 4:
                f = stage
                if f == 0:
                    pe.wait_ge(s_kv[k], (b - k) * 16 + 32)
                    pe.wait_ge(das_act["pv"], das_act.after(b - 1, "pv"))
                elif f % 2:
                    pe.wait_ge(das_act[f"f{f - 1}"], das_act.after(b, f"f{f - 1}"))
                else:
                    pe.wait_ge(das_dve[f"f{f - 1}"], das_dve.after(b, f"f{f - 1}"))
                for i in range(4):
                    mm = nc.tensor.transpose(quarters(bank[6])[:, i, :], kk[:, i, f * P:(f + 1) * P], ident)
                mm.then_inc(das_pe.step(f"f{f}"), 1)
            elif stage == 4:
                pe.wait_ge(das_dve["f3"], das_dve.after(b, "f3"))
                pe.wait_ge(das_act["f2"], das_act.after(b, "f2"))
                pe.wait_ge(das_act["o"], das_act.after(b - 1, "o"))
                kt = s_KT.rearrange("p (h m) -> p h m", h=H)
                for h in range(H):
                    nc.tensor.matmul(bank[7][32 * h:32 * h + 32, :], s_q[:, h, :], kt[:, h, :], start=True, stop=True)
                for h in range(H):
                    mm = nc.tensor.matmul(bank[6][32 * h:32 * h + 32, 0:P], s_q[:, h, :], sk_[:, h, :], start=True, stop=True)
                mm.then_inc(das_pe.step("sc"), 1)
            elif stage == 5:
                pe.wait_ge(das_dve["cm"], das_dve.after(b, "cm"))
                for c in range(5):
                    mm = nc.tensor.matmul(bank[7][:, 64 * c:64 * c + 64], s_P[:, c * P:(c + 1) * P], s_cm, start=True, stop=True)
                mm.then_inc(das_pe.step("pT"), 1)
            elif stage == 6:
                pe.wait_ge(das_dve["pT"], das_dve.after(b, "pT"))
                for c in range(5):
                    for h in range(H):
                        v = vv[:, c, h * P:(h + 1) * P] if c < 4 else sv_[:, h * P:(h + 1) * P]
                        mm = nc.tensor.matmul(bank[6][32 * h:32 * h + 32, 0:P], s_aT[:, 64 * c + 16 * h:64 * c + 16 * h + 32], v,
                                              start=c == 0, stop=c == 4, skip_group_check=True)
                mm.then_inc(das_pe.step("pv"), 1)
            else:
                pe.wait_ge(das_act["pv"], das_act.after(b, "pv"))
                nc.tensor.transpose(bank[7][:, 0:P], s_o[:, 0:P], ident).then_inc(das_pe.step("oT"), 1)

        def das_act_stage(act, b, stage):
            if stage in (0, 2):
                act.wait_ge(das_pe[f"f{stage}"], das_pe.after(b, f"f{stage}"))
                nc.scalar.copy(s_KT[:, 512 * stage:512 * stage + 512], bank[6][:, :]).then_inc(das_act.step(f"f{stage}"), 1)
            elif stage == 4:
                act.wait_ge(das_dve["mxm"], das_dve.after(b, "mxm"))
                nc.scalar.activation(s_P[:, 0:512], bank[7][:, :], ACT.Exp, bias=s_mx[:, 0:1],
                                     accum_out=s_sum[:, 0:1]).then_inc(das_act.step("p"), 1)
                nc.scalar.activation(s_P[:, 512:640], s_sn, ACT.Exp, bias=s_mx[:, 0:1],
                                     accum_out=s_sum[:, 1:2]).then_inc(das_act.step("pn"), 1)
            elif stage == 6:
                act.wait_ge(das_pe["pv"], das_pe.after(b, "pv"))
                nc.scalar.copy(s_o[:, 0:P], bank[6][:, 0:P]).then_inc(das_act.step("pv"), 1)
            elif stage == 7:
                act.wait_ge(das_pe["oT"], das_pe.after(b, "oT"))
                nc.scalar.copy(da_oT[:, :, bass.ds(b * TB, TB)],
                               bank[7][:, 0:P].rearrange("p (h t) -> p h t", h=H)[:, :, 0:TB]).then_inc(das_act.step("o"), 1)

        def das_dve_stage(dve, b, stage):
            if stage == 0:
                dve.wait_ge(das_pe["sc"], das_pe.after(b - 1, "sc"))
                nc.vector.tensor_copy(s_q[0:64, 0:4, 0:16], sq_[0:64, :, bass.ds(b * TB, TB)])
                nc.vector.tensor_copy(s_q[64:128, 0:4, 16:32], sq_[64:128, :, bass.ds(b * TB, TB)]).then_inc(das_dve.step("q"), 1)
            elif stage in (1, 3):
                dve.wait_ge(das_pe[f"f{stage}"], das_pe.after(b, f"f{stage}"))
                nc.vector.tensor_copy(s_KT[:, 512 * stage:512 * stage + 512], bank[6][:, :]).then_inc(das_dve.step(f"f{stage}"), 1)
            elif stage == 4:
                dve.wait_ge(das_pe["sc"], das_pe.after(b, "sc"))
                w = C("stream_off")[:, bass.ds(b * P, P)]
                nc.vector.tensor_tensor(s_sn, bank[6][:, 0:P], w, ALU.add).then_inc(das_dve.step("sn"), 1)
                nc.vector.tensor_reduce(s_mx[:, 1:2], bank[7][:, :], AX.X, ALU.max).then_inc(das_dve.step("mx"), 1)
                dve.wait_ge(das_dve["mx"], das_dve.after(b, "mx"))
                nc.vector.tensor_reduce(s_mx[:, 2:3], s_sn, AX.X, ALU.max).then_inc(das_dve.step("mx2"), 1)
                dve.wait_ge(das_dve["mx2"], das_dve.after(b, "mx2"))
                nc.vector.scalar_tensor_tensor(s_mx[:, 0:1], s_mx[:, 1:2], s_mx[:, 2:3], C("minus_one"),
                                               ALU.max, ALU.mult).then_inc(das_dve.step("mxm"), 1)
            elif stage == 5:
                dve.wait_ge(das_act["pn"], das_act.after(b, "pn"))
                nc.vector.tensor_tensor(s_sum[:, 2:3], s_sum[:, 0:1], s_sum[:, 1:2], ALU.add).then_inc(das_dve.step("sum"), 1)
                dve.wait_ge(das_dve["sum"], das_dve.after(b, "sum"))
                nc.vector.reciprocal(s_sum[:, 3:4], s_sum[:, 2:3]).then_inc(das_dve.step("r"), 1)
                dve.wait_ge(das_dve["r"], das_dve.after(b, "r"))
                nc.vector.tensor_tensor(s_sum[:, 2:3], s_sum[:, 3:4], row_sign, ALU.mult).then_inc(das_dve.step("c"), 1)
                dve.wait_ge(das_dve["c"], das_dve.after(b, "c"))
                nc.vector.tensor_scalar(s_cm, C("pick"), s_sum[:, 2:3], None, ALU.mult).then_inc(das_dve.step("cm"), 1)
            elif stage == 6:
                dve.wait_ge(das_pe["pT"], das_pe.after(b, "pT"))
                nc.vector.tensor_copy(s_aT[:, 0:320], bank[7][:, 0:320]).then_inc(das_dve.step("pT"), 1)

        def das_start(dve):
            das_dve.arm(dve)
            das_copy.arm(dve)
            nc.vector.tensor_copy(sq_, dq[:, :, SEQ:]).then_inc(das_copy.step("q"), 1)
            nc.vector.tensor_copy(sk_, dk[:, :, SEQ:]).then_inc(das_copy.step("k"), 1)
            nc.vector.tensor_copy(sv_, dv[:, 4, :]).then_inc(das_copy.step("v"), 1)
            dve.wait_ge(moved["moved"], moved.after(0, "moved"))
            nc.vector.memset(s_q, 0.0).then_inc(das_copy.step("zq"), 1)
            nc.vector.memset(s_aT[:, 320:336], 0.0).then_inc(das_copy.step("za"), 1)
            dve.wait_ge(das_copy["za"], das_copy.after(0, "za"))

        t_pe = steps("da_s_pe", "turn oT")
        t_act = steps("da_s_act", "sq mix")
        t_dve = steps("da_s_dve", "ss on og")
        t_pool = steps("da_s_pool", "ms rn")

        t_on, t_sq = spare[0][:, 1344:1856], spare[1][:, 0:512]

        def das_out_pe(pe, i):
            if i == 0:
                t_pe.arm(pe)
                pe.wait_ge(das_act["o"], das_act.after(NB - 1, "o"))
                for h in range(H):
                    mm = nc.tensor.transpose(quarters(bank[6])[:, h, :], da_oT[:, h, :], ident)
                mm.then_inc(t_pe.step("turn"), 1)
            elif i == 4:
                pe.wait_ge(t_dve["og"], t_dve.after(0, "og"))
                for h in range(H):
                    mm = nc.tensor.transpose(quarters(bank[6])[:, h, :], t_on[:, h * P:(h + 1) * P], ident)
                mm.then_inc(t_pe.step("oT"), 1)

        def das_out_act(act, i):
            if i == 0:
                t_act.arm(act)
                act.wait_ge(t_pe["turn"], t_pe.after(0, "turn"))
                nc.scalar.activation(t_sq, bank[6][:, :], ACT.Square).then_inc(t_act.step("sq"), 1)
            elif i == 4:
                act.wait_ge(t_pe["oT"], t_pe.after(0, "oT"))
                nc.scalar.copy(act_a[:, 0:4, SEQ:], quarters(bank[6])).then_inc(t_act.step("mix"), 1)

        def das_out_dve(dve, i):
            if i == 1:
                t_dve.arm(dve)
                head_norm_dve(dve, t_dve, t_act, t_pool, 0, bank[6], gdn_g[:, 0:128], t_sq, t_on, 0)
            elif i == 3:
                head_norm_dve(dve, t_dve, t_act, t_pool, 0, bank[6], gdn_g[:, 0:128], t_sq, t_on, 1)

        g_act, g_pe, g_dve, g_pool = (steps("gdn_" + e, n) for e, n in
                                      (("act", GDN_ACT), ("pe", GDN_PE), ("dve", GDN_DVE), ("pool", GDN_POOL)))
        gs_act, gs_pe, gs_dve, gs_pool = (steps("gdn_s_" + e, n) for e, n in (
            ("act", "sq0 sq1 EG eg qT D DT Mt M2 M2t M4 M4t M8 w osq | mix"),
            ("pe", "tokqk cum gcum chq chk kk kq Mt tokv sq2 sq2t x1 sq4 sq4t x2 sq8 x3 w | oT"),
            ("dve", "gb gB ss ssq gc S qk0 qk1 SD SU kT SDb L M X0 vb be kbg X1 kl ktail X2 AT X3 qd | oss oms on og oz"),
            ("pool", GDN_POOL)))
        staged = steps("gdn_staged", "tile")
        gh_pe = steps("gdn_state_pe", "vn o s")
        gh_dve = steps("gdn_state_dve", "vn vM sg s0 s1 | wM | qM")
        s_state = sem("states_loaded")

        stage = attn[:, 0:1536].rearrange("p (m t) -> p m t", m=12)
        qk_tok = attn[:, 1536:2560]
        qT, kT, vb, kbg, ktail, EG, SD, DT, S_, AT = (attn[:, 2560 + 512 * i:3072 + 512 * i] for i in range(10))
        gB, L, M, Mt, M2, M2t, X, Bm, T_, Wb = (x_buf[:, 512 * i:512 * i + 512] for i in range(10))
        scr_ = scr[:, :, :].rearrange("p a b -> p (a b)")
        wTn, qdT, vnew, gon = (scr_[:, 512 * i:512 * i + 512] for i in range(4))
        gsq = wTn
        gsq2 = scr_[:, 2048:3072]
        state = act_b[:, 4096:4608]
        states = act_b[:, 0:4096].rearrange("p (h b v) -> p h b v", h=H, b=NB)
        wM = attn[:, 0:1024].rearrange("p (b t) -> p b t", b=NB)
        qM = qk_tok.rearrange("p (b t) -> p b t", b=NB)
        vM = x_buf[:, 1024:2048].rearrange("p (b t) -> p b t", b=NB)
        g_t, b_t, gc, eg, be, kl, goss = (little(4) for _ in range(7))
        rqk = little(8)

        def m4(name):
            return C(name, 4)

        def mul4(pe, out, lhs, rhs, start=True, stop=True):
            for h in range(H):
                mm = nc.tensor.matmul(quarters(out)[:, h, :], h4(lhs)[:, h, :], h4(rhs)[:, h, :], start=start, stop=stop)
            return mm

        def turn4(pe, out, src):
            for h in range(H):
                mm = nc.tensor.transpose(quarters(out)[:, h, :], h4(src)[:, h, :], ident)
            return mm

        BESIDE = [0, 1, 2, 3, 4, 5, 6, 7, 15, 16, 17, 18, 19, 20, 21, 22]
        mix_out = conv[:, 0:NTP * D].rearrange("p (t d) -> p t d", t=NTP)
        x_add = steps("mix_added_to_x", " ".join(f"t{t}" for t in range(NTP)))

        def mix_out_dve(dve):
            x_add.arm(dve)
            all_taken(dve, MIX_JOBS[-1])
            for t in range(NTP):
                dve.wait_ge(s_x[t], 32)
                nc.vector.tensor_tensor(x[:, t, :], x[:, t, :], mix_out[:, t, :], ALU.add).then_inc(x_add.step(f"t{t}"), 1)

        def gdn_pe_out(pe, s, sd, t):
            pe.wait_ge(sd["oz"], sd.after(t, "oz"))
            turn4(pe, bank[3], gon).then_inc(s.step("oT"), 1)

        def gdn_pe_tile(pe, t, sample, side, before):
            s, sa, sd = (gs_pe, gs_act, gs_dve) if sample else (g_pe, g_act, g_dve)
            cum = C("cum_s" if sample else "cum_p")
            at = NTP if sample else t
            pe.wait_ge(staged["tile"], staged.after(at, "tile"))
            for i in range(8):
                mm = nc.tensor.transpose(quarters(bank[i // 4])[:, i % 4, :], stage[:, i, :], ident)
            mm.then_inc(s.step("tokqk"), 1)
            side(0)
            pe.wait_ge(sd["gB"], sd.after(t, "gB"))
            nc.tensor.matmul(bank[3][:, 0:4], cum, g_t, start=True, stop=True).then_inc(s.step("cum"), 1)
            for h in range(H):
                mm = nc.tensor.matmul(quarters(bank[4])[:, h, :], h4(gB)[:, h, :], cum, start=True, stop=True)
            mm.then_inc(s.step("gcum"), 1)
            side(1)
            pe.wait_ge(sd["qk1"], sd.after(t, "qk1"))
            turn4(pe, bank[0], qk_tok[:, 0:512]).then_inc(s.step("chq"), 1)
            turn4(pe, bank[1], qk_tok[:, 512:1024]).then_inc(s.step("chk"), 1)
            side(2)
            pe.wait_ge(sd["kT"], sd.after(t, "kT"))
            pe.wait_ge(sd["S"], sd.after(t, "S"))
            pe.wait_ge(sa["qT"], sa.after(t, "qT"))
            mul4(pe, bank[3], kT, kT).then_inc(s.step("kk"), 1)
            mul4(pe, bank[4], kT, qT).then_inc(s.step("kq"), 1)
            side(3)
            pe.wait_ge(sd["M"], sd.after(t, "M"))
            turn4(pe, bank[5], M).then_inc(s.step("Mt"), 1)
            if before:
                gdn_pe_out(pe, g_pe, g_dve, at - 1)
            for i in range(4):
                mm = nc.tensor.transpose(quarters(bank[2])[:, i, :], stage[:, 8 + i, :], ident)
            mm.then_inc(s.step("tokv"), 1)
            side(4)
            pe.wait_ge(sa["Mt"], sa.after(t, "Mt"))
            mul4(pe, bank[0], Mt, M).then_inc(s.step("sq2"), 1)
            mul4(pe, bank[1], M, Mt).then_inc(s.step("sq2t"), 1)
            pe.wait_ge(sd["X0"], sd.after(t, "X0"))
            pe.wait_ge(sa["M2t"], sa.after(t, "M2t"))
            mul4(pe, bank[5], M2, X).then_inc(s.step("x1"), 1)
            mul4(pe, bank[0], M2t, M2).then_inc(s.step("sq4"), 1)
            mul4(pe, bank[1], M2, M2t).then_inc(s.step("sq4t"), 1)
            side(5)
            pe.wait_ge(sd["X1"], sd.after(t, "X1"))
            pe.wait_ge(sa["M4t"], sa.after(t, "M4t"))
            mul4(pe, bank[5], M, X).then_inc(s.step("x2"), 1)
            mul4(pe, bank[0], Mt, M).then_inc(s.step("sq8"), 1)
            side(6)
            pe.wait_ge(sd["X2"], sd.after(t, "X2"))
            pe.wait_ge(sa["M8"], sa.after(t, "M8"))
            mul4(pe, bank[5], M2, X).then_inc(s.step("x3"), 1)
            side(7)
            side(8)
            if not sample:
                for l in range(3):
                    pe.wait_ge(sd[f"B{l}"], sd.after(t, f"B{l}"))
                    if l == 0:
                        pe.wait_ge(sd["X3"], sd.after(t, "X3"))
                    turn4(pe, bank[0], X).then_inc(s.step(f"T{l}"), 1)
                    mul4(pe, bank[1], Bm, X).then_inc(s.step(f"BX{l}"), 1)
                    if l < 2:
                        side(9 + 2 * l)
                    pe.wait_ge(sa[f"T{l}"], sa.after(t, f"T{l}"))
                    pe.wait_ge(sd[f"W{l}"], sd.after(t, f"W{l}"))
                    mul4(pe, bank[5], T_, Wb).then_inc(s.step(f"Y{l}"), 1)
                    side(10 + 2 * l if l < 2 else 13)
            pe.wait_ge(sd["X3" if sample else "Y2"], sd.after(t, "X3" if sample else "Y2"))
            pe.wait_ge(sa["M8"], sa.after(t, "M8"))
            mul4(pe, bank[0], kbg, X).then_inc(s.step("w"), 1)
            side(15 if sample else 14)

        def gdn_pe_prompt(pe):
            g_pe.arm(pe)
            das_pe.arm(pe)

            def tile(t, before):
                def side(i):
                    das_pe_stage(pe, 2 * t + i // STAGES, i // STAGES, i % STAGES)

                gdn_pe_tile(pe, t, False, side, before)
                pe.wait_ge(g_act["w"], g_act.after(t, "w"))
                mm = None
                for h in range(H):
                    nc.tensor.matmul(quarters(bank[1])[:, h, :], h4(X)[:, h, :], h4(vb)[:, h, :], start=True, stop=False)
                    mm = nc.tensor.matmul(quarters(bank[1])[:, h, :], h4(wTn)[:, h, :], h4(state)[:, h, :], start=False, stop=True)
                mm.then_inc(g_pe.step("vn"), 1)
                side(15)
                pe.wait_ge(g_dve["vn"], g_dve.after(t, "vn"))
                for h in range(H):
                    nc.tensor.matmul(quarters(bank[2])[:, h, :], h4(qdT)[:, h, :], h4(state)[:, h, :], start=True, stop=False)
                    mm = nc.tensor.matmul(quarters(bank[2])[:, h, :], h4(AT)[:, h, :], h4(vnew)[:, h, :], start=False, stop=True)
                mm.then_inc(g_pe.step("o"), 1)
                mul4(pe, bank[3], ktail, vnew).then_inc(g_pe.step("s"), 1)

            tile(0, False)
            with pe.Fori(1, NTP) as t:
                tile(t, True)

        def gdn_pe_sample(pe):
            gs_pe.arm(pe)
            gh_pe.arm(pe)

            def side(i):
                if i not in BESIDE:
                    return
                das_out_pe(pe, i)
                k = BESIDE.index(i)
                if k == 6:
                    pe.wait_ge(g_act["mix"], g_act.after(NTP - 1, "mix"))
                run_jobs(pe, ("mix",), act_a, None, [MIX_JOBS[k // 2]], range(4 * (k % 2), 4 * (k % 2) + 4))

            gdn_pe_tile(pe, 0, True, side, True)
            pe.wait_ge(s_state, 16 * H)
            for h in range(H):
                pe.wait_ge(gh_dve["wM"], gh_dve.after(h, "wM"))
                nc.tensor.matmul(quarters(bank[1])[:, h, :], h4(X)[:, h, :], h4(vb)[:, h, :], start=True, stop=False)
                for b in range(NB):
                    mm = nc.tensor.matmul(quarters(bank[1])[:, h, :], wM[:, b, :], states[:, h, b, :], start=False, stop=b == NB - 1)
                mm.then_inc(gh_pe.step("vn"), 1)
                side(16 + 2 * h)
                pe.wait_ge(gh_dve["qM"], gh_dve.after(h, "qM"))
                pe.wait_ge(gh_dve["vM"], gh_dve.after(h, "vM"))
                for b in range(NB):
                    nc.tensor.matmul(quarters(bank[2])[:, h, :], qM[:, b, :], states[:, h, b, :], start=b == 0, stop=False)
                mm = nc.tensor.matmul(quarters(bank[2])[:, h, :], h4(AT)[:, h, :], h4(vnew)[:, h, :], start=False, stop=True)
                mm.then_inc(gh_pe.step("o"), 1)
                side(17 + 2 * h)
                pe.wait_ge(gh_dve["s1"], gh_dve.after(h - 1, "s1"))
                for i in range(2):
                    mm = nc.tensor.matmul(bank[3 + i][:, :], h4(ktail)[:, h, :], vM[:, 4 * i:4 * i + 4, :], start=True, stop=True)
                mm.then_inc(gh_pe.step("s"), 1)
            gdn_pe_out(pe, gs_pe, gs_dve, 0)

        def tile_cols(t):
            return bass.ds(t * P, P) if not isinstance(t, int) else slice(t * P, t * P + P)

        def gdn_act_out(act, s, sp_, t, dst):
            act.wait_ge(sp_["oT"], sp_.after(t, "oT"))
            nc.scalar.copy(dst, quarters(bank[3])).then_inc(s.step("mix"), 1)

        def gdn_act_tile(act, t, sample, side, before):
            s, sp_, sd = (gs_act, gs_pe, gs_dve) if sample else (g_act, g_pe, g_dve)
            act.wait_ge(sp_["tokqk"], sp_.after(t, "tokqk"))
            nc.scalar.activation(gsq2[:, 0:512], bank[0][:, :], ACT.Square).then_inc(s.step("sq0"), 1)
            nc.scalar.activation(gsq2[:, 512:1024], bank[1][:, :], ACT.Square).then_inc(s.step("sq1"), 1)
            side(0)
            act.wait_ge(sp_["gcum"], sp_.after(t, "gcum"))
            nc.scalar.activation(EG, bank[4][:, :], ACT.Exp).then_inc(s.step("EG"), 1)
            act.wait_ge(sd["gc"], sd.after(t, "gc"))
            nc.scalar.activation(eg, gc, ACT.Exp).then_inc(s.step("eg"), 1)
            side(1)
            act.wait_ge(sp_["chq"], sp_.after(t, "chq"))
            nc.scalar.copy(qT, bank[0][:, :]).then_inc(s.step("qT"), 1)
            act.wait_ge(sd["SU"], sd.after(t, "SU"))
            nc.scalar.activation(SD, SD, ACT.Exp).then_inc(s.step("D"), 1)
            nc.scalar.activation(DT, DT, ACT.Exp).then_inc(s.step("DT"), 1)
            side(2)
            side(3)
            act.wait_ge(sp_["Mt"], sp_.after(t, "Mt"))
            nc.scalar.copy(Mt, bank[5][:, :]).then_inc(s.step("Mt"), 1)
            for n in ("sq2", "sq4"):
                act.wait_ge(sp_[n], sp_.after(t, n))
                nc.scalar.copy(M2 if n == "sq2" else M, bank[0][:, :]).then_inc(s.step("M2" if n == "sq2" else "M4"), 1)
                act.wait_ge(sp_[n + "t"], sp_.after(t, n + "t"))
                nc.scalar.copy(M2t if n == "sq2" else Mt, bank[1][:, :]).then_inc(s.step("M2t" if n == "sq2" else "M4t"), 1)
                if n == "sq2" and before:
                    at = NTP if sample else t
                    gdn_act_out(act, g_act, g_pe, at - 1, act_a[:, 4:8, tile_cols(at - 1)])
                side(4 if n == "sq2" else 5)
            act.wait_ge(sp_["sq8"], sp_.after(t, "sq8"))
            nc.scalar.copy(M2, bank[0][:, :]).then_inc(s.step("M8"), 1)
            side(6)
            side(7)
            side(8)
            if not sample:
                for l in range(3):
                    act.wait_ge(sp_[f"T{l}"], sp_.after(t, f"T{l}"))
                    nc.scalar.copy(T_, bank[0][:, :]).then_inc(s.step(f"T{l}"), 1)
                    side(9 + 2 * l)
                    if l < 2:
                        side(10 + 2 * l)
            act.wait_ge(sp_["w"], sp_.after(t, "w"))
            nc.scalar.copy(wTn, bank[0][:, :]).then_inc(s.step("w"), 1)
            if sample:
                for i in BESIDE[BESIDE.index(15):]:
                    side(i)
                act.wait_ge(gh_pe["o"], gh_pe.after(H - 1, "o"))
            else:
                side(14)
                side(15)
                act.wait_ge(sp_["o"], sp_.after(t, "o"))
            nc.scalar.activation(gsq, bank[2][:, :], ACT.Square).then_inc(s.step("osq"), 1)

        def gdn_act(act):
            g_act.arm(act)
            das_act.arm(act)
            gs_act.arm(act)

            def tile(t, before):
                gdn_act_tile(act, t, False, lambda i: das_act_stage(act, 2 * t + i // STAGES, i % STAGES), before)

            tile(0, False)
            with act.Fori(1, NTP) as t:
                tile(t, True)

            def side(i):
                if i not in BESIDE:
                    return
                das_out_act(act, i)
                k = BESIDE.index(i)
                if k % 2:
                    take_jobs("act", act, ("mix",), rest_dst, None, [MIX_JOBS[k // 2]])

            gdn_act_tile(act, 0, True, side, True)
            gdn_act_out(act, gs_act, gs_pe, 0, act_a[:, 4:8, SEQ:])

        def gdn_pool(pool):
            g_pool.arm(pool)
            gs_pool.arm(pool)
            staged.arm(pool)

            def take_tile(t):
                pool.wait_ge(g_pe["tokv"], g_pe.after(t - 1, "tokv"))
                nc.gpsimd.tensor_copy(stage[:, :, :], cv[:, :, tile_cols(t)]).then_inc(staged.step("tile"), 1)

            def norms(s, sd, t):
                pool.wait_ge(sd["ssq"], sd.after(t, "ssq"))
                nc.gpsimd.tensor_tensor(rqk, rqk, C("minus_half"), ALU.pow).then_inc(s.step("rn"), 1)

            def out_norm(s, sd, t):
                pool.wait_ge(sd["oms"], sd.after(t, "oms"))
                nc.gpsimd.tensor_tensor(goss, goss, C("minus_half")[:, 0:4], ALU.pow).then_inc(s.step("orn"), 1)

            pool.wait_ge(c_act["silu9"], c_act.after(0, "silu9"))
            pool.wait_ge(d_pe["pv"], d_pe.after(UN - 1, "pv"))
            pool.wait_ge(das_copy["v"], das_copy.after(0, "v"))
            take_tile(0)
            norms(g_pool, g_dve, 0)
            take_tile(1)
            with pool.Fori(1, NTP - 1) as t:
                norms(g_pool, g_dve, t)
                out_norm(g_pool, g_dve, t - 1)
                take_tile(t + 1)
            norms(g_pool, g_dve, NTP - 1)
            out_norm(g_pool, g_dve, NTP - 2)
            pool.wait_ge(g_pe["tokv"], g_pe.after(NTP - 1, "tokv"))
            for i in range(3):
                src = cv[:, 4 * i:4 * i + 4, GS:GW].rearrange("p m (b c) -> p m b c", b=NB)[:, :, :, 0:TB]
                ins = nc.gpsimd.tensor_copy(stage[:, 4 * i:4 * i + 4, :].rearrange("p m (b c) -> p m b c", b=NB), src)
            ins.then_inc(staged.step("tile"), 1)
            norms(gs_pool, gs_dve, 0)
            out_norm(g_pool, g_dve, NTP - 1)
            t_pool.arm(pool)
            head_norm_pool(pool, t_pool, t_dve, 0)
            out_norm(gs_pool, gs_dve, 0)

        def gdn_dve_out(dve, t, sample, part):
            s, sa, spo = (gs_dve, gs_act, gs_pool) if sample else (g_dve, g_act, g_pool)
            tt = nc.vector.tensor_tensor
            if part == 0:
                dve.wait_ge(sa["osq"], sa.after(t, "osq"))
                nc.vector.tensor_reduce(goss, h4(gsq), AX.X, ALU.add).then_inc(s.step("oss"), 1)
                dve.wait_ge(s["oss"], s.after(t, "oss"))
                nc.vector.tensor_scalar(goss, goss, 1.0 / P, EPS, ALU.mult, ALU.add).then_inc(s.step("oms"), 1)
            elif part == 1:
                dve.wait_ge(spo["orn"], spo.after(t, "orn"))
                tt(h4(gon), quarters(bank[2]), b4(goss), ALU.mult).then_inc(s.step("on"), 1)
            elif part == 2:
                dve.wait_ge(s["on"], s.after(t, "on"))
                tt(h4(gon), h4(gon), gdn_g[:, 128:256].unsqueeze(1).to_broadcast([P, 4, P]), ALU.mult).then_inc(s.step("og"), 1)
            else:
                dve.wait_ge(s["og"], s.after(t, "og"))
                gate = gz[:, NT - 1, :] if sample else gz[:, bass.ds(t, 1), :].rearrange("p o c -> p (o c)")
                tt(gon, gon, gate, ALU.mult).then_inc(s.step("oz"), 1)

        def gdn_dve_tile(dve, t, sample, side, before):
            s, sp_, sa, spo = (gs_dve, gs_pe, gs_act, gs_pool) if sample else (g_dve, g_pe, g_act, g_pool)
            at = NTP if sample else t
            sfx = "_s" if sample else "_p"
            tt = nc.vector.tensor_tensor
            gcols = slice(4 * (NT - 1), 4 * NT) if sample else bass.ds(t * 4, 4)
            nc.vector.tensor_copy(b_t, beta[:, gcols])
            nc.vector.tensor_copy(g_t, glog[:, gcols]).then_inc(s.step("gb"), 1)
            dve.wait_ge(s["gb"], s.after(t, "gb"))
            dve.wait_ge(sp_["gcum"], sp_.after(t - 1, "gcum"))
            nc.vector.tensor_copy(h4(gB), b4(g_t)).then_inc(s.step("gB"), 1)
            side(0)
            if before:
                gdn_dve_out(dve, at - 1, False, 0)
            dve.wait_ge(sa["sq1"], sa.after(t, "sq1"))
            nc.vector.tensor_reduce(rqk, gsq2.rearrange("p (h c) -> p h c", h=8), AX.X, ALU.add).then_inc(s.step("ss"), 1)
            dve.wait_ge(s["ss"], s.after(t, "ss"))
            nc.vector.scalar_tensor_tensor(rqk, rqk, EPS, C("qk_scale"), ALU.add, ALU.mult).then_inc(s.step("ssq"), 1)
            dve.wait_ge(sp_["gcum"], sp_.after(t, "gcum"))
            nc.vector.tensor_copy(gc, bank[3][:, 0:4]).then_inc(s.step("gc"), 1)
            dve.wait_ge(s["gc"], s.after(t, "gc"))
            dve.wait_ge(sa["eg"], sa.after(t, "eg"))
            tt(h4(S_), quarters(bank[4]), b4(gc), ALU.subtract).then_inc(s.step("S"), 1)
            dve.wait_ge(spo["rn"], spo.after(t, "rn"))
            tt(h4(qk_tok[:, 0:512]), quarters(bank[0]), b4(rqk[:, 0:4]), ALU.mult).then_inc(s.step("qk0"), 1)
            tt(h4(qk_tok[:, 512:1024]), quarters(bank[1]), b4(rqk[:, 4:8]), ALU.mult).then_inc(s.step("qk1"), 1)
            dve.wait_ge(s["S"], s.after(t, "S"))
            tt(h4(SD), m4("low" + sfx), h4(S_), ALU.subtract).then_inc(s.step("SD"), 1)
            tt(h4(DT), m4("up" + sfx), h4(S_), ALU.add).then_inc(s.step("SU"), 1)
            side(1)
            dve.wait_ge(sp_["chk"], sp_.after(t, "chk"))
            nc.vector.tensor_copy(kT, bank[1][:, :]).then_inc(s.step("kT"), 1)
            if before:
                gdn_dve_out(dve, at - 1, False, 1)
            side(2)
            dve.wait_ge(sa["D"], sa.after(t, "D"))
            tt(h4(SD), h4(SD), b4(b_t), ALU.mult).then_inc(s.step("SDb"), 1)
            dve.wait_ge(s["SDb"], s.after(t, "SDb"))
            dve.wait_ge(sp_["kk"], sp_.after(t, "kk"))
            tt(h4(L), quarters(bank[3]), h4(SD), ALU.mult).then_inc(s.step("L"), 1)
            dve.wait_ge(s["L"], s.after(t, "L"))
            tt(h4(M), h4(L), m4("blk16"), ALU.mult).then_inc(s.step("M"), 1)
            if before:
                gdn_dve_out(dve, at - 1, False, 2)
                gdn_dve_out(dve, at - 1, False, 3)
            side(3)
            dve.wait_ge(sp_["Mt"], sp_.after(t, "Mt"))
            dve.wait_ge(sa["Mt"], sa.after(t, "Mt"))
            tt(h4(X), m4("ident"), quarters(bank[5]), ALU.subtract).then_inc(s.step("X0"), 1)
            side(4)
            dve.wait_ge(sp_["tokv"], sp_.after(t, "tokv"))
            tt(h4(vb), quarters(bank[2]), b4(b_t), ALU.mult).then_inc(s.step("vb"), 1)
            nc.vector.scalar_tensor_tensor(be, b_t, -1.0, eg, ALU.mult, ALU.mult).then_inc(s.step("be"), 1)
            dve.wait_ge(s["be"], s.after(t, "be"))
            tt(h4(kbg), h4(qk_tok[:, 512:1024]), b4(be), ALU.mult).then_inc(s.step("kbg"), 1)
            side(5)
            dve.wait_ge(sp_["x1"], sp_.after(t, "x1"))
            tt(h4(X), h4(X), quarters(bank[5]), ALU.add).then_inc(s.step("X1"), 1)
            dve.wait_ge(sa["DT"], sa.after(t, "DT"))
            if sample:
                last = h4(DT)[:, :, TB - 1:P:TB]
                nc.vector.tensor_reduce(kl, last, AX.X, ALU.add).then_inc(s.step("kl"), 1)
            else:
                nc.vector.tensor_copy(kl, h4(DT)[:, :, P - 1]).then_inc(s.step("kl"), 1)
            dve.wait_ge(s["kl"], s.after(t, "kl"))
            tt(h4(ktail), h4(qk_tok[:, 512:1024]), b4(kl), ALU.mult).then_inc(s.step("ktail"), 1)
            side(6)
            dve.wait_ge(sp_["x2"], sp_.after(t, "x2"))
            tt(h4(X), h4(X), quarters(bank[5]), ALU.add).then_inc(s.step("X2"), 1)
            dve.wait_ge(sp_["kq"], sp_.after(t, "kq"))
            tt(h4(AT), quarters(bank[4]), h4(DT), ALU.mult).then_inc(s.step("AT"), 1)
            if not sample:
                tt(h4(Bm), h4(L), m4("lev32"), ALU.mult).then_inc(s.step("B0"), 1)
            side(7)
            dve.wait_ge(sp_["x3"], sp_.after(t, "x3"))
            tt(h4(X), h4(X), quarters(bank[5]), ALU.add).then_inc(s.step("X3"), 1)
            side(8)
            if not sample:
                for l in range(3):
                    if l:
                        dve.wait_ge(sp_[f"BX{l - 1}"], sp_.after(t, f"BX{l - 1}"))
                        tt(h4(Bm), h4(L), m4(f"lev{32 << l}"), ALU.mult).then_inc(s.step(f"B{l}"), 1)
                    dve.wait_ge(sp_[f"BX{l}"], sp_.after(t, f"BX{l}"))
                    nc.vector.tensor_copy(Wb, bank[1][:, :]).then_inc(s.step(f"W{l}"), 1)
                    side(9 + 2 * l)
                    dve.wait_ge(sp_[f"Y{l}"], sp_.after(t, f"Y{l}"))
                    tt(h4(X), h4(X), quarters(bank[5]), ALU.subtract).then_inc(s.step(f"Y{l}"), 1)
                    side(10 + 2 * l)
            dve.wait_ge(sa["qT"], sa.after(t, "qT"))
            tt(qdT, qT, EG, ALU.mult).then_inc(s.step("qd"), 1)
            side(15)
            if not sample:
                dve.wait_ge(sp_["vn"], sp_.after(t, "vn"))
                nc.vector.tensor_copy(vnew, bank[1][:, :]).then_inc(s.step("vn"), 1)
                dve.wait_ge(sp_["o"], sp_.after(t, "o"))
                tt(h4(state), h4(state), b4(h4(EG)[:, :, P - 1]), ALU.mult).then_inc(s.step("sg"), 1)
                dve.wait_ge(s["sg"], s.after(t, "sg"))
                dve.wait_ge(sp_["s"], sp_.after(t, "s"))
                tt(state, state, bank[3][:, :], ALU.add).then_inc(s.step("s"), 1)
            else:
                gdn_dve_states(dve)

        def gdn_dve_states(dve):
            gh_dve.arm(dve)
            tt = nc.vector.tensor_tensor
            dve.wait_ge(gs_dve["qd"], gs_dve.after(0, "qd"))
            dve.wait_ge(gs_act["w"], gs_act.after(0, "w"))
            dve.wait_ge(s_state, 16 * H)
            off = C("stream_off").rearrange("p (b t) -> p b t", b=NB)
            def over(v, h):
                return h4(v)[:, h, :].unsqueeze(1).to_broadcast([P, NB, P])

            def w_by_stream(h):
                dve.wait_ge(gh_pe["vn"], gh_pe.after(h - 1, "vn"))
                nc.vector.scalar_tensor_tensor(wM, off, 0.0, over(wTn, h), ALU.is_equal, ALU.mult).then_inc(gh_dve.step("wM"), 1)

            def q_by_stream(h):
                dve.wait_ge(gh_pe["o"], gh_pe.after(h - 1, "o"))
                nc.vector.scalar_tensor_tensor(qM, off, 0.0, over(qdT, h), ALU.is_equal, ALU.mult).then_inc(gh_dve.step("qM"), 1)

            w_by_stream(0)
            q_by_stream(0)
            for h in range(H):
                dve.wait_ge(gh_pe["vn"], gh_pe.after(h, "vn"))
                nc.vector.tensor_copy(h4(vnew)[:, h, :], quarters(bank[1])[:, h, :]).then_inc(gh_dve.step("vn"), 1)
                dve.wait_ge(gh_dve["vn"], gh_dve.after(h, "vn"))
                dve.wait_ge(gh_pe["s"], gh_pe.after(h - 1, "s"))
                tt(vM, over(vnew, h), C("stream_row").unsqueeze(2).to_broadcast([P, NB, P]), ALU.mult).then_inc(gh_dve.step("vM"), 1)
                if h < H - 1:
                    w_by_stream(h + 1)
                dve.wait_ge(gh_pe["o"], gh_pe.after(h, "o"))
                last = h4(EG)[:, h, TB - 1:P:TB].unsqueeze(2).to_broadcast([P, NB, P])
                tt(states[:, h, :, :], states[:, h, :, :], last, ALU.mult).then_inc(gh_dve.step("sg"), 1)
                if h < H - 1:
                    q_by_stream(h + 1)
                dve.wait_ge(gh_dve["sg"], gh_dve.after(h, "sg"))
                dve.wait_ge(gh_pe["s"], gh_pe.after(h, "s"))
                for i in range(2):
                    o = states[:, h, 4 * i:4 * i + 4, :]
                    tt(o, o, quarters(bank[3 + i]), ALU.add).then_inc(gh_dve.step(f"s{i}"), 1)

        def gdn_dve(dve):
            g_dve.arm(dve)
            gs_dve.arm(dve)
            g0.arm(dve)
            nc.vector.memset(state, 0.0).then_inc(g0.step("state"), 1)
            dve.wait_ge(g0["state"], g0.after(0, "state"))

            def tile(t, before):
                gdn_dve_tile(dve, t, False, lambda i: das_dve_stage(dve, 2 * t + i // STAGES, i % STAGES), before)

            tile(0, False)
            with dve.Fori(1, NTP) as t:
                tile(t, True)
            gdn_dve_tile(dve, 0, True, lambda i: das_out_dve(dve, i), True)
            for part in range(4):
                gdn_dve_out(dve, 0, True, part)

        g0 = steps("gdn_state_zero", "state")

        mem_rows = conv[:, 4096:6144].rearrange("p (t d) -> p t d", t=2)
        mem_act = spare[1].rearrange("p (c t) -> p c t", c=KC)
        mk_tok = conv[:, 0:2048].rearrange("p (t d) -> p t d", t=2)
        mkT = conv[:, 2048:4096].rearrange("p (c m) -> p c m", c=KC)
        mv = conv[:, 4096:6144].rearrange("p (t d) -> p t d", t=2)
        m_pe = steps("mem_pe", "t0 t1 t2 t3")
        m_dve = steps("mem_dve", "t0 t1 t2 t3")
        s_mem = sem("memory_rows_loaded")

        def mem_turn_pe(pe):
            m_pe.arm(pe)
            all_taken(pe, LAST_OF["mk"])
            for g in range(4):
                pe.wait_ge(n_dve["cross"][f"ev{NT - 1}b"], n_dve["cross"].after(0, f"ev{NT - 1}b"))
                if g >= 2:
                    pe.wait_ge(m_dve[f"t{g - 2}"], m_dve.after(0, f"t{g - 2}"))
                for i in range(4):
                    c, m = 2 * g + i // 2, i % 2
                    mm = nc.tensor.transpose(quarters(bank[4 + g % 2])[:, i, :], mk_tok[:, m, c * P:(c + 1) * P], ident)
                mm.then_inc(m_pe.step(f"t{g}"), 1)

        def mem_turn_dve(dve):
            m_dve.arm(dve)
            for g in range(4):
                dve.wait_ge(m_pe[f"t{g}"], m_pe.after(0, f"t{g}"))
                nc.vector.tensor_copy(mkT[:, 2 * g:2 * g + 2, :].rearrange("p a b -> p (a b)"), bank[4 + g % 2][:, :]).then_inc(m_dve.step(f"t{g}"), 1)

        xq = act_b[:, :].rearrange("p (c t) -> p c t", c=KC)
        x_pe = steps("xp_pe", "sc | tr0 tr1 pv0 pv1")
        x_dve = steps("xp_dve", "m0 m1 | r pn T1 o1")
        x_act = steps("xp_act", "p0 p1 p2 p3 | T0 o0")
        xP = [gz[:, 2 * i:2 * i + 2, :].rearrange("p a b -> p (a b)") for i in range(2)]
        xPT = [scr[:, i, :] for i in range(2)]
        xmx = [little(4) for _ in range(2)]
        xsum = [little(4) for _ in range(2)]

        def xp_pe(pe):
            x_pe.arm(pe)
            all_taken(pe, LAST_OF["cq"])
            pe.wait_ge(m_dve["t3"], m_dve.after(0, "t3"))
            pe.wait_ge(n_dve["cross"][f"ev{NT - 1}b"], n_dve["cross"].after(0, f"ev{NT - 1}b"))
            def scores(u, heads):
                for h in heads:
                    for c in range(2):
                        mm = nc.tensor.matmul(bank[2 * (u % 2) + h // 2][:, MEM * (h % 2):MEM * (h % 2) + MEM],
                                              xq[:, 2 * h + c, u * P:(u + 1) * P], mkT[:, 2 * h + c, :], start=c == 0, stop=c == 1)
                return mm

            for u in range(NTP + 1):
                v = u - 1
                if u < NTP:
                    pe.wait_ge(x_act["p3"], x_act.after(u - 2, "p3"))
                    scores(u, (0, 1))
                if u >= 1:
                    pe.wait_ge(x_dve["pn"], x_dve.after(v, "pn"))
                    for g, s in ((0, x_act), (1, x_dve)):
                        pe.wait_ge(s[f"T{g}"], s.after(v - 1, f"T{g}"))
                        for i in range(4):
                            q = 4 * g + i
                            mm = nc.tensor.transpose(quarters(bank[4 + g])[:, i, :], xP[v % 2][:, q * P:(q + 1) * P], ident)
                        mm.then_inc(x_pe.step(f"tr{g}"), 1)
                if u < NTP:
                    scores(u, (2, 3)).then_inc(x_pe.step("sc"), 1)
                if u >= 1:
                    pe.wait_ge(x_act["T0"], x_act.after(v, "T0"))
                    pe.wait_ge(x_dve["T1"], x_dve.after(v, "T1"))
                    for g, s in ((0, x_act), (1, x_dve)):
                        pe.wait_ge(s[f"o{g}"], s.after(v - 1, f"o{g}"))
                        for i in range(4):
                            q = 4 * g + i
                            for m in range(2):
                                mm = nc.tensor.matmul(quarters(bank[6 + g])[:, i, :], mv[:, m, q * P:(q + 1) * P],
                                                      xPT[v % 2][:, (2 * (q // 2) + m) * P:(2 * (q // 2) + m + 1) * P], start=m == 0, stop=m == 1)
                        mm.then_inc(x_pe.step(f"pv{g}"), 1)

        def xp_dve(dve):
            x_dve.arm(dve)
            for u in range(NTP + 1):
                v = u - 1
                if u >= 1:
                    dve.wait_ge(x_act["p3"], x_act.after(v, "p3"))
                    nc.vector.reciprocal(xsum[v % 2], xsum[v % 2]).then_inc(x_dve.step("r"), 1)
                    dve.wait_ge(x_dve["r"], x_dve.after(v, "r"))
                    pp = xP[v % 2].rearrange("p (h m) -> p h m", h=H)
                    nc.vector.tensor_tensor(pp, pp, xsum[v % 2].unsqueeze(2).to_broadcast([P, H, MEM]), ALU.mult).then_inc(x_dve.step("pn"), 1)
                    dve.wait_ge(x_pe["tr1"], x_pe.after(v, "tr1"))
                    nc.vector.tensor_copy(xPT[v % 2][:, 512:1024], bank[5][:, :]).then_inc(x_dve.step("T1"), 1)
                if u < NTP:
                    dve.wait_ge(x_pe["sc"], x_pe.after(u, "sc"))
                    for g in range(2):
                        ins = nc.vector.tensor_reduce(xmx[u % 2][:, 2 * g:2 * g + 2],
                                                      bank[2 * (u % 2) + g][:, :].rearrange("p (h m) -> p h m", h=2), AX.X, ALU.max, negate=True)
                        ins.then_inc(x_dve.step(f"m{g}"), 1)
                if u >= 1:
                    dve.wait_ge(x_pe["pv1"], x_pe.after(v, "pv1"))
                    nc.vector.tensor_copy(act_a[:, 4:8, v * P:(v + 1) * P], quarters(bank[7])).then_inc(x_dve.step("o1"), 1)

        def xp_act(act):
            x_act.arm(act)
            for u in range(NTP + 1):
                v = u - 1
                if u >= 1:
                    act.wait_ge(x_pe["tr0"], x_pe.after(v, "tr0"))
                    nc.scalar.copy(xPT[v % 2][:, 0:512], bank[4][:, :]).then_inc(x_act.step("T0"), 1)
                if u < NTP:
                    q = u % 2
                    act.wait_ge(x_dve["m1"], x_dve.after(u, "m1"))
                    act.wait_ge(x_pe["tr1"], x_pe.after(u - 2, "tr1"))
                    for h in range(H):
                        c = slice(MEM * (h % 2), MEM * (h % 2) + MEM)
                        nc.scalar.activation(xP[q][:, MEM * h:MEM * h + MEM], bank[2 * q + h // 2][:, c], ACT.Exp,
                                                        bias=xmx[q][:, h:h + 1], accum_out=xsum[q][:, h:h + 1]).then_inc(x_act.step(f"p{h}"), 1)
                if u >= 1:
                    act.wait_ge(x_pe["pv0"], x_pe.after(v, "pv0"))
                    nc.scalar.copy(act_a[:, 0:4, v * P:(v + 1) * P], quarters(bank[6])).then_inc(x_act.step("o0"), 1)

        X_STAGES = [[0, 1], [2, 3], [4], [], [5], [6], [7], []]
        xs_pe = steps("x_stream_pe", "f0 f1 f2 f3 sc pT pv oT")
        xs_dve = steps("x_stream_dve", "q f1 f3 mx r pn pT")
        xs_act = steps("x_stream_act", "f0 f2 p pv o")
        xs_zero = steps("x_stream_zero", "q")
        c_KT = attn[:, 0:2048].rearrange("p (c m) -> p c m", c=KC)
        c_q = attn[:, 2048:2304].rearrange("p (c r) -> p c r", r=32)
        c_P, c_aT, c_o = (attn[:, 2304 + MEM * i:2304 + MEM * (i + 1)] for i in range(3))
        c_mx, c_sum = little(1), little(1)

        def xs_pe_stage(pe, b, k, stage):
            kk, vv = kv_slot(UNIT["x0"], k, True)
            if stage < 4:
                f = stage
                if f == 0:
                    pe.wait_ge(s_kv[k], (b - k) * 16 + 32 + 32 * (NB // 2))
                    pe.wait_ge(xs_act["o"], xs_act.after(b - 1, "o"))
                elif f == 2:
                    pe.wait_ge(xs_act["f0"], xs_act.after(b, "f0"))
                elif f == 3:
                    pe.wait_ge(xs_dve["f1"], xs_dve.after(b, "f1"))
                for i in range(4):
                    src = kk[:, i % 2, (2 * f + i // 2) * P:(2 * f + i // 2 + 1) * P]
                    mm = nc.tensor.transpose(quarters(bank[6 + f % 2])[:, i, :], src, ident)
                mm.then_inc(xs_pe.step(f"f{f}"), 1)
            elif stage == 4:
                pe.wait_ge(xs_dve["f3"], xs_dve.after(b, "f3"))
                pe.wait_ge(xs_act["f2"], xs_act.after(b, "f2"))
                for c in range(2):
                    for h in range(H):
                        mm = nc.tensor.matmul(bank[7][32 * h:32 * h + 32, 0:MEM], c_q[:, 2 * h + c, :], c_KT[:, 2 * h + c, :],
                                              start=c == 0, stop=c == 1, skip_group_check=True)
                mm.then_inc(xs_pe.step("sc"), 1)
            elif stage == 5:
                pe.wait_ge(xs_dve["pn"], xs_dve.after(b, "pn"))
                for m in range(2):
                    mm = nc.tensor.transpose(bank[6][:, m * P:(m + 1) * P], c_P[:, m * P:(m + 1) * P], ident)
                mm.then_inc(xs_pe.step("pT"), 1)
            elif stage == 6:
                pe.wait_ge(xs_dve["pT"], xs_dve.after(b, "pT"))
                for m in range(2):
                    for h in range(H):
                        mm = nc.tensor.matmul(bank[7][32 * h:32 * h + 32, 0:MEM], c_aT[:, m * P + 32 * h:m * P + 32 * h + 32],
                                              vv[:, m, MEM * h:MEM * h + MEM], start=m == 0, stop=m == 1, skip_group_check=True)
                mm.then_inc(xs_pe.step("pv"), 1)
            else:
                pe.wait_ge(xs_act["pv"], xs_act.after(b, "pv"))
                for e in range(2):
                    mm = nc.tensor.transpose(bank[6][:, e * P:(e + 1) * P], c_o[:, e * P:(e + 1) * P], ident)
                mm.then_inc(xs_pe.step("oT"), 1)

        def xs_act_stage(act, b, stage):
            if stage in (0, 2):
                act.wait_ge(xs_pe[f"f{stage}"], xs_pe.after(b, f"f{stage}"))
                nc.scalar.copy(c_KT[:, 2 * stage:2 * stage + 2, :],
                               bank[6][:, :].rearrange("p (c m) -> p c m", c=2)).then_inc(xs_act.step(f"f{stage}"), 1)
            elif stage == 4:
                act.wait_ge(xs_dve["mx"], xs_dve.after(b, "mx"))
                nc.scalar.activation(c_P, bank[7][:, 0:MEM], ACT.Exp, bias=c_mx, accum_out=c_sum).then_inc(xs_act.step("p"), 1)
            elif stage == 6:
                act.wait_ge(xs_pe["pv"], xs_pe.after(b, "pv"))
                nc.scalar.copy(c_o, bank[7][:, 0:MEM]).then_inc(xs_act.step("pv"), 1)
            elif stage == 7:
                act.wait_ge(xs_pe["oT"], xs_pe.after(b, "oT"))
                src = bank[6][:, 0:2 * P].rearrange("p (e h t) -> p e h t", e=2, h=H)
                dst = act_a[:, :, SEQ + b * TB:SEQ + (b + 1) * TB].rearrange("p (h e) t -> p e h t", h=H)
                for e in range(2):
                    ins = nc.scalar.copy(dst[:, e, :, :], src[:, e, :, 0:TB])
                ins.then_inc(xs_act.step("o"), 1)

        def xs_dve_stage(dve, b, stage):
            if stage == 0:
                dve.wait_ge(xs_pe["sc"], xs_pe.after(b - 1, "sc"))
                nc.vector.tensor_copy(c_q[:, :, 0:TB], xq[:, :, SEQ + b * TB:SEQ + (b + 1) * TB]).then_inc(xs_dve.step("q"), 1)
            elif stage in (1, 3):
                dve.wait_ge(xs_pe[f"f{stage}"], xs_pe.after(b, f"f{stage}"))
                nc.vector.tensor_copy(c_KT[:, 2 * stage:2 * stage + 2, :],
                                      bank[7][:, :].rearrange("p (c m) -> p c m", c=2)).then_inc(xs_dve.step(f"f{stage}"), 1)
            elif stage == 4:
                dve.wait_ge(xs_pe["sc"], xs_pe.after(b, "sc"))
                nc.vector.tensor_reduce(c_mx, bank[7][:, 0:MEM], AX.X, ALU.max, negate=True).then_inc(xs_dve.step("mx"), 1)
            elif stage == 5:
                dve.wait_ge(xs_act["p"], xs_act.after(b, "p"))
                nc.vector.reciprocal(c_sum, c_sum).then_inc(xs_dve.step("r"), 1)
                dve.wait_ge(xs_dve["r"], xs_dve.after(b, "r"))
                nc.vector.tensor_scalar(c_P, c_P, c_sum, None, ALU.mult).then_inc(xs_dve.step("pn"), 1)
            elif stage == 6:
                dve.wait_ge(xs_pe["pT"], xs_pe.after(b, "pT"))
                nc.vector.tensor_copy(c_aT, bank[6][:, 0:MEM]).then_inc(xs_dve.step("pT"), 1)

        h_row = conv[:, 4 * D:6 * D].rearrange("p (t d) -> p t d", t=2)
        gffn_row = conv[:, 6144:7168]
        w_route = conv[:, 7168:7168 + 36 * KC].rearrange("p (c n) -> p c n", c=KC)
        b_route = conv[:, 7456:7492]
        at_r = [0]

        def rs(*shape):
            n = int(np.prod(shape))
            at_r[0] += n
            v = attn[:, at_r[0] - n:at_r[0]]
            if len(shape) == 2:
                v = v.rearrange("p (a b) -> p a b", a=shape[0])
            return v

        lg = rs(NT, 36)
        g_s, g_e, g_q = rs(NT, 4), rs(NT, 4), rs(NT, 4)
        gmax, gsum, gidx, m1, m2, i1, i2, ee, w1, w2 = (rs(NT) for _ in range(10))
        sl12, place = rs(2 * NT), rs(2 * NT)
        sl1, sl2 = sl12[:, 0:NT], sl12[:, NT:]
        msk, ml, dd, oh1, oh2, pos, slotv = (rs(NT, NE) for _ in range(7))
        A0 = rs(NT + 1, NE)
        A = A0[:, 0:NT, :]
        cnt, nblk, ends, starts, one32 = (rs(NE) for _ in range(5))
        capq = rs(NE, NT * P // CAP)
        cmp_ = rs(BLKPAD + 1, NE)
        blk_e = rs(BLKPAD + 1)
        cmp2, n_rounds = rs((BLKPAD + 1) // 2), rs(1)
        pair_f, over_f, token_f = rs(NBLK), rs(NBLK), rs(NBLK)
        in_block, off = rs(2 * NT, NBLK), rs(2 * NT, NBLK)
        lgT = attn[0:36, 5504:5504 + NT * P]
        at_place = cmp_.rearrange("p a b -> p (a b)")[:, 0:2 * NT * CAP].rearrange("p (a b) -> p a b", b=CAP)
        assert at_r[0] <= 5120
        at_u = [5120]

        def us(n):
            at_u[0] += n
            return attn[:, at_u[0] - n:at_u[0]].bitcast(U32)

        table_u = us(64)
        pair_all = us(64)
        token_all = us(64)
        token_col, pair_col = [us(1), us(1)], [us(1), us(1)]
        e_pe = steps("moe_pe", "tr0 tr1 | gate up d0 d1")
        r_pe = steps("route_pe", "lgp lgs lg cum table")
        r_act = steps("route_act", "lgp lgs ge ee")
        r_dve = steps("route_dve",
                      "A0 lg gmax gs ge4 gsum gtop gq gq2 gidx msk0 msk1 ml m1 d1 q1 q1b i1 oh1 ml2 m2 d2 q2 q2b i2 oh2 "
                      "dm w0 w1a w1 w2 A cnt pos capq nblk one ends "
                      "cmp blk min tab cmp2 nr tabn starts base slotv s1a s1 s2a s2 off ib0 ib off2 place ap pairs "
                      "e0 e1 pf pu p1 p2 p3 p4 token")
        s_route = sem("route_weights_loaded")
        s_bias = sem("group_bias_loaded")
        s_rows = [sem(f"rows_stored{k}") for k in range(2)]
        H_ROWS = [16 * len(range(k, NT, 2)) for k in range(2)]

        def route_prompt_pe(pe):
            r_pe.arm(pe)
            e_pe.arm(pe)
            pe.wait_ge(s_route, 64)
            pe.wait_ge(n_dve["ffn"][f"ev{NTP - 1}b"], n_dve["ffn"].after(0, f"ev{NTP - 1}b"))
            pe.wait_ge(taken(LAST_OF["co"]), taken_count(LAST_OF["co"]))
            for c in range(KC):
                mm = nc.tensor.matmul(bank[1][0:36, :], w_route[:, c, :], act_a[:, c, 0:SEQ], start=c == 0, stop=c == KC - 1)
            mm.then_inc(r_pe.step("lgp"), 1)

        def route_pe(pe):
            pe.wait_ge(n_dve["ffn"][f"ev{NT - 1}b"], n_dve["ffn"].after(0, f"ev{NT - 1}b"))
            for c in range(KC):
                mm = nc.tensor.matmul(bank[2][0:36, 0:P], w_route[:, c, :], act_a[:, c, SEQ:], start=c == 0, stop=c == KC - 1)
            mm.then_inc(r_pe.step("lgs"), 1)
            pe.wait_ge(r_act["lgs"], r_act.after(0, "lgs"))
            for t in range(NT):
                mm = nc.tensor.transpose(bank[0][:, 36 * t:36 * t + 36], lgT[:, t * P:(t + 1) * P], ident[0:36, 0:36])
            mm.then_inc(r_pe.step("lg"), 1)
            pe.wait_ge(r_dve["A"], r_dve.after(0, "A"))
            mm = nc.tensor.matmul(bank[1][:, 0:NE * (NT + 1)], C("cum_p"), A0.rearrange("p t n -> p (t n)"), start=True, stop=False)
            for d in range(1, NT + 1):
                mm = nc.tensor.matmul(bank[1][:, NE * d:NE * (NT + 1)], C("ones"), A0[:, 0:NT + 1 - d, :].rearrange("p t n -> p (t n)"),
                                      start=False, stop=d == NT)
            mm.then_inc(r_pe.step("cum"), 1)
            pe.wait_ge(r_dve["pairs"], r_dve.after(0, "pairs"))
            for i in range(2 * NT):
                mm = nc.tensor.matmul(bank[2][0:CAP, 0:NBLK], at_place[:, i, :], in_block[:, i, :], start=i == 0, stop=i == 2 * NT - 1)
            mm.then_inc(r_pe.step("table"), 1)

        def route_act(act):
            r_act.arm(act)
            act.wait_ge(r_pe["lgp"], r_pe.after(0, "lgp"))
            nc.scalar.copy(lgT[:, 0:SEQ], bank[1][0:36, :]).then_inc(r_act.step("lgp"), 1)
            act.wait_ge(r_pe["lgs"], r_pe.after(0, "lgs"))
            nc.scalar.copy(lgT[:, SEQ:], bank[2][0:36, 0:P]).then_inc(r_act.step("lgs"), 1)
            act.wait_ge(r_dve["gs"], r_dve.after(0, "gs"))
            nc.scalar.activation(g_e, g_s, ACT.Exp).then_inc(r_act.step("ge"), 1)
            act.wait_ge(r_dve["dm"], r_dve.after(0, "dm"))
            nc.scalar.activation(ee, ee, ACT.Exp).then_inc(r_act.step("ee"), 1)

        def route_dve(dve):
            r_dve.arm(dve)
            tt, ts, red = nc.vector.tensor_tensor, nc.vector.tensor_scalar, nc.vector.tensor_reduce
            stt = nc.vector.scalar_tensor_tensor

            def over(v, n):
                return v.unsqueeze(2).to_broadcast([P, NT, n])

            def row(v, n):
                return v.unsqueeze(1).to_broadcast([P, NT, n])

            dve.wait_ge(xs_act["o"], xs_act.after(NB - 1, "o"))
            nc.vector.memset(A0[:, NT, :], 0.0).then_inc(r_dve.step("A0"), 1)
            dve.wait_ge(r_pe["lg"], r_pe.after(0, "lg"))
            tt(lg, bank[0][:, 0:36 * NT].rearrange("p (t n) -> p t n", t=NT), row(b_route, 36), ALU.add).then_inc(r_dve.step("lg"), 1)
            dve.wait_ge(r_dve["lg"], r_dve.after(0, "lg"))
            gl, el = lg[:, :, 0:4], lg[:, :, 4:36]
            red(gmax, gl, AX.X, ALU.max).then_inc(r_dve.step("gmax"), 1)
            dve.wait_ge(r_dve["gmax"], r_dve.after(0, "gmax"))
            tt(g_s, gl, over(gmax, 4), ALU.subtract).then_inc(r_dve.step("gs"), 1)
            dve.wait_ge(r_dve["gs"], r_dve.after(0, "gs"))
            dve.wait_ge(r_act["ge"], r_act.after(0, "ge"))
            red(gsum, g_e, AX.X, ALU.add).then_inc(r_dve.step("ge4"), 1)
            dve.wait_ge(r_dve["ge4"], r_dve.after(0, "ge4"))
            nc.vector.reciprocal(gsum, gsum).then_inc(r_dve.step("gsum"), 1)
            dve.wait_ge(r_dve["gsum"], r_dve.after(0, "gsum"))
            ts(g_q, g_s, 0.0, None, ALU.is_equal).then_inc(r_dve.step("gtop"), 1)
            dve.wait_ge(r_dve["gtop"], r_dve.after(0, "gtop"))
            ts(g_q, g_q, -100.0, 100.0, ALU.mult, ALU.add).then_inc(r_dve.step("gq"), 1)
            dve.wait_ge(r_dve["gq"], r_dve.after(0, "gq"))
            tt(g_q, g_q, row(C("iota8")[:, 0:4], 4), ALU.add).then_inc(r_dve.step("gq2"), 1)
            dve.wait_ge(r_dve["gq2"], r_dve.after(0, "gq2"))
            red(gidx, g_q, AX.X, ALU.min).then_inc(r_dve.step("gidx"), 1)
            dve.wait_ge(r_dve["gidx"], r_dve.after(0, "gidx"))
            tt(msk, row(C("group"), NE), over(gidx, NE), ALU.is_equal).then_inc(r_dve.step("msk0"), 1)
            dve.wait_ge(r_dve["msk0"], r_dve.after(0, "msk0"))
            ts(msk, msk, BIG, -BIG, ALU.mult, ALU.add).then_inc(r_dve.step("msk1"), 1)
            dve.wait_ge(r_dve["msk1"], r_dve.after(0, "msk1"))
            tt(ml, el, msk, ALU.add).then_inc(r_dve.step("ml"), 1)
            dve.wait_ge(r_dve["ml"], r_dve.after(0, "ml"))
            for k, m, i, oh in ((1, m1, i1, oh1), (2, m2, i2, oh2)):
                red(m, ml, AX.X, ALU.max).then_inc(r_dve.step(f"m{k}"), 1)
                dve.wait_ge(r_dve[f"m{k}"], r_dve.after(0, f"m{k}"))
                tt(dd, ml, over(m, NE), ALU.is_equal).then_inc(r_dve.step(f"d{k}"), 1)
                dve.wait_ge(r_dve[f"d{k}"], r_dve.after(0, f"d{k}"))
                ts(dd, dd, -100.0, 100.0, ALU.mult, ALU.add).then_inc(r_dve.step(f"q{k}"), 1)
                dve.wait_ge(r_dve[f"q{k}"], r_dve.after(0, f"q{k}"))
                tt(dd, dd, row(C("iota32"), NE), ALU.add).then_inc(r_dve.step(f"q{k}b"), 1)
                dve.wait_ge(r_dve[f"q{k}b"], r_dve.after(0, f"q{k}b"))
                red(i, dd, AX.X, ALU.min).then_inc(r_dve.step(f"i{k}"), 1)
                dve.wait_ge(r_dve[f"i{k}"], r_dve.after(0, f"i{k}"))
                tt(oh, row(C("iota32"), NE), over(i, NE), ALU.is_equal).then_inc(r_dve.step(f"oh{k}"), 1)
                dve.wait_ge(r_dve[f"oh{k}"], r_dve.after(0, f"oh{k}"))
                if k == 1:
                    stt(ml, oh, -BIG, ml, ALU.mult, ALU.add).then_inc(r_dve.step("ml2"), 1)
                    dve.wait_ge(r_dve["ml2"], r_dve.after(0, "ml2"))
            tt(ee, m2, m1, ALU.subtract).then_inc(r_dve.step("dm"), 1)
            dve.wait_ge(r_dve["dm"], r_dve.after(0, "dm"))
            dve.wait_ge(r_act["ee"], r_act.after(0, "ee"))
            ts(w1, ee, 1.0, None, ALU.add).then_inc(r_dve.step("w0"), 1)
            dve.wait_ge(r_dve["w0"], r_dve.after(0, "w0"))
            nc.vector.reciprocal(w1, w1).then_inc(r_dve.step("w1a"), 1)
            dve.wait_ge(r_dve["w1a"], r_dve.after(0, "w1a"))
            tt(w1, w1, gsum, ALU.mult).then_inc(r_dve.step("w1"), 1)
            dve.wait_ge(r_dve["w1"], r_dve.after(0, "w1"))
            tt(w2, w1, ee, ALU.mult).then_inc(r_dve.step("w2"), 1)
            dve.wait_ge(r_dve["w2"], r_dve.after(0, "w2"))
            tt(A, oh1, oh2, ALU.add).then_inc(r_dve.step("A"), 1)
            dve.wait_ge(r_dve["A"], r_dve.after(0, "A"))
            dve.wait_ge(r_pe["cum"], r_pe.after(0, "cum"))
            nc.vector.tensor_copy(cnt, bank[1][:, NE * NT:NE * NT + NE]).then_inc(r_dve.step("cnt"), 1)
            dve.wait_ge(r_dve["cnt"], r_dve.after(0, "cnt"))
            tt(pos, bank[1][:, 0:NE * NT].rearrange("p (t n) -> p t n", t=NT), A, ALU.subtract).then_inc(r_dve.step("pos"), 1)
            dve.wait_ge(r_dve["pos"], r_dve.after(0, "pos"))
            nc_ = NT * P // CAP
            tt(capq, cnt.unsqueeze(2).to_broadcast([P, NE, nc_]), C("capacities").unsqueeze(1).to_broadcast([P, NE, nc_]), ALU.is_gt).then_inc(r_dve.step("capq"), 1)
            dve.wait_ge(r_dve["capq"], r_dve.after(0, "capq"))
            red(nblk, capq, AX.X, ALU.add).then_inc(r_dve.step("nblk"), 1)
            dve.wait_ge(r_dve["nblk"], r_dve.after(0, "nblk"))
            nc.vector.memset(one32, 1.0).then_inc(r_dve.step("one"), 1)
            dve.wait_ge(r_dve["one"], r_dve.after(0, "one"))
            nc.vector.tensor_tensor_scan(ends, one32, nblk, 0.0, ALU.mult, ALU.add).then_inc(r_dve.step("ends"), 1)
            dve.wait_ge(r_dve["ends"], r_dve.after(0, "ends"))
            nb = BLKPAD + 1
            tt(cmp_, C("block").unsqueeze(2).to_broadcast([P, nb, NE]), ends.unsqueeze(1).to_broadcast([P, nb, NE]), ALU.is_ge).then_inc(r_dve.step("cmp"), 1)
            dve.wait_ge(r_dve["cmp"], r_dve.after(0, "cmp"))
            red(blk_e, cmp_, AX.X, ALU.add).then_inc(r_dve.step("blk"), 1)
            dve.wait_ge(r_dve["blk"], r_dve.after(0, "blk"))
            ts(blk_e, blk_e, float(NE - 1), None, ALU.min).then_inc(r_dve.step("min"), 1)
            dve.wait_ge(r_dve["min"], r_dve.after(0, "min"))
            nc.vector.tensor_copy(table_u[:, 1:1 + nb], blk_e).then_inc(r_dve.step("tab"), 1)
            dve.wait_ge(r_dve["tab"], r_dve.after(0, "tab"))
            tt(cmp2, ends[:, NE - 1:NE].to_broadcast([P, nb // 2]), C("block")[:, 0:nb:2], ALU.is_gt).then_inc(r_dve.step("cmp2"), 1)
            dve.wait_ge(r_dve["cmp2"], r_dve.after(0, "cmp2"))
            red(n_rounds, cmp2, AX.X, ALU.add).then_inc(r_dve.step("nr"), 1)
            dve.wait_ge(r_dve["nr"], r_dve.after(0, "nr"))
            nc.vector.tensor_copy(table_u[:, 0:1], n_rounds).then_inc(r_dve.step("tabn"), 1)
            tt(starts, ends, nblk, ALU.subtract).then_inc(r_dve.step("starts"), 1)
            dve.wait_ge(r_dve["starts"], r_dve.after(0, "starts"))
            ts(starts, starts, float(CAP), None, ALU.mult).then_inc(r_dve.step("base"), 1)
            dve.wait_ge(r_dve["base"], r_dve.after(0, "base"))
            tt(slotv, pos, row(starts, NE), ALU.add).then_inc(r_dve.step("slotv"), 1)
            dve.wait_ge(r_dve["slotv"], r_dve.after(0, "slotv"))
            for k, oh, sl in ((1, oh1, sl1), (2, oh2, sl2)):
                tt(dd, oh, slotv, ALU.mult).then_inc(r_dve.step(f"s{k}a"), 1)
                dve.wait_ge(r_dve[f"s{k}a"], r_dve.after(0, f"s{k}a"))
                red(sl, dd, AX.X, ALU.add).then_inc(r_dve.step(f"s{k}"), 1)
                dve.wait_ge(r_dve[f"s{k}"], r_dve.after(0, f"s{k}"))
            tt(off, sl12.unsqueeze(2).to_broadcast([P, 2 * NT, NBLK]), C("slot0").unsqueeze(1).to_broadcast([P, 2 * NT, NBLK]),
               ALU.subtract).then_inc(r_dve.step("off"), 1)
            dve.wait_ge(r_dve["off"], r_dve.after(0, "off"))
            ts(in_block, off, 0.0, None, ALU.is_ge).then_inc(r_dve.step("ib0"), 1)
            dve.wait_ge(r_dve["ib0"], r_dve.after(0, "ib0"))
            stt(in_block, off, float(CAP), in_block, ALU.is_lt, ALU.mult).then_inc(r_dve.step("ib"), 1)
            dve.wait_ge(r_dve["ib"], r_dve.after(0, "ib"))
            tt(off, off, in_block, ALU.mult).then_inc(r_dve.step("off2"), 1)
            dve.wait_ge(r_dve["off2"], r_dve.after(0, "off2"))
            red(place, off, AX.X, ALU.add).then_inc(r_dve.step("place"), 1)
            dve.wait_ge(r_dve["place"], r_dve.after(0, "place"))
            tt(at_place, C("iota_cap").unsqueeze(1).to_broadcast([P, 2 * NT, CAP]), place.unsqueeze(2).to_broadcast([P, 2 * NT, CAP]),
               ALU.is_equal).then_inc(r_dve.step("ap"), 1)
            tt(in_block, in_block, C("pair").unsqueeze(2).to_broadcast([P, 2 * NT, NBLK]), ALU.mult).then_inc(r_dve.step("pairs"), 1)
            r_ = slice(0, CAP)
            pf, ov, tf, table = pair_f[r_], over_f[r_], token_f[r_], bank[2][r_, 0:NBLK]
            dve.wait_ge(r_pe["table"], r_pe.after(0, "table"))
            ts(ov, table, 0.0, None, ALU.is_equal).then_inc(r_dve.step("e0"), 1)
            dve.wait_ge(r_dve["e0"], r_dve.after(0, "e0"))
            tt(ov, ov, C("empty")[r_], ALU.mult).then_inc(r_dve.step("e1"), 1)
            dve.wait_ge(r_dve["e1"], r_dve.after(0, "e1"))
            stt(pf, table, -1.0, ov, ALU.add, ALU.add).then_inc(r_dve.step("pf"), 1)
            dve.wait_ge(r_dve["pf"], r_dve.after(0, "pf"))
            nc.vector.tensor_copy(pair_all[r_, 0:NBLK], pf).then_inc(r_dve.step("pu"), 1)
            ts(ov, pf, float(NT * P), -float(NT * P), ALU.is_ge, ALU.mult).then_inc(r_dve.step("p1"), 1)
            dve.wait_ge(r_dve["p1"], r_dve.after(0, "p1"))
            tt(tf, pf, ov, ALU.add).then_inc(r_dve.step("p2"), 1)
            dve.wait_ge(r_dve["p2"], r_dve.after(0, "p2"))
            ts(ov, pf, float(NPAIR), -float(NT * P), ALU.is_ge, ALU.mult).then_inc(r_dve.step("p3"), 1)
            dve.wait_ge(r_dve["p3"], r_dve.after(0, "p3"))
            tt(tf, tf, ov, ALU.add).then_inc(r_dve.step("p4"), 1)
            dve.wait_ge(r_dve["p4"], r_dve.after(0, "p4"))
            nc.vector.tensor_copy(token_all[r_, 0:NBLK], tf).then_inc(r_dve.step("token"), 1)
            dve.wait_ge(r_dve["token"], r_dve.after(0, "token"))

        def ffn_rows_pool(pool):
            s = n_pool["ffn"]
            pool.wait_ge(s_route, 64)
            for u in range(NT + 1):
                if u < NT:
                    norm_pool_tile(pool, "ffn", u)
                if u >= 1:
                    t = u - 1
                    pool.wait_ge(n_dve["ffn"][f"xn{t}"], n_dve["ffn"].after(0, f"xn{t}"))
                    if t >= 2:
                        pool.wait_ge(s_rows[t % 2], 16 * (t // 2))
                    nc.gpsimd.tensor_tensor(h_row[:, t % 2, :], scr[:, t % 2, :], gffn_row, ALU.mult).then_inc(s.step(f"g{t}"), 1)
                    pool.wait_ge(s[f"g{t}"], s.after(0, f"g{t}"))
                    pool.dma_start(a["h_rows"][t * P:(t + 1) * P, :], h_row[:, t % 2, :]).then_inc(s_rows[t % 2], 16)
            for k in range(2):
                pool.wait_ge(s_rows[k], H_ROWS[k])

        xg = [act_a[:, :, :].rearrange("p c t -> p (c t)")[:, 1024 * i:1024 * i + 1024] for i in range(2)]
        xgT = [act_b[:, 640 * i:640 * i + 640].rearrange("p (c s) -> p c s", c=KC) for i in range(2)]
        sgate = [act_b[:, 1280 + 160 * i:1440 + 160 * i] for i in range(2)]
        hT = [act_b[:, 1600 + 160 * i:1760 + 160 * i].rearrange("p (f s) -> p f s", f=2) for i in range(2)]
        yb = [act_b[:, 2048 + 1024 * i:3072 + 1024 * i] for i in range(2)]
        e_act = steps("moe_act", "x0 | silu y0")
        e_dve = steps("moe_dve", "x1 | ix | h pc y1")
        s_ew = [sem(f"expert_loaded{k}") for k in range(2)]
        s_xg = [sem(f"tokens_gathered{k}") for k in range(2)]
        s_go = sem("indirect_dma_may_go")

        def rounds(eng):
            eng.wait_ge(r_dve["tabn"], r_dve.after(0, "tabn"))
            return eng.value_load(table_u[0:1, 0:1], min_val=1, max_val=(BLKPAD + 1) // 2)

        def moe_sync(sp):
            def load(i, k):
                j = 2 * i + k if isinstance(i, int) else sp.snap(2 * i + k)
                at = slice(j + 1, j + 2) if isinstance(i, int) else bass.ds(j + 1, 1)
                e = sp.value_load(table_u[0:1, at], min_val=0, max_val=NE - 1)
                if k == 1:
                    sp.wait_ge(s_xg[0], i * 16 + 16)
                w = W[:, k, :]
                for m, (name, step) in enumerate((("w_gate", "gate"), ("w_up", "up"))):
                    sp.wait_ge(e_pe[step], e_pe.after(j - 2, step))
                    sp.dma_start(w[:, 2048 * m:2048 * m + 2048].rearrange("p (c f) -> p c f", c=KC),
                                 a[name][0][bass.ds(e, 1)].rearrange("o (c p) f -> p (o c) f", p=P)).then_inc(s_ew[k], 16)
                sp.wait_ge(e_pe["d1"], e_pe.after(j - 2, "d1"))
                sp.dma_start(w[:, 4096:6144].rearrange("p (f d) -> p f d", f=2),
                             a["w_down"][0][bass.ds(e, 1)].rearrange("o (f p) d -> p (o f) d", p=P)).then_inc(s_ew[k], 16)

            sp.wait_ge(r_dve["tab"], r_dve.after(0, "tab"))
            for k in range(2):
                load(0, k)
            n = rounds(sp)
            with sp.Fori(1, n) as i:
                for k in range(2):
                    load(i, k)

        def moe_pool(pool):
            def gather(j, k):
                pool.wait_ge(e_pe["tr1"], e_pe.after(j - 2, "tr1"))
                pool.wait_ge(e_dve["ix"], e_dve.after(j, "ix"))
                pool.sem_inc(s_go, 1)
                pool.indirect_dma_start(xg[k][0:CAP, :], None, a["h_rows"], bass.IndirectOffsetOnAxis(token_col[k][0:CAP, :], 0))\
                    .then_inc(s_xg[k], 16)

            n = rounds(pool)
            for k in range(2):
                gather(k, k)
            with pool.Fori(0, n) as i:
                for k in range(2):
                    j = pool.snap(2 * i + k)
                    gather(j + 2, k)
                    pool.wait_ge(e_act["y0"], e_act.after(j, "y0"))
                    pool.wait_ge(e_dve["y1"], e_dve.after(j, "y1"))
                    pool.sem_inc(s_go, 1)
                    pool.indirect_dma_start(a["pair_rows"], bass.IndirectOffsetOnAxis(pair_col[k][0:CAP, :], 0), yb[k][0:CAP, :], None)\
                        .then_inc(s_rows[k], 16)

        def moe_pe(pe):
            n = rounds(pe)

            def turn(j, k, count):
                pe.wait_ge(s_xg[k], count)
                for g, s, name in ((0, e_act, "x0"), (1, e_dve, "x1")):
                    pe.wait_ge(s[name], s.after(j - 1, name))
                    for c in range(4):
                        mm = nc.tensor.transpose(bank[g][:, c * CAP:(c + 1) * CAP], xg[k][0:CAP, (4 * g + c) * P:(4 * g + c + 1) * P],
                                                 ident[0:CAP, 0:CAP])
                    mm.then_inc(e_pe.step(f"tr{g}"), 1)

            turn(0, 0, 16)
            with pe.Fori(0, n) as i:
                for k in range(2):
                    j = pe.snap(2 * i + k)
                    pe.wait_ge(e_act["x0"], e_act.after(j, "x0"))
                    pe.wait_ge(e_dve["x1"], e_dve.after(j, "x1"))
                    pe.wait_ge(e_dve["h"], e_dve.after(j - 1, "h"))
                    pe.wait_ge(s_ew[k], i * 48 + 48)
                    for m, name in enumerate(("gate", "up")):
                        w = W[:, k, 2048 * m:2048 * m + 2048].rearrange("p (c f) -> p c f", c=KC)
                        for f in range(2):
                            for c in range(KC):
                                mm = nc.tensor.matmul(bank[2 + m][:, CAP * f:CAP * f + CAP], w[:, c, f * P:(f + 1) * P], xgT[k][:, c, :],
                                                      start=c == 0, stop=c == KC - 1)
                        mm.then_inc(e_pe.step(name), 1)
                    turn(j + 1, 1 - k, i * 16 + 16 + 16 * k)
                    pe.wait_ge(e_dve["h"], e_dve.after(j, "h"))
                    w = W[:, k, 4096:6144].rearrange("p (f d) -> p f d", f=2)
                    for g, s, name in ((0, e_act, "y0"), (1, e_dve, "y1")):
                        pe.wait_ge(s[name], s.after(j - 1, name))
                        for f in range(2):
                            mm = nc.tensor.matmul(bank[4 + g][0:CAP, :], hT[k][:, f, :], w[:, f, 512 * g:512 * g + 512], start=f == 0, stop=f == 1)
                        mm.then_inc(e_pe.step(f"d{g}"), 1)

        def moe_act(act):
            e_act.arm(act)
            n = rounds(act)

            def turned(j, k):
                act.wait_ge(e_pe["tr0"], e_pe.after(j, "tr0"))
                nc.scalar.copy(xgT[k][:, 0:4, :], bank[0][:, 0:4 * CAP].rearrange("p (c s) -> p c s", c=4)).then_inc(e_act.step("x0"), 1)

            turned(0, 0)
            with act.Fori(0, n) as i:
                for k in range(2):
                    j = act.snap(2 * i + k)
                    act.wait_ge(e_pe["gate"], e_pe.after(j, "gate"))
                    nc.scalar.activation(sgate[k], bank[2][:, 0:2 * CAP], ACT.Silu).then_inc(e_act.step("silu"), 1)
                    turned(j + 1, 1 - k)
                    act.wait_ge(e_pe["d0"], e_pe.after(j, "d0"))
                    act.wait_ge(s_rows[k], i * 16 + H_ROWS[k])
                    nc.scalar.copy(yb[k][0:CAP, 0:512], bank[4][0:CAP, :]).then_inc(e_act.step("y0"), 1)

        def moe_dve(dve):
            e_dve.arm(dve)
            n = rounds(dve)
            rows = slice(0, CAP)

            def columns(j, k):
                nc.vector.tensor_copy(token_col[k][rows, :], token_all[rows, bass.ds(j, 1)]).then_inc(e_dve.step("ix"), 1)

            def turned(j, k, j2):
                dve.wait_ge(e_pe["tr1"], e_pe.after(j, "tr1"))
                nc.vector.tensor_copy(xgT[k][:, 4:8, :], bank[1][:, 0:4 * CAP].rearrange("p (c s) -> p c s", c=4)).then_inc(e_dve.step("x1"), 1)
                columns(j2, k)

            for k in range(2):
                columns(k, k)
            turned(0, 0, 2)
            with dve.Fori(0, n) as i:
                for k in range(2):
                    j = dve.snap(2 * i + k)
                    ahead = dve.snap(2 * i + (k + 3))
                    dve.wait_ge(e_pe["up"], e_pe.after(j, "up"))
                    dve.wait_ge(e_act["silu"], e_act.after(j, "silu"))
                    nc.vector.tensor_tensor(hT[k][:, :, :].rearrange("p f s -> p (f s)"), bank[3][:, 0:2 * CAP], sgate[k], ALU.mult).then_inc(e_dve.step("h"), 1)
                    turned(j + 1, 1 - k, ahead)
                    dve.wait_ge(s_rows[k], i * 16 + H_ROWS[k])
                    nc.vector.tensor_copy(pair_col[k][rows, :], pair_all[rows, bass.ds(j, 1)]).then_inc(e_dve.step("pc"), 1)
                    dve.wait_ge(e_pe["d1"], e_pe.after(j, "d1"))
                    nc.vector.tensor_copy(yb[k][0:CAP, 512:1024], bank[5][0:CAP, :]).then_inc(e_dve.step("y1"), 1)

        Wf = W[:, :, :].rearrange("p a b -> p (a b)")
        back = [Wf[:, 1024 * i:1024 * i + 1024] for i in range(2 * NT)]
        gfin_row = Wf[:, 10240:11264]
        s_back = [sem(f"rows_back{i}") for i in range(2 * NT)]
        s_gfin = sem("g_final_loaded")
        ss_f, rstd_f = little(NT), little(NT)
        f_dve = steps("final_dve", "x1 x2")
        f2_dve = steps("final_norm_dve", "y")
        f_act = steps("final_act", "sq")
        f_pool = steps("final_pool", "ms rn")
        s_store = sem("y_stored")

        def final_pool(pool):
            n = rounds(pool)
            for k in range(2):
                pool.wait_ge(s_rows[k], n * 16 + H_ROWS[k])
            for k in range(2):
                pool.wait_ge(s_xg[k], n * 16 + 16)
            pool.wait_ge(e_pe["d1"], e_pe.after(2 * n - 1, "d1"))
            pool.sem_inc(s_go, 1)
            for t in range(NT):
                for i in (t, t + NT):
                    pool.dma_start(back[i], a["pair_rows"][i * P:(i + 1) * P, :]).then_inc(s_back[i], 16)
            f_pool.arm(pool)
            for t in range(NT):
                c = slice(t, t + 1)
                pool.wait_ge(f_act["sq"], f_act.after(t, "sq"))
                nc.gpsimd.tensor_scalar(rstd_f[:, c], ss_f[:, c], 1.0 / D, EPS, ALU.mult, ALU.add).then_inc(f_pool.step("ms"), 1)
                pool.wait_ge(f_pool["ms"], f_pool.after(t, "ms"))
                nc.gpsimd.tensor_tensor(rstd_f[:, c], rstd_f[:, c], C("minus_half")[:, 0:1], ALU.pow).then_inc(f_pool.step("rn"), 1)

        def final_dve(dve):
            f_dve.arm(dve)
            f2_dve.arm(dve)
            dve.wait_ge(s_gfin, 16)
            for u in range(NT + 1):
                if u < NT:
                    for k, w in ((0, w1), (1, w2)):
                        dve.wait_ge(s_back[u + NT * k], 16)
                        nc.vector.scalar_tensor_tensor(x[:, u, :], back[u + NT * k], w[:, u:u + 1], x[:, u, :], ALU.mult, ALU.add).then_inc(f_dve.step(f"x{k + 1}"), 1)
                        dve.wait_ge(f_dve[f"x{k + 1}"], f_dve.after(u, f"x{k + 1}"))
                if u >= 1:
                    t = u - 1
                    dve.wait_ge(f_pool["rn"], f_pool.after(t, "rn"))
                    nc.vector.scalar_tensor_tensor(x[:, t, :], x[:, t, :], rstd_f[:, t:t + 1], gfin_row, ALU.mult, ALU.mult).then_inc(f2_dve.step("y"), 1)

        def final_act(act):
            f_act.arm(act)
            for t in range(NT):
                act.wait_ge(f_dve["x2"], f_dve.after(t, "x2"))
                nc.scalar.activation(scr[:, 2, :], x[:, t, :], ACT.Square, accum_out=ss_f[:, t:t + 1]).then_inc(f_act.step("sq"), 1)
                act.wait_ge(f_act["sq"], f_act.after(t, "sq"))

        def final_sync(sp):
            n = rounds(sp)
            sp.wait_ge(e_pe["d1"], e_pe.after(2 * n - 1, "d1"))
            sp.dma_start(gfin_row, a["g_final"].partition_broadcast(P)).then_inc(s_gfin, 16)
            for t in range(NT):
                sp.wait_ge(f2_dve["y"], f2_dve.after(t, "y"))
                dst = a["y_prompt"][0][t * P:(t + 1) * P, :] if t < NTP else a["y_sample"].rearrange("b t d -> (b t) d")
                sp.dma_start(dst, x[:, t, :]).then_inc(s_store, 16)
            sp.wait_ge(s_store, 16 * NT)

        def store(eng, dst, src):
            n_out[0] += 16
            eng.dma_start(dst, src).then_inc(s_out, 16)

        block = ctx.enter_context(nc.Block())

        w_in = a["w_in"][0]

        def cols(i):
            return slice(512 * i, 512 * i + 512)

        def rest_dst(job, b):
            what, ja, jb = job
            if what == "mix" and ja < NTP:
                return [(mix_out[:, ja, 512 * jb:512 * jb + 512], b[:, :], 1.0)]
            if what in ("mix", "co"):
                return [(x[:, ja, 512 * jb:512 * jb + 512], b[:, :], 1.0)]
            if what == "cq":
                n = 512 if jb == 0 else P
                return [(xq[:, ja, 512 * jb:512 * jb + n], b[:, 0:n], 1.0 / 16)]
            return [((mk_tok if what == "mk" else mv)[:, ja, 512 * jb:512 * jb + 512], b[:, :], 1.0)]

        @block.sync
        def _(sp):
            sp.dma_start(const[:, 0:P + 8], a["const"][:, 0:P + 8]).then_inc(s_ident, 16)
            for t in range(NTP):
                sp.dma_start(x[:, t, :], a["x_prompt"][0][t * P:(t + 1) * P, :]).then_inc(s_x[t], 16)
            sp.dma_start(x[:, 4, :], a["x_sample"].rearrange("b t d -> (b t) d")).then_inc(s_x[4], 16)
            for i, n in enumerate(("g_mix", "g_mem", "g_cross", "g_ffn")):
                sp.dma_start(gains[:, i, :], a[n][0].rearrange("(c p) -> p c", p=P), allow_slow_non_contiguous=True).then_inc(s_gain, 16)
            load_weight(sp, "dq", w_in, cols(0))
            load_weight(sp, "dk", w_in, cols(1))
            sp.dma_start(const[:, P + 8:], a["const"][:, P + 8:]).then_inc(s_const, 16)
            sp.dma_start(hist, a["state_gdn_conv"][0].rearrange("b j c -> (b j) c")).then_inc(s_hist, 16)
            prep_sync_load(sp)
            load_weight(sp, "dv", w_in, cols(2))
            for i in range(3):
                load_weight(sp, f"conv{i}", w_in, cols(3 + i))
            load_weight(sp, "gz", w_in, slice(3080, 3592))
            for t in range(NT):
                for what, src, out in (("dk", dk_tok, "new_diff_k"), ("dv", dv, "new_diff_v")):
                    sp.wait_ge(taken(ORDER.index((what, t, 0))), taken_count(ORDER.index((what, t, 0))))
                    dst = (a[out + "_p"][0, 0].rearrange("t h c -> t (h c)")[t * P:(t + 1) * P] if t < NTP
                           else a[out + "_s"][0].rearrange("b t h c -> (b t) (h c)"))
                    store(sp, dst, src[:, t, :])
            streams_sync(sp, UNIT["da0"], a["cache_diff_k"], a["cache_diff_v"], das_pe)
            load_weight(sp, "mix0", a["w_out"][0], cols(0))
            load_weight(sp, "mix1", a["w_out"][0], cols(1))
            sp.wait_ge(das_pe["sc"], das_pe.after(NB - 1, "sc"))
            for h in range(H):
                sp.dma_start(states[:, h, :, :], a["state_gdn"][0].rearrange("b h k v -> h k b v")[h]).then_inc(s_state, 16)
            sp.wait_ge(staged["tile"], staged.after(NTP, "tile"))
            sp.dma_start(mem_rows[:, :, :], a["mem_prompt"][0].rearrange("(t p) d -> p t d", p=P)).then_inc(s_mem, 16)
            sp.wait_ge(gs_act["mix"], gs_act.after(0, "mix"))
            sp.wait_ge(gh_dve["s1"], gh_dve.after(H - 1, "s1"))
            for t in range(NTP):
                sp.dma_start(x[:, t, :], a["x_prompt"][0][t * P:(t + 1) * P, :]).then_inc(s_x[t], 16)
            sp.dma_start(x[:, 4, :], a["x_sample"].rearrange("b t d -> (b t) d")).then_inc(s_x[4], 16)
            load_weight(sp, "mk0", a["w_ck"][0], cols(0))
            store(sp, a["new_gdn_p"][0, 0].rearrange("h k v -> k h v"), h4(state))
            for h in range(H):
                store(sp, a["new_gdn_s"][0].rearrange("b h k v -> h k b v")[h], states[:, h, :, :])
            for i, n in enumerate(("w_ck", "w_cv", "w_cq")):
                for j in range(1 if i == 0 else 0, 2):
                    load_weight(sp, f"{('mk', 'mv', 'cq')[i]}{j}", a[n][0], cols(j))
            sp.dma_start(gffn_row, a["g_ffn"][0].partition_broadcast(P)).then_inc(s_route, 16)
            w_r = a["w_rt"][0].rearrange("(c p) n -> p c n", p=P)
            w_g = a["w_grp"][0].rearrange("(c p) n -> p c n", p=P)
            sp.dma_start(w_route[:, :, 0:4], w_g).then_inc(s_route, 16)
            sp.dma_start(w_route[:, :, 4:36], w_r).then_inc(s_route, 16)
            sp.dma_start(b_route[:, 0:4], a["b_grp"][0].partition_broadcast(P)).then_inc(s_bias, 16)
            sp.dma_start(b_route[:, 4:36], a["b_rt"][0].partition_broadcast(P)).then_inc(s_route, 16)
            sp.wait_ge(s_bias, 16)
            all_taken(sp, LAST_OF["mv"])
            store(sp, a["new_mem_k_p"][0, 0].rearrange("(t p) h c -> p t (h c)", p=P), mk_tok)
            store(sp, a["new_mem_v_p"][0, 0].rearrange("(t p) h c -> p t (h c)", p=P), mv)
            w_co = a["w_co"][0].rearrange("(c p) n -> p c n", p=P)
            for i in range(2):
                sp.dma_start(spare[i].rearrange("p (c n) -> p c n", n=512), w_co[:, 4 * i:4 * i + 4, cols(0)]).then_inc(s_co[0], 16)
            sp.wait_ge(x_dve["o1"], x_dve.after(NTP - 1, "o1"))
            sp.wait_ge(x_pe["pv1"], x_pe.after(NTP - 1, "pv1"))
            sp.wait_ge(s_out, n_out[0])
            sp.dma_start(conv[:, 0:4096].rearrange("p (c n) -> p c n", n=512), w_co[:, :, cols(1)]).then_inc(s_co[1], 16)
            streams_sync(sp, UNIT["x0"], a["cache_mem_k"], a["cache_mem_v"], xs_pe)
            moe_sync(sp)
            final_sync(sp)
            sp.wait_ge(s_out, n_out[0])
            sp.wait_ge(s_tails, 32)

        @block.tensor
        def _(pe):
            pe.wait_ge(s_ident, 16)
            for t in range(NT):
                norm_pe_tile(pe, "mix", t)
            pe.wait_ge(n_dve["mix"][f"ev{NT - 1}b"], n_dve["mix"].after(0, f"ev{NT - 1}b"))
            run_jobs(pe, ("dq", "dk", "dv"), act_a)
            pe.wait_ge(s_small, N_SMALL)
            prep_pe_a(pe)
            prep_pe_b(pe)
            da_pe(pe)
            tails_pe(pe)

            pe.wait_ge(o_act["mix"], o_act.after(NTP - 1, "mix"))
            pe.wait_ge(das_copy["za"], das_copy.after(0, "za"))
            gdn_pe_prompt(pe)
            gdn_pe_sample(pe)
            pe.wait_ge(gs_act["mix"], gs_act.after(0, "mix"))
            run_jobs(pe, ("mix",), act_a, None, [MIX_JOBS[-1] + 1, MIX_JOBS[-1] + 2])
            for t in range(2):
                norm_pe_tile(pe, "mem", t)
            pe.wait_ge(n_dve["mem"]["ev1b"], n_dve["mem"].after(0, "ev1b"))
            for i in range(len(MEM_JOBS)):
                run_jobs(pe, ("mk", "mv"), mem_act, None, MEM_JOBS[i:i + 1])
                if i < NT:
                    norm_pe_tile(pe, "cross", i)
            mem_turn_pe(pe)
            pe.wait_ge(n_dve["cross"][f"ev{NT - 1}b"], n_dve["cross"].after(0, f"ev{NT - 1}b"))
            run_jobs(pe, ("cq",), act_a)
            xp_pe(pe)
            pe.wait_ge(x_act["o0"], x_act.after(NTP - 1, "o0"))
            pe.wait_ge(x_dve["o1"], x_dve.after(NTP - 1, "o1"))
            xs_pe.arm(pe)

            for i, n in enumerate(CO_JOBS):
                def between(job, c):
                    for stage in X_STAGES[c]:
                        xs_pe_stage(pe, i, i % 2, stage)

                run_jobs(pe, ("co",), act_a, between if i < NB else None, [n])
                if i >= NB:
                    for t in range(2 * (i - NB), 2 * (i - NB) + 2):
                        norm_pe_tile(pe, "ffn", t)
            norm_pe_tile(pe, "ffn", NT - 1)
            route_prompt_pe(pe)
            route_pe(pe)
            moe_pe(pe)

        @block.scalar
        def _(act):
            for t in range(NT):
                norm_act_tile(act, "mix", t, x_tile(t), s_x[t], 16)
            take_jobs("act", act, ("dq", "dk", "dv"), project_dst)
            prep_act_a(act)
            act.wait_ge(n_dve["mix"][f"xn{NT - 1}"], n_dve["mix"].after(0, f"xn{NT - 1}"))
            da_act(act)
            prep_act_b(act)
            act.wait_ge(p_dve["tt2"], p_dve.after(0, "tt2"))
            act.dma_start(a["new_conv_p"][0, 0], tails_tok[0:3, :]).then_inc(s_tails, 16)
            act.dma_start(a["new_conv_s"][0].rearrange("b j c -> (b j) c"), tails_tok[3:27, :]).then_inc(s_tails, 16)
            act.wait_ge(s_out, 16 * 2 * NT)
            act.wait_ge(s_tails, 32)
            act.wait_ge(d_pe["pv"], d_pe.after(UN - 1, "pv"))
            act.wait_ge(o_pe["oT"], o_pe.after(NTP - 1, "oT"))
            act.wait_ge(das_copy["za"], das_copy.after(0, "za"))
            act.wait_ge(c_act["gz"], c_act.after(0, "gz"))
            gdn_act(act)
            for t in range(2):
                norm_act_tile(act, "mem", t, mem_rows[:, t, :], s_mem, 16)

            def x_sum(what, t):
                return ORDER.index((what, t, 1))

            for t in range(NTP):
                norm_act_tile(act, "cross", t, x_tile(t), x_add[f"t{t}"], x_add.after(0, f"t{t}"))
            n = x_sum("mix", NTP)
            norm_act_tile(act, "cross", NTP, x_tile(NTP), taken(n), taken_count(n))
            take_jobs("act", act, ("mk", "mv"), rest_dst)
            take_jobs("act", act, ("cq",), rest_dst)
            xp_act(act)
            xs_act.arm(act)
            for b in range(NB):
                for stage in range(STAGES):
                    xs_act_stage(act, b, stage)
                if b >= 5:
                    n = x_sum("co", b - 5)
                    norm_act_tile(act, "ffn", b - 5, x_tile(b - 5), taken(n), taken_count(n))
            for t in (3, 4):
                n = x_sum("co", t)
                norm_act_tile(act, "ffn", t, x_tile(t), taken(n), taken_count(n))
            route_act(act)
            moe_act(act)
            final_act(act)

        @block.vector
        def _(dve):
            dve.wait_ge(s_gain, 64)
            norm_dve(dve, "mix", x_tile, gains[:, 0, :], act_a)
            take_jobs("dve", dve, ("dq", "dk", "dv"), project_dst)
            prep_dve_a(dve)
            turn_k_dve(dve)
            da_dve(dve)
            das_start(dve)
            prep_dve_b(dve)
            dve.wait_ge(d_pe["pv"], d_pe.after(UN - 1, "pv"))
            dve.wait_ge(o_pe["oT"], o_pe.after(NTP - 1, "oT"))
            dve.wait_ge(s_out, 16 * 2 * NT)
            dve.wait_ge(s_tails, 32)
            dve.wait_ge(c_act["gz"], c_act.after(0, "gz"))
            gdn_dve(dve)
            for t in range(2):
                norm_dve_rows(dve, "mem", t, mem_rows[:, t, :])
            mix_out_dve(dve)
            dve.wait_ge(s_x[NTP], 32)
            take_jobs("dve", dve, ("mix",), rest_dst)
            for t in range(2):
                norm_dve_out(dve, "mem", t, gains[:, 1, :], mem_act)
            norm_dve_rows(dve, "cross", 0, x_tile(0))
            for i in range(len(MEM_JOBS)):
                if i + 1 < NT:
                    norm_dve_rows(dve, "cross", i + 1, x_tile(i + 1))
                take_jobs("dve", dve, ("mk", "mv"), rest_dst, None, MEM_JOBS[i:i + 1])
                if i < NT:
                    norm_dve_out(dve, "cross", i, gains[:, 2, :], act_a)
            mem_turn_dve(dve)
            take_jobs("dve", dve, ("cq",), rest_dst)
            xp_dve(dve)
            xs_dve.arm(dve)
            xs_zero.arm(dve)
            nc.vector.memset(c_q, 0.0).then_inc(xs_zero.step("q"), 1)
            dve.wait_ge(xs_zero["q"], xs_zero.after(0, "q"))

            for i, n in enumerate(CO_JOBS):
                if i < NB:
                    for stage in range(STAGES):
                        xs_dve_stage(dve, i, stage)
                take_jobs("dve", dve, ("co",), rest_dst, None, [n])
                if i == NB - 1:
                    for t in range(2):
                        norm_dve_rows(dve, "ffn", t, x_tile(t))
                if i >= NB:
                    for t in range(2 * (i - NB), 2 * (i - NB) + 2):
                        norm_dve_out(dve, "ffn", t, gains[:, 3, :], act_a)
                        if t + 2 < NT:
                            norm_dve_rows(dve, "ffn", t + 2, x_tile(t + 2))
            norm_dve_out(dve, "ffn", NT - 1, gains[:, 3, :], act_a)
            route_dve(dve)
            moe_dve(dve)
            final_dve(dve)

        @block.gpsimd
        def _(pool):
            prep_pool_a(pool)
            pool.wait_ge(s_ident, 16)
            for t in range(NT):
                norm_pool_tile(pool, "mix", t)
            da_pool(pool)
            gdn_pool(pool)
            for k in ("mem", "cross"):
                for t in range(NORMS[k]):
                    norm_pool_tile(pool, k, t)
            ffn_rows_pool(pool)
            moe_pool(pool)
            final_pool(pool)


SCRATCH = {"h_rows": ((NT * P, D), F32), "pair_rows": ((NPAIR + 2 * CAP, D), F32)}

OUTPUTS = [
    ("y_prompt", (1, SEQ, D)), ("y_sample", (NB, TB, D)),
    ("new_diff_k_p", (1, 1, SEQ, H, 128)), ("new_diff_v_p", (1, 1, SEQ, H, 128)),
    ("new_conv_p", (1, 1, CONV - 1, 1536)), ("new_gdn_p", (1, 1, H, 128, 128)),
    ("new_mem_k_p", (1, 1, MEM, H, 256)), ("new_mem_v_p", (1, 1, MEM, H, 256)),
    ("new_diff_k_s", (1, NB, TB, H, 128)), ("new_diff_v_s", (1, NB, TB, H, 128)),
    ("new_conv_s", (1, NB, CONV - 1, 1536)), ("new_gdn_s", (1, NB, H, 128, 128)),
]


def kernel(**inputs):
    import numpy as _np
    import concourse.bacc as _bacc
    from concourse import mybir as _mybir
    from concourse.bass_utils import run_bass_kernel_spmd as _run

    nc = _bacc.Bacc("TRN2", target_bir_lowering=False, num_devices=1)
    arrays = {name: _np.ascontiguousarray(value) for name, value in inputs.items()}
    arrays["const"] = _np.concatenate([CONST[k] for k in CONST_AT], axis=1)
    aps = {}
    for name, value in arrays.items():
        aps[name] = nc.dram_tensor(name, value.shape, _mybir.dt.from_np(value.dtype), kind="ExternalInput").ap()
    for name, shape in OUTPUTS:
        aps[name] = nc.dram_tensor(name, shape, F32, kind="ExternalOutput").ap()
    for name, (shape, dt) in SCRATCH.items():
        aps[name] = nc.dram_tensor(name, shape, dt, kind="Internal").ap()
    build_encoder_step(nc, aps)
    r = _run(nc, [arrays], core_ids=[0])
    return tuple(r.results[0][name] for name, _ in OUTPUTS)
```
